# Optimizing a Trainium2 kernel written in Bass

```python
import math
import jax, jax.numpy as jnp
from jax import lax
import numpy as np

D_MODEL = 1024
BATCH = 1
SEQ = 1024
DEPTH = 2
DEC_BATCH = 8
DEC_SEQ = 8
PAST_LEN = 8192
PAGE_SIZE = 128

EPS = 1e-6
A_HEADS = 4
A_DK = 128
A_DV = 128
A_CONV = 4
A_CHUNK = 64
B_HEADS = 8
B_N = 64
B_LORA_W = 64
B_LORA_A = 64
B_GN_EPS = 64e-5
B_DECAY_SCALE = math.exp(-0.5)
C_HEADS = 8
C_DQK = 64
C_DV = 128
C_CHUNK = 64
C_GATE_CAP = 15.0

A_KEY = A_HEADS * A_DK
A_VAL = A_HEADS * A_DV
A_QKV = 2 * A_KEY + A_VAL
B_W = B_HEADS * B_N
C_QK = C_HEADS * C_DQK
C_V = C_HEADS * C_DV
A_COLS = A_QKV + A_VAL + 2 * A_HEADS
B_COLS = 4 * B_W + B_LORA_W + B_LORA_A
P0 = A_COLS + B_COLS
MIX0 = A_VAL + B_W
P1 = 2 * C_QK + 3 * C_V + 2 * C_HEADS
MIX1 = C_V

kernel_name = 'hybrid_gdn_rwkv7_mlstm_decode_step'

def rms_norm(x, w):
    xf = x.astype(jnp.float32)
    y = xf * lax.rsqrt(jnp.mean(xf * xf, axis=-1, keepdims=True) + EPS)
    return (y * w.astype(jnp.float32)).astype(x.dtype)

def l2_normalize(x):
    xf = x.astype(jnp.float32)
    return xf * lax.rsqrt(jnp.sum(xf * xf, axis=-1, keepdims=True) + EPS)

def soft_cap(t):
    return C_GATE_CAP * jnp.tanh(t / C_GATE_CAP)

def _to_blocks(t, c):
    bsz, L = t.shape[0], t.shape[1]
    t = t.astype(jnp.float32).reshape((bsz, L // c, c) + t.shape[2:])
    return jnp.moveaxis(t, 3, 1)

def _from_blocks(o):
    n, bsz, h, c, d = o.shape
    return jnp.transpose(o, (1, 0, 3, 2, 4)).reshape(bsz, n * c, h, d)

def causal_conv_silu(u, buf, w):
    K = w.shape[0]
    L = u.shape[1]
    ext = jnp.concatenate([buf.astype(u.dtype), u], axis=1)
    y = sum(ext[:, j:j + L] * w[j] for j in range(K))
    return jax.nn.silu(y.astype(jnp.float32)), ext[:, L:]

def gated_delta_chunked(q, k, v, beta, logd, s0):
    L = q.shape[1]
    c = math.gcd(L, A_CHUNK)
    qc, kc, vc = _to_blocks(q, c), _to_blocks(k, c), _to_blocks(v, c)
    bc = _to_blocks(beta, c)
    g = jnp.cumsum(_to_blocks(logd, c), axis=-1)
    idx = jnp.arange(c)
    causal = idx[:, None] >= idx[None, :]
    strict = idx[:, None] > idx[None, :]
    decay = jnp.exp(jnp.where(causal, g[..., :, None] - g[..., None, :], -jnp.inf))
    amat = jnp.where(strict, bc[..., :, None] * decay * jnp.einsum('bhntd,bhnsd->bhnts', kc, kc), 0.0)
    rhs = jnp.concatenate([bc[..., None] * vc, (bc * jnp.exp(g))[..., None] * kc], axis=-1)
    sol = lax.linalg.triangular_solve(amat + jnp.eye(c, dtype=jnp.float32), rhs,
                                      left_side=True, lower=True, unit_diagonal=True)
    dv = v.shape[-1]
    u_blk, w_blk = sol[..., :dv], sol[..., dv:]
    attn = decay * jnp.einsum('bhntd,bhnsd->bhnts', qc, kc)
    qg = qc * jnp.exp(g)[..., None]
    kd = kc * jnp.exp(g[..., -1:] - g)[..., None]
    g_end = jnp.exp(g[..., -1])

    def step(s, blk):
        u_, w_, attn_, qg_, kd_, ge_ = blk
        nv = u_ - jnp.einsum('bhtk,bhkv->bhtv', w_, s)
        o = jnp.einsum('bhtk,bhkv->bhtv', qg_, s) + jnp.einsum('bhts,bhsv->bhtv', attn_, nv)
        s = ge_[..., None, None] * s + jnp.einsum('bhsk,bhsv->bhkv', kd_, nv)
        return s, o

    xs = tuple(jnp.moveaxis(t, 2, 0) for t in (u_blk, w_blk, attn, qg, kd, g_end))
    s, o = lax.scan(step, s0.astype(jnp.float32), xs)
    return _from_blocks(o), s

def rwkv7_scan(r, w, k, v, a, b, s0):
    def step(s, inp):
        r_, w_, k_, v_, a_, b_ = inp
        sa = jnp.einsum('bhvk,bhk->bhv', s, a_)
        s = s * w_[:, :, None, :] + sa[..., None] * b_[:, :, None, :] + v_[..., None] * k_[:, :, None, :]
        return s, jnp.einsum('bhvk,bhk->bhv', s, r_)

    xs = tuple(jnp.moveaxis(t.astype(jnp.float32), 1, 0) for t in (r, w, k, v, a, b))
    s, o = lax.scan(step, s0.astype(jnp.float32), xs)
    return jnp.moveaxis(o, 0, 1), s

def mlstm_chunked(q, k, v, logi, logf, c0, n0, m0):
    L = q.shape[1]
    c = math.gcd(L, C_CHUNK)
    qc, kc, vc = _to_blocks(q, c), _to_blocks(k, c), _to_blocks(v, c)
    ic = _to_blocks(logi, c)
    bcum = jnp.cumsum(_to_blocks(logf, c), axis=-1)
    idx = jnp.arange(c)
    causal = idx[:, None] >= idx[None, :]
    dmat = jnp.where(causal, bcum[..., :, None] - bcum[..., None, :] + ic[..., None, :], -jnp.inf)
    dmax = jnp.max(dmat, axis=-1)
    qk = jnp.einsum('bhntd,bhnsd->bhnts', qc, kc)

    def step(carry, blk):
        cm, nm, m = carry
        q_, k_, v_, b_, i_, d_, dmax_, qk_ = blk
        inter = b_ + m[..., None]
        mt = jnp.maximum(inter, dmax_)
        pm = jnp.exp(d_ - mt[..., None]) * qk_
        e_inter = jnp.exp(inter - mt)
        num = e_inter[..., None] * jnp.einsum('bhtk,bhkv->bhtv', q_, cm) + jnp.einsum('bhts,bhsv->bhtv', pm, v_)
        den = e_inter * jnp.einsum('bhtk,bhk->bht', q_, nm) + jnp.sum(pm, axis=-1)
        h = num / jnp.maximum(jnp.abs(den), jnp.exp(-mt))[..., None]
        m_new = mt[..., -1]
        w_s = jnp.exp(b_[..., -1:] - b_ + i_ - m_new[..., None])
        e_c = jnp.exp(b_[..., -1] + m - m_new)
        cm = e_c[..., None, None] * cm + jnp.einsum('bhs,bhsk,bhsv->bhkv', w_s, k_, v_)
        nm = e_c[..., None] * nm + jnp.einsum('bhs,bhsk->bhk', w_s, k_)
        return (cm, nm, m_new), h

    xs = tuple(jnp.moveaxis(t, 2, 0) for t in (qc, kc, vc, bcum, ic, dmat, dmax, qk))
    init = (c0.astype(jnp.float32), n0.astype(jnp.float32), m0.astype(jnp.float32))
    (cm, nm, m), h = lax.scan(step, init, xs)
    return _from_blocks(h), cm, nm, m

def mixer_ab_layer(x, conv_buf, s_gdn, x_prev, s_rwkv, p):
    f32 = jnp.float32
    bsz, L, _ = x.shape
    xn = rms_norm(x, p['norm0_w'])
    proj = xn @ p['w_in0']
    pa, pb = proj[..., :A_COLS], proj[..., A_COLS:]
    qkv, conv_new = causal_conv_silu(pa[..., :A_QKV], conv_buf, p['gdn_conv_w'])
    q = l2_normalize(qkv[..., :A_KEY].reshape(bsz, L, A_HEADS, A_DK)) * (A_DK ** -0.5)
    k = l2_normalize(qkv[..., A_KEY:2 * A_KEY].reshape(bsz, L, A_HEADS, A_DK))
    v = qkv[..., 2 * A_KEY:].reshape(bsz, L, A_HEADS, A_DV)
    z_a = pa[..., A_QKV:A_QKV + A_VAL].astype(f32)
    beta = jax.nn.sigmoid(pa[..., A_QKV + A_VAL:A_QKV + A_VAL + A_HEADS].astype(f32))
    logd = -jnp.exp(p['gdn_a_log'].astype(f32)) * jax.nn.softplus(
        pa[..., A_QKV + A_VAL + A_HEADS:].astype(f32) + p['gdn_dt_bias'].astype(f32))
    o_a, s_gdn_new = gated_delta_chunked(q, k, v, beta, logd, s_gdn)
    o_a = rms_norm(o_a, p['gdn_norm_w']).reshape(bsz, L, A_VAL) * jax.nn.silu(z_a)
    prev_row = (x_prev.astype(xn.dtype) @ p['w_in0'][:, A_COLS:])[:, None]
    pb_prev = jnp.concatenate([prev_row, pb[:, :-1]], axis=1)
    pb = (pb + (pb_prev - pb) * p['rwkv_mu']).astype(f32)
    r, kb, vb, gb = (pb[..., i * B_W:(i + 1) * B_W] for i in range(4))
    w_lo = pb[..., 4 * B_W:4 * B_W + B_LORA_W]
    a_lo = pb[..., 4 * B_W + B_LORA_W:]
    logw = -B_DECAY_SCALE * jax.nn.sigmoid(p['rwkv_w0'] + jnp.tanh(w_lo) @ p['rwkv_w2'])
    a = jax.nn.sigmoid(p['rwkv_a0'] + a_lo @ p['rwkv_a2'])
    heads = lambda t: t.reshape(bsz, L, B_HEADS, B_N)
    kk = l2_normalize(heads(kb * p['rwkv_k_k']))
    kb = kb * (1.0 + (a - 1.0) * p['rwkv_k_a'])
    rh, kh, vh = heads(r), heads(kb), heads(vb)
    o_b, s_rwkv_new = rwkv7_scan(rh, heads(jnp.exp(logw)), kh, vh, -kk, kk * heads(a), s_rwkv)
    gmean = jnp.mean(o_b, axis=-1, keepdims=True)
    gvar = jnp.mean(jnp.square(o_b - gmean), axis=-1, keepdims=True)
    o_b = ((o_b - gmean) * lax.rsqrt(gvar + B_GN_EPS)).reshape(bsz, L, B_W)
    bonus = (jnp.sum(rh * kh * p['rwkv_r_k'], axis=-1, keepdims=True) * vh).reshape(bsz, L, B_W)
    o_b = (o_b * p['rwkv_ln_w'] + p['rwkv_ln_b'] + bonus) * jax.nn.silu(gb)
    y = jnp.concatenate([o_a, o_b], axis=-1).astype(x.dtype) @ p['w_out0']
    return x + y, conv_new, s_gdn_new, xn[:, -1], s_rwkv_new

def mlstm_layer(x, c0, n0, m0, p):
    bsz, L, _ = x.shape
    xn = rms_norm(x, p['norm1_w'])
    proj = (xn @ p['w_in1']).astype(jnp.float32)
    q = proj[..., :C_QK].reshape(bsz, L, C_HEADS, C_DQK) * (C_DQK ** -0.5)
    k = proj[..., C_QK:2 * C_QK].reshape(bsz, L, C_HEADS, C_DQK)
    off = 2 * C_QK
    v = proj[..., off:off + C_V].reshape(bsz, L, C_HEADS, C_DV)
    o_gate = proj[..., off + C_V:off + 2 * C_V]
    z = proj[..., off + 2 * C_V:off + 3 * C_V]
    gi = proj[..., off + 3 * C_V:off + 3 * C_V + C_HEADS] + p['mlstm_b_i']
    gf = proj[..., off + 3 * C_V + C_HEADS:] + p['mlstm_b_f']
    logi = soft_cap(gi)
    logf = jax.nn.log_sigmoid(soft_cap(gf))
    h, cm, nm, m = mlstm_chunked(q, k, v, logi, logf, c0, n0, m0)
    h = h.reshape(bsz, L, C_V) * jax.nn.sigmoid(o_gate) * jax.nn.silu(z)
    return x + h.astype(x.dtype) @ p['w_out1'], cm, nm, m

def trunk(x, state, p):
    conv_buf, s_gdn, x_prev, s_rwkv, c0, n0, m0 = state
    for layer in range(DEPTH):
        if layer % 2 == 0:
            x, conv_buf, s_gdn, x_prev, s_rwkv = mixer_ab_layer(x, conv_buf, s_gdn, x_prev, s_rwkv, p)
        else:
            x, c0, n0, m0 = mlstm_layer(x, c0, n0, m0, p)
    return rms_norm(x, p['norm_f_w']), (conv_buf, s_gdn, x_prev, s_rwkv, c0, n0, m0)

def setup_inputs(seed: int = 0) -> dict:
    key = jax.random.key(seed)
    ks = jax.random.split(key, 32)
    f32 = jnp.float32
    nrm = lambda i, shape, scale: scale * jax.random.normal(ks[i], shape, f32)
    dt = jnp.exp(jax.random.uniform(ks[14], (A_HEADS,), f32, math.log(1e-3), math.log(1e-1)))
    return {
        'x_prompt': nrm(0, (BATCH, SEQ, D_MODEL), 1.0),
        'x_sample': nrm(1, (DEC_BATCH, DEC_SEQ, D_MODEL), 1.0),
        'state_gdn_conv': nrm(2, (DEC_BATCH, A_CONV - 1, A_QKV), 1.0),
        'state_gdn': nrm(3, (DEC_BATCH, A_HEADS, A_DK, A_DV), 0.5),
        'state_rwkv_shift': nrm(4, (DEC_BATCH, D_MODEL), 1.0),
        'state_rwkv': nrm(5, (DEC_BATCH, B_HEADS, B_N, B_N), 0.3),
        'state_mlstm_c': nrm(6, (DEC_BATCH, C_HEADS, C_DQK, C_DV), 0.3),
        'state_mlstm_n': nrm(7, (DEC_BATCH, C_HEADS, C_DQK), 0.3),
        'state_mlstm_m': nrm(8, (DEC_BATCH, C_HEADS), 0.5),
        'norm0_w': 1.0 + nrm(9, (D_MODEL,), 0.02),
        'w_in0': nrm(10, (D_MODEL, P0), D_MODEL ** -0.5),
        'w_out0': nrm(11, (MIX0, D_MODEL), MIX0 ** -0.5),
        'gdn_conv_w': nrm(12, (A_CONV, A_QKV), A_CONV ** -0.5),
        'gdn_a_log': jnp.log(jax.random.uniform(ks[13], (A_HEADS,), f32, 1.0, 16.0)),
        'gdn_dt_bias': dt + jnp.log(-jnp.expm1(-dt)),
        'gdn_norm_w': 1.0 + nrm(15, (A_DV,), 0.02),
        'rwkv_mu': jax.random.uniform(ks[16], (B_COLS,), f32, 0.0, 1.0),
        'rwkv_w0': nrm(17, (B_W,), 0.5),
        'rwkv_w2': nrm(18, (B_LORA_W, B_W), 0.5 * B_LORA_W ** -0.5),
        'rwkv_a0': nrm(19, (B_W,), 0.1),
        'rwkv_a2': nrm(20, (B_LORA_A, B_W), 0.5 * B_LORA_A ** -0.5),
        'rwkv_k_k': 0.85 + nrm(21, (B_W,), 0.05),
        'rwkv_k_a': 1.0 + nrm(22, (B_W,), 0.05),
        'rwkv_r_k': nrm(23, (B_HEADS, B_N), 0.1),
        'rwkv_ln_w': 1.0 + nrm(24, (B_W,), 0.02),
        'rwkv_ln_b': nrm(25, (B_W,), 0.01),
        'norm1_w': 1.0 + nrm(26, (D_MODEL,), 0.02),
        'w_in1': nrm(27, (D_MODEL, P1), D_MODEL ** -0.5),
        'w_out1': nrm(28, (MIX1, D_MODEL), MIX1 ** -0.5),
        'mlstm_b_i': nrm(29, (C_HEADS,), 0.1),
        'mlstm_b_f': jnp.linspace(3.0, 6.0, C_HEADS, dtype=f32) + nrm(30, (C_HEADS,), 0.1),
        'norm_f_w': 1.0 + nrm(31, (D_MODEL,), 0.02),
    }

def reference(x_prompt, x_sample, state_gdn_conv, state_gdn, state_rwkv_shift, state_rwkv,
              state_mlstm_c, state_mlstm_n, state_mlstm_m,
              norm0_w, w_in0, w_out0, gdn_conv_w, gdn_a_log, gdn_dt_bias, gdn_norm_w,
              rwkv_mu, rwkv_w0, rwkv_w2, rwkv_a0, rwkv_a2, rwkv_k_k, rwkv_k_a, rwkv_r_k,
              rwkv_ln_w, rwkv_ln_b, norm1_w, w_in1, w_out1, mlstm_b_i, mlstm_b_f, norm_f_w):
    p = {
        'norm0_w': norm0_w, 'w_in0': w_in0, 'w_out0': w_out0, 'gdn_conv_w': gdn_conv_w,
        'gdn_a_log': gdn_a_log, 'gdn_dt_bias': gdn_dt_bias, 'gdn_norm_w': gdn_norm_w,
        'rwkv_mu': rwkv_mu, 'rwkv_w0': rwkv_w0, 'rwkv_w2': rwkv_w2, 'rwkv_a0': rwkv_a0,
        'rwkv_a2': rwkv_a2, 'rwkv_k_k': rwkv_k_k, 'rwkv_k_a': rwkv_k_a, 'rwkv_r_k': rwkv_r_k,
        'rwkv_ln_w': rwkv_ln_w, 'rwkv_ln_b': rwkv_ln_b, 'norm1_w': norm1_w, 'w_in1': w_in1,
        'w_out1': w_out1, 'mlstm_b_i': mlstm_b_i, 'mlstm_b_f': mlstm_b_f, 'norm_f_w': norm_f_w,
    }
    f32 = jnp.float32
    bsz = x_prompt.shape[0]
    prompt_state = (
        jnp.zeros((bsz, A_CONV - 1, A_QKV), x_prompt.dtype),
        jnp.zeros((bsz, A_HEADS, A_DK, A_DV), f32),
        jnp.zeros((bsz, D_MODEL), x_prompt.dtype),
        jnp.zeros((bsz, B_HEADS, B_N, B_N), f32),
        jnp.zeros((bsz, C_HEADS, C_DQK, C_DV), f32),
        jnp.zeros((bsz, C_HEADS, C_DQK), f32),
        jnp.zeros((bsz, C_HEADS), f32),
    )
    y_prompt, (p_conv, p_gdn, p_shift, p_rwkv, p_c, p_n, p_m) = trunk(x_prompt, prompt_state, p)
    sample_state = (state_gdn_conv, state_gdn, state_rwkv_shift, state_rwkv,
                    state_mlstm_c, state_mlstm_n, state_mlstm_m)
    y_sample, (s_conv, s_gdn, s_shift, s_rwkv, s_c, s_n, s_m) = trunk(x_sample, sample_state, p)
    return (y_prompt, y_sample, p_conv, p_gdn, p_shift, p_rwkv, p_c, p_n, p_m,
            s_conv, s_gdn, s_shift, s_rwkv, s_c, s_n, s_m)


_drawn_inputs = setup_inputs


def setup_inputs(seed=0):
    import zlib

    import numpy as np

    out = dict(_drawn_inputs(seed))
    spreads = {}
    factors = {}
    for name, (base, spread) in spreads.items():
        noise = np.random.default_rng([zlib.crc32(name.encode()), seed]).standard_normal(out[name].shape)
        drawn = base * np.exp(spread * noise) if base else spread * noise
        out[name] = __import__('jax').numpy.asarray(drawn.astype(out[name].dtype))
    for name, factor in factors.items():
        out[name] = (out[name] * factor).astype(out[name].dtype)
    return out
```

```python
import math
from contextlib import ExitStack

import concourse.bass as bass
from concourse import mybir

F32 = mybir.dt.float32
ALU = mybir.AluOpType
ACT = mybir.ActivationFunctionType
AX_X = mybir.AxisListType.X

P = 128
D = 1024
KT = D // P
SEQ = 1024
TILES = SEQ // P
DB, DS = 8, 8
SR = DB * DS
TOK = SEQ + SR
XC = TOK + DB
XW = (TILES + 1) * P
EPS = 1e-6
AH, AKEY = 4, 512
AQKV = 3 * AKEY
AZ = AQKV
AGATE = AQKV + AKEY
ACOLS = AGATE + 2 * AH
BW, BH = 512, 8
NP = BW // P
B_GN_EPS = 64e-5
DECAY = math.exp(-0.5)
CH, CQK, CV = 8, 64, 128
CAP = 15.0
NEG = -30000.0
CONV = 4
GROUPS = ((0, 512), (512, 512), (SEQ, SR))


def alone(eng, K):
    eng.sem_inc(K.idle[eng.engine.name], 1)


class Events:

    def __init__(self, nc, ctx, prefix):
        self.nc, self.prefix, self.sems = nc, prefix, {}
        ctx.callback(self.close)

    def __call__(self, name):
        if name not in self.sems:
            self.sems[name] = self.nc.alloc_semaphore(self.prefix + name)
        return self.sems[name]

    def close(self):
        self.nc.clear_and_free_semaphores(list(self.sems.values()))
        self.nc.all_engine_barrier()


class Seq:

    def __init__(self, sem, eng, per):
        self.sem, self.eng, self.per, self.n, self.base = sem, eng, per, 0, 0

    def start(self, i):
        self.base, self.n = i * self.per, 0

    def __call__(self, ins):
        self.n += 1
        ins.then_inc(self.sem, 1)
        self.eng.wait_ge(self.sem, self.base + self.n)

    def end(self):
        assert self.n == self.per


def as_row(v):
    n = v.shape[0]
    return v.rearrange("(a n) -> a n", a=1).broadcast_to([P, n])


def phase_norm(nc, K, x_prompt, x_sample, shift, norm_w, p_shift, s_shift):
    with ExitStack() as ctx:
        sb = lambda n, s: ctx.enter_context(nc.sbuf_tensor(n, s, F32))
        ev = Events(nc, ctx, "n_")
        x = sb("n_x", [P, 2, D])
        xn = sb("n_xn", [P, 2, D])
        sq = sb("n_sq", [P, D])
        st = sb("n_st", [P, 2, 4])
        wb = sb("n_wb", [P, D])
        pt = [ctx.enter_context(nc.psum_tensor(f"n_pt{i}", [P, 4, P], F32)) for i in range(4)]
        x_in0, x_in1, w_in, ssq, mean, rstd, norm, turned, turned2, kept, kept2, shifts, consts, tmp, prev_rows = [ev(n) for n in (
            "x_in0", "x_in1", "w_in", "ssq", "mean", "rstd", "norm", "turned", "turned2", "kept", "kept2", "shifts", "consts", "tmp", "prev_rows")]

        x_in = (x_in0, x_in1)

        with nc.Block() as block:
            @block.sync
            def _(sp):
                sp.dma_start(wb[:, :], as_row(norm_w)).then_inc(w_in, 16)
                for b in range(2):
                    sp.dma_start(x[:, b, :], x_prompt[0, b * P:(b + 1) * P, :]).then_inc(x_in[b], 16)
                with sp.Fori(0, TILES // 2 - 1) as g:
                    for b in range(2):
                        sp.wait_ge(norm, 2 * g + b + 1)
                        sp.dma_start(x[:, b, :], x_prompt[0, bass.ds((2 * g + b + 2) * P, P), :]).then_inc(x_in[b], 16)
                sp.wait_ge(norm, TILES - 1)
                sp.dma_start(x[0:SR, 0, :], x_sample.rearrange("b t d -> (b t) d")).then_inc(x_in[0], 16)
                sp.dma_start(x[SR:SR + DB, 0, :], shift).then_inc(x_in[0], 16)
                sp.wait_ge(norm, TILES)
                sp.dma_start(p_shift, xn[P - 1:P, 1, :]).then_inc(shifts, 16)
                sp.wait_ge(norm, TILES + 1)
                for b in range(DB):
                    r = b * DS + DS - 1
                    sp.dma_start(s_shift[b:b + 1, :], xn[r:r + 1, 0, :]).then_inc(shifts, 16)
                sp.wait_ge(shifts, 16 * (DB + 1))

            @block.gpsimd
            def _(pool):
                done = Seq(tmp, pool, 33)
                done.start(0)
                done(pool.memset(K.ident[:, :], 0.0))
                done(pool.affine_select(out=K.ident[:, :], in_=K.ident[:, :], compare_op=ALU.not_equal, fill=1.0,
                                        base=0, pattern=[[-1, P]], channel_multiplier=1))
                pool.sem_inc(consts, 1)
                done(pool.memset(K.half_neg[:, :], -0.5))
                done(pool.memset(K.ones[:, :], 1.0))
                done(pool.memset(K.pair_ones[:, :], 0.0))
                done(pool.memset(K.pair_ones[0:64, 0:64], 1.0))
                done(pool.memset(K.pair_ones[64:128, 64:128], 1.0))
                for out, cmp in ((K.causal, ALU.is_ge), (K.strict, ALU.is_gt)):
                    done(pool.affine_select(out=out[:, :], in_=K.ones[:, :], compare_op=cmp, fill=0.0,
                                            base=0, pattern=[[1, P]], channel_multiplier=-1))
                v = K.same[0:SR, 0:SR].rearrange("s (b t) -> s b t", b=DB)
                done(pool.affine_select(out=v, in_=K.ones[0:SR, 0:SR].rearrange("s (b t) -> s b t", b=DB),
                                        compare_op=ALU.is_ge, fill=0.0, base=0, pattern=[[-DS, DB], [0, DS]],
                                        channel_multiplier=1))
                done(pool.affine_select(out=v, in_=v, compare_op=ALU.is_ge, fill=0.0, base=DS - 1,
                                        pattern=[[DS, DB], [0, DS]], channel_multiplier=-1))
                for out, m in ((K.causal_s, K.causal), (K.strict_s, K.strict)):
                    done(pool.tensor_tensor(out[:, :], K.same[0:SR, 0:SR], m[0:SR, 0:SR], ALU.mult))
                done(pool.memset(K.last[:, :], 0.0))
                done(pool.tensor_copy(K.last[:, DS - 1:SR:DS], K.same[0:SR, DS - 1:SR:DS]))
                done(pool.memset(K.restart[:, :], 1.0))
                done(pool.memset(K.restart[:, 0:SEQ:P], 0.0))
                done(pool.memset(K.restart[:, SEQ:TOK:DS], 0.0))
                done(pool.memset(K.batch_cols[:, :, :], 0.0))
                for b in range(DB):
                    done(pool.memset(K.batch_cols[:, b, b * DS:(b + 1) * DS], 1.0))
                done(pool.memset(K.head_cols[:, :], 0.0))
                done(pool.memset(K.head_cols[0:64, 0:1], 1.0))
                done(pool.memset(K.head_cols[64:128, 1:2], 1.0))
                done(pool.tensor_scalar(K.lcausal[:, :], K.causal[:, :], -NEG, NEG, ALU.mult, ALU.add))
                done(pool.tensor_scalar(K.lcausal_s[:, :], K.causal_s[:, :], -NEG, NEG, ALU.mult, ALU.add))
                done(pool.memset(K.xnT[:, :, XC:XW], 0.0))
                done.end()

                def one(i, n, k):
                    pool.wait_ge(mean, n)
                    pool.tensor_tensor(st[:, k, 2:3], st[:, k, 1:2], K.half_neg[:, 0:1], ALU.pow).then_inc(rstd, 1)
                with pool.Fori(0, TILES // 2) as g:
                    for b in range(2):
                        one(g, 2 * g + b + 1, b)
                pool.wait_ge(mean, TILES + 1)
                pool.tensor_tensor(st[0:SR, 0, 2:3], st[0:SR, 0, 1:2], K.half_neg[0:SR, 0:1], ALU.pow).then_inc(rstd, 1)

            @block.scalar
            def _(act):
                def one(n, k, r):
                    act.wait_ge(mean, n)
                    act.activation(sq[0:r, :], x[0:r, k, :], ACT.Square, accum_out=st[0:r, k, 0:1]).then_inc(ssq, 1)

                def keep(n, k, cols, r):
                    act.wait_ge(turned2, n + 1)
                    act.activation(K.xnT[:, 4:8, cols], pt[2 * k + 1][:, :, 0:r], ACT.Copy).then_inc(kept2, 1)
                with act.Fori(0, TILES // 2) as g:
                    for b in range(2):
                        act.wait_ge(x_in[b], 16 * (g + 1))
                        one(2 * g + b, b, P)
                        keep(2 * g + b, b, bass.ds((2 * g + b) * P, P), P)
                act.wait_ge(x_in[0], 16 * (TILES // 2 + 2))
                one(TILES, 0, SR)
                keep(TILES, 0, slice(SEQ, XC), SR + DB)

            @block.vector
            def _(dve):
                dve.wait_ge(w_in, 16)

                def one(n, k, r, cols):
                    m = SR if r != P else P
                    dve.wait_ge(ssq, n + 1)
                    dve.wait_ge(rstd, n)
                    dve.tensor_scalar(st[0:m, k, 1:2], st[0:m, k, 0:1], 1.0 / D, EPS, ALU.mult, ALU.add).then_inc(mean, 1)
                    if r != P:
                        dve.wait_ge(kept2, n)
                        dve.tensor_copy(xn[SR:SR + DB, k, :], x[SR:SR + DB, k, :]).then_inc(prev_rows, 1)
                    dve.wait_ge(rstd, n + 1)
                    dve.wait_ge(turned2, n)
                    dve.scalar_tensor_tensor(out=xn[0:m, k, :], in0=x[0:m, k, :], scalar=st[0:m, k, 2:3],
                                             in1=wb[0:m, :], op0=ALU.mult, op1=ALU.mult).then_inc(norm, 1)
                    dve.wait_ge(turned, n + 1)
                    dve.tensor_copy(K.xnT[:, 0:4, cols], pt[2 * k][:, :, 0:r]).then_inc(kept, 1)
                with dve.Fori(0, TILES // 2) as g:
                    for b in range(2):
                        one(2 * g + b, b, P, bass.ds((2 * g + b) * P, P))
                one(TILES, 0, SR + DB, slice(SEQ, XC))

            @block.tensor
            def _(pe):
                pe.wait_ge(consts, 1)

                def one(n, k, r, first):
                    pe.wait_ge(norm, n + 1)
                    if r != P:
                        pe.wait_ge(prev_rows, 1)
                    if first is not True:
                        pe.wait_ge(kept, n - 1 if isinstance(n, int) else first)
                        pe.wait_ge(kept2, n - 1 if isinstance(n, int) else first)
                    for kt in range(KT):
                        mm = pe.transpose(pt[2 * k + kt // 4][:, kt % 4, 0:r], xn[0:r, k, kt * P:(kt + 1) * P],
                                          K.ident[0:r, 0:r])
                        if kt == 3:
                            mm.then_inc(turned, 1)
                    mm.then_inc(turned2, 1)
                one(0, 0, P, True)
                one(1, 1, P, True)
                with pe.Fori(1, TILES // 2) as g:
                    for b in range(2):
                        one(2 * g + b, b, P, 2 * g + b - 1)
                one(TILES, 0, SR + DB, False)


CONSTS = (("ident", [P, P]), ("ones", [P, P]), ("half_neg", [P, 16]), ("pair_ones", [P, P]), 
          ("causal", [P, P]), ("strict", [P, P]), ("same", [SR, SR]), ("causal_s", [SR, SR]), ("strict_s", [SR, SR]),
          ("last", [SR, SR]), ("restart", [P, TOK]), ("batch_cols", [P, DB, SR]),
          ("head_cols", [P, 2]), ("lcausal", [P, P]), ("lcausal_s", [SR, SR]))


def w_block(w, col, n):
    return w.rearrange("(kt p) c -> p kt c", p=P)[:, :, bass.ds(col, n)]


def phase_gdn_in(nc, K, w_in, conv_w, conv_state, a_log, dt_bias, S, p_conv, s_conv):
    with ExitStack() as ctx:
        sb = lambda n, s: ctx.enter_context(nc.sbuf_tensor("a_" + n, s, F32))
        sem = Events(nc, ctx, "a_")
        W = [sb(f"w{m}", [P, KT, P]) for m in range(4)]
        wg = sb("wg", [P, KT, 2 * AH])
        U = [sb(f"u{m}", [P, CONV - 1 + SEQ]) for m in range(3)]
        US = [sb(f"us{m}", [P, DB, CONV - 1 + DS]) for m in range(3)]
        Y = [sb(f"y{m}", [P, TOK]) for m in range(3)]
        T = [sb(f"t{m}", [P, TOK]) for m in range(3)]
        O = [sb(f"o{m}", [P, TOK]) for m in range(3)]
        TZ = sb("tz", [P, TILES + 1, P])
        Z = sb("z", [P, TILES + 1, P])
        cw_rows = sb("cw_rows", [CONV, AQKV])
        cw = sb("cw", [P, 3 * AH, CONV])
        cs_rows = sb("cs_rows", [DB * (CONV - 1), AQKV])
        cs = sb("cs", [P, 3 * AH, DB, CONV - 1])
        tail = sb("tail", [P, 3, 27])
        tails = sb("tails", [27, 3, P])
        gp = sb("gp", [P, 2, AH])
        g1 = sb("g1", [P, TILES + 1, AH])
        g2 = sb("g2", [P, TILES + 1, AH])
        g3 = sb("g3", [P, TILES + 1, AH])
        bank = [ctx.enter_context(nc.psum_tensor(f"a_bank{i}", [P, 512], F32)) for i in range(8)]
        w_ld = [sem(f"w_ld{m}") for m in range(4)]
        proj = [sem(f"proj{m}") for m in range(4)]
        evac = [sem(f"evac{m}") for m in range(3)]
        conv = [sem(f"conv{m}") for m in range(3)]
        tanh = [sem(f"tanh{m}") for m in range(4)]
        silu = [sem(f"silu{m}") for m in range(4)]
        square = [sem(f"square{m}") for m in range(2)]
        ssq = [sem(f"ssq{m}") for m in range(2)]
        logn = [sem(f"logn{m}") for m in range(2)]
        rs = [sem(f"rs{m}") for m in range(2)]
        normed = [sem(f"normed{m}") for m in range(2)]
        stored = [sem(f"stored{m}") for m in range(4)]
        halo, tailed, tails_t, tails_kept, tails_out, par, par2, pre_t, pre_k, gates, gate_a, gate_v, padded, dseq, pseq = [sem(n) for n in (
            "halo", "tailed", "tails_t", "tails_kept", "tails_out", "par", "par2", "pre_t", "pre_k", "gates", "gate_a",
            "gate_v", "padded", "dseq", "pseq")]
        ready = [silu[2], normed[0], normed[1]]

        with nc.Block() as block:
            @block.sync
            def _(sp):
                for m in range(4):
                    alone(sp, K)
                    sp.dma_start(W[m][:, :, :], w_block(w_in, m * AKEY, P)).then_inc(w_ld[m], 16)
                sp.dma_start(cw_rows[:, :], conv_w).then_inc(par, 16)
                sp.dma_start(cs_rows[:, :], conv_state.rearrange("b r c -> (b r) c")).then_inc(par, 16)
                sp.dma_start(wg[:, :, :], w_block(w_in, AGATE, 2 * AH)).then_inc(par, 16)
                sp.dma_start(gp[:, 0, :], as_row(a_log)).then_inc(par2, 16)
                sp.dma_start(gp[:, 1, :], as_row(dt_bias)).then_inc(par2, 16)

                def load(m, j):
                    sp.wait_ge(proj[m], 3 * (j + 1))
                    alone(sp, K)
                    sp.dma_start(W[m][:, :, :], w_block(w_in, m * AKEY + (j + 1) * P, P)).then_inc(w_ld[m], 16)

                def body(j, more):
                    for m in range(3):
                        if more:
                            load(m, j)
                    sp.wait_ge(silu[2], j + 1)
                    alone(sp, K)
                    sp.dma_start(S.qkv[2, bass.ds(j * P, P), :], O[2][:, :]).then_inc(stored[2], 16)
                    sp.wait_ge(silu[3], j + 1)
                    alone(sp, K)
                    sp.dma_start(S.z[0:SEQ, bass.ds(j * P, P)].rearrange("(n p) c -> p n c", p=P),
                                 Z[:, 0:TILES, :]).then_inc(stored[3], 16)
                    alone(sp, K)
                    sp.dma_start(S.z[SEQ:TOK, bass.ds(j * P, P)], Z[0:SR, TILES, :]).then_inc(stored[3], 16)
                    if more:
                        load(3, j)
                    for m in range(2):
                        sp.wait_ge(normed[m], j + 1)
                        alone(sp, K)
                        sp.dma_start(S.qkv[m, bass.ds(j * P, P), :], O[m][:, :]).then_inc(stored[m], 16)
                    sp.wait_ge(tails_kept, j + 1)
                    col = lambda t: t.rearrange("r (m c) -> r m c", m=3)[:, :, bass.ds(j * P, P)]
                    alone(sp, K)
                    sp.dma_start(col(p_conv[0]), tails[0:3, :, :]).then_inc(tails_out, 16)
                    alone(sp, K)
                    sp.dma_start(col(s_conv.rearrange("b r c -> (b r) c")), tails[3:27, :, :]).then_inc(tails_out, 16)
                with sp.Fori(0, AH - 1) as j:
                    body(j, True)
                body(AH - 1, False)
                for s, n in ((stored[0], 1), (stored[1], 1), (stored[2], 1), (stored[3], 2), (tails_out, 2)):
                    sp.wait_ge(s, 16 * n * AH)

            @block.gpsimd
            def _(pool):
                done = Seq(pseq, pool, 7)
                done.start(0)
                for m in range(3):
                    done(pool.memset(U[m][:, 0:CONV - 1], 0.0))
                for m in range(3):
                    done(pool.memset(US[m][:, :, :], 0.0))
                done(pool.memset(tail[:, :, :], 0.0))
                done.end()
                pool.sem_inc(padded, 1)
                pool.wait_ge(pre_k, 2)
                with pool.Fori(0, AH) as j:
                    for m in range(3):
                        pool.wait_ge(conv[m], j)
                        alone(pool, K)
                        pool.tensor_copy(US[m][:, :, 0:CONV - 1], cs[:, bass.ds(m * AH + j, 1), :, :].rearrange(
                            "p a b r -> p (a b) r")).then_inc(halo, 1)
                        pool.wait_ge(halo, 3 * j + m + 1)
                    pool.wait_ge(tails_t, j)
                    for m in range(3):
                        pool.wait_ge(evac[m], 3 * (j + 1))
                        alone(pool, K)
                        pool.tensor_copy(tail[:, m, 0:3], U[m][:, SEQ:SEQ + 3]).then_inc(tailed, 1)
                        pool.wait_ge(tailed, 6 * j + 2 * m + 1)
                        alone(pool, K)
                        pool.tensor_copy(tail[:, m, 3:27].rearrange("p (b r) -> p b r", b=DB),
                                         US[m][:, :, DS:DS + CONV - 1]).then_inc(tailed, 1)
                        pool.wait_ge(tailed, 6 * j + 2 * m + 2)

            @block.scalar
            def _(act):
                act.wait_ge(padded, 1)
                act.wait_ge(gate_v, 1)
                x = bank[0][:, 0:72].rearrange("p (n h) -> p n h", h=2 * AH)
                act.activation(K.beta[:, :, :], x[:, :, 0:AH], ACT.Tanh, scale=0.5).then_inc(gate_a, 1)
                act.wait_ge(par2, 32)
                act.activation(gp[:, 0, :], gp[:, 0, :], ACT.Exp).then_inc(gate_a, 1)
                act.wait_ge(gate_v, 1)
                act.activation(g2[:, :, :], g1[:, :, :], ACT.Abs).then_inc(gate_a, 1)
                act.wait_ge(gate_a, 3)
                act.activation(g2[:, :, :], g2[:, :, :], ACT.Exp, scale=-1.0).then_inc(gate_a, 1)
                act.wait_ge(gate_a, 4)
                act.activation(g2[:, :, :], g2[:, :, :], ACT.Ln, bias=1.0).then_inc(gate_a, 1)

                def keep(m, j):
                    b0 = 3 * (m % 2)
                    act.wait_ge(conv[m], j)
                    act.wait_ge(tailed, 6 * j)
                    if m < 3:
                        act.wait_ge(halo, 3 * j + m + 1)
                    for g in range(2):
                        act.wait_ge(proj[m], 3 * j + g + 1)
                        act.activation(U[m][:, 3 + 512 * g:3 + 512 * (g + 1)], bank[b0 + g][:, :], ACT.Copy).then_inc(evac[m], 1)
                    act.wait_ge(proj[m], 3 * j + 3)
                    act.activation(US[m][:, :, 3:11], bank[b0 + 2][:, 0:SR].rearrange("p (b t) -> p b t", b=DB),
                                   ACT.Copy).then_inc(evac[m], 1)

                def tanhs(m, j):
                    act.wait_ge(conv[m], j + 1)
                    act.wait_ge(silu[m], j)
                    if m < 2:
                        act.wait_ge(normed[m], j)
                    act.activation(T[m][:, :], Y[m][:, :], ACT.Tanh).then_inc(tanh[m], 1)

                def squares(m, j):
                    act.wait_ge(silu[m], j + 1)
                    act.activation(T[m][:, :], O[m][:, :], ACT.Square).then_inc(square[m], 1)

                with act.Fori(0, AH) as j:
                    keep(0, j)
                    keep(1, j)
                    tanhs(0, j)
                    squares(0, j)
                    keep(2, j)
                    tanhs(1, j)
                    squares(1, j)
                    tanhs(2, j)
                    act.wait_ge(silu[3], j)
                    for g in range(2):
                        act.wait_ge(proj[3], 3 * j + g + 1)
                        act.activation(TZ[:, 4 * g:4 * g + 4, :], bank[3 + g][:, :].rearrange("p (n c) -> p n c", n=4),
                                       ACT.Tanh, scale=0.5).then_inc(tanh[3], 1)
                    act.wait_ge(proj[3], 3 * j + 3)
                    act.activation(TZ[0:SR, TILES, :], bank[5][0:SR, 0:P], ACT.Tanh, scale=0.5).then_inc(tanh[3], 1)
                    for m in range(2):
                        act.wait_ge(ssq[m], j + 1)
                        for g, (c, n) in enumerate(GROUPS):
                            src = bank[6 + g][:, 0:n] if g < 2 else bank[2][:, 128:128 + n]
                            act.activation(T[m][:, c:c + n], src, ACT.Ln, bias=EPS).then_inc(logn[m], 1)
                    for m in range(2):
                        act.wait_ge(logn[m], 3 * (j + 1))
                        act.activation(T[m][:, :], T[m][:, :], ACT.Exp, scale=-0.5,
                                       bias=-0.5 * math.log(P) if m == 0 else 0.0).then_inc(rs[m], 1)

            @block.vector
            def _(dve):
                done = Seq(dseq, dve, 7)
                done.start(0)
                dve.wait_ge(pre_t, 1)
                dve.tensor_scalar(cw[:, :, :], bank[6][:, 0:48].rearrange("p (c r) -> p c r", r=CONV), 0.5, None,
                                  ALU.mult).then_inc(pre_k, 1)
                dve.wait_ge(pre_t, 2)
                dve.tensor_copy(cs[:, :, :, :], bank[7][:, 0:288].rearrange("p (c b r) -> p c b r", b=DB, r=3)).then_inc(pre_k, 1)
                dve.wait_ge(pre_t, 3)
                dve.wait_ge(par2, 32)
                dve.tensor_tensor(g1[:, :, :], bank[0][:, 0:72].rearrange("p (n h) -> p n h", h=2 * AH)[:, :, AH:2 * AH],
                                  gp[:, 1:2, :].broadcast_to([P, TILES + 1, AH]), ALU.add).then_inc(gate_v, 1)
                dve.wait_ge(gate_a, 5)
                done(dve.tensor_scalar(K.beta[:, :, :], K.beta[:, :, :], 0.5, 0.5, ALU.mult, ALU.add))
                done(dve.tensor_scalar(g3[:, :, :], g1[:, :, :], 0.0, None, ALU.max))
                done(dve.tensor_tensor(g3[:, :, :], g3[:, :, :], g2[:, :, :], ALU.add))
                done(dve.scalar_tensor_tensor(out=K.logd[:, :, :], in0=g3[:, :, :], scalar=-1.0,
                                              in1=gp[:, 0:1, :].broadcast_to([P, TILES + 1, AH]),
                                              op0=ALU.mult, op1=ALU.mult))
                done(dve.memset(g1[:, :, :], 0.0))
                done(dve.memset(g1[:, :, :], 0.0))
                done(dve.memset(g1[:, :, :], 0.0))
                dve.sem_inc(gates, 1)

                step = Seq(gates, dve, 21)

                def convolve(m, j):
                    dve.wait_ge(evac[m], 3 * (j + 1))
                    dve.wait_ge(halo, 3 * j + m + 1)
                    y, ys = Y[m][:, 0:SEQ], Y[m][:, SEQ:TOK].rearrange("p (b t) -> p b t", b=DB)
                    for r in range(CONV):
                        w = cw[:, bass.ds(m * AH + j, 1), r]
                        for o, u in ((y, U[m][:, r:r + SEQ]), (ys, US[m][:, :, r:r + DS])):
                            if r == 0:
                                ins = dve.tensor_scalar(o, u, w, None, ALU.mult)
                            else:
                                ins = dve.scalar_tensor_tensor(out=o, in0=u, scalar=w, in1=o, op0=ALU.mult, op1=ALU.add)
                            if r < CONV - 1 or o is y:
                                step(ins)
                    ins.then_inc(conv[m], 1)

                def silus(m, j):
                    dve.wait_ge(tanh[m], j + 1)
                    dve.wait_ge(conv[m], j + 1)
                    dve.wait_ge(stored[m], 16 * j)
                    dve.scalar_tensor_tensor(out=O[m][:, :], in0=T[m][:, :], scalar=1.0, in1=Y[m][:, :],
                                             op0=ALU.add, op1=ALU.mult).then_inc(silu[m], 1)

                with dve.Fori(0, AH) as j:
                    step.start(j)
                    step.base = step.base + 1
                    convolve(0, j)
                    silus(0, j)
                    convolve(1, j)
                    silus(1, j)
                    convolve(2, j)
                    silus(2, j)
                    dve.wait_ge(stored[3], 32 * j)
                    for g in range(2):
                        dve.wait_ge(tanh[3], 3 * j + g + 1)
                        dve.scalar_tensor_tensor(out=Z[:, 4 * g:4 * g + 4, :], in0=TZ[:, 4 * g:4 * g + 4, :], scalar=1.0,
                                                 in1=bank[3 + g][:, :].rearrange("p (n c) -> p n c", n=4),
                                                 op0=ALU.add, op1=ALU.mult).then_inc(padded, 1)
                    dve.wait_ge(tanh[3], 3 * j + 3)
                    dve.wait_ge(padded, 2 * j + 3)
                    dve.scalar_tensor_tensor(out=Z[0:SR, TILES, :], in0=TZ[0:SR, TILES, :], scalar=1.0,
                                             in1=bank[5][0:SR, 0:P], op0=ALU.add, op1=ALU.mult).then_inc(silu[3], 1)
                    for m in range(2):
                        dve.wait_ge(rs[m], j + 1)
                        dve.tensor_tensor(O[m][:, :], O[m][:, :], T[m][:, :], ALU.mult).then_inc(normed[m], 1)
                    dve.wait_ge(tails_t, j + 1)
                    dve.wait_ge(tails_out, 32 * j)
                    dve.tensor_copy(tails[:, :, :], bank[5][0:27, P:4 * P].rearrange("p (m c) -> p m c", m=3)).then_inc(tails_kept, 1)
                    step.end()

            @block.tensor
            def _(pe):
                pe.wait_ge(par, 48)
                for c in range(3 * AH):
                    mm = pe.transpose(bank[6][:, c * CONV:(c + 1) * CONV], cw_rows[:, c * P:(c + 1) * P], K.ident[0:CONV, 0:CONV])
                mm.then_inc(pre_t, 1)
                for c in range(3 * AH):
                    mm = pe.transpose(bank[7][:, c * 24:(c + 1) * 24], cs_rows[:, c * P:(c + 1) * P], K.ident[0:24, 0:24])
                mm.then_inc(pre_t, 1)
                for n in range(TILES + 1):
                    r = P
                    for kt in range(KT):
                        mm = pe.matmul(bank[0][0:r, n * 8:(n + 1) * 8], K.xnT[:, kt, n * P:n * P + r], wg[:, kt, :],
                                       start=(kt == 0), stop=(kt == KT - 1))
                mm.then_inc(pre_t, 1)
                pe.wait_ge(gate_v, 1)
                pe.wait_ge(gate_a, 1)
                pe.wait_ge(pre_k, 2)

                def sums(m, j):
                    pe.wait_ge(square[m], j + 1)
                    if m == 0:
                        pe.wait_ge(logn[1], 3 * j)
                    else:
                        pe.wait_ge(logn[0], 3 * (j + 1))
                    for g, (c, n) in enumerate(GROUPS):
                        dst = bank[6 + g][:, 0:n] if g < 2 else bank[2][:, 128:128 + n]
                        mm = pe.matmul(dst, K.ones[:, :], T[m][:, c:c + n], start=True, stop=True)
                    mm.then_inc(ssq[m], 1)

                with pe.Fori(0, AH) as j:
                    for m in range(3):
                        b0 = 3 * (m % 2)
                        if m == 0:
                            pe.wait_ge(evac[2], 3 * j)
                            pe.wait_ge(logn[1], 3 * j)
                        elif m == 1:
                            pe.wait_ge(silu[3], j)
                            pe.wait_ge(tails_kept, j)
                        else:
                            pe.wait_ge(evac[0], 3 * (j + 1))
                        pe.wait_ge(w_ld[m], 16 * (j + 1))
                        for g, (c, n) in enumerate(GROUPS):
                            for kt in range(KT):
                                mm = pe.matmul(bank[b0 + g][:, 0:n], W[m][:, kt, :], K.xnT[:, kt, c:c + n],
                                               start=(kt == 0), stop=(kt == KT - 1))
                            mm.then_inc(proj[m], 1)
                    pe.wait_ge(evac[2], 3 * (j + 1))
                    sums(0, j)
                    pe.wait_ge(evac[1], 3 * (j + 1))
                    pe.wait_ge(w_ld[3], 16 * (j + 1))
                    for n in range(TILES + 1):
                        r = P
                        for kt in range(KT):
                            mm = pe.matmul(bank[3 + n // 4][0:r, (n % 4) * P:(n % 4 + 1) * P], K.xnT[:, kt, n * P:n * P + r],
                                           W[3][:, kt, :], start=(kt == 0), stop=(kt == KT - 1))
                        if n in (3, 7, 8):
                            mm.then_inc(proj[3], 1)
                    sums(1, j)
                    pe.wait_ge(silu[3], j + 1)
                    pe.wait_ge(tailed, 6 * (j + 1))
                    for m in range(3):
                        mm = pe.transpose(bank[5][0:27, (m + 1) * P:(m + 2) * P], tail[:, m, :], K.ident[:, :])
                    mm.then_inc(tails_t, 1)


def phase_rwkv_in(nc, K, w_in, mu, w0, w2, a0, a2, k_k, k_a, r_k, S):
    with ExitStack() as ctx:
        sb = lambda n, s: ctx.enter_context(nc.sbuf_tensor("b_" + n, s, F32))
        sem = Events(nc, ctx, "b_")
        W = [sb(f"w{m}", [P, KT, P]) for m in range(4)]
        U = [sb(f"u{m}", [P, 1 + SEQ]) for m in range(4)]
        US = [sb(f"us{m}", [P, DB, 1 + DS]) for m in range(4)]
        X = [sb(f"x{m}", [P, TOK]) for m in range(4)]
        LO = sb("lo", [P, TOK])
        lora = sb("lora", [P, P])
        T1 = sb("t1", [P, XW])
        par_rows = sb("par_rows", [24, P])
        par = sb("par", [P, 24])
        mu_rows = sb("mu_rows", [17, P])
        mus = sb("mus", [P, 17])
        lw, kk, G, E1, E2, E3, A = [sb(n, [P, TOK]) for n in ("lw", "kk", "g", "e1", "e2", "e3", "a")]
        bank = [ctx.enter_context(nc.psum_tensor(f"b_bank{i}", [P, 512], F32)) for i in range(8)]
        w_ld = [sem(f"w_ld{m}") for m in range(4)]
        proj = [sem(f"proj{m}") for m in range(4)]
        evac = [sem(f"evac{m}") for m in range(4)]
        mixed = [sem(f"mixed{m}") for m in range(4)]
        outs = [sem(f"out{m}") for m in range(6)]
        stored = [sem(f"stored{m}") for m in range(6)]
        (par_in, lora_in, turned, par_kept, lo_ready, lo_a, gate_mm, gate_t, sq, ssq, ssq_free, rs, gt, expo, gc, gsub,
         rk_ready, bonus_mm, bonus_kept, dseq, pseq, zeroed, ends, kk_ready) = [sem(n) for n in (
             "par_in", "lora_in", "turned", "par_kept", "lo_ready", "lo_a", "gate_mm", "gate_t", "sq", "ssq", "ssq_free",
             "rs", "gt", "expo", "gc", "gsub", "rk_ready", "bonus_mm", "bonus_kept", "dseq", "pseq", "zeroed", "ends", "kk_ready")]
        B0 = ACOLS
        KK, KA, RK, W0, A0 = 0, 4, 8, 12, 16

        def shifted(m):
            return ((U[m][:, 1:1 + SEQ], U[m][:, 0:SEQ]), (US[m][:, :, 1:1 + DS], US[m][:, :, 0:DS]))

        def halves(t):
            return t[:, 0:SEQ], t[:, SEQ:TOK].rearrange("p (b t) -> p b t", b=DB)

        with nc.Block() as block:
            @block.sync
            def _(sp):
                sp.dma_start(W[0][:, :, :], w_block(w_in, B0 + 4 * BW, P)).then_inc(w_ld[0], 16)
                for n, t in enumerate((k_k, k_a, r_k.rearrange("h n -> (h n)"), w0, a0)):
                    sp.dma_start(par_rows[4 * n:4 * n + 4, :], t.rearrange("(j p) -> j p", p=P)).then_inc(par_in, 16)
                sp.dma_start(mu_rows[:, :], mu.rearrange("(j p) -> j p", p=P)).then_inc(par_in, 16)
                sp.dma_start(lora[0:64, :], w2[:, 0:P]).then_inc(lora_in, 16)
                sp.dma_start(lora[64:128, :], a2[:, 0:P]).then_inc(lora_in, 16)
                for m in range(1, 4):
                    sp.dma_start(W[m][:, :, :], w_block(w_in, B0 + m * BW, P)).then_inc(w_ld[m], 16)
                sp.wait_ge(proj[0], 3)
                sp.dma_start(W[0][:, :, :], w_block(w_in, B0, P)).then_inc(w_ld[0], 16)

                def body(j, more):
                    for m in range(4):
                        if more:
                            sp.wait_ge(proj[m], 3 * (j + 1) + (3 if m == 0 else 0))
                            alone(sp, K)
                            sp.dma_start(W[m][:, :, :], w_block(w_in, B0 + m * BW + (j + 1) * P, P)).then_inc(w_ld[m], 16)
                    if more:
                        sp.wait_ge(gate_mm, 2 * (j + 1))
                        alone(sp, K)
                        sp.dma_start(lora[0:64, :], w2[:, bass.ds((j + 1) * P, P)]).then_inc(lora_in, 16)
                        sp.dma_start(lora[64:128, :], a2[:, bass.ds((j + 1) * P, P)]).then_inc(lora_in, 16)
                    for m, t in ((4, X[2]), (5, X[3]), (0, X[0]), (1, E2), (2, kk), (3, X[1])):
                        sp.wait_ge(outs[m], j + 1)
                        alone(sp, K)
                        sp.dma_start(S.rw[m, bass.ds(j * P, P), :], t[:, :]).then_inc(stored[m], 16)
                with sp.Fori(0, NP - 1) as j:
                    body(j, True)
                body(NP - 1, False)
                for s in stored:
                    sp.wait_ge(s, 16 * NP)

            @block.gpsimd
            def _(pool):
                done = Seq(pseq, pool, 5)
                done.start(0)
                for m in range(4):
                    done(pool.memset(U[m][:, 0:1], 0.0))
                done(pool.memset(T1[:, TOK:XW], 0.0))
                done.end()
                pool.sem_inc(zeroed, 1)

            @block.scalar
            def _(act):
                act.wait_ge(zeroed, 1)

                def keep(m, j, base):
                    act.wait_ge(mixed[m], j + (1 if base else 0))
                    b0 = 3 * (m % 2)
                    for g in range(2):
                        act.wait_ge(proj[m], 3 * j + base + g + 1)
                        act.activation(U[m][:, 1 + 512 * g:1 + 512 * (g + 1)], bank[b0 + g][:, :], ACT.Copy).then_inc(evac[m], 1)
                    act.wait_ge(proj[m], 3 * j + base + 3)
                    act.activation(US[m][:, :, 1:1 + DS], bank[b0 + 2][:, 0:SR].rearrange("p (b t) -> p b t", b=DB),
                                   ACT.Copy).then_inc(evac[m], 1)
                    act.activation(US[m][:, :, 0], bank[b0 + 2][:, SR:SR + DB], ACT.Copy).then_inc(evac[m], 1)
                keep(0, 0, 0)
                act.wait_ge(mixed[0], 1)
                act.activation(LO[0:64, :], LO[0:64, :], ACT.Tanh).then_inc(lo_a, 1)

                with act.Fori(0, NP) as j:
                    act.wait_ge(expo, 3 * j)
                    act.wait_ge(gsub, j)
                    act.wait_ge(outs[3], j)
                    act.wait_ge(outs[2], j)
                    act.wait_ge(gate_mm, 2 * j + 1)
                    act.wait_ge(par_kept, 2)
                    for g, (c, n) in enumerate(GROUPS):
                        src = bank[6 + g][:, 0:n] if g < 2 else bank[5][:, 128:128 + n]
                        act.activation(lw[:, c:c + n], src, ACT.Tanh, scale=0.5, bias=par[:, bass.ds(W0 + j, 1)]).then_inc(gate_t, 1)
                    act.wait_ge(gate_mm, 2 * j + 2)
                    for g, (c, n) in enumerate(GROUPS):
                        src = bank[6 + g][:, 0:n] if g < 2 else bank[5][:, 128:128 + n]
                        act.activation(A[:, c:c + n], src, ACT.Tanh, scale=0.5, bias=par[:, bass.ds(A0 + j, 1)]).then_inc(gate_t, 1)
                    keep(0, j, 3)
                    keep(1, j, 0)
                    act.wait_ge(mixed[1], j + 1)
                    act.wait_ge(outs[0], j)
                    act.activation(E1[:, :], X[1][:, :], ACT.Square, scale=par[:, bass.ds(KK + j, 1)]).then_inc(sq, 1)
                    keep(2, j, 0)
                    keep(3, j, 0)
                    act.wait_ge(mixed[3], j + 1)
                    act.wait_ge(stored[1], 16 * j)
                    act.activation(E2[:, :], X[3][:, :], ACT.Tanh, scale=0.5).then_inc(gt, 1)
                    act.wait_ge(ssq, j + 1)
                    for g, (c, n) in enumerate(GROUPS):
                        src = bank[6 + g][:, 0:n] if g < 2 else bank[5][:, 128:128 + n]
                        act.activation(E3[:, c:c + n], src, ACT.Ln, bias=EPS).then_inc(ssq_free, 1)
                    act.wait_ge(ssq_free, 3 * (j + 1))
                    act.activation(E3[:, :], E3[:, :], ACT.Exp, scale=-0.5).then_inc(rs, 1)
                    act.wait_ge(gc, j + 1)
                    act.wait_ge(ssq, j + 1)
                    act.activation(E1[:, :], G[:, :], ACT.Exp).then_inc(expo, 1)
                    act.wait_ge(gsub, j + 1)
                    act.wait_ge(outs[5], j + 1)
                    act.activation(E2[:, :], lw[:, :], ACT.Exp).then_inc(expo, 1)
                    act.wait_ge(kk_ready, j + 1)
                    act.activation(E3[:, :], G[:, :], ACT.Exp, scale=-1.0).then_inc(expo, 1)
                    act.activation(K.rw_in[:, bass.ds(j, 1), :], K.rw_mid[:, bass.ds(j, 1), :], ACT.Exp).then_inc(ends, 1)
                    act.activation(K.rw_out[:, bass.ds(j, 1), 0:TILES], G[:, P - 1:SEQ:P], ACT.Exp).then_inc(ends, 1)
                    act.activation(K.rw_out[:, bass.ds(j, 1), TILES:TILES + DB], G[:, SEQ + DS - 1:TOK:DS], ACT.Exp).then_inc(ends, 1)

            @block.vector
            def _(dve):
                dve.wait_ge(turned, 2)
                dve.tensor_copy(mus[:, :], bank[6][:, 0:17]).then_inc(par_kept, 1)
                dve.tensor_copy(par[:, 0:12], bank[6][:, 32:44]).then_inc(dseq, 1)
                dve.tensor_scalar(par[:, 12:20], bank[6][:, 44:52], 0.5, None, ALU.mult).then_inc(par_kept, 1)
                dve.wait_ge(dseq, 1)
                dve.tensor_scalar(par[:, 4:8], par[:, 4:8], 0.5, None, ALU.mult).then_inc(dseq, 1)
                dve.wait_ge(dseq, 2)
                dve.tensor_scalar(par[:, 20:24], par[:, 4:8], -1.0, 1.0, ALU.mult, ALU.add).then_inc(dseq, 1)
                dve.wait_ge(dseq, 3)
                dve.wait_ge(par_kept, 2)

                one = Seq(dseq, dve, 19)

                def blend(m, dst, col, n):
                    dve.wait_ge(evac[m], n)
                    now_s, now_d = shifted(m)
                    ds_, dd_ = halves(dst)
                    one(dve.tensor_tensor(ds_, now_s[1], now_s[0], ALU.subtract))
                    one(dve.tensor_tensor(dd_, now_d[1], now_d[0], ALU.subtract))
                    one(dve.scalar_tensor_tensor(out=ds_, in0=ds_, scalar=mus[:, col], in1=now_s[0], op0=ALU.mult, op1=ALU.add))
                    dve.scalar_tensor_tensor(out=dd_, in0=dd_, scalar=mus[:, col], in1=now_d[0],
                                             op0=ALU.mult, op1=ALU.add).then_inc(mixed[m], 1)
                one.start(0)
                one.n = 3
                blend(0, LO, slice(16, 17), 4)
                assert one.n == 6

                with dve.Fori(0, NP) as j:
                    one.start(j)
                    one.base = one.base + 6
                    dve.wait_ge(stored[0], 16 * j)
                    blend(0, X[0], bass.ds(0 + j, 1), 4 * j + 8)
                    dve.wait_ge(gate_t, 6 * j + 3)
                    one(dve.tensor_scalar(lw[:, :], lw[:, :], 1.0, -0.5 * DECAY, ALU.add, ALU.mult))
                    dve.wait_ge(ends, 3 * j)
                    one(dve.tensor_tensor_scan(G[:, :], K.restart[:, :], lw[:, :], 0.0, ALU.mult, ALU.add))
                    one(dve.tensor_copy(K.rw_mid[:, bass.ds(j, 1), :], G[:, P // 2 - 1:SEQ:P]))
                    g3 = G[:, 0:SEQ].rearrange("p (n t) -> p n t", n=TILES)
                    mid = K.rw_mid[:, bass.ds(j, 1), :].rearrange("p a n -> p (a n)")
                    one(dve.tensor_tensor(g3, g3, mid.rearrange("p (n a) -> p n a", a=1).broadcast_to([P, TILES, P]), ALU.subtract))
                    dve.sem_inc(gc, 1)
                    dve.tensor_tensor(lw[:, :], G[:, :], lw[:, :], ALU.subtract).then_inc(gsub, 1)
                    dve.wait_ge(stored[3], 16 * j)
                    blend(1, X[1], bass.ds(4 + j, 1), 4 * j + 4)
                    dve.wait_ge(stored[4], 16 * j)
                    blend(2, X[2], bass.ds(8 + j, 1), 4 * j + 4)
                    dve.wait_ge(mixed[2], j + 1)
                    dve.sem_inc(outs[4], 1)
                    dve.wait_ge(stored[5], 16 * j)
                    blend(3, X[3], bass.ds(12 + j, 1), 4 * j + 4)
                    dve.wait_ge(gt, j + 1)
                    dve.wait_ge(mixed[3], j + 1)
                    dve.scalar_tensor_tensor(out=X[3][:, :], in0=E2[:, :], scalar=1.0, in1=X[3][:, :],
                                             op0=ALU.add, op1=ALU.mult).then_inc(outs[5], 1)
                    dve.wait_ge(rs, j + 1)
                    dve.wait_ge(mixed[1], j + 1)
                    dve.wait_ge(stored[2], 16 * j)
                    dve.scalar_tensor_tensor(out=kk[:, :], in0=X[1][:, :], scalar=par[:, bass.ds(KK + j, 1)], in1=E3[:, :],
                                             op0=ALU.mult, op1=ALU.mult).then_inc(kk_ready, 1)
                    dve.wait_ge(gate_t, 6 * j + 6)
                    dve.wait_ge(bonus_kept, j)
                    one(dve.tensor_scalar(T1[:, 0:TOK], A[:, :], par[:, bass.ds(KA + j, 1)],
                                          par[:, bass.ds(20 + j, 1)], ALU.mult, ALU.add))
                    one(dve.tensor_tensor(X[1][:, :], X[1][:, :], T1[:, 0:TOK], ALU.mult))
                    dve.wait_ge(mixed[0], j + 2)
                    dve.scalar_tensor_tensor(out=T1[:, 0:TOK], in0=X[1][:, :], scalar=par[:, bass.ds(RK + j, 1)], in1=X[0][:, :],
                                             op0=ALU.mult, op1=ALU.mult).then_inc(rk_ready, 1)
                    dve.wait_ge(expo, 3 * j + 1)
                    dve.wait_ge(rk_ready, j + 1)
                    dve.tensor_tensor(X[0][:, :], X[0][:, :], E1[:, :], ALU.mult).then_inc(outs[0], 1)
                    dve.wait_ge(expo, 3 * j + 3)
                    dve.wait_ge(kk_ready, j + 1)
                    dve.wait_ge(stored[1], 16 * j)
                    dve.tensor_tensor(E2[:, :], kk[:, :], E2[:, :], ALU.mult).then_inc(outs[1], 1)
                    one(dve.scalar_tensor_tensor(out=A[:, :], in0=A[:, :], scalar=1.0, in1=kk[:, :], op0=ALU.add, op1=ALU.mult))
                    dve.wait_ge(outs[1], j + 1)
                    dve.scalar_tensor_tensor(out=kk[:, :], in0=A[:, :], scalar=0.5, in1=E3[:, :],
                                             op0=ALU.mult, op1=ALU.mult).then_inc(outs[2], 1)
                    dve.tensor_tensor(X[1][:, :], X[1][:, :], E3[:, :], ALU.mult).then_inc(outs[3], 1)
                    dve.wait_ge(bonus_mm, j + 1)
                    dve.tensor_copy(K.bonus[:, :, bass.ds(2 * j, 2)], bank[5][:, 256:256 + 18].rearrange("p (n h) -> p n h", h=2)
                                    ).then_inc(bonus_kept, 1)
                    one.end()

            @block.tensor
            def _(pe):
                pe.wait_ge(par_in, 96)
                pe.transpose(bank[6][:, 0:17], mu_rows[:, :], K.ident[0:17, 0:17]).then_inc(turned, 1)
                pe.transpose(bank[6][:, 32:52], par_rows[0:20, :], K.ident[0:20, 0:20]).then_inc(turned, 1)

                def project(m, n_w):
                    b0 = 3 * (m % 2)
                    pe.wait_ge(w_ld[m], 16 * n_w)
                    for g, (c, n) in enumerate(GROUPS[:2] + ((SEQ, SR + DB),)):
                        for kt in range(KT):
                            mm = pe.matmul(bank[b0 + g][:, 0:n], W[m][:, kt, :], K.xnT[:, kt, c:c + n],
                                           start=(kt == 0), stop=(kt == KT - 1))
                        mm.then_inc(proj[m], 1)

                def gate(half, j):
                    r = slice(64 * half, 64 * half + 64)
                    for g, (c, n) in enumerate(GROUPS):
                        dst = bank[6 + g][:, 0:n] if g < 2 else bank[5][:, 128:128 + n]
                        mm = pe.matmul(dst, lora[r, :], LO[r, c:c + n], start=True, stop=True)
                    mm.then_inc(gate_mm, 1)
                project(0, 1)
                pe.wait_ge(lora_in, 32)
                pe.wait_ge(lo_a, 1)
                pe.wait_ge(par_kept, 2)
                pe.wait_ge(evac[0], 4)

                with pe.Fori(0, NP) as j:
                    pe.wait_ge(bonus_kept, j)
                    pe.wait_ge(ssq_free, 3 * j)
                    pe.wait_ge(evac[3], 4 * j)
                    pe.wait_ge(lora_in, 32 * (j + 1))
                    gate(0, j)
                    pe.wait_ge(evac[2], 4 * j)
                    project(0, j + 2)
                    pe.wait_ge(gate_t, 6 * j + 3)
                    gate(1, j)
                    pe.wait_ge(gate_t, 6 * j + 6)
                    project(1, j + 1)
                    pe.wait_ge(evac[0], 4 * j + 8)
                    project(2, j + 1)
                    pe.wait_ge(evac[1], 4 * j + 4)
                    project(3, j + 1)
                    pe.wait_ge(evac[3], 4 * j + 4)
                    pe.wait_ge(sq, j + 1)
                    for g, (c, n) in enumerate(GROUPS):
                        dst = bank[6 + g][:, 0:n] if g < 2 else bank[5][:, 128:128 + n]
                        mm = pe.matmul(dst, K.pair_ones[:, :], E1[:, c:c + n], start=True, stop=True)
                    mm.then_inc(ssq, 1)
                    pe.wait_ge(rk_ready, j + 1)
                    pe.wait_ge(ssq_free, 3 * j + 3)
                    for n in range(TILES + 1):
                        r = P
                        mm = pe.matmul(bank[5][0:r, 256 + 2 * n:258 + 2 * n], T1[:, n * P:n * P + r], K.head_cols[:, :],
                                       start=True, stop=True)
                    mm.then_inc(bonus_mm, 1)


LEVELS = 7
LEVELS_S = 3


def phase_mix0(nc, K, w_out, norm_w, gdn_norm, ln_w, ln_b, x_prompt, x_sample, gdn0, rwkv0, S,
               p_gdn, p_rwkv, s_gdn, s_rwkv):
    with ExitStack() as ctx:
        sb = lambda n, s: ctx.enter_context(nc.sbuf_tensor("c_" + n, s, F32))
        ev = Events(nc, ctx, "c_")

        QK = sb("qk", [P, 2, AH, P])
        V = sb("v", [P, AH, P])
        RW = sb("rw", [P, 4, NP, P])
        VG = sb("vg", [P, 2, NP, P])
        Z = sb("z", [P, AKEY])
        XR = sb("xr", [P, D])
        wo = sb("wo", [P, KT, D])
        nw = sb("nw", [P, D])
        gnw = sb("gnw", [P, P])
        lnw = sb("lnw", [P, BW])
        lnb = sb("lnb", [P, BW])
        ld, bt, nbt, bo = sb("ld", [P, AH]), sb("bt", [P, AH]), sb("nbt", [P, AH]), sb("bo", [P, BH])
        g, eg = sb("g", [P, AH]), sb("eg", [P, AH])
        dend = sb("dend", [P, AH])
        dec = sb("dec", [P, AH, P])
        eGB = sb("egb", [P, AH, P])
        attn = sb("attn", [P, AH, P])
        NT = sb("nt", [P, AH, P])
        SC = sb("sc", [P, BH, 4, P])
        mask4 = sb("mask4", [P, 4, P])
        mask4s = sb("mask4s", [SR, 4, SR])
        lev = sb("lev", [P, LEVELS, P])
        kr, vr = sb("kr", [P, AH, P]), sb("vr", [P, AH, P])
        Br, Kr, Vr, Gr = [sb(n, [P, BW]) for n in ("br", "krr", "vrr", "grr")]
        X = [sb(f"inv{u}", [P, 4, P]) for u in range(3)]
        XT = [sb(f"invt{u}", [P, 4, P]) for u in range(3)]
        Yall = sb("y", [P, 3, 4, P])
        Y = [Yall[:, u, :, :] for u in range(3)]
        M = [sb(f"m{u}", [P, 4, P]) for u in range(3)]
        Wr = sb("wr", [P, AH, P])
        NV = sb("nv", [P, AH, P])
        NVd = sb("nvd", [P, AH, P])
        RH = sb("rh", [P, BW])
        SA = sb("sa", [P, BW])
        St = sb("st", [P, AH, P])
        Tt = sb("tt", [P, NP, P])
        Th = sb("th", [P, NP, P])
        sqa, sqb = sb("sqa", [P, BW]), sb("sqb", [P, BW])
        st = sb("stats", [P, 12])
        rstd = sb("rstd", [P, 12])
        mean = sb("mean", [P, BH])
        OR = sb("or", [P, D])
        bv = sb("bv", [P, BW])
        gw = sb("gw", [P, BW])
        OT = sb("ot", [P, KT, P])
        x1 = XR
        n1 = sb("n1", [P, 4])
        xn = sb("xn", [P, D])
        QG = sb("qg", [P, AH, P])
        tr = Wr
        bank = [ctx.enter_context(nc.psum_tensor(f"c_bank{i}", [P, 512], F32)) for i in range(8)]
        Sb = sb("sb", [P, DB, AH, P])
        Tb = sb("tb", [P, DB, NP, 64])
        Rb = Yall[0:64, 0:2, :, :]
        Q1 = sb("q1", [P, DB, SR])

        def v4(b, r=P, c=P):
            return bank[b][0:r, 0:4 * P].rearrange("p (h c) -> p h c", h=4)[:, :, 0:c]

        def half(t, l, T, s):
            if len(t.shape) == 2:
                return t[:, 0:T].rearrange("p (b u h) -> p b u h", u=2, h=1 << l)[:, :, s, :]
            return t[:, :, 0:T].rearrange("p k (b u h) -> p k b u h", u=2, h=1 << l)[:, :, :, s, :]

        def packed(b, l, T, r):
            return bank[b][0:r, :].rearrange("p (k c) -> p k c", k=4)[:, :, 0:T // 2].rearrange("p k (b h) -> p k b h", h=1 << l)

        def bc(t, shape):
            return t.broadcast_to(shape)

        with nc.Block() as block:
            @block.sync
            def _(sp):
                sp.dma_start(wo[:, :, :], w_block(w_out, 0, D)).then_inc(ev("ld_wo"), 16)
                for t, v in ((nw, norm_w), (gnw, gdn_norm), (lnw, ln_w), (lnb, ln_b)):
                    sp.dma_start(t[:, :], as_row(v)).then_inc(ev("ld_par"), 16)

                col = lambda t, c, T: t.rearrange("(h p) t -> p h t", p=P)[:, :, bass.ds(c, T)]

                def load_qkv(c, T):
                    for m in range(2):
                        sp.dma_start(QK[:, m, :, 0:T], col(S.qkv[m], c, T)).then_inc(ev("ld_qk"), 16)
                    sp.dma_start(V[:, :, 0:T], col(S.qkv[2], c, T)).then_inc(ev("ld_v"), 16)

                def load_abk(c, T):
                    for m in range(1, 4):
                        sp.dma_start(RW[:, m, :, 0:T], col(S.rw[m], c, T)).then_inc(ev("ld_rw"), 16)
                    for m in range(2):
                        sp.dma_start(VG[:, m, :, 0:T], col(S.rw[4 + m], c, T)).then_inc(ev("ld_vg"), 16)

                def load_r(c, T):
                    sp.dma_start(RW[:, 0, :, 0:T], col(S.rw[0], c, T)).then_inc(ev("ld_r"), 16)

                def load_z(c, T):
                    sp.dma_start(Z[0:T, :], S.z[bass.ds(c, T), :]).then_inc(ev("ld_z"), 16)

                def load_x(c, T):
                    x = x_prompt[0, bass.ds(c, T), :] if T == P else x_sample.rearrange("b t d -> (b t) d")
                    sp.dma_start(XR[0:T, :], x).then_inc(ev("ld_x"), 16)

                def during(i, ahead):
                    n, c = i + 1, i * P
                    sp.wait_ge(ev("rows_a"), n)
                    sp.wait_ge(ev("rhs_a"), n)
                    sp.wait_ge(ev("qg"), n)
                    alone(sp, K)
                    load_qkv(c + P, ahead)
                    sp.wait_ge(ev("rows_vg"), n)
                    sp.wait_ge(ev("rows_b"), n)
                    sp.wait_ge(ev("rhs_b"), n)
                    alone(sp, K)
                    load_abk(c + P, ahead)
                    if not (isinstance(i, int) and i == 0):
                        sp.wait_ge(ev("oa"), i)
                        alone(sp, K)
                        load_z(c, P)
                        sp.wait_ge(ev("x1"), i)
                        alone(sp, K)
                        sp.dma_start(S.x1[bass.ds(c - P, P), :], x1[:, :]).then_inc(ev("stored"), 16)
                    sp.wait_ge(ev("out_b"), n)
                    alone(sp, K)
                    load_r(c + P, ahead)
                    if not (isinstance(i, int) and i == 0):
                        sp.wait_ge(ev("xn1"), i)
                        alone(sp, K)
                        sp.wait_ge(ev("stored"), 16 * i)
                        alone(sp, K)
                        load_x(c, P)
                        sp.wait_ge(ev("xk_a"), i)
                        sp.wait_ge(ev("xk_b"), i)
                        alone(sp, K)
                        sp.dma_start(S.xnT[:, :, bass.ds(c - P, P)], OT[:, :, :]).then_inc(ev("xn_out"), 16)

                def after(i, T):
                    c = i * P
                    if i < TILES:
                        sp.wait_ge(ev("oa"), i + 1)
                        load_z(SEQ, SR)
                    sp.wait_ge(ev("x1"), i + 1)
                    sp.dma_start(S.x1[c:c + T, :], x1[0:T, :]).then_inc(ev("stored"), 16)
                    if i < TILES:
                        sp.wait_ge(ev("xn1"), i + 1)
                        sp.wait_ge(ev("stored"), 16 * (i + 1))
                        load_x(SEQ, SR)
                    sp.wait_ge(ev("xk_a"), i + 1)
                    sp.wait_ge(ev("xk_b"), i + 1)
                    sp.dma_start(S.xnT[:, :, c:c + T], OT[:, :, 0:T]).then_inc(ev("xn_out"), 16)
                load_qkv(0, P)
                load_abk(0, P)
                load_r(0, P)
                load_z(0, P)
                load_x(0, P)
                for i in range(2):
                    during(i, P)
                with sp.Fori(2, TILES - 1) as i:
                    during(i, P)
                during(TILES - 1, SR)
                after(TILES - 1, P)
                sp.wait_ge(ev("state_a"), TILES)
                sp.dma_start(p_gdn[0].rearrange("h d v -> d h v"), St[:, :, :]).then_inc(ev("st_out"), 16)
                sp.dma_start(Sb[:, :, :, :], gdn0.rearrange("b h d v -> d b h v")).then_inc(ev("ld_sb"), 16)
                for b in range(DB):
                    if b >= 2:
                        sp.wait_ge(ev("tb_mm"), b // 2)
                    sp.dma_start(Rb[:, b % 2, :, :].rearrange("v j (h k) -> v (j h) k", h=2),
                                 rwkv0[b].rearrange("h v k -> v h k")).then_inc(ev("ld_rb"), 16)
                sp.wait_ge(ev("tr"), 1)
                for h in range(2):
                    r = slice(64 * h, 64 * h + 64)
                    sp.dma_start(p_rwkv[0].rearrange("(j h) v k -> h v j k", h=2)[h], tr[r, :, r]).then_inc(ev("tr_out"), 16)
                after(TILES, SR)
                for b in range(DB):
                    sp.wait_ge(ev("rb_new"), b + 1)
                    sp.dma_start(s_rwkv[b].rearrange("h v k -> v h k"),
                                 Rb[:, b % 2, :, :].rearrange("v j (h k) -> v (j h) k", h=2)).then_inc(ev(f"rb_out{b % 2}"), 16)
                sp.wait_ge(ev("sb_new"), DB)
                sp.dma_start(s_gdn.rearrange("b h d v -> d b h v"), Sb[:, :, :, :]).then_inc(ev("st_out"), 16)
                sp.wait_ge(ev("st_out"), 16 * 2)
                sp.wait_ge(ev("tr_out"), 16 * 2)
                for m in range(2):
                    sp.wait_ge(ev(f"rb_out{m}"), 16 * DB // 2)
                sp.wait_ge(ev("stored"), 16 * (TILES + 1))
                sp.wait_ge(ev("xn_out"), 16 * (TILES + 1))

            @block.gpsimd
            def _(pool):
                done = Seq(ev("pool_seq"), pool, 8 + 4 * LEVELS)
                done.start(0)
                m4 = ((K.causal, -1.0), (K.strict, 1.0), (K.causal, 1.0), (K.strict, 1.0))
                for n, (m, f) in enumerate(m4):
                    done(pool.tensor_scalar(mask4[:, n, :], m[:, :], f, None, ALU.mult))
                for n, (m, f) in enumerate(((K.causal_s, -1.0), (K.strict_s, 1.0), (K.causal_s, 1.0), (K.strict_s, 1.0))):
                    done(pool.tensor_scalar(mask4s[:, n, :], m[:, :], f, None, ALU.mult))
                for l in range(LEVELS):
                    h = 1 << l
                    nb = P // (2 * h)
                    done(pool.memset(lev[:, l, :], 0.0))
                    v = lev[:, l, :].rearrange("s (b u t) -> s b u t", u=2, t=h)[:, :, 1, :]
                    done(pool.memset(v, 1.0))
                    done(pool.affine_select(out=v, in_=v, compare_op=ALU.is_ge, fill=0.0, base=0,
                                            pattern=[[-2 * h, nb], [0, h]], channel_multiplier=1))
                    done(pool.affine_select(out=v, in_=v, compare_op=ALU.is_ge, fill=0.0, base=h - 1,
                                            pattern=[[2 * h, nb], [0, h]], channel_multiplier=-1))
                done.end()
                pool.sem_inc(ev("masks"), 1)

                def norms(f, T):
                    pool.wait_ge(ev("stats"), f + 1)
                    pool.wait_ge(ev("ob1"), f)
                    pool.tensor_tensor(rstd[0:T, :], st[0:T, :], K.half_neg[0:T, 0:12], ALU.pow).then_inc(ev("rstd"), 1)

                def norm(f, T):
                    pool.wait_ge(ev("n1"), f + 1)
                    pool.tensor_tensor(n1[0:T, 2:3], n1[0:T, 1:2], K.half_neg[0:T, 0:1], ALU.pow).then_inc(ev("n1r"), 1)

                def tile(i, T, levels, last):
                    n = i + 1
                    for l in range(levels):
                        if l == 3 and last is not None:
                            norms(last, P)
                        for u in range(3):
                            if l == 0:
                                pool.wait_ge(ev("nt_a") if u == 0 else ev("sc"), n if u == 0 else 8 * i + 4 * u)
                                pool.wait_ge(ev(f"ymm{u}"), (LEVELS - 1) * i)
                                pool.wait_ge(ev(f"xt1_{u}"), i)
                            elif l == 1:
                                pool.wait_ge(ev(f"xt1_{u}"), n)
                            else:
                                pool.wait_ge(ev(f"ymm{u}"), (LEVELS - 1) * i + l - 1)
                            src = NT[0:T, :, 0:T] if u == 0 else SC[0:T, 4 * (u - 1):4 * u, 1, 0:T]
                            pool.tensor_tensor(M[u][0:T, :, 0:T], src, bc(lev[0:T, l:l + 1, 0:T], [T, 4, T]),
                                               ALU.mult).then_inc(ev(f"m{u}"), 1)
                    pool.wait_ge(ev("ld_z"), 16 * n)
                    z = Z[0:T, :].rearrange("p (h c) -> p h c", h=AH)
                    pool.wait_ge(ev("gnw"), 1)
                    pool.tensor_tensor(z, z, bc(gnw[0:T, :].rearrange("p (a c) -> p a c", a=1), [T, AH, P]),
                                       ALU.mult).then_inc(ev("zw"), 1)
                    pool.wait_ge(ev("vr_b"), n)
                    pool.wait_ge(ev("bo"), n)
                    pool.wait_ge(ev("ob"), i)
                    v8 = lambda t: t[0:T, :].rearrange("p (h c) -> p h c", h=BH)
                    pool.tensor_tensor(v8(bv), v8(Vr), bc(bo[0:T, :].rearrange("p (h a) -> p h a", a=1), [T, BH, 64]),
                                       ALU.mult).then_inc(ev("bv1"), 1)
                    pool.wait_ge(ev("bv1"), n)
                    pool.tensor_tensor(bv[0:T, :], bv[0:T, :], lnb[0:T, :], ALU.add).then_inc(ev("bv2"), 1)
                    pool.wait_ge(ev("bv2"), n)
                    pool.wait_ge(ev("gr"), n)
                    pool.tensor_tensor(bv[0:T, :], bv[0:T, :], Gr[0:T, :], ALU.mult).then_inc(ev("bv"), 1)
                    pool.tensor_tensor(gw[0:T, :], lnw[0:T, :], Gr[0:T, :], ALU.mult).then_inc(ev("gw"), 1)
                    if last is not None:
                        norm(last, P)
                pool.wait_ge(ev("ld_par"), 64)
                for i in range(2):
                    tile(i, P, LEVELS, i - 1 if i else None)
                with pool.Fori(2, TILES) as i:
                    tile(i, P, LEVELS, i - 1)
                norms(TILES - 1, P)
                norm(TILES - 1, P)
                tile(TILES, SR, LEVELS_S, None)
                norms(TILES, SR)
                norm(TILES, SR)

            @block.scalar
            def _(act):
                def end_rows(f, T):
                    act.wait_ge(ev("ot_mm"), f + 1)
                    act.wait_ge(ev("prj"), 2 * f)
                    act.wait_ge(ev("xn_out"), 16 * f)
                    act.activation(OT[:, 0:4, 0:T], v4(6, P, T), ACT.Copy).then_inc(ev("ot"), 1)

                def end_square(f, T):
                    act.wait_ge(ev("x1"), f + 1)
                    act.wait_ge(ev("nt_mm"), f)
                    act.activation(xn[0:T, :], x1[0:T, :], ACT.Square, accum_out=n1[0:T, 0:1]).then_inc(ev("n1s"), 1)

                def end_keep(f, T):
                    act.wait_ge(ev("nt_mm"), f + 1)
                    act.activation(OT[:, 4:8, 0:T], v4(7, P, T), ACT.Copy).then_inc(ev("xk_b"), 1)

                def tile(i, T, levels, last):
                    n = i + 1
                    act.wait_ge(ev("gB"), i)
                    act.wait_ge(ev("gcol_mm"), i)
                    act.activation(ld[:, :], K.logd[:, bass.ds(i, 1), :].rearrange("p a h -> p (a h)"), ACT.Copy).then_inc(ev("ldc"), 1)
                    act.wait_ge(ev("nv"), i)
                    act.wait_ge(ev("nt_a"), i)
                    act.activation(bt[:, :], K.beta[:, bass.ds(i, 1), :].rearrange("p a h -> p (a h)"), ACT.Copy).then_inc(ev("bt"), 1)
                    act.activation(nbt[:, :], K.beta[:, bass.ds(i, 1), :].rearrange("p a h -> p (a h)"), ACT.Copy,
                                   scale=-1.0).then_inc(ev("bt"), 1)
                    act.wait_ge(ev("bv1"), i)
                    act.activation(bo[:, :], K.bonus[:, bass.ds(i, 1), :].rearrange("p a h -> p (a h)"), ACT.Copy).then_inc(ev("bo"), 1)
                    act.wait_ge(ev("gcol_mm"), n)
                    act.wait_ge(ev("dm"), i)
                    act.activation(g[0:T, :], bank[1][0:T, 0:AH], ACT.Copy).then_inc(ev("g"), 1)
                    act.wait_ge(ev("wr"), i)
                    act.activation(eg[0:T, :], bank[1][0:T, 0:AH], ACT.Exp).then_inc(ev("eg"), 1)
                    act.wait_ge(ev("dm"), n)
                    act.wait_ge(ev("attn"), i)
                    act.activation(dec[0:T, :, 0:T], dec[0:T, :, 0:T], ACT.Exp).then_inc(ev("dec"), 1)
                    act.wait_ge(ev("state_a"), i)
                    act.activation(eGB[:, :, 0:T], v4(0, P, T), ACT.Exp).then_inc(ev("egb"), 1)
                    act.wait_ge(ev("rows_a"), n)
                    act.wait_ge(ev("upd_a"), i)
                    act.activation(kr[0:T, :, :], v4(4, T), ACT.Copy).then_inc(ev("kr"), 1)
                    act.wait_ge(ev("rows_b"), n)
                    act.wait_ge(ev("upd_b"), i)
                    act.activation(Br[0:T, :], bank[6][0:T, :], ACT.Copy, scale=-1.0).then_inc(ev("br"), 1)
                    act.wait_ge(ev("rows_vg"), n)
                    act.wait_ge(ev("bv1"), i)
                    act.activation(Vr[0:T, :], bank[0][0:T, :], ACT.Copy).then_inc(ev("vr_b"), 1)
                    for l in range(levels):
                        for u in range(3):
                            b = 2 * u
                            if l == 0:
                                act.wait_ge(ev(f"x1mm{u}"), n)
                                act.activation(X[u][0:T, :, 0:T], v4(b, T, T), ACT.Copy).then_inc(ev(f"xk{u}"), 1)
                            else:
                                act.wait_ge(ev(f"ymm{u}"), (LEVELS - 1) * i + l)
                                w = P // 2 if l == LEVELS - 1 else T
                                act.activation(Y[u][0:T, :, 0:w], v4(b, T, w), ACT.Copy).then_inc(ev(f"y{u}"), 1)
                        if last is not None and l == 3:
                            end_rows(last, P)
                        if last is not None and l == 6:
                            end_square(last, P)
                    act.wait_ge(ev("sa_mm"), n)
                    act.activation(SA[0:T, :], bank[2][0:T, :], ACT.Copy).then_inc(ev("sa"), 1)
                    act.wait_ge(ev("out_a"), n)
                    act.wait_ge(ev("suma"), i)
                    act.wait_ge(ev("ot_mm"), i)
                    act.activation(sqa[0:T, :], bank[1][0:T, :], ACT.Square).then_inc(ev("sqa"), 1)
                    act.activation(OR[0:T, 0:AKEY], bank[1][0:T, :], ACT.Copy).then_inc(ev("raw"), 1)
                    act.wait_ge(ev("cent"), n)
                    act.wait_ge(ev("sumb"), i)
                    act.activation(sqb[0:T, :], OR[0:T, AKEY:D], ACT.Square).then_inc(ev("sqb"), 1)
                    if last is not None:
                        end_keep(last, P)
                for i in range(2):
                    tile(i, P, LEVELS, i - 1 if i else None)
                with act.Fori(2, TILES) as i:
                    tile(i, P, LEVELS, i - 1)
                for i, T in ((TILES - 1, P), (TILES, SR)):
                    if i == TILES:
                        tile(i, T, LEVELS_S, None)
                    end_rows(i, T)
                    end_square(i, T)
                    end_keep(i, T)
                for b in range(DB):
                    if b == 0:
                        act.wait_ge(ev("xk_b"), TILES + 1)
                    act.wait_ge(ev("upd_s"), b)
                    row = K.same[:, b * DS:b * DS + 1]
                    act.activation(Wr[0:SR, :, :], NVd[0:SR, :, :], ACT.Copy, scale=row).then_inc(ev("pick"), 1)
                    act.activation(RH[0:SR, :], SA[0:SR, :], ACT.Copy, scale=row).then_inc(ev("pick"), 1)
                    act.activation(sqa[0:SR, :], Vr[0:SR, :], ACT.Copy, scale=row).then_inc(ev("pick"), 1)
                    act.wait_ge(ev("rb_mm"), b + 1)
                    if b >= 2:
                        act.wait_ge(ev(f"rb_out{b % 2}"), 16 * (b // 2))
                    act.activation(Rb[:, b % 2, :, :], bank[6][0:64, :].rearrange("v (j c) -> v j c", j=NP), ACT.Copy).then_inc(ev("rb_new"), 1)

            @block.vector
            def _(dve):
                def spread(half):
                    for r in range(AH + BH):
                        k = (AH + BH) * half + r
                        j = (r - AH) // 2
                        if half == 0:
                            src = QK[:, 1, r, 0:SR] if r < AH else RW[:, 1, j, 0:SR]
                        else:
                            src = QG[:, r, 0:SR] if r < AH else RW[:, 0, j, 0:SR]
                        if k > 0:
                            dve.wait_ge(ev("q1_used"), k)
                        keep = K.ones[:, 0:1] if r < AH else K.head_cols[:, (r - AH) % 2:(r - AH) % 2 + 1]
                        dve.scalar_tensor_tensor(out=Q1[:, :, :], in0=bc(src.rearrange("p (a t) -> p a t", a=1), [P, DB, SR]),
                                                 scalar=keep, in1=K.batch_cols[:, :, :], op0=ALU.mult,
                                                 op1=ALU.mult).then_inc(ev("q1"), 1)

                dve.memset(St[:, :, :], 0.0).then_inc(ev("init"), 1)
                dve.memset(Tt[:, :, :], 0.0).then_inc(ev("init"), 1)
                dve.wait_ge(ev("ld_par"), 64)
                dve.tensor_scalar(gnw[:, :], gnw[:, :], 0.5, None, ALU.mult).then_inc(ev("gnw"), 1)
                dve.wait_ge(ev("init"), 2)
                dve.wait_ge(ev("masks"), 1)

                v8 = lambda t: t.rearrange("p (h c) -> p h c", h=BH)
                wide = lambda t, T, w: bc(t.rearrange("p (h a) -> p h a", a=1), [T, t.shape[1], w])

                def end_sums(f, T):
                    n = f + 1
                    dve.wait_ge(ev("sqa"), n)
                    dve.tensor_reduce(st[0:T, 0:4], sqa[0:T, :].rearrange("p (h c) -> p h c", h=AH), AX_X, ALU.add).then_inc(ev("suma"), 1)
                    dve.wait_ge(ev("sqb"), n)
                    dve.tensor_reduce(st[0:T, 4:12], v8(sqb[0:T, :]), AX_X, ALU.add).then_inc(ev("sumb"), 1)
                    dve.wait_ge(ev("suma"), n)
                    dve.tensor_scalar(st[0:T, 0:4], st[0:T, 0:4], 1.0 / P, EPS, ALU.mult, ALU.add).then_inc(ev("st1"), 1)
                    dve.wait_ge(ev("sumb"), n)
                    dve.tensor_scalar(st[0:T, 4:12], st[0:T, 4:12], 1.0 / 64, B_GN_EPS, ALU.mult, ALU.add).then_inc(ev("stats"), 1)

                def end_gate(f, T):
                    n = f + 1
                    dve.wait_ge(ev("rstd"), n)
                    dve.wait_ge(ev("raw"), n)
                    oa = OR[0:T, 0:AKEY].rearrange("p (h c) -> p h c", h=AH)
                    dve.tensor_tensor(oa, oa, wide(rstd[0:T, 0:4], T, P), ALU.mult).then_inc(ev("oa1"), 1)
                    ob = v8(OR[0:T, AKEY:D])
                    dve.tensor_tensor(ob, ob, wide(rstd[0:T, 4:12], T, 64), ALU.mult).then_inc(ev("ob1"), 1)
                    dve.wait_ge(ev("oa1"), n)
                    dve.wait_ge(ev("zw"), n)
                    dve.tensor_tensor(OR[0:T, 0:AKEY], OR[0:T, 0:AKEY], Z[0:T, :], ALU.mult).then_inc(ev("oa"), 1)
                    o = OR[0:T, AKEY:D]
                    dve.wait_ge(ev("ob1"), n)
                    dve.wait_ge(ev("gw"), n)
                    dve.tensor_tensor(o, o, gw[0:T, :], ALU.mult).then_inc(ev("ob2"), 1)
                    dve.wait_ge(ev("ob2"), n)
                    dve.wait_ge(ev("bv"), n)
                    dve.tensor_tensor(o, o, bv[0:T, :], ALU.add).then_inc(ev("ob"), 1)

                def end_rows(f, T):
                    dve.wait_ge(ev("ot_mm"), f + 1)
                    dve.wait_ge(ev("prj"), 2 * f)
                    dve.wait_ge(ev("xn_out"), 16 * f)
                    dve.tensor_copy(OT[:, 4:8, 0:T], v4(7, P, T)).then_inc(ev("ot2"), 1)

                def end_add(f, T):
                    for c in range(2):
                        dve.wait_ge(ev("prj"), 2 * f + c + 1)
                        if c == 0:
                            dve.wait_ge(ev("ld_x"), 16 * (f + 1))
                        ins = dve.tensor_tensor(x1[0:T, 512 * c:512 * c + 512], bank[6 + c][0:T, :], XR[0:T, 512 * c:512 * c + 512], ALU.add)
                    ins.then_inc(ev("x1"), 1)

                def end_norm(f, T):
                    dve.wait_ge(ev("n1s"), f + 1)
                    dve.tensor_scalar(n1[0:T, 1:2], n1[0:T, 0:1], 1.0 / D, EPS, ALU.mult, ALU.add).then_inc(ev("n1"), 1)
                    dve.wait_ge(ev("n1r"), f + 1)
                    dve.wait_ge(ev("nt_mm"), f)
                    dve.scalar_tensor_tensor(out=xn[0:T, :], in0=x1[0:T, :], scalar=n1[0:T, 2:3], in1=nw[0:T, :],
                                             op0=ALU.mult, op1=ALU.mult).then_inc(ev("xn1"), 1)

                def end_keep(f, T):
                    dve.wait_ge(ev("nt_mm"), f + 1)
                    dve.tensor_copy(OT[:, 0:4, 0:T], v4(6, P, T)).then_inc(ev("xk_a"), 1)

                def center(i, T):
                    n = i + 1
                    dve.wait_ge(ev("out_b"), n)
                    dve.tensor_reduce(mean[0:T, :], v8(bank[3][0:T, :]), AX_X, ALU.add).then_inc(ev("mean"), 1)
                    dve.wait_ge(ev("mean"), n)
                    dve.wait_ge(ev("ot_mm"), i)
                    dve.scalar_tensor_tensor(out=v8(OR[0:T, AKEY:D]), in0=wide(mean[0:T, :], T, 64), scalar=-1.0 / 64,
                                             in1=v8(bank[3][0:T, :]), op0=ALU.mult, op1=ALU.add).then_inc(ev("cent"), 1)

                def tile(i, T, levels, mask, lmask, last):
                    n = i + 1
                    dve.wait_ge(ev("gB"), n)
                    dve.wait_ge(ev("g"), n)
                    dve.wait_ge(ev("attn"), i)
                    for h in range(AH):
                        ins = dve.scalar_tensor_tensor(out=dec[0:T, h, 0:T], in0=v4(0, T, T)[:, h, :], scalar=g[0:T, h:h + 1],
                                                       in1=lmask[0:T, 0:T], op0=ALU.subtract, op1=ALU.min)
                    ins.then_inc(ev("dm"), 1)
                    if T == P:
                        dve.wait_ge(ev("out_b"), i)
                        dve.wait_ge(ev("rhs_b"), i)
                        dve.wait_ge(ev("state_b"), i)
                        dve.tensor_tensor(Th[:, :, :], Tt[:, :, :], bc(K.rw_in[:, :, bass.ds(i, 1)], [P, NP, P]),
                                          ALU.mult).then_inc(ev("th"), 1)
                    dve.wait_ge(ev("dec"), n)
                    dve.wait_ge(ev("kkqk"), n)
                    dve.wait_ge(ev("bt"), 2 * n)
                    dve.wait_ge(ev("m0"), LEVELS * i)
                    dve.wait_ge(ev("out_a"), i)
                    for h in range(AH):
                        b = v4(2 + h // 2, T, T)
                        ins = dve.scalar_tensor_tensor(out=NT[0:T, h, 0:T], in0=b[:, 2 * (h % 2) + 1, :], scalar=bt[0:T, h:h + 1],
                                                       in1=dec[0:T, h, 0:T], op0=ALU.mult, op1=ALU.mult)
                    ins.then_inc(ev("nt_a"), 1)
                    for h in range(0, AH, 2):
                        b = v4(2 + h // 2, T, T)
                        ins = dve.tensor_tensor(attn[0:T, h:h + 2, 0:T], b[:, 0::2, :], dec[0:T, h:h + 2, 0:T], ALU.mult)
                    ins.then_inc(ev("attn"), 1)
                    dve.wait_ge(ev("egb"), n)
                    dve.tensor_tensor(QG[:, :, 0:T], QK[:, 0, :, 0:T], eGB[:, :, 0:T], ALU.mult).then_inc(ev("qg"), 1)
                    if T == P:
                        dve.wait_ge(ev("nvd"), i)
                        dve.tensor_copy(dend[:, :], dec[:, :, P - 1]).then_inc(ev("dend"), 1)
                    else:
                        dve.wait_ge(ev("w_mm"), i)
                        dve.tensor_tensor(Wr[0:T, :, 0:T], dec[0:T, :, 0:T], bc(K.last[:, :].rearrange("s (a t) -> s a t", a=1),
                                                                                [T, AH, T]), ALU.mult).then_inc(ev("dend_m"), 1)
                        dve.wait_ge(ev("dend_m"), 1)
                        dve.tensor_reduce(dend[0:T, :], Wr[0:T, :, 0:T], AX_X, ALU.add).then_inc(ev("dend"), 1)
                    dve.wait_ge(ev("rows_a"), n)
                    dve.wait_ge(ev("wr"), i)
                    dve.tensor_copy(vr[0:T, :, :], v4(5, T)).then_inc(ev("vr_a"), 1)
                    dve.wait_ge(ev("rows_b"), n)
                    dve.wait_ge(ev("upd_b"), i)
                    dve.tensor_copy(Kr[0:T, :], bank[7][0:T, :]).then_inc(ev("krr"), 1)
                    for h in range(BH):
                        dve.wait_ge(ev("score"), 8 * i + h + 1)
                        if h == 0:
                            dve.wait_ge(ev("m1"), LEVELS * i)
                            dve.wait_ge(ev("m2"), LEVELS * i)
                            dve.wait_ge(ev("out_b"), i)
                        dve.tensor_tensor(SC[0:T, h, :, 0:T], v4(2 + h % 6, T, T), mask[0:T, :, 0:T],
                                          ALU.mult).then_inc(ev("sc"), 1)
                    dve.wait_ge(ev("rows_vg"), n)
                    dve.wait_ge(ev("gw"), i)
                    dve.wait_ge(ev("bv"), i)
                    dve.tensor_scalar(Gr[0:T, :], bank[1][0:T, :], 0.5, None, ALU.mult).then_inc(ev("gr"), 1)
                    for u in range(3):
                        dve.wait_ge(ev(f"m{u}"), LEVELS * i + 1)
                        dve.wait_ge(ev("w_mm" if u == 0 else "sa_mm"), i)
                        dve.tensor_tensor(XT[u][0:T, :, 0:T], bc(K.ident[0:T, 0:T].rearrange("p (a c) -> p a c", a=1), [T, 4, T]),
                                          M[u][0:T, :, 0:T], ALU.subtract).then_inc(ev(f"xt1_{u}"), 1)
                    if T != P:
                        spread(0)
                    dve.wait_ge(ev("rhs_a"), n)
                    dve.wait_ge(ev("eg"), n)
                    dve.wait_ge(ev("w_mm"), i)
                    dve.wait_ge(ev("vr_a"), n)
                    for h in range(AH):
                        ins = dve.scalar_tensor_tensor(out=Wr[0:T, h, :], in0=v4(6, T)[:, h, :], scalar=eg[0:T, h:h + 1],
                                                       in1=vr[0:T, h, :], op0=ALU.mult, op1=ALU.subtract)
                    ins.then_inc(ev("wr"), 1)
                    dve.wait_ge(ev("rhs_b"), n)
                    dve.wait_ge(ev("sa_mm"), i)
                    dve.tensor_copy(RH[0:T, :], bank[7][0:T, :]).then_inc(ev("rh"), 1)
                    for l in range(1, levels):
                        for u in range(3):
                            if l < levels - 1:
                                dve.wait_ge(ev(f"zmm{u}"), (2 * LEVELS - 3) * i + 2 * l - 1)
                                if l == 1:
                                    dve.wait_ge(ev(f"xk{u}"), n)
                                dve.wait_ge(ev(f"xd{u}"), (2 * LEVELS - 3) * i + 2 * l - 2)
                                x = half(X[u][0:T, :, :], l, T, 0)
                                dve.tensor_tensor(x, x, packed(2 * u + 1, l, T, T), ALU.subtract).then_inc(ev(f"xd{u}"), 1)
                                dve.wait_ge(ev(f"zmm{u}"), (2 * LEVELS - 3) * i + 2 * l)
                                xt = half(XT[u][0:T, :, :], l, T, 1)
                                dve.tensor_tensor(xt, xt, packed(2 * u, l, T, T), ALU.subtract).then_inc(ev(f"xd{u}"), 1)
                            else:
                                dve.wait_ge(ev(f"zmm{u}"), (2 * LEVELS - 3) * i + 2 * l - 1)
                                dve.wait_ge(ev(f"xd{u}"), (2 * LEVELS - 3) * i + 2 * l - 2)
                                r = P // 2 if l == LEVELS - 1 else T
                                xt = half(XT[u][0:r, :, :], l, T, 1)
                                dve.tensor_tensor(xt, xt, packed(2 * u, l, T, r), ALU.subtract).then_inc(ev(f"xd{u}"), 1)
                        if last is not None:
                            if l == 1:
                                end_sums(last, P)
                            if l == 2:
                                end_gate(last, P)
                            if l == 3:
                                end_rows(last, P)
                            if l == 5:
                                end_add(last, P)
                    dve.wait_ge(ev("w_mm"), n)
                    dve.wait_ge(ev("out_a"), i)
                    dve.tensor_tensor(NV[0:T, :, :], v4(0, T), bc(nbt[0:T, :].rearrange("p (h a) -> p h a", a=1), [T, AH, P]),
                                      ALU.mult).then_inc(ev("nv"), 1)
                    dve.wait_ge(ev("nv"), n)
                    dve.wait_ge(ev("dend"), n)
                    dve.wait_ge(ev("upd_a"), i)
                    dve.tensor_tensor(NVd[0:T, :, :], NV[0:T, :, :], bc(dend[0:T, :].rearrange("p (h a) -> p h a", a=1),
                                                                        [T, AH, P]), ALU.mult).then_inc(ev("nvd"), 1)
                    if last is not None:
                        end_norm(last, P)
                    if T != P:
                        spread(1)
                    center(i, T)

                def whole_tile(i, last):
                    n = i + 1
                    tile(i, P, LEVELS, mask4, K.lcausal, last)
                    dve.wait_ge(ev("upd_a"), n)
                    for h in range(AH):
                        ins = dve.scalar_tensor_tensor(out=St[:, h, :], in0=St[:, h, :], scalar=eGB[:, h, P - 1:P],
                                                       in1=v4(4)[:, h, :], op0=ALU.mult, op1=ALU.add)
                    ins.then_inc(ev("state_a"), 1)
                    dve.wait_ge(ev("upd_b"), n)
                    for h in range(2):
                        r = slice(64 * h, 64 * h + 64)
                        ins = dve.tensor_tensor(Tt[r, :, r], Th[r, :, r], v4(5)[r, :, r], ALU.add)
                    ins.then_inc(ev("tt1"), 1)
                    dve.wait_ge(ev("tt1"), n)
                    dve.tensor_tensor(Tt[:, :, :], Tt[:, :, :], bc(K.rw_out[:, :, bass.ds(i, 1)], [P, NP, P]),
                                      ALU.mult).then_inc(ev("state_b"), 1)
                    if last is not None:
                        end_keep(last, P)

                def end(f, T):
                    end_sums(f, T)
                    end_gate(f, T)
                    end_rows(f, T)
                    end_add(f, T)
                    end_norm(f, T)
                    end_keep(f, T)
                for i in range(2):
                    whole_tile(i, i - 1 if i else None)
                with dve.Fori(2, TILES) as i:
                    whole_tile(i, i - 1)
                end(TILES - 1, P)
                dve.wait_ge(ev("tr_mm"), 1)
                dve.tensor_copy(tr[:, :, :], v4(4)).then_inc(ev("tr"), 1)
                for r in range(4):
                    dve.wait_ge(ev("tb_mm"), r + 1)
                    dve.tensor_copy(Tb[:, 2 * r:2 * r + 2, :, :], bank[6 + r % 2][:, :].rearrange("p (b j v) -> p b j v", b=2, j=NP)
                                    ).then_inc(ev("tb"), 1)
                dve.wait_ge(ev("ld_sb"), 16)
                dve.wait_ge(ev("tr_out"), 32)
                tile(TILES, SR, LEVELS_S, mask4s, K.lcausal_s, None)
                end(TILES, SR)
                for b in range(DB):
                    dve.wait_ge(ev("upd_s"), b + 1)
                    for h in range(AH):
                        dve.scalar_tensor_tensor(out=Sb[:, b, h, :], in0=Sb[:, b, h, :], scalar=eGB[:, h, b * DS + DS - 1:(b + 1) * DS],
                                                 in1=v4(4)[:, h, :], op0=ALU.mult, op1=ALU.add).then_inc(ev("sb_step"), 1)
                    dve.wait_ge(ev("sb_step"), AH * (b + 1))
                    dve.tensor_tensor(Tb[:, b, :, :], Tb[:, b, :, :], bank[5][:, 0:256].rearrange("p (j v) -> p j v", j=NP),
                                      ALU.add).then_inc(ev("tb1"), 1)
                    dve.wait_ge(ev("tb1"), b + 1)
                    dve.sem_inc(ev("sb_new"), 1)
                    dve.tensor_tensor(Tb[:, b, :, :], Tb[:, b, :, :], bc(K.rw_out[:, :, TILES + b:TILES + b + 1], [P, NP, 64]),
                                      ALU.mult).then_inc(ev("tb_new"), 1)

            @block.tensor
            def _(pe):
                def end_rows(f, T, used):
                    pe.wait_ge(ev("oa"), f + 1)
                    pe.wait_ge(ev("ob"), f + 1)
                    pe.wait_ge(ev("wr"), used)
                    pe.wait_ge(ev("rh"), used)
                    for c in range(KT):
                        mm = pe.transpose(v4(6 + c // 4, P, T)[:, c % 4, :], OR[0:T, c * P:(c + 1) * P], K.ident[0:T, 0:T])
                    mm.then_inc(ev("ot_mm"), 1)

                def end_project(f, T, c):
                    if c == 0:
                        pe.wait_ge(ev("ot"), f + 1)
                        pe.wait_ge(ev("ot2"), f + 1)
                    for kt in range(KT):
                        mm = pe.matmul(bank[6 + c][0:T, :], OT[:, kt, 0:T], wo[:, kt, 512 * c:512 * c + 512],
                                       start=(kt == 0), stop=(kt == KT - 1))
                    mm.then_inc(ev("prj"), 1)

                def end_norm(f, T):
                    pe.wait_ge(ev("xn1"), f + 1)
                    for c in range(KT):
                        mm = pe.transpose(v4(6 + c // 4, P, T)[:, c % 4, :], xn[0:T, c * P:(c + 1) * P], K.ident[0:T, 0:T])
                    mm.then_inc(ev("nt_mm"), 1)

                def tile(i, T, levels, ks, kd, last):
                    n = i + 1
                    pe.wait_ge(ev("ldc"), n)
                    pe.wait_ge(ev("nv"), i)
                    pe.wait_ge(ev("sqa"), i)
                    pe.wait_ge(ev("raw"), i)
                    pe.wait_ge(ev("cent"), i)
                    caus = K.causal if T == P else K.causal_s
                    for h in range(AH):
                        mm = pe.matmul(v4(0, P, T)[:, h, :], ld[0:T, h:h + 1].broadcast_to([T, P]), caus[0:T, 0:T], start=True, stop=True)
                    mm.then_inc(ev("gB"), 1)
                    pe.matmul(bank[1][0:T, 0:AH], caus[0:T, 0:T], ld[0:T, :], start=True, stop=True).then_inc(ev("gcol_mm"), 1)
                    pe.wait_ge(ev("ld_qk"), 32 * n)
                    for h in range(AH):
                        o = v4(2 + h // 2, T, T)[:, 2 * (h % 2):2 * (h % 2) + 2, :]
                        mm = pe.matmul(o, QK[:, 1, h, 0:T], QK[:, :, h, 0:T], start=True, stop=True)
                    mm.then_inc(ev("kkqk"), 1)
                    pe.wait_ge(ev("state_a"), i)
                    pe.wait_ge(ev("state_b"), i)
                    pe.wait_ge(ev("ld_v"), 16 * n)
                    for h in range(AH):
                        pe.transpose(v4(4, T)[:, h, :], QK[:, 1, h, 0:T], K.ident[:, :])
                        mm = pe.transpose(v4(5, T)[:, h, :], V[:, h, 0:T], K.ident[:, :])
                    mm.then_inc(ev("rows_a"), 1)
                    kept = i if T != P else 0 if isinstance(i, int) and i == 0 else i - 1
                    pe.wait_ge(ev("xk_a"), kept)
                    pe.wait_ge(ev("xk_b"), kept)
                    pe.wait_ge(ev("ld_rw"), 48 * n)
                    pe.wait_ge(ev("ld_r"), 16 * n)
                    for j in range(NP):
                        pe.transpose(v4(6, T)[:, j, :], RW[:, 2, j, 0:T], K.ident[:, :])
                        mm = pe.transpose(v4(7, T)[:, j, :], RW[:, 3, j, 0:T], K.ident[:, :])
                    mm.then_inc(ev("rows_b"), 1)
                    for h in range(BH):
                        if h == 0:
                            pe.wait_ge(ev("attn"), n)
                        if h == 2:
                            pe.wait_ge(ev("kr"), n)
                        if h == 3:
                            pe.wait_ge(ev("vr_a"), n)
                        if h == 4:
                            pe.wait_ge(ev("br"), n)
                        if h == 5:
                            pe.wait_ge(ev("krr"), n)
                        if h >= 6:
                            pe.wait_ge(ev("sc"), 8 * i + h - 5)
                        r = slice(64 * (h % 2), 64 * (h % 2) + 64)
                        o = v4(2 + h % 6, T, T)
                        pe.matmul(o[:, 0:2, :], RW[r, 2, h // 2, 0:T], RW[r, 0:2, h // 2, 0:T], start=True, stop=True)
                        pe.matmul(o[:, 2:4, :], RW[r, 3, h // 2, 0:T], RW[r, 0:2, h // 2, 0:T], start=True, stop=True
                                  ).then_inc(ev("score"), 1)
                    pe.wait_ge(ev("egb"), n)
                    pe.wait_ge(ev("eg"), n)
                    pe.wait_ge(ev("ld_vg"), 32 * n)
                    for j in range(NP):
                        pe.transpose(v4(0, T)[:, j, :], VG[:, 0, j, 0:T], K.ident[:, :])
                        mm = pe.transpose(v4(1, T)[:, j, :], VG[:, 1, j, 0:T], K.ident[:, :])
                    mm.then_inc(ev("rows_vg"), 1)
                    pe.wait_ge(ev("sc"), 8 * i + 5)
                    ks(6)
                    pe.wait_ge(ev("vr_b"), n)
                    if T == P:
                        pe.wait_ge(ev("th"), n)
                    pe.wait_ge(ev("sc"), 8 * n)
                    kd(7)
                    pe.wait_ge(ev("gr"), n)
                    for u in range(3):
                        pe.wait_ge(ev(f"xt1_{u}"), n)
                        for k in range(4):
                            mm = pe.transpose(v4(2 * u, T, T)[:, k, :], XT[u][0:T, k, 0:T], K.ident[0:T, 0:T])
                        mm.then_inc(ev(f"x1mm{u}"), 1)
                    for l in range(1, levels):
                        for u in range(3):
                            if l == 1:
                                pe.wait_ge(ev(f"xk{u}"), n)
                            else:
                                pe.wait_ge(ev(f"xd{u}"), (2 * LEVELS - 3) * i + 2 * l - 2)
                            pe.wait_ge(ev(f"m{u}"), LEVELS * i + l + 1)
                            for k in range(4):
                                w = P // 2 if l == LEVELS - 1 else T
                                mm = pe.matmul(v4(2 * u, T, w)[:, k, :], M[u][0:T, k, 0:T], X[u][0:T, k, 0:w], start=True, stop=True)
                            mm.then_inc(ev(f"ymm{u}"), 1)
                        for u in range(3):
                            pe.wait_ge(ev(f"y{u}"), (LEVELS - 1) * i + l)
                            if l < levels - 1:
                                for k in range(4):
                                    mm = pe.matmul(packed(2 * u + 1, l, T, T)[:, k], XT[u][0:T, k, 0:T], half(Y[u][0:T, k, :], l, T, 0), start=True, stop=True)
                                mm.then_inc(ev(f"zmm{u}"), 1)
                            r = P // 2 if l == LEVELS - 1 else T
                            for k in range(4):
                                mm = pe.matmul(packed(2 * u, l, T, r)[:, k], Y[u][0:T, k, 0:r], half(XT[u][0:T, k, :], l, T, 1), start=True, stop=True)
                            mm.then_inc(ev(f"zmm{u}"), 1)
                        if last is not None and l == 3:
                            end_rows(last, P, n)
                        if last is not None and l in (4, 5):
                            end_project(last, P, l - 4)
                    pe.wait_ge(ev("xd0"), (2 * LEVELS - 3) * i + 2 * levels - 3)
                    pe.wait_ge(ev("wr"), n)
                    for h in range(AH):
                        mm = pe.matmul(v4(0, T)[:, h, :], XT[0][0:T, h, 0:T], Wr[0:T, h, :], start=True, stop=True)
                    mm.then_inc(ev("w_mm"), 1)
                    pe.wait_ge(ev("xd1"), (2 * LEVELS - 3) * i + 2 * levels - 3)
                    pe.wait_ge(ev("xd2"), (2 * LEVELS - 3) * i + 2 * levels - 3)
                    pe.wait_ge(ev("rh"), n)
                    for h in range(BH):
                        mm = pe.matmul(bank[2][0:T, 64 * h:64 * h + 64], XT[1 + h // 4][0:T, h % 4, 0:T],
                                       RH[0:T, 64 * h:64 * h + 64], start=True, stop=True)
                    mm.then_inc(ev("sa_mm"), 1)

                def end(f, T):
                    pe.wait_ge(ev("xk_a"), f)
                    pe.wait_ge(ev("xk_b"), f)
                    end_rows(f, T, f + 1)
                    end_project(f, T, 0)
                    end_project(f, T, 1)
                    end_norm(f, T)

                pe.wait_ge(ev("ld_wo"), 16)
                pe.wait_ge(ev("init"), 2)

                def whole_tile(i, last):
                    n = i + 1

                    def ks(b):
                        for h in range(AH):
                            mm = pe.matmul(v4(b)[:, h, :], QK[:, 1, h, :], St[:, h, :], start=True, stop=True)
                        mm.then_inc(ev("rhs_a"), 1)

                    def kd(b):
                        for j in range(NP):
                            pe.matmul(v4(b)[:, j, :], RW[:, 1, j, :], Th[:, j, :], start=(j == 0), stop=False, skip_group_check=True)
                            for h in (2 * j, 2 * j + 1):
                                mm = pe.matmul(bank[b][:, 64 * h:64 * h + 64], SC[:, h, 3, :], Vr[:, 64 * h:64 * h + 64],
                                               start=False, stop=(h == BH - 1), skip_group_check=True)
                        mm.then_inc(ev("rhs_b"), 1)
                    tile(i, P, LEVELS, ks, kd, last)
                    pe.wait_ge(ev("nv"), n)
                    pe.wait_ge(ev("qg"), n)
                    for h in range(AH):
                        pe.matmul(v4(1)[:, h, :], QG[:, h, :], St[:, h, :], start=True, stop=False)
                        mm = pe.matmul(v4(1)[:, h, :], attn[:, h, :], NV[:, h, :], start=False, stop=True)
                    mm.then_inc(ev("out_a"), 1)
                    pe.wait_ge(ev("sa"), n)
                    for j in range(NP):
                        pe.matmul(v4(3)[:, j, :], RW[:, 0, j, :], Th[:, j, :], start=(j == 0), stop=False, skip_group_check=True)
                        for h in (2 * j, 2 * j + 1):
                            o = bank[3][:, 64 * h:64 * h + 64]
                            pe.matmul(o, SC[:, h, 0, :], SA[:, 64 * h:64 * h + 64], start=False, stop=False, skip_group_check=True)
                            mm = pe.matmul(o, SC[:, h, 2, :], Vr[:, 64 * h:64 * h + 64], start=False, stop=(h == BH - 1), skip_group_check=True)
                    mm.then_inc(ev("out_b"), 1)
                    pe.wait_ge(ev("nvd"), n)
                    pe.wait_ge(ev("kr"), n)
                    for h in range(AH):
                        mm = pe.matmul(v4(4)[:, h, :], kr[:, h, :], NVd[:, h, :], start=True, stop=True)
                    mm.then_inc(ev("upd_a"), 1)
                    for j in range(NP):
                        c = slice(j * P, (j + 1) * P)
                        pe.matmul(v4(5)[:, j, :], Br[:, c], SA[:, c], start=True, stop=False)
                        mm = pe.matmul(v4(5)[:, j, :], Kr[:, c], Vr[:, c], start=False, stop=True)
                    mm.then_inc(ev("upd_b"), 1)
                    if last is not None:
                        end_norm(last, P)
                for i in range(2):
                    whole_tile(i, i - 1 if i else None)
                with pe.Fori(2, TILES) as i:
                    whole_tile(i, i - 1)
                end(TILES - 1, P)
                pe.wait_ge(ev("state_b"), TILES)
                for j in range(NP):
                    mm = pe.transpose(v4(4)[:, j, :], Tt[:, j, :], K.ident[:, :])
                mm.then_inc(ev("tr_mm"), 1)
                pe.wait_ge(ev("xk_a"), TILES)
                pe.wait_ge(ev("xk_b"), TILES)
                for r in range(4):
                    pe.wait_ge(ev("ld_rb"), 32 * (r + 1))
                    if r >= 2:
                        pe.wait_ge(ev("tb"), r - 1)
                    for b in range(2):
                        for j in range(NP):
                            o = bank[6 + r % 2][:, b * 256 + j * 64:b * 256 + j * 64 + 64]
                            mm = pe.transpose(o, Rb[:, b, j, :], K.ident[0:64, 0:64])
                    mm.then_inc(ev("tb_mm"), 1)
                pe.wait_ge(ev("tb"), 4)
                pe.wait_ge(ev("tr"), 1)

                def ks_s(bk):
                    for h in range(AH):
                        pe.wait_ge(ev("q1"), h + 1)
                        for b in range(DB):
                            mm = pe.matmul(v4(bk, SR)[:, h, :], Q1[:, b, :], Sb[:, b, h, :], start=(b == 0), stop=(b == DB - 1))
                        mm.then_inc(ev("q1_used"), 1)
                        pe.wait_ge(ev("q1_used"), h + 1)
                    pe.sem_inc(ev("rhs_a"), 1)

                def kd_s(bk):
                    for h in range(BH):
                        pe.wait_ge(ev("q1"), AH + h + 1)
                        o = bank[bk][0:SR, 64 * h:64 * h + 64]
                        pe.matmul(o, SC[0:SR, h, 3, 0:SR], Vr[0:SR, 64 * h:64 * h + 64], start=True, stop=False)
                        for b in range(DB):
                            mm = pe.matmul(o, Q1[:, b, :], Tb[:, b, h // 2, :], start=False, stop=(b == DB - 1))
                        mm.then_inc(ev("q1_used"), 1)
                        pe.wait_ge(ev("q1_used"), AH + h + 1)
                    pe.sem_inc(ev("rhs_b"), 1)
                tile(TILES, SR, LEVELS_S, ks_s, kd_s, None)
                pe.wait_ge(ev("nv"), TILES + 1)
                for h in range(AH):
                    pe.matmul(v4(1, SR)[:, h, :], attn[0:SR, h, 0:SR], NV[0:SR, h, :], start=True, stop=False)
                    pe.wait_ge(ev("q1"), AH + BH + h + 1)
                    for b in range(DB):
                        mm = pe.matmul(v4(1, SR)[:, h, :], Q1[:, b, :], Sb[:, b, h, :], start=False, stop=(b == DB - 1))
                    mm.then_inc(ev("q1_used"), 1)
                    pe.wait_ge(ev("q1_used"), AH + BH + h + 1)
                pe.sem_inc(ev("out_a"), 1)
                pe.wait_ge(ev("sa"), TILES + 1)
                for h in range(BH):
                    pe.wait_ge(ev("q1"), 2 * AH + BH + h + 1)
                    o = bank[3][0:SR, 64 * h:64 * h + 64]
                    pe.matmul(o, SC[0:SR, h, 0, 0:SR], SA[0:SR, 64 * h:64 * h + 64], start=True, stop=False)
                    pe.matmul(o, SC[0:SR, h, 2, 0:SR], Vr[0:SR, 64 * h:64 * h + 64], start=False, stop=False)
                    for b in range(DB):
                        mm = pe.matmul(o, Q1[:, b, :], Tb[:, b, h // 2, :], start=False, stop=(b == DB - 1))
                    mm.then_inc(ev("q1_used"), 1)
                    pe.wait_ge(ev("q1_used"), 2 * AH + BH + h + 1)
                pe.sem_inc(ev("out_b"), 1)
                end(TILES, SR)
                for b in range(DB):
                    pe.wait_ge(ev("pick"), 3 * (b + 1))
                    if b > 0:
                        pe.wait_ge(ev("tb_new"), b)
                    for h in range(AH):
                        pe.matmul(v4(4)[:, h, :], kr[0:SR, h, :], Wr[0:SR, h, :], start=True, stop=True)
                    for h in range(BH):
                        r = slice(64 * (h % 2), 64 * (h % 2) + 64)
                        o = bank[5][r, 64 * (h // 2):64 * (h // 2) + 64]
                        c = slice(64 * h, 64 * h + 64)
                        pe.matmul(o, Br[0:SR, c], RH[0:SR, c], start=True, stop=False)
                        mm = pe.matmul(o, Kr[0:SR, c], sqa[0:SR, c], start=False, stop=True)
                    mm.then_inc(ev("upd_s"), 1)
                    pe.wait_ge(ev("tb_new"), b + 1)
                    if b > 0:
                        pe.wait_ge(ev("rb_new"), b)
                    for j in range(NP):
                        mm = pe.transpose(bank[6][0:64, j * P:(j + 1) * P], Tb[:, b, j, :], K.ident[:, :])
                    mm.then_inc(ev("rb_mm"), 1)


QKC, VC = CH * CQK, CH * CV
OG, ZG, IG = 2 * QKC + VC, 2 * QKC + 2 * VC, 2 * QKC + 3 * VC
VA1 = CV + 1


def phase_mlstm_in(nc, K, w_in, b_i, b_f, m0, S, p_m, s_m):
    with ExitStack() as ctx:
        sb = lambda n, s: ctx.enter_context(nc.sbuf_tensor("e_" + n, s, F32))
        ev = Events(nc, ctx, "e_")
        xnT = sb("xnT", [P, KT, XW])
        W = [sb(f"w{m}", [P, KT, 512]) for m in range(3)]
        WQ = [sb(f"wq{m}", [P, KT, P]) for m in range(2)]
        wg = sb("wg", [P, KT, 2 * CH])
        VB = sb("vb", [P, TILES + 1, 512])
        GO = sb("go", [P, TILES + 1, 512])
        T2 = sb("t2", [P, 2, 512])
        QB = [sb(f"qb{m}", [P, TOK]) for m in range(2)]
        bias = sb("bias", [CH, 2])
        li, lf, bc_, m, u, e = [sb(n, [CH, TOK]) for n in ("li", "lf", "b", "m", "u", "e")]
        pad = sb("pad", [CH, 2, DB, DS + 1])
        ms = sb("ms", [CH, DB, DS + 1])
        m0t = sb("m0t", [CH, DB])
        mp = sb("mp", [CH, TILES])
        bank = [ctx.enter_context(nc.psum_tensor(f"e_bank{i}", [P, 512], F32)) for i in range(8)]
        NB = TILES + 1

        def cols(b, r, n):
            return bank[b][0:r, 0:8 * NB].rearrange("p (n h) -> p n h", h=CH)[:, n, :]

        with nc.Block() as block:
            @block.sync
            def _(sp):
                sp.wait_ge(ev("pad"), 1)
                sp.dma_start(xnT[:, :, 0:TOK], S.xnT).then_inc(ev("ld_x"), 16)
                sp.dma_start(wg[:, :, :], w_block(w_in, IG, 2 * CH)).then_inc(ev("ld_g"), 16)
                sp.dma_start(bias[:, 0:1], b_i.rearrange("(h a) -> h a", a=1)).then_inc(ev("ld_g"), 16)
                sp.dma_start(bias[:, 1:2], b_f.rearrange("(h a) -> h a", a=1)).then_inc(ev("ld_g"), 16)
                sp.dma_start(m0t[:, :], m0.rearrange("b h -> h b"), allow_slow_non_contiguous=True).then_inc(ev("ld_g"), 16)
                for k in range(2):
                    sp.dma_start(WQ[k][:, :, :], w_block(w_in, k * QKC, P)).then_inc(ev(f"ld_q{k}"), 16)
                for k in range(3):
                    sp.dma_start(W[k][:, :, :], w_block(w_in, 2 * QKC + k * VC, 512)).then_inc(ev(f"ld_w{k}"), 16)

                def qk(j, more):
                    for k in range(2):
                        if more:
                            sp.wait_ge(ev(f"proj_q{k}"), 3 * (j + 1))
                            alone(sp, K)
                            sp.dma_start(WQ[k][:, :, :], w_block(w_in, k * QKC + (j + 1) * P, P)).then_inc(ev(f"ld_q{k}"), 16)
                    for k in range(2):
                        sp.wait_ge(ev(f"kept_q{k}"), 3 * (j + 1))
                        alone(sp, K)
                        sp.dma_start(S.ql[k, bass.ds(j * P, P), :], QB[k][:, :]).then_inc(ev(f"out_q{k}"), 16)
                with sp.Fori(0, NP - 1) as j:
                    qk(j, True)
                qk(NP - 1, False)

                def store(c, dram, t, done):
                    sp.dma_start(dram[0:SEQ, c * 512:c * 512 + 512].rearrange("(n p) c -> p n c", p=P), t[:, 0:TILES, :]).then_inc(done, 16)
                    sp.dma_start(dram[SEQ:TOK, c * 512:c * 512 + 512], t[0:SR, TILES, :]).then_inc(done, 16)
                for c in range(2):
                    for k in range(3):
                        sp.wait_ge(ev(f"proj_w{k}"), NB * (c + 1))
                        if c == 0:
                            sp.dma_start(W[k][:, :, :], w_block(w_in, 2 * QKC + k * VC + 512, 512)).then_inc(ev(f"ld_w{k}"), 16)
                        if k == 0:
                            sp.wait_ge(ev("kept_w0"), NB * (c + 1))
                            store(c, S.v, VB, ev("out_v"))
                    sp.wait_ge(ev("gated"), NB * (c + 1))
                    store(c, S.g, GO, ev("out_g"))
                sp.wait_ge(ev("m_end"), 2)
                sp.dma_start(p_m.rearrange("b h -> h b"), m[:, SEQ - 1:SEQ], allow_slow_non_contiguous=True).then_inc(ev("out_m"), 16)
                sp.dma_start(s_m.rearrange("b h -> h b"), ms[:, :, DS], allow_slow_non_contiguous=True).then_inc(ev("out_m"), 16)
                for n, k in (("out_q0", NP), ("out_q1", NP), ("out_v", 4), ("out_g", 4), ("out_m", 2)):
                    sp.wait_ge(ev(n), 16 * k)

            @block.gpsimd
            def _(pool):
                pool.memset(xnT[:, :, TOK:XW], 0.0).then_inc(ev("pad"), 1)
                done = Seq(ev("pseq"), pool, 2 + 2 * 1)
                done.start(0)
                done(pool.memset(K.sel[:, :, :], 1.0))
                done(pool.affine_select(out=K.sel[:, :, :], in_=K.sel[:, :, :], compare_op=ALU.is_equal, fill=0.0, base=0,
                                        pattern=[[-1, CH], [0, P]], channel_multiplier=1))
                done(pool.memset(K.sel2[:, :, :], 1.0))
                done(pool.affine_select(out=K.sel2[:, :, :].rearrange("g j (u c) -> g (j u) c", u=2),
                                        in_=K.sel2[:, :, :].rearrange("g j (u c) -> g (j u) c", u=2),
                                        compare_op=ALU.is_equal, fill=0.0, base=0,
                                        pattern=[[-1, CH], [0, 64]], channel_multiplier=1))
                done.end()

            @block.scalar
            def _(act):
                act.wait_ge(ev("bias"), 1)
                for t in range(2):
                    for g, (c, n) in enumerate(GROUPS):
                        act.wait_ge(ev("gate_mm"), 3 * t + g + 1)
                        dst = (li, lf)[t]
                        act.activation(dst[:, c:c + n], bank[4 * (t % 2) + g][0:CH, 0:n], ACT.Tanh, scale=1.0 / CAP,
                                       bias=bias[:, t:t + 1]).then_inc(ev("gate_t"), 1)
                act.wait_ge(ev("gate_t"), 6)
                act.activation(lf[:, :], lf[:, :], ACT.Exp, scale=-CAP).then_inc(ev("gate_e"), 1)
                act.wait_ge(ev("gate_e"), 1)
                act.activation(lf[:, :], lf[:, :], ACT.Ln, bias=1.0).then_inc(ev("gate_e"), 1)
                act.wait_ge(ev("u"), 1)
                act.activation(e[:, :], e[:, :], ACT.Exp).then_inc(ev("e"), 1)
                act.wait_ge(ev("turned"), 2)
                for r, n in ((P, slice(0, TILES)), (SR, slice(TILES, NB))):
                    ins = act.activation(K.em[0:r, n, :], cols(3, r, n), ACT.Exp, scale=-1.0)
                ins.then_inc(ev("em"), 1)
                act.activation(K.u[:, :], u[:, :], ACT.Copy).then_inc(ev("em"), 1)
                act.wait_ge(ev("e"), 1)
                act.activation(K.e[:, :], e[:, :], ACT.Copy).then_inc(ev("em"), 1)

                with act.Fori(0, NP) as j:
                    for k in range(2):
                        act.wait_ge(ev(f"out_q{k}"), 16 * j)
                        for g, (c, n) in enumerate(GROUPS):
                            act.wait_ge(ev(f"proj_q{k}"), 3 * j + g + 1)
                            act.activation(QB[k][:, c:c + n], bank[3 * k + g][:, 0:n], ACT.Copy,
                                           scale=CQK ** -0.5 if k == 0 else 1.0).then_inc(ev(f"kept_q{k}"), 1)
                for c in range(2):
                    for n in range(NB):
                        if n == 0:
                            act.wait_ge(ev("out_v"), 32 * c)
                        act.wait_ge(ev("proj_w0"), NB * c + n + 1)
                        act.activation(VB[:, n, :], bank[(27 * c + n) % 8][:, :], ACT.Copy).then_inc(ev("kept_w0"), 1)
                    for n in range(NB):
                        if n == 0:
                            act.wait_ge(ev("out_g"), 32 * c)
                        act.wait_ge(ev("proj_w1"), NB * c + n + 1)
                        act.activation(GO[:, n, :], bank[(27 * c + 9 + n) % 8][:, :], ACT.Tanh, scale=0.5).then_inc(ev("kept_w1"), 1)
                    for n in range(NB):
                        act.wait_ge(ev("proj_w2"), NB * c + n + 1)
                        if NB * c + n >= 2:
                            act.wait_ge(ev("gated"), NB * c + n - 1)
                        act.activation(T2[:, n % 2, :] if c == 0 else T2[:, (n + 1) % 2, :], bank[(27 * c + 18 + n) % 8][:, :], ACT.Tanh,
                                       scale=0.5).then_inc(ev("tz"), 1)

            @block.vector
            def _(dve):
                dve.wait_ge(ev("ld_g"), 64)
                dve.tensor_scalar(bias[:, :], bias[:, :], 1.0 / CAP, None, ALU.mult).then_inc(ev("bias"), 1)
                done = Seq(ev("dseq"), dve, 14)
                done.start(0)
                dve.wait_ge(ev("gate_e"), 2)
                done(dve.tensor_scalar(li[:, :], li[:, :], CAP, None, ALU.mult))
                done(dve.tensor_scalar(lf[:, :], lf[:, :], -1.0, None, ALU.mult))
                done(dve.tensor_tensor_scan(bc_[:, :], K.restart[0:CH, :], lf[:, :], 0.0, ALU.mult, ALU.add))
                done(dve.tensor_tensor_scan(m[:, 0:SEQ], lf[:, 0:SEQ], li[:, 0:SEQ], 0.0, ALU.add, ALU.max))
                done(dve.memset(pad[:, 0, :, 0], -1e30))
                done(dve.tensor_copy(pad[:, 1, :, 0], m0t[:, :]))
                done(dve.tensor_copy(pad[:, 0, :, 1:DS + 1], lf[:, SEQ:TOK].rearrange("h (b t) -> h b t", b=DB)))
                done(dve.tensor_copy(pad[:, 1, :, 1:DS + 1], li[:, SEQ:TOK].rearrange("h (b t) -> h b t", b=DB)))
                done(dve.tensor_tensor_scan(ms[:, :, :].rearrange("h b t -> h (b t)"), pad[:, 0, :, :].rearrange("h b t -> h (b t)"),
                                            pad[:, 1, :, :].rearrange("h b t -> h (b t)"), 0.0, ALU.add, ALU.max))
                done(dve.tensor_copy(m[:, SEQ:TOK].rearrange("h (b t) -> h b t", b=DB), ms[:, :, 1:DS + 1]))
                dve.sem_inc(ev("m_end"), 2)
                done(dve.tensor_tensor(u[:, :], bc_[:, :], m[:, :], ALU.subtract))
                done(dve.tensor_tensor(li[:, :], li[:, :], bc_[:, :], ALU.subtract))
                done(dve.memset(mp[:, 0:1], 0.0))
                done(dve.tensor_copy(mp[:, 1:TILES], m[:, P - 1:SEQ - P:P]))
                done.end()
                dve.sem_inc(ev("w"), 1)
                dve.tensor_tensor(e[:, 0:SEQ].rearrange("h (n t) -> h n t", n=TILES), u[:, 0:SEQ].rearrange("h (n t) -> h n t", n=TILES),
                                  mp[:, :].rearrange("h (n a) -> h n a", a=1).broadcast_to([CH, TILES, P]), ALU.add)
                dve.tensor_tensor(e[:, SEQ:TOK].rearrange("h (b t) -> h b t", b=DB), u[:, SEQ:TOK].rearrange("h (b t) -> h b t", b=DB),
                                  m0t[:, :].rearrange("h (b a) -> h b a", a=1).broadcast_to([CH, DB, DS]), ALU.add).then_inc(ev("u"), 1)
                dve.wait_ge(ev("turned"), 1)
                for r, n in ((P, slice(0, TILES)), (SR, slice(TILES, NB))):
                    ins = dve.tensor_copy(K.w[0:r, n, :], cols(7, r, n))
                ins.then_inc(ev("w_kept"), 1)
                for c in range(2):
                    for n in range(NB):
                        k = NB * c + n
                        t2 = T2[:, n % 2, :] if c == 0 else T2[:, (n + 1) % 2, :]
                        dve.wait_ge(ev("tz"), k + 1)
                        dve.scalar_tensor_tensor(out=t2, in0=t2, scalar=1.0, in1=bank[(27 * c + 18 + n) % 8][:, :],
                                                 op0=ALU.add, op1=ALU.mult).then_inc(ev("silu_z"), 1)
                        dve.wait_ge(ev("silu_z"), k + 1)
                        dve.wait_ge(ev("kept_w1"), k + 1)
                        dve.scalar_tensor_tensor(out=GO[:, n, :], in0=GO[:, n, :], scalar=1.0, in1=t2,
                                                 op0=ALU.add, op1=ALU.mult).then_inc(ev("gated"), 1)

            @block.tensor
            def _(pe):
                pe.wait_ge(ev("ld_x"), 16)
                pe.wait_ge(ev("ld_g"), 64)
                for t in range(2):
                    for g, (c, n) in enumerate(GROUPS):
                        for kt in range(KT):
                            mm = pe.matmul(bank[4 * t + g][0:CH, 0:n], wg[:, kt, CH * t:CH * t + CH], xnT[:, kt, c:c + n],
                                           start=(kt == 0), stop=(kt == KT - 1))
                        mm.then_inc(ev("gate_mm"), 1)
                pe.wait_ge(ev("w"), 1)
                pe.wait_ge(ev("pad"), 1)
                for src, b in ((li, 7), (m, 3)):
                    for n in range(NB):
                        r = P if n < TILES else SR
                        mm = pe.transpose(bank[b][0:r, 8 * n:8 * n + 8], src[:, n * P:n * P + r], K.ident[0:CH, 0:CH])
                    mm.then_inc(ev("turned"), 1)
                pe.wait_ge(ev("w_kept"), 1)
                pe.wait_ge(ev("em"), 3)

                def qk(j):
                    for k in range(2):
                        pe.wait_ge(ev(f"ld_q{k}"), 16 * (j + 1))
                        pe.wait_ge(ev(f"kept_q{k}"), 3 * j)
                        for g, (c, n) in enumerate(GROUPS):
                            for kt in range(KT):
                                mm = pe.matmul(bank[3 * k + g][:, 0:n], WQ[k][:, kt, :], xnT[:, kt, c:c + n],
                                               start=(kt == 0), stop=(kt == KT - 1))
                            mm.then_inc(ev(f"proj_q{k}"), 1)
                with pe.Fori(0, NP) as j:
                    qk(j)
                pe.wait_ge(ev("kept_q1"), 3 * NP)
                kinds = ("kept_w0", "kept_w1", "gated")
                for c in range(2):
                    for k in range(3):
                        pe.wait_ge(ev(f"ld_w{k}"), 16 * (c + 1))
                        for n in range(NB):
                            q = 27 * c + 9 * k + n
                            if q >= 8:
                                o = q - 8
                                pe.wait_ge(ev(kinds[o % 27 // 9]), NB * (o // 27) + o % 9 + 1)
                            for kt in range(KT):
                                mm = pe.matmul(bank[q % 8][:, :], xnT[:, kt, n * P:(n + 1) * P], W[k][:, kt, :],
                                               start=(kt == 0), stop=(kt == KT - 1))
                            mm.then_inc(ev(f"proj_w{k}"), 1)


def phase_mix1(nc, K, w_out, norm_w, c0, n0, S, y_p, y_s, p_c, p_n, s_c, s_n):
    with ExitStack() as ctx:
        sb = lambda n, s: ctx.enter_context(nc.sbuf_tensor("f_" + n, s, F32))
        ev = Events(nc, ctx, "f_")
        QL = sb("ql", [P, 2, NP, P])
        VA = sb("va", [P, CH, VA1])
        GR = sb("gr", [P, D])
        XR = sb("xr", [P, D])
        wo = sb("wo", [P, KT, D])
        nw = sb("nw", [P, D])
        ut, et = sb("ut", [CH, P]), sb("et", [CH, P])
        wt, emt = sb("wt", [P, CH]), sb("emt", [P, CH])
        Dm = sb("dm", [P, CH, P])
        PM = sb("pm", [P, CH, P])
        qe = sb("qe", [P, NP, P])
        ec = sb("ec", [P, NP, DB])
        wk = sb("wk", [P, CH])
        KW = sb("kw", [P, QKC])
        den = sb("den", [P, 2, CH])
        H = sb("h", [P, D])
        OT = sb("ot", [P, KT, P])
        C = sb("c", [P, NP, VA1])
        n1 = sb("n1", [P, 4])
        yo = sb("yo", [P, D])
        Cb = sb("cb", [P, DB, NP, VA1])
        Q1 = sb("q1", [P, DB, SR])
        KM = sb("km", [P, QKC])
        bank = [ctx.enter_context(nc.psum_tensor(f"f_bank{i}", [P, 512], F32)) for i in range(8)]
        place = {h: (6 + h % 2, VA1 * (h // 2)) if h < 6 else (3 + h % 2, 0) for h in range(CH)}

        def v4(b, r=P, c=P):
            return bank[b][0:r, :].rearrange("p (h c) -> p h c", h=4)[:, :, 0:c]

        def split(b, r):
            if b >= 6:
                t = bank[b][0:r, 0:3 * VA1].rearrange("p (h c) -> p h c", h=3)
                return slice(b % 2, 6, 2), t[:, :, 0:CV], t[:, :, CV]
            t = bank[b][0:r, 0:VA1].rearrange("p (h c) -> p h c", h=1)
            return slice(3 + b, 4 + b), t[:, :, 0:CV], t[:, :, CV]

        with nc.Block() as block:
            @block.sync
            def _(sp):
                sp.dma_start(wo[:, :, :], w_block(w_out, 0, D)).then_inc(ev("ld_wo"), 16)
                sp.dma_start(nw[:, :], as_row(norm_w)).then_inc(ev("ld_nw"), 16)

                def load(i, c, T):
                    sp.wait_ge(ev("qk"), i)
                    sp.wait_ge(ev("rows"), i)
                    sp.wait_ge(ev("qe"), i)
                    alone(sp, K)
                    for m in range(2):
                        sp.dma_start(QL[:, m, :, 0:T], S.ql[m].rearrange("(j p) t -> p j t", p=P)[:, :, bass.ds(c, T)]).then_inc(ev("ld_q"), 16)
                    sp.wait_ge(ev("num"), i)
                    sp.wait_ge(ev("upd"), i)
                    alone(sp, K)
                    sp.dma_start(VA[0:T, :, 0:CV], S.v[bass.ds(c, T), :].rearrange("t (h v) -> t h v", h=CH)).then_inc(ev("ld_v"), 16)
                    sp.wait_ge(ev("gate"), i)
                    alone(sp, K)
                    sp.dma_start(GR[0:T, :], S.g[bass.ds(c, T), :]).then_inc(ev("ld_gr"), 16)
                    sp.wait_ge(ev("y"), i)
                    alone(sp, K)
                    sp.dma_start(XR[0:T, :], S.x1[bass.ds(c, T), :]).then_inc(ev("ld_x"), 16)

                def store(i, c, T):
                    sp.wait_ge(ev("y"), i + 1)
                    alone(sp, K)
                    y = y_p[0, bass.ds(c, T), :] if T == P else y_s.rearrange("b t d -> (b t) d")
                    sp.dma_start(y, yo[0:T, :]).then_inc(ev("stored"), 16)
                with sp.Fori(0, TILES) as i:
                    load(i, i * P, P)
                    store(i, i * P, P)
                sp.wait_ge(ev("state"), TILES)
                pair = lambda t: t.rearrange("(j h) k v -> (h k) j v", h=2)
                pair2 = lambda t: t.rearrange("(j h) k -> (h k) j", h=2)
                for h in range(2):
                    r = slice(64 * h, 64 * h + 64)
                    sp.dma_start(p_c[0].rearrange("(j h) k v -> h k j v", h=2)[h], C[r, :, 0:CV], allow_slow_non_contiguous=True).then_inc(ev("c_out"), 16)
                    sp.dma_start(p_n[0].rearrange("(j h) k -> h k j", h=2)[h], C[r, :, CV], allow_slow_non_contiguous=True).then_inc(ev("c_out"), 16)
                    for b in range(DB):
                        sp.dma_start(Cb[r, b, :, 0:CV], c0[b].rearrange("(j h) k v -> h k j v", h=2)[h]).then_inc(ev("ld_c"), 16)
                        sp.dma_start(Cb[r, b, :, CV], n0[b].rearrange("(j h) k -> h k j", h=2)[h], allow_slow_non_contiguous=True).then_inc(ev("ld_c"), 16)
                load(TILES, SEQ, SR)
                store(TILES, SEQ, SR)
                for b in range(DB):
                    sp.wait_ge(ev("cb"), b + 1)
                    for h in range(2):
                        r = slice(64 * h, 64 * h + 64)
                        sp.dma_start(s_c[b].rearrange("(j h) k v -> h k j v", h=2)[h], Cb[r, b, :, 0:CV], allow_slow_non_contiguous=True).then_inc(ev("cb_out"), 16)
                        sp.dma_start(s_n[b].rearrange("(j h) k -> h k j", h=2)[h], Cb[r, b, :, CV], allow_slow_non_contiguous=True).then_inc(ev("cb_out"), 16)
                sp.wait_ge(ev("stored"), 16 * (TILES + 1))
                sp.wait_ge(ev("c_out"), 64)
                sp.wait_ge(ev("cb_out"), 64 * DB)

            @block.gpsimd
            def _(pool):
                pool.memset(VA[:, :, CV:VA1], 1.0).then_inc(ev("va1"), 1)
                pool.memset(C[:, :, :], 0.0).then_inc(ev("init"), 1)

                def tile(i, T):
                    n = i + 1
                    pool.wait_ge(ev("n1"), n)
                    pool.tensor_tensor(n1[0:T, 2:3], n1[0:T, 1:2], K.half_neg[0:T, 0:1], ALU.pow).then_inc(ev("n1r"), 1)
                with pool.Fori(0, TILES) as i:
                    tile(i, P)
                tile(TILES, SR)

            @block.scalar
            def _(act):
                def tile(i, c, T):
                    n = i + 1
                    act.wait_ge(ev("ub"), i)
                    act.activation(ut[:, 0:T], K.u[:, bass.ds(c, T)], ACT.Copy).then_inc(ev("ut"), 1)
                    act.wait_ge(ev("eb"), i)
                    act.activation(et[:, 0:T], K.e[:, bass.ds(c, T)], ACT.Copy).then_inc(ev("et"), 1)
                    act.wait_ge(ev("dmin"), i)
                    act.activation(wt[0:T, :], K.w[0:T, bass.ds(i, 1), :].rearrange("p a h -> p (a h)"), ACT.Copy).then_inc(ev("wt"), 1)
                    act.wait_ge(ev("rden"), i)
                    act.activation(emt[0:T, :], K.em[0:T, bass.ds(i, 1), :].rearrange("p a h -> p (a h)"), ACT.Copy).then_inc(ev("emt"), 1)
                    act.wait_ge(ev("dmin"), n)
                    act.activation(Dm[0:T, :, 0:T], Dm[0:T, :, 0:T], ACT.Exp).then_inc(ev("dexp"), 1)
                    act.wait_ge(ev("num"), n)
                    for b in (6, 7, 3, 4):
                        hs, _, dn = split(b, T)
                        ins = act.activation(den[0:T, 0, hs], dn, ACT.Abs)
                    ins.then_inc(ev("den"), 1)
                    act.wait_ge(ev("ot_mm"), n)
                    act.wait_ge(ev("prj"), i)
                    act.activation(OT[:, 0:4, 0:T], v4(0, P, T), ACT.Copy).then_inc(ev("ot"), 1)
                    act.wait_ge(ev("x2"), n)
                    act.wait_ge(ev("stored"), 16 * i)
                    act.activation(yo[0:T, :], XR[0:T, :], ACT.Square, accum_out=n1[0:T, 0:1]).then_inc(ev("n1s"), 1)
                with act.Fori(0, TILES) as i:
                    tile(i, i * P, P)
                tile(TILES, SEQ, SR)
                for b in range(DB):
                    act.wait_ge(ev("upd_s"), b)
                    act.activation(KM[0:SR, :], KW[0:SR, :], ACT.Copy, scale=K.same[:, b * DS:b * DS + 1]).then_inc(ev("pick"), 1)

            @block.vector
            def _(dve):
                bc = lambda t, s: t.broadcast_to(s)

                def tile(i, T, lmask):
                    n = i + 1
                    dve.wait_ge(ev("ub"), n)
                    dve.wait_ge(ev("wt"), n)
                    dve.wait_ge(ev("kw"), i)
                    dve.wait_ge(ev("pm"), 2 * i)
                    for h in range(CH):
                        ins = dve.scalar_tensor_tensor(out=Dm[0:T, h, 0:T], in0=v4(h // 4, T, T)[:, h % 4, :], scalar=wt[0:T, h:h + 1],
                                                       in1=lmask[0:T, 0:T], op0=ALU.add, op1=ALU.min)
                    ins.then_inc(ev("dmin"), 1)
                    dve.wait_ge(ev("eb"), n)
                    dve.wait_ge(ev("ld_q"), 32 * n)
                    dve.wait_ge(ev("num"), i)
                    dve.wait_ge(ev("state"), i)
                    dve.tensor_tensor(qe[:, :, 0:T], QL[:, 0, :, 0:T], v4(2, P, T), ALU.mult).then_inc(ev("qe"), 1)
                    if T == P:
                        dve.tensor_copy(ec[:, :, 0], v4(2)[:, :, P - 1]).then_inc(ev("ec"), 1)
                    else:
                        dve.tensor_copy(ec[:, :, :], v4(2, P, T)[:, :, DS - 1:SR:DS]).then_inc(ev("ec"), 1)
                    dve.wait_ge(ev("dexp"), n)
                    dve.wait_ge(ev("qk"), n)
                    for k in range(2):
                        dve.tensor_tensor(PM[0:T, k::2, 0:T], Dm[0:T, k::2, 0:T], v4(3 + k, T, T), ALU.mult).then_inc(ev("pm"), 1)
                    dve.wait_ge(ev("rows"), n)
                    dve.wait_ge(ev("upd"), i)
                    if T == P:
                        w = Dm[:, :, P - 1]
                    else:
                        dve.wait_ge(ev("pm"), 2 * n)
                        dve.tensor_tensor(Dm[0:T, :, 0:T], Dm[0:T, :, 0:T], bc(K.last[:, :].rearrange("s (a t) -> s a t", a=1),
                                                                            [T, CH, T]), ALU.mult).then_inc(ev("wk"), 1)
                        dve.wait_ge(ev("wk"), 1)
                        dve.tensor_reduce(wk[0:T, :], Dm[0:T, :, 0:T], AX_X, ALU.add).then_inc(ev("wk"), 1)
                        dve.wait_ge(ev("wk"), 2)
                        w = wk[0:T, :]
                    dve.tensor_tensor(KW[0:T, :].rearrange("p (h k) -> p h k", h=CH), bank[5][0:T, :].rearrange("p (h k) -> p h k", h=CH),
                                      bc(w.rearrange("p (h a) -> p h a", a=1), [T, CH, 64]), ALU.mult).then_inc(ev("kw"), 1)
                    if T != P:
                        for h in range(CH):
                            if h:
                                dve.wait_ge(ev("q1_used"), h)
                            dve.wait_ge(ev("qe"), n)
                            dve.scalar_tensor_tensor(out=Q1[:, :, :], in0=bc(qe[:, h // 2, 0:T].rearrange("p (a t) -> p a t", a=1), [P, DB, SR]),
                                                     scalar=K.head_cols[:, h % 2:h % 2 + 1], in1=K.batch_cols[:, :, :],
                                                     op0=ALU.mult, op1=ALU.mult).then_inc(ev("q1"), 1)
                    dve.wait_ge(ev("den"), n)
                    dve.wait_ge(ev("emt"), n)
                    dve.tensor_tensor(den[0:T, 0, :], den[0:T, 0, :], emt[0:T, :], ALU.max).then_inc(ev("den2"), 1)
                    dve.wait_ge(ev("den2"), n)
                    dve.tensor_scalar(den[0:T, 0, :], den[0:T, 0, :], 4.0, None, ALU.mult).then_inc(ev("den3"), 1)
                    dve.wait_ge(ev("den3"), n)
                    dve.wait_ge(ev("ot_mm"), i)
                    dve.reciprocal(den[0:T, 1, :], den[0:T, 0, :]).then_inc(ev("rden"), 1)
                    dve.wait_ge(ev("rden"), n)
                    h3 = H[0:T, :].rearrange("p (h c) -> p h c", h=CH)
                    for b in (6, 7, 3, 4):
                        hs, nm, _ = split(b, T)
                        w = nm.shape[1]
                        ins = dve.tensor_tensor(h3[:, hs, :], nm, bc(den[0:T, 1, hs].rearrange("p (h a) -> p h a", a=1), [T, w, CV]), ALU.mult)
                    ins.then_inc(ev("hr"), 1)
                    dve.wait_ge(ev("hr"), n)
                    dve.wait_ge(ev("ld_gr"), 16 * n)
                    dve.tensor_tensor(H[0:T, :], H[0:T, :], GR[0:T, :], ALU.mult).then_inc(ev("gate"), 1)
                    if T == P:
                        dve.wait_ge(ev("upd"), n)
                        dve.wait_ge(ev("ec"), n)
                        for j in range(NP):
                            src = bank[2][:, VA1 * j:VA1 * (j + 1)] if j < 3 else bank[5][:, 0:VA1]
                            ins = dve.scalar_tensor_tensor(out=C[:, j, :], in0=C[:, j, :], scalar=ec[:, j, 0:1], in1=src,
                                                           op0=ALU.mult, op1=ALU.add)
                        ins.then_inc(ev("state"), 1)
                    dve.wait_ge(ev("ot_mm"), n)
                    dve.wait_ge(ev("prj"), i)
                    dve.tensor_copy(OT[:, 4:8, 0:T], v4(1, P, T)).then_inc(ev("ot2"), 1)
                    dve.wait_ge(ev("prj"), n)
                    dve.wait_ge(ev("ld_x"), 16 * n)
                    for c in range(2):
                        ins = dve.tensor_tensor(XR[0:T, 512 * c:512 * c + 512], bank[6 + c][0:T, :], XR[0:T, 512 * c:512 * c + 512], ALU.add)
                    ins.then_inc(ev("x2"), 1)
                    dve.wait_ge(ev("n1s"), n)
                    dve.tensor_scalar(n1[0:T, 1:2], n1[0:T, 0:1], 1.0 / D, EPS, ALU.mult, ALU.add).then_inc(ev("n1"), 1)
                    dve.wait_ge(ev("n1r"), n)
                    dve.scalar_tensor_tensor(out=yo[0:T, :], in0=XR[0:T, :], scalar=n1[0:T, 2:3], in1=nw[0:T, :],
                                             op0=ALU.mult, op1=ALU.mult).then_inc(ev("y"), 1)
                dve.wait_ge(ev("ld_nw"), 16)
                with dve.Fori(0, TILES) as i:
                    tile(i, P, K.lcausal)
                tile(TILES, SR, K.lcausal_s)
                for b in range(DB):
                    dve.wait_ge(ev("upd_s"), b + 1)
                    for j in range(NP):
                        src = bank[2][:, VA1 * j:VA1 * (j + 1)] if j < 3 else bank[5][:, 0:VA1]
                        ins = dve.scalar_tensor_tensor(out=Cb[:, b, j, :], in0=Cb[:, b, j, :], scalar=ec[:, j, b:b + 1], in1=src,
                                                       op0=ALU.mult, op1=ALU.add)
                    ins.then_inc(ev("cb"), 1)

            @block.tensor
            def _(pe):
                def update(T, keys, name):
                    for h in range(CH):
                        r = slice(64 * (h % 2), 64 * (h % 2) + 64)
                        j = h // 2
                        o = bank[2][r, VA1 * j:VA1 * (j + 1)] if j < 3 else bank[5][r, 0:VA1]
                        mm = pe.matmul(o, keys[0:T, 64 * h:64 * h + 64], VA[0:T, h, :], start=True, stop=True)
                    mm.then_inc(ev(name), 1)

                def tile(i, T):
                    n = i + 1
                    pe.wait_ge(ev("ut"), n)
                    pe.wait_ge(ev("ot"), i)
                    pe.wait_ge(ev("ot2"), i)
                    for h in range(CH):
                        mm = pe.matmul(v4(h // 4, T, T)[:, h % 4, :], K.sel[:, h, 0:T], ut[:, 0:T], start=True, stop=True)
                    mm.then_inc(ev("ub"), 1)
                    pe.wait_ge(ev("et"), n)
                    pe.wait_ge(ev("state"), i)
                    for j in range(NP):
                        mm = pe.matmul(v4(2, P, T)[:, j, :], K.sel2[:, j, :], et[:, 0:T], start=True, stop=True)
                    mm.then_inc(ev("eb"), 1)
                    pe.wait_ge(ev("hr"), i)
                    pe.wait_ge(ev("ld_q"), 32 * n)
                    for h in range(CH):
                        r = slice(64 * (h % 2), 64 * (h % 2) + 64)
                        mm = pe.matmul(v4(3 + h % 2, T, T)[:, h // 2, :], QL[r, 1, h // 2, 0:T], QL[r, 0, h // 2, 0:T], start=True, stop=True)
                    mm.then_inc(ev("qk"), 1)
                    for j in range(NP):
                        mm = pe.transpose(v4(5, T)[:, j, :], QL[:, 1, j, 0:T], K.ident[:, :])
                    mm.then_inc(ev("rows"), 1)
                    pe.wait_ge(ev("ld_v"), 16 * n)
                    pe.wait_ge(ev("qe"), n)
                    pe.wait_ge(ev("x2"), i)
                    pe.wait_ge(ev("pm"), 2 * n)
                    for h in range(CH):
                        r = slice(64 * (h % 2), 64 * (h % 2) + 64)
                        b, c = place[h]
                        o = bank[b][0:T, c:c + VA1]
                        pe.matmul(o, PM[0:T, h, 0:T], VA[0:T, h, :], start=True, stop=False)
                        if T == P:
                            mm = pe.matmul(o, qe[r, h // 2, :], C[r, h // 2, :], start=False, stop=True)
                        else:
                            pe.wait_ge(ev("q1"), h + 1)
                            for b in range(DB):
                                mm = pe.matmul(o, Q1[:, b, :], Cb[:, b, h // 2, :], start=False, stop=(b == DB - 1))
                            mm.then_inc(ev("q1_used"), 1)
                            pe.wait_ge(ev("q1_used"), h + 1)
                    if T == P:
                        mm.then_inc(ev("num"), 1)
                        pe.wait_ge(ev("kw"), n)
                        pe.wait_ge(ev("ec"), n)
                        update(T, KW, "upd")
                    else:
                        pe.sem_inc(ev("num"), 1)
                    pe.wait_ge(ev("gate"), n)
                    pe.wait_ge(ev("dmin"), n)
                    for c in range(KT):
                        mm = pe.transpose(v4(c // 4, P, T)[:, c % 4, :], H[0:T, c * P:(c + 1) * P], K.ident[0:T, 0:T])
                    mm.then_inc(ev("ot_mm"), 1)
                    pe.wait_ge(ev("ot"), n)
                    pe.wait_ge(ev("ot2"), n)
                    for c in range(2):
                        for kt in range(KT):
                            mm = pe.matmul(bank[6 + c][0:T, :], OT[:, kt, 0:T], wo[:, kt, 512 * c:512 * c + 512],
                                           start=(kt == 0), stop=(kt == KT - 1))
                    mm.then_inc(ev("prj"), 1)
                pe.wait_ge(ev("ld_wo"), 16)
                pe.wait_ge(ev("va1"), 1)
                pe.wait_ge(ev("init"), 1)
                with pe.Fori(0, TILES) as i:
                    tile(i, P)
                pe.wait_ge(ev("ld_c"), 32 * DB * 2)
                tile(TILES, SR)
                for b in range(DB):
                    pe.wait_ge(ev("pick"), b + 1)
                    pe.wait_ge(ev("cb"), b)
                    pe.wait_ge(ev("kw"), TILES + 1)
                    pe.wait_ge(ev("ec"), TILES + 1)
                    update(SR, KM, "upd_s")


_INS = ("x_prompt", "x_sample", "state_gdn_conv", "state_gdn", "state_rwkv_shift", "state_rwkv",
        "state_mlstm_c", "state_mlstm_n", "state_mlstm_m",
        "norm0_w", "w_in0", "w_out0", "gdn_conv_w", "gdn_a_log", "gdn_dt_bias", "gdn_norm_w",
        "rwkv_mu", "rwkv_w0", "rwkv_w2", "rwkv_a0", "rwkv_a2", "rwkv_k_k", "rwkv_k_a", "rwkv_r_k",
        "rwkv_ln_w", "rwkv_ln_b", "norm1_w", "w_in1", "w_out1", "mlstm_b_i", "mlstm_b_f", "norm_f_w")
_OUTS = (("y_prompt", (1, SEQ, D)), ("y_sample", (DB, DS, D)),
         ("p_conv", (1, CONV - 1, AQKV)), ("p_gdn", (1, AH, P, P)), ("p_shift", (1, D)), ("p_rwkv", (1, BH, 64, 64)),
         ("p_c", (1, CH, CQK, CV)), ("p_n", (1, CH, CQK)), ("p_m", (1, CH)),
         ("s_conv", (DB, CONV - 1, AQKV)), ("s_gdn", (DB, AH, P, P)), ("s_shift", (DB, D)), ("s_rwkv", (DB, BH, 64, 64)),
         ("s_c", (DB, CH, CQK, CV)), ("s_n", (DB, CH, CQK)), ("s_m", (DB, CH)))


class Scope:
    pass


def build(nc, A, O):
    K, S = Scope(), Scope()
    dram = lambda name, shape: nc.dram_tensor("scratch_" + name, shape, F32, kind="Internal").ap()
    S.qkv, S.z, S.rw = dram("qkv", [3, AKEY, TOK]), dram("z", [TOK, AKEY]), dram("rw", [6, BW, TOK])
    S.x1, S.xnT = dram("x1", [TOK, D]), dram("xnT", [P, KT, TOK])
    S.ql, S.v, S.g = dram("ql", [2, CH * CQK, TOK]), dram("v", [TOK, D]), dram("g", [TOK, D])
    chip = lambda ctx, name, shape: ctx.enter_context(nc.sbuf_tensor("k_" + name, shape, F32))
    NB = TILES + 1

    with ExitStack() as kept:
        (K.ident, K.ones, K.half_neg, K.pair_ones, K.causal, K.strict, K.same, K.causal_s, K.strict_s, K.last, K.restart,
         K.batch_cols, K.head_cols, K.lcausal, K.lcausal_s) = [chip(kept, name, shape) for name, shape in CONSTS]
        K.idle = {n: kept.enter_context(nc.semaphore("idle_" + n)) for n in ("SP", "Pool", "PE", "DVE", "Activation")}
        with ExitStack() as layer:
            K.beta, K.logd, K.bonus = [chip(layer, n, [P, NB, h]) for n, h in (("beta", AH), ("logd", AH), ("bonus", BH))]
            K.rw_mid, K.rw_in, K.rw_out = [chip(layer, n, [P, NP, h]) for n, h in (("rw_mid", TILES), ("rw_in", TILES), ("rw_out", TILES + DB))]
            with ExitStack() as rows:
                K.xnT = chip(rows, "xnT", [P, KT, XW])
                phase_norm(nc, K, A["x_prompt"], A["x_sample"], A["state_rwkv_shift"], A["norm0_w"], O["p_shift"], O["s_shift"])
                phase_gdn_in(nc, K, A["w_in0"], A["gdn_conv_w"], A["state_gdn_conv"], A["gdn_a_log"], A["gdn_dt_bias"], S,
                             O["p_conv"], O["s_conv"])
                phase_rwkv_in(nc, K, A["w_in0"], A["rwkv_mu"], A["rwkv_w0"], A["rwkv_w2"], A["rwkv_a0"], A["rwkv_a2"],
                              A["rwkv_k_k"], A["rwkv_k_a"], A["rwkv_r_k"], S)
            phase_mix0(nc, K, A["w_out0"], A["norm1_w"], A["gdn_norm_w"], A["rwkv_ln_w"], A["rwkv_ln_b"],
                       A["x_prompt"], A["x_sample"], A["state_gdn"], A["state_rwkv"], S,
                       O["p_gdn"], O["p_rwkv"], O["s_gdn"], O["s_rwkv"])
        with ExitStack() as layer:
            K.sel, K.sel2 = chip(layer, "sel", [CH, CH, P]), chip(layer, "sel2", [CH, NP, P])
            K.w, K.em = chip(layer, "w", [P, NB, CH]), chip(layer, "em", [P, NB, CH])
            K.u, K.e = chip(layer, "u", [CH, TOK]), chip(layer, "e", [CH, TOK])
            phase_mlstm_in(nc, K, A["w_in1"], A["mlstm_b_i"], A["mlstm_b_f"], A["state_mlstm_m"], S, O["p_m"], O["s_m"])
            phase_mix1(nc, K, A["w_out1"], A["norm_f_w"], A["state_mlstm_c"], A["state_mlstm_n"], S,
                       O["y_prompt"], O["y_sample"], O["p_c"], O["p_n"], O["s_c"], O["s_n"])


def kernel(**inputs):
    import numpy as _np
    import concourse.bacc as _bacc
    from concourse import mybir as _mybir
    from concourse.bass_utils import run_bass_kernel_spmd as _run

    nc = _bacc.Bacc("TRN2", target_bir_lowering=False, num_devices=1)
    arrays, A, O = {}, {}, {}
    for name in _INS:
        arrays[f"in_{name}_dram"] = a = _np.ascontiguousarray(inputs[name])
        A[name] = nc.dram_tensor(f"in_{name}_dram", a.shape, _mybir.dt.from_np(a.dtype), kind="ExternalInput").ap()
    for name, shape in _OUTS:
        O[name] = nc.dram_tensor(f"out_{name}_dram", shape, _mybir.dt.float32, kind="ExternalOutput").ap()
    build(nc, A, O)
    r = _run(nc, [arrays], core_ids=[0])
    return tuple(r.results[0][f"out_{name}_dram"] for name, _ in _OUTS)
```

```python
import math
from contextlib import ExitStack

import concourse.bass as bass
from concourse import mybir

F32 = mybir.dt.float32
F32R = mybir.dt.float32r
ALU = mybir.AluOpType
ACT = mybir.ActivationFunctionType
AX_X = mybir.AxisListType.X

P = 128
D = 1024
KT = D // P
SEQ = 1024
TILES = SEQ // P
DB, DS = 8, 8
SR = DB * DS
TOK = SEQ + SR
XC = TOK + DB
XW = (TILES + 1) * P
EPS = 1e-6
AH, AKEY = 4, 512
AQKV = 3 * AKEY
AZ = AQKV
AGATE = AQKV + AKEY
ACOLS = AGATE + 2 * AH
BW, BH = 512, 8
NP = BW // P
B_GN_EPS = 64e-5
DECAY = math.exp(-0.5)
CH, CQK, CV = 8, 64, 128
CAP = 15.0
NEG = -30000.0
CONV = 4
GROUPS = ((0, 512), (512, 512), (SEQ, SR))
THIRDS = ((0, 364), (364, 364), (728, TOK - 728))


def alone(eng, K):
    eng.sem_inc(K.idle[eng.engine.name], 1)


class Events:

    def __init__(self, nc, ctx, prefix):
        self.nc, self.prefix, self.sems = nc, prefix, {}
        ctx.callback(self.close)

    def __call__(self, name):
        if name not in self.sems:
            self.sems[name] = self.nc.alloc_semaphore(self.prefix + name)
        return self.sems[name]

    def close(self):
        self.nc.clear_and_free_semaphores(list(self.sems.values()))
        self.nc.all_engine_barrier()


class Seq:

    def __init__(self, sem, eng, per):
        self.sem, self.eng, self.per, self.n, self.base = sem, eng, per, 0, 0

    def start(self, i):
        self.base, self.n = i * self.per, 0

    def __call__(self, ins):
        self.n += 1
        ins.then_inc(self.sem, 1)
        self.eng.wait_ge(self.sem, self.base + self.n)

    def end(self):
        assert self.n == self.per


def products(pe, out, w, x, first, last):
    pe.matmul(out, w[0], x[0], start=first, stop=False)
    pe.matmul(out, w[0], x[1], start=False, stop=False)
    return pe.matmul(out, w[1], x[0], start=False, stop=last)


def as_row(v):
    n = v.shape[0]
    return v.rearrange("(a n) -> a n", a=1).broadcast_to([P, n])


def phase_norm(nc, K, x_prompt, x_sample, shift, norm_w, p_shift, s_shift):
    with ExitStack() as ctx:
        sb = lambda n, s: ctx.enter_context(nc.sbuf_tensor(n, s, F32))
        ev = Events(nc, ctx, "n_")
        x = sb("n_x", [P, 2, D])
        xn = sb("n_xn", [P, 2, D])
        sq = sb("n_sq", [P, D])
        st = sb("n_st", [P, 2, 4])
        wb = sb("n_wb", [P, D])
        pt = [ctx.enter_context(nc.psum_tensor(f"n_pt{i}", [P, 4, P], F32)) for i in range(4)]
        x_in0, x_in1, w_in, ssq, mean, rstd, norm, turned, high, low, shifts, consts, tmp, prev_rows = [ev(n) for n in (
            "x_in0", "x_in1", "w_in", "ssq", "mean", "rstd", "norm", "turned", "high", "low", "shifts", "consts", "tmp", "prev_rows")]

        x_in = (x_in0, x_in1)

        with nc.Block() as block:
            @block.sync
            def _(sp):
                sp.dma_start(wb[:, :], as_row(norm_w)).then_inc(w_in, 16)
                for b in range(2):
                    sp.dma_start(x[:, b, :], x_prompt[0, b * P:(b + 1) * P, :]).then_inc(x_in[b], 16)
                with sp.Fori(0, TILES // 2 - 1) as g:
                    for b in range(2):
                        sp.wait_ge(norm, 2 * g + b + 1)
                        sp.dma_start(x[:, b, :], x_prompt[0, bass.ds((2 * g + b + 2) * P, P), :]).then_inc(x_in[b], 16)
                sp.wait_ge(norm, TILES - 1)
                sp.dma_start(x[0:SR, 0, :], x_sample.rearrange("b t d -> (b t) d")).then_inc(x_in[0], 16)
                sp.dma_start(x[SR:SR + DB, 0, :], shift).then_inc(x_in[0], 16)
                sp.wait_ge(norm, TILES)
                sp.dma_start(p_shift, xn[P - 1:P, 1, :]).then_inc(shifts, 16)
                sp.wait_ge(norm, TILES + 1)
                for b in range(DB):
                    r = b * DS + DS - 1
                    sp.dma_start(s_shift[b:b + 1, :], xn[r:r + 1, 0, :]).then_inc(shifts, 16)
                sp.wait_ge(shifts, 16 * (DB + 1))

            @block.gpsimd
            def _(pool):
                done = Seq(tmp, pool, 34)
                done.start(0)
                done(pool.memset(K.ident[:, :], 0.0))
                done(pool.affine_select(out=K.ident[:, :], in_=K.ident[:, :], compare_op=ALU.not_equal, fill=1.0,
                                        base=0, pattern=[[-1, P]], channel_multiplier=1))
                pool.sem_inc(consts, 1)
                done(pool.memset(K.half_neg[:, :], -0.5))
                done(pool.memset(K.ones[:, :], 1.0))
                done(pool.memset(K.pair_ones[:, :], 0.0))
                done(pool.memset(K.pair_ones[0:64, 0:64], 1.0))
                done(pool.memset(K.pair_ones[64:128, 64:128], 1.0))
                for out, cmp in ((K.causal, ALU.is_ge), (K.strict, ALU.is_gt)):
                    done(pool.affine_select(out=out[:, :], in_=K.ones[:, :], compare_op=cmp, fill=0.0,
                                            base=0, pattern=[[1, P]], channel_multiplier=-1))
                v = K.same[0:SR, 0:SR].rearrange("s (b t) -> s b t", b=DB)
                done(pool.affine_select(out=v, in_=K.ones[0:SR, 0:SR].rearrange("s (b t) -> s b t", b=DB),
                                        compare_op=ALU.is_ge, fill=0.0, base=0, pattern=[[-DS, DB], [0, DS]],
                                        channel_multiplier=1))
                done(pool.affine_select(out=v, in_=v, compare_op=ALU.is_ge, fill=0.0, base=DS - 1,
                                        pattern=[[DS, DB], [0, DS]], channel_multiplier=-1))
                for out, m in ((K.causal_s, K.causal), (K.strict_s, K.strict)):
                    done(pool.tensor_tensor(out[:, :], K.same[0:SR, 0:SR], m[0:SR, 0:SR], ALU.mult))
                done(pool.memset(K.last[:, :], 0.0))
                done(pool.tensor_copy(K.last[:, DS - 1:SR:DS], K.same[0:SR, DS - 1:SR:DS]))
                done(pool.memset(K.restart[:, :], 1.0))
                done(pool.memset(K.restart[:, 0:SEQ:P], 0.0))
                done(pool.memset(K.restart[:, SEQ:TOK:DS], 0.0))
                done(pool.memset(K.batch_cols[:, :, :], 0.0))
                for b in range(DB):
                    done(pool.memset(K.batch_cols[:, b, b * DS:(b + 1) * DS], 1.0))
                done(pool.memset(K.head_cols[:, :], 0.0))
                done(pool.memset(K.head_cols[0:64, 0:1], 1.0))
                done(pool.memset(K.head_cols[64:128, 1:2], 1.0))
                done(pool.tensor_scalar(K.lcausal[:, :], K.causal[:, :], -NEG, NEG, ALU.mult, ALU.add))
                done(pool.tensor_scalar(K.lcausal_s[:, :], K.causal_s[:, :], -NEG, NEG, ALU.mult, ALU.add))
                for t in (K.xh, K.xl):
                    done(pool.memset(t[:, :, XC:XW].bitcast(F32), 0.0))
                done.end()

                def one(i, n, k):
                    pool.wait_ge(mean, n)
                    pool.tensor_tensor(st[:, k, 2:3], st[:, k, 1:2], K.half_neg[:, 0:1], ALU.pow).then_inc(rstd, 1)
                with pool.Fori(0, TILES // 2) as g:
                    for b in range(2):
                        one(g, 2 * g + b + 1, b)
                pool.wait_ge(mean, TILES + 1)
                pool.tensor_tensor(st[0:SR, 0, 2:3], st[0:SR, 0, 1:2], K.half_neg[0:SR, 0:1], ALU.pow).then_inc(rstd, 1)

            @block.scalar
            def _(act):
                def square(n, k, r):
                    act.wait_ge(mean, n)
                    act.activation(sq[0:r, :], x[0:r, k, :], ACT.Square, accum_out=st[0:r, k, 0:1]).then_inc(ssq, 1)

                def keep(n, k, cols, r):
                    act.wait_ge(turned, n + 1)
                    for h in range(2):
                        act.activation(K.xh[:, 4 * h:4 * h + 4, cols], pt[2 * k + h][:, :, 0:r], ACT.Copy).then_inc(high, 1)
                act.wait_ge(x_in[0], 16)
                square(0, 0, P)
                act.wait_ge(x_in[1], 16)
                square(1, 1, P)
                keep(0, 0, slice(0, P), P)
                with act.Fori(1, TILES // 2) as g:
                    for b in range(2):
                        act.wait_ge(x_in[b], 16 * (g + 1))
                        square(2 * g + b, b, P)
                        keep(2 * g + b - 1, 1 - b, bass.ds((2 * g + b - 1) * P, P), P)
                act.wait_ge(x_in[0], 16 * (TILES // 2 + 2))
                square(TILES, 0, SR)
                keep(TILES - 1, 1, slice(SEQ - P, SEQ), P)
                keep(TILES, 0, slice(SEQ, XC), SR + DB)

            @block.vector
            def _(dve):
                dve.wait_ge(w_in, 16)

                def one(n, k, r):
                    m = SR if r != P else P
                    dve.wait_ge(ssq, n + 1)
                    dve.tensor_scalar(st[0:m, k, 1:2], st[0:m, k, 0:1], 1.0 / D, EPS, ALU.mult, ALU.add).then_inc(mean, 1)
                    if isinstance(n, int) and n < 2:
                        pass
                    else:
                        dve.wait_ge(turned, n - 1)
                    if r != P:
                        dve.tensor_copy(xn[SR:SR + DB, k, :], x[SR:SR + DB, k, :]).then_inc(prev_rows, 1)
                    dve.wait_ge(rstd, n + 1)
                    dve.scalar_tensor_tensor(out=xn[0:m, k, :], in0=x[0:m, k, :], scalar=st[0:m, k, 2:3],
                                             in1=wb[0:m, :], op0=ALU.mult, op1=ALU.mult).then_inc(norm, 1)

                def rest(n, k, cols, r):
                    for h in range(2):
                        dve.wait_ge(high, 2 * n + h + 1)
                        dve.tensor_tensor(K.xl[:, 4 * h:4 * h + 4, cols], pt[2 * k + h][:, :, 0:r],
                                          K.xh[:, 4 * h:4 * h + 4, cols].bitcast(F32), ALU.subtract).then_inc(low, 1)
                one(0, 0, P)
                one(1, 1, P)
                rest(0, 0, slice(0, P), P)
                with dve.Fori(1, TILES // 2) as g:
                    for b in range(2):
                        one(2 * g + b, b, P)
                        rest(2 * g + b - 1, 1 - b, bass.ds((2 * g + b - 1) * P, P), P)
                one(TILES, 0, SR + DB)
                rest(TILES - 1, 1, slice(SEQ - P, SEQ), P)
                rest(TILES, 0, slice(SEQ, XC), SR + DB)

            @block.tensor
            def _(pe):
                pe.wait_ge(consts, 1)

                def one(n, k, r):
                    pe.wait_ge(norm, n + 1)
                    if r != P:
                        pe.wait_ge(prev_rows, 1)
                    if not isinstance(n, int) or n >= 2:
                        pe.wait_ge(low, 2 * n - 2)
                    for kt in range(KT):
                        mm = pe.transpose(pt[2 * k + kt // 4][:, kt % 4, 0:r], xn[0:r, k, kt * P:(kt + 1) * P],
                                          K.ident[0:r, 0:r])
                    mm.then_inc(turned, 1)
                one(0, 0, P)
                one(1, 1, P)
                with pe.Fori(1, TILES // 2) as g:
                    for b in range(2):
                        one(2 * g + b, b, P)
                one(TILES, 0, SR + DB)


CONSTS = (("ident", [P, P]), ("ones", [P, P]), ("half_neg", [P, 16]), ("pair_ones", [P, P]), 
          ("causal", [P, P]), ("strict", [P, P]), ("same", [SR, SR]), ("causal_s", [SR, SR]), ("strict_s", [SR, SR]),
          ("last", [SR, SR]), ("restart", [P, TOK]), ("batch_cols", [P, DB, SR]),
          ("head_cols", [P, 2]), ("lcausal", [P, P]), ("lcausal_s", [SR, SR]))


def w_block(w, col, n):
    return w.rearrange("(kt p) c -> p kt c", p=P)[:, :, bass.ds(col, n)]


def over(eng, count, body):
    body(0, True)
    with eng.Fori(1, count - 1) as j:
        body(j, True)
    body(count - 1, False)


def phase_gdn_in(nc, K, w_in, conv_w, conv_state, a_log, dt_bias, S, p_conv, s_conv):
    with ExitStack() as ctx:
        sb = lambda n, s: ctx.enter_context(nc.sbuf_tensor("a_" + n, s, F32))
        sem = Events(nc, ctx, "a_")
        W = [sb(f"w{m}", [P, KT, P]) for m in range(4)]
        parts = lambda n, s: [ctx.enter_context(nc.sbuf_tensor(f"a_{n}{h}", s, F32R)) for h in "hl"]
        WP = [parts(f"wp{m}", [P, KT, P]) for m in range(4)]
        wg = sb("wg", [P, KT, 2 * AH])
        wgp = parts("wgp", [P, KT, 2 * AH])
        gT = sb("gt", [2 * AH, XW])
        U = [sb(f"u{m}", [P, CONV - 1 + SEQ]) for m in range(3)]
        US = [sb(f"us{m}", [P, DB, CONV - 1 + DS]) for m in range(3)]
        Y = [sb(f"y{m}", [P, TOK]) for m in range(3)]
        T = [sb(f"t{m}", [P, TOK]) for m in range(3)]
        O = [sb(f"o{m}", [P, TOK]) for m in range(3)]
        TZ = sb("tz", [P, TOK])
        Z = sb("z", [P, TILES + 1, P])
        rows = sb("rows", [64, AQKV])
        cw_rows, cs_rows = rows[0:CONV, :], rows[32:32 + DB * (CONV - 1), :]
        cw = sb("cw", [P, 3 * AH, CONV])
        cs = sb("cs", [P, 3 * AH, DB, CONV - 1])
        tail = sb("tail", [P, 3, 27])
        tails = sb("tails", [27, 3, P])
        gp = sb("gp", [P, 2, AH])
        g1 = sb("g1", [P, TILES + 1, AH])
        g2 = sb("g2", [P, TILES + 1, AH])
        g3 = sb("g3", [P, TILES + 1, AH])
        bank = [ctx.enter_context(nc.psum_tensor(f"a_bank{i}", [P, 512], F32)) for i in range(8)]
        w_ld = [sem(f"w_ld{m}") for m in range(4)]
        proj = [sem(f"proj{m}") for m in range(4)]
        evac = [sem(f"evac{m}") for m in range(3)]
        conv = [sem(f"conv{m}") for m in range(3)]
        tanh = [sem(f"tanh{m}") for m in range(4)]
        silu = [sem(f"silu{m}") for m in range(4)]
        square = [sem(f"square{m}") for m in range(2)]
        ssq = [sem(f"ssq{m}") for m in range(2)]
        logn = [sem(f"logn{m}") for m in range(2)]
        rs = [sem(f"rs{m}") for m in range(2)]
        normed = [sem(f"normed{m}") for m in range(2)]
        stored = [sem(f"stored{m}") for m in range(4)]
        high = [sem(f"high{m}") for m in range(4)]
        low = [sem(f"low{m}") for m in range(4)]
        z_t, z_kept, z_last = sem("z_t"), sem("z_kept"), sem("z_last")
        g_high, g_low, g_rows = sem("g_high"), sem("g_low"), sem("g_rows")
        halo, tailed, tails_t, tails_kept, tails_out, par, par2, pre_t, pre_k, gates, gate_a, gate_v, padded, dseq, pseq = [sem(n) for n in (
            "halo", "tailed", "tails_t", "tails_kept", "tails_out", "par", "par2", "pre_t", "pre_k", "gates", "gate_a",
            "gate_v", "padded", "dseq", "pseq")]
        ready = [silu[2], normed[0], normed[1]]

        with nc.Block() as block:
            @block.sync
            def _(sp):
                sp.dma_start(W[0][:, :, :], w_block(w_in, 0, P)).then_inc(w_ld[0], 16)
                sp.dma_start(cw_rows[:, :], conv_w).then_inc(par, 16)
                sp.dma_start(cs_rows[:, :], conv_state.rearrange("b r c -> (b r) c")).then_inc(par, 16)
                sp.dma_start(wg[:, :, :], w_block(w_in, AGATE, 2 * AH)).then_inc(par, 16)
                sp.dma_start(gp[:, 0, :], as_row(a_log)).then_inc(par2, 16)
                sp.dma_start(gp[:, 1, :], as_row(dt_bias)).then_inc(par2, 16)
                for m in range(1, 4):
                    sp.dma_start(W[m][:, :, :], w_block(w_in, m * AKEY, P)).then_inc(w_ld[m], 16)

                def load(m, j):
                    sp.wait_ge(low[m], j + 1)
                    alone(sp, K)
                    sp.dma_start(W[m][:, :, :], w_block(w_in, m * AKEY + (j + 1) * P, P)).then_inc(w_ld[m], 16)

                def body(j, more):
                    for m in range(3):
                        if more:
                            load(m, j)
                    sp.wait_ge(silu[2], j + 1)
                    alone(sp, K)
                    sp.dma_start(S.qkv[2, bass.ds(j * P, P), :], O[2][:, :]).then_inc(stored[2], 16)
                    sp.wait_ge(z_last, j + 1)
                    alone(sp, K)
                    sp.wait_ge(z_kept, 2 * (j + 1))
                    alone(sp, K)
                    sp.dma_start(S.z[0:SEQ, bass.ds(j * P, P)].rearrange("(n p) c -> p n c", p=P),
                                 Z[:, 0:TILES, :]).then_inc(stored[3], 16)
                    alone(sp, K)
                    sp.dma_start(S.z[SEQ:TOK, bass.ds(j * P, P)], Z[0:SR, TILES, :]).then_inc(stored[3], 16)
                    if more:
                        load(3, j)
                    for m in range(2):
                        sp.wait_ge(normed[m], j + 1)
                        alone(sp, K)
                        sp.dma_start(S.qkv[m, bass.ds(j * P, P), :], O[m][:, :]).then_inc(stored[m], 16)
                    sp.wait_ge(tails_kept, j + 1)
                    col = lambda t: t.rearrange("r (m c) -> r m c", m=3)[:, :, bass.ds(j * P, P)]
                    alone(sp, K)
                    sp.dma_start(col(p_conv[0]), tails[0:3, :, :]).then_inc(tails_out, 16)
                    alone(sp, K)
                    sp.dma_start(col(s_conv.rearrange("b r c -> (b r) c")), tails[3:27, :, :]).then_inc(tails_out, 16)
                over(sp, AH, body)
                for s, n in ((stored[0], 1), (stored[1], 1), (stored[2], 1), (stored[3], 2), (tails_out, 2)):
                    sp.wait_ge(s, 16 * n * AH)

            @block.gpsimd
            def _(pool):
                done = Seq(pseq, pool, 7)
                done.start(0)
                for m in range(3):
                    done(pool.memset(U[m][:, 0:CONV - 1], 0.0))
                for m in range(3):
                    done(pool.memset(US[m][:, :, :], 0.0))
                done(pool.memset(tail[:, :, :], 0.0))
                done.end()
                pool.sem_inc(padded, 1)
                pool.wait_ge(pre_k, 2)
                pool.wait_ge(g_high, 1)
                pool.tensor_tensor(wgp[1][:, :, :], wg[:, :, :], wgp[0][:, :, :].bitcast(F32), ALU.subtract).then_inc(g_low, 1)

                def split(m, j):
                    pool.wait_ge(high[m], j + 1)
                    pool.tensor_tensor(WP[m][1][:, :, :], W[m][:, :, :], WP[m][0][:, :, :].bitcast(F32), ALU.subtract
                                       ).then_inc(low[m], 1)
                for m in range(4):
                    split(m, 0)

                def body(j, more):
                    for m in range(3):
                        pool.wait_ge(conv[m], j)
                        alone(pool, K)
                        pool.tensor_copy(US[m][:, :, 0:CONV - 1], cs[:, bass.ds(m * AH + j, 1), :, :].rearrange(
                            "p a b r -> p (a b) r")).then_inc(halo, 1)
                        pool.wait_ge(halo, 3 * j + m + 1)
                    pool.wait_ge(tails_t, j)
                    for m in range(3):
                        pool.wait_ge(evac[m], 3 * (j + 1))
                        alone(pool, K)
                        pool.tensor_copy(tail[:, m, 0:3], U[m][:, SEQ:SEQ + 3]).then_inc(tailed, 1)
                        pool.wait_ge(tailed, 6 * j + 2 * m + 1)
                        alone(pool, K)
                        pool.tensor_copy(tail[:, m, 3:27].rearrange("p (b r) -> p b r", b=DB),
                                         US[m][:, :, DS:DS + CONV - 1]).then_inc(tailed, 1)
                        pool.wait_ge(tailed, 6 * j + 2 * m + 2)
                        if more:
                            split(m, j + 1)
                    if more:
                        split(3, j + 1)
                over(pool, AH, body)

            @block.scalar
            def _(act):
                def split(m, j):
                    act.wait_ge(w_ld[m], 16 * (j + 1))
                    act.wait_ge(low[m], j)
                    act.wait_ge(proj[m], 3 * j)
                    act.activation(WP[m][0][:, :, :], W[m][:, :, :], ACT.Copy).then_inc(high[m], 1)
                act.wait_ge(par, 48)
                act.activation(wgp[0][:, :, :], wg[:, :, :], ACT.Copy).then_inc(g_high, 1)
                for m in range(4):
                    split(m, 0)
                for g in range(3):
                    act.wait_ge(pre_t, g + 3)
                    n = 512 if g < 2 else P
                    act.activation(gT[:, 512 * g:512 * g + n], bank[g][0:2 * AH, 0:n], ACT.Copy).then_inc(g_rows, 1)
                act.wait_ge(padded, 1)
                act.wait_ge(gate_v, 1)
                x = bank[3][:, 0:72].rearrange("p (n h) -> p n h", h=2 * AH)
                act.activation(K.beta[:, :, :], x[:, :, 0:AH], ACT.Tanh, scale=0.5).then_inc(gate_a, 1)
                act.wait_ge(par2, 32)
                act.activation(gp[:, 0, :], gp[:, 0, :], ACT.Exp).then_inc(gate_a, 1)
                act.wait_ge(gate_v, 1)
                act.activation(g2[:, :, :], g1[:, :, :], ACT.Abs).then_inc(gate_a, 1)
                act.wait_ge(gate_a, 3)
                act.activation(g2[:, :, :], g2[:, :, :], ACT.Exp, scale=-1.0).then_inc(gate_a, 1)
                act.wait_ge(gate_a, 4)
                act.activation(g2[:, :, :], g2[:, :, :], ACT.Ln, bias=1.0).then_inc(gate_a, 1)

                def keep(m, j):
                    b0 = 3 * (m % 2)
                    act.wait_ge(conv[m], j)
                    act.wait_ge(tailed, 6 * j)
                    if m < 3:
                        act.wait_ge(halo, 3 * j + m + 1)
                    for g, (c, n) in enumerate(THIRDS):
                        act.wait_ge(proj[m], 3 * j + g + 1)
                        n = min(n, SEQ - c)
                        ins = act.activation(U[m][:, 3 + c:3 + c + n], bank[b0 + g][:, 0:n], ACT.Copy)
                        if g == 2:
                            ins = act.activation(US[m][:, :, 3:11], bank[b0 + 2][:, n:n + SR].rearrange("p (b t) -> p b t", b=DB), ACT.Copy)
                        ins.then_inc(evac[m], 1)

                def tanhs(m, j):
                    act.wait_ge(conv[m], j + 1)
                    act.wait_ge(silu[m], j)
                    if m < 2:
                        act.wait_ge(normed[m], j)
                    act.activation(T[m][:, :], Y[m][:, :], ACT.Tanh).then_inc(tanh[m], 1)

                def squares(m, j):
                    act.wait_ge(silu[m], j + 1)
                    act.activation(T[m][:, :], O[m][:, :], ACT.Square).then_inc(square[m], 1)

                def logs(m, j):
                    act.wait_ge(ssq[m], j + 1)
                    for g, (c, n) in enumerate(GROUPS):
                        src = bank[6 + g][:, 0:n] if g < 2 else bank[2][:, 128:128 + n]
                        act.activation(T[m][:, c:c + n], src, ACT.Ln, bias=EPS).then_inc(logn[m], 1)

                def body(j, more):
                    keep(0, j)
                    if more:
                        split(0, j + 1)
                    keep(1, j)
                    if more:
                        split(1, j + 1)
                    tanhs(0, j)
                    squares(0, j)
                    keep(2, j)
                    if more:
                        split(2, j + 1)
                    tanhs(1, j)
                    squares(1, j)
                    tanhs(2, j)
                    logs(0, j)
                    act.wait_ge(z_t, j)
                    for g, (c, n) in enumerate(THIRDS):
                        act.wait_ge(proj[3], 3 * j + g + 1)
                        act.activation(TZ[:, c:c + n], bank[3 + g][:, 0:n], ACT.Tanh, scale=0.5).then_inc(tanh[3], 1)
                    logs(1, j)
                    act.wait_ge(z_t, j + 1)
                    act.wait_ge(stored[3], 32 * j)
                    for g in range(2):
                        act.activation(Z[:, 4 * g:4 * g + 4, :], bank[3 + g][:, :].rearrange("p (n c) -> p n c", n=4), ACT.Copy).then_inc(z_kept, 1)
                    for m in range(2):
                        act.wait_ge(logn[m], 3 * (j + 1))
                        act.activation(T[m][:, :], T[m][:, :], ACT.Exp, scale=-0.5,
                                       bias=-0.5 * math.log(P) if m == 0 else 0.0).then_inc(rs[m], 1)
                    if more:
                        split(3, j + 1)
                over(act, AH, body)

            @block.vector
            def _(dve):
                done = Seq(dseq, dve, 4)
                done.start(0)
                dve.wait_ge(pre_t, 1)
                dve.tensor_scalar(cw[:, :, :], bank[6][:, 0:48].rearrange("p (c r) -> p c r", r=CONV), 0.5, None,
                                  ALU.mult).then_inc(pre_k, 1)
                dve.wait_ge(pre_t, 2)
                dve.tensor_copy(cs[:, :, :, :], bank[7][:, 0:288].rearrange("p (c b r) -> p c b r", b=DB, r=3)).then_inc(pre_k, 1)
                dve.wait_ge(pre_t, 6)
                dve.wait_ge(par2, 32)
                dve.tensor_tensor(g1[:, :, :], bank[3][:, 0:72].rearrange("p (n h) -> p n h", h=2 * AH)[:, :, AH:2 * AH],
                                  gp[:, 1:2, :].broadcast_to([P, TILES + 1, AH]), ALU.add).then_inc(gate_v, 1)
                dve.wait_ge(gate_a, 5)
                done(dve.tensor_scalar(K.beta[:, :, :], K.beta[:, :, :], 0.5, 0.5, ALU.mult, ALU.add))
                done(dve.tensor_scalar(g3[:, :, :], g1[:, :, :], 0.0, None, ALU.max))
                done(dve.tensor_tensor(g3[:, :, :], g3[:, :, :], g2[:, :, :], ALU.add))
                done(dve.scalar_tensor_tensor(out=K.logd[:, :, :], in0=g3[:, :, :], scalar=-1.0,
                                              in1=gp[:, 0:1, :].broadcast_to([P, TILES + 1, AH]),
                                              op0=ALU.mult, op1=ALU.mult))
                step = Seq(gates, dve, 21)

                def convolve(m, j):
                    dve.wait_ge(evac[m], 3 * (j + 1))
                    dve.wait_ge(halo, 3 * j + m + 1)
                    y, ys = Y[m][:, 0:SEQ], Y[m][:, SEQ:TOK].rearrange("p (b t) -> p b t", b=DB)
                    for r in range(CONV):
                        w = cw[:, bass.ds(m * AH + j, 1), r]
                        for o, u in ((y, U[m][:, r:r + SEQ]), (ys, US[m][:, :, r:r + DS])):
                            if r == 0:
                                ins = dve.tensor_scalar(o, u, w, None, ALU.mult)
                            else:
                                ins = dve.scalar_tensor_tensor(out=o, in0=u, scalar=w, in1=o, op0=ALU.mult, op1=ALU.add)
                            if r < CONV - 1 or o is y:
                                step(ins)
                    ins.then_inc(conv[m], 1)

                def silus(m, j):
                    dve.wait_ge(tanh[m], j + 1)
                    dve.wait_ge(conv[m], j + 1)
                    dve.wait_ge(stored[m], 16 * j)
                    dve.scalar_tensor_tensor(out=O[m][:, :], in0=T[m][:, :], scalar=1.0, in1=Y[m][:, :],
                                             op0=ALU.add, op1=ALU.mult).then_inc(silu[m], 1)

                def body(j, more):
                    step.start(j)
                    convolve(0, j)
                    silus(0, j)
                    convolve(1, j)
                    silus(1, j)
                    convolve(2, j)
                    silus(2, j)
                    for g, (c, n) in enumerate(THIRDS):
                        dve.wait_ge(tanh[3], 3 * j + g + 1)
                        dve.scalar_tensor_tensor(out=TZ[:, c:c + n], in0=TZ[:, c:c + n], scalar=1.0, in1=bank[3 + g][:, 0:n],
                                                 op0=ALU.add, op1=ALU.mult).then_inc(silu[3], 1)
                    for m in range(2):
                        dve.wait_ge(rs[m], j + 1)
                        dve.tensor_tensor(O[m][:, :], O[m][:, :], T[m][:, :], ALU.mult).then_inc(normed[m], 1)
                    dve.wait_ge(tails_t, j + 1)
                    dve.wait_ge(tails_out, 32 * j)
                    dve.wait_ge(stored[3], 32 * j)
                    dve.tensor_copy(Z[0:SR, TILES, :], bank[5][0:SR, 0:P]).then_inc(z_last, 1)
                    dve.tensor_copy(tails[:, :, :], bank[5][0:27, P:4 * P].rearrange("p (m c) -> p m c", m=3)).then_inc(tails_kept, 1)
                    step.end()
                over(dve, AH, body)

            @block.tensor
            def _(pe):
                pe.wait_ge(par, 48)
                for c in range(3 * AH):
                    mm = pe.transpose(bank[6][:, c * CONV:(c + 1) * CONV], cw_rows[:, c * P:(c + 1) * P], K.ident[0:CONV, 0:CONV])
                mm.then_inc(pre_t, 1)
                for c in range(3 * AH):
                    mm = pe.transpose(bank[7][:, c * 24:(c + 1) * 24], cs_rows[:, c * P:(c + 1) * P], K.ident[32:56, 32:56])
                mm.then_inc(pre_t, 1)
                pe.wait_ge(g_high, 1)
                pe.wait_ge(g_low, 1)
                for g in range(3):
                    n = 512 if g < 2 else P
                    for kt in range(KT):
                        x = K.xh[:, kt, 512 * g:512 * g + n], K.xl[:, kt, 512 * g:512 * g + n]
                        mm = products(pe, bank[g][0:2 * AH, 0:n], (wgp[0][:, kt, :], wgp[1][:, kt, :]), x, kt == 0, kt == KT - 1)
                    mm.then_inc(pre_t, 1)
                pe.wait_ge(g_rows, 3)
                for n in range(TILES + 1):
                    mm = pe.transpose(bank[3][:, n * 8:(n + 1) * 8], gT[:, n * P:(n + 1) * P], K.ident[0:2 * AH, 0:2 * AH])
                mm.then_inc(pre_t, 1)
                pe.wait_ge(gate_v, 1)
                pe.wait_ge(gate_a, 1)
                pe.wait_ge(pre_k, 2)

                def sums(m, j):
                    pe.wait_ge(square[m], j + 1)
                    if m == 0:
                        pe.wait_ge(logn[1], 3 * j)
                    else:
                        pe.wait_ge(logn[0], 3 * (j + 1))
                    for g, (c, n) in enumerate(GROUPS):
                        dst = bank[6 + g][:, 0:n] if g < 2 else bank[2][:, 128:128 + n]
                        mm = pe.matmul(dst, K.ones[:, :], T[m][:, c:c + n], start=True, stop=True)
                    mm.then_inc(ssq[m], 1)

                def body(j, more):
                    for m in range(3):
                        b0 = 3 * (m % 2)
                        if m == 0:
                            pe.wait_ge(evac[2], 3 * j)
                        elif m == 1:
                            pe.wait_ge(z_kept, 2 * j)
                            pe.wait_ge(tails_kept, j)
                        else:
                            pe.wait_ge(evac[0], 3 * (j + 1))
                        pe.wait_ge(high[m], j + 1)
                        pe.wait_ge(low[m], j + 1)
                        for g, (c, n) in enumerate(THIRDS):
                            if m == 0 and g == 2:
                                pe.wait_ge(logn[1], 3 * j)
                            for kt in range(KT):
                                w = WP[m][0][:, kt, :], WP[m][1][:, kt, :]
                                x = K.xh[:, kt, c:c + n], K.xl[:, kt, c:c + n]
                                mm = products(pe, bank[b0 + g][:, 0:n], w, x, kt == 0, kt == KT - 1)
                            mm.then_inc(proj[m], 1)
                    pe.wait_ge(evac[2], 3 * (j + 1))
                    sums(0, j)
                    pe.wait_ge(evac[1], 3 * (j + 1))
                    pe.wait_ge(high[3], j + 1)
                    pe.wait_ge(low[3], j + 1)
                    for g, (c, n) in enumerate(THIRDS):
                        for kt in range(KT):
                            w = WP[3][0][:, kt, :], WP[3][1][:, kt, :]
                            x = K.xh[:, kt, c:c + n], K.xl[:, kt, c:c + n]
                            mm = products(pe, bank[3 + g][:, 0:n], w, x, kt == 0, kt == KT - 1)
                        mm.then_inc(proj[3], 1)
                    sums(1, j)
                    pe.wait_ge(silu[3], 3 * (j + 1))
                    for n in range(TILES + 1):
                        r = P if n < TILES else SR
                        mm = pe.transpose(bank[3 + n // 4][0:r, (n % 4) * P:(n % 4 + 1) * P], TZ[:, n * P:n * P + r], K.ident[:, :])
                    mm.then_inc(z_t, 1)
                    pe.wait_ge(tailed, 6 * (j + 1))
                    for m in range(3):
                        mm = pe.transpose(bank[5][0:27, (m + 1) * P:(m + 2) * P], tail[:, m, :], K.ident[:, :])
                    mm.then_inc(tails_t, 1)
                over(pe, AH, body)


def phase_rwkv_in(nc, K, w_in, mu, w0, w2, a0, a2, k_k, k_a, r_k, S):
    with ExitStack() as ctx:
        sb = lambda n, s: ctx.enter_context(nc.sbuf_tensor("b_" + n, s, F32))
        sem = Events(nc, ctx, "b_")
        W = [sb(f"w{m}", [P, KT, P]) for m in range(4)]
        WP = [[ctx.enter_context(nc.sbuf_tensor(f"b_wp{m}{h}", [P, KT, P], F32R)) for h in "hl"] for m in range(4)]
        U = [sb(f"u{m}", [P, 1 + SEQ]) for m in range(4)]
        US = [sb(f"us{m}", [P, DB, 1 + DS]) for m in range(4)]
        X = [sb(f"x{m}", [P, TOK]) for m in range(4)]
        LO = sb("lo", [P, TOK])
        lora = sb("lora", [P, P])
        T1 = sb("t1", [P, XW])
        par_rows = sb("par_rows", [24, P])
        par = sb("par", [P, 24])
        mu_rows = sb("mu_rows", [17, P])
        mus = sb("mus", [P, 17])
        lw, kk, G, E1, E2, E3, A = [sb(n, [P, TOK]) for n in ("lw", "kk", "g", "e1", "e2", "e3", "a")]
        bank = [ctx.enter_context(nc.psum_tensor(f"b_bank{i}", [P, 512], F32)) for i in range(8)]
        w_ld = [sem(f"w_ld{m}") for m in range(4)]
        proj = [sem(f"proj{m}") for m in range(4)]
        evac = [sem(f"evac{m}") for m in range(4)]
        mixed = [sem(f"mixed{m}") for m in range(4)]
        outs = [sem(f"out{m}") for m in range(6)]
        stored = [sem(f"stored{m}") for m in range(6)]
        high = [sem(f"high{m}") for m in range(4)]
        low = [sem(f"low{m}") for m in range(4)]
        (par_in, lora_in, turned, par_kept, lo_ready, lo_a, gate_mm, gate_t, sq, ssq, ssq_free, rs, gt, expo, gc, gsub,
         rk_ready, bonus_mm, bonus_kept, dseq, pseq, zeroed, ends, kk_ready) = [sem(n) for n in (
             "par_in", "lora_in", "turned", "par_kept", "lo_ready", "lo_a", "gate_mm", "gate_t", "sq", "ssq", "ssq_free",
             "rs", "gt", "expo", "gc", "gsub", "rk_ready", "bonus_mm", "bonus_kept", "dseq", "pseq", "zeroed", "ends", "kk_ready")]
        B0 = ACOLS
        SUM, BONUS = 376, 440
        KK, KA, RK, W0, A0 = 0, 4, 8, 12, 16

        def shifted(m):
            return ((U[m][:, 1:1 + SEQ], U[m][:, 0:SEQ]), (US[m][:, :, 1:1 + DS], US[m][:, :, 0:DS]))

        def halves(t):
            return t[:, 0:SEQ], t[:, SEQ:TOK].rearrange("p (b t) -> p b t", b=DB)

        with nc.Block() as block:
            @block.sync
            def _(sp):
                sp.dma_start(W[0][:, :, :], w_block(w_in, B0 + 4 * BW, P)).then_inc(w_ld[0], 16)
                for n, t in enumerate((k_k, k_a, r_k.rearrange("h n -> (h n)"), w0, a0)):
                    sp.dma_start(par_rows[4 * n:4 * n + 4, :], t.rearrange("(j p) -> j p", p=P)).then_inc(par_in, 16)
                sp.dma_start(mu_rows[:, :], mu.rearrange("(j p) -> j p", p=P)).then_inc(par_in, 16)
                sp.dma_start(lora[0:64, :], w2[:, 0:P]).then_inc(lora_in, 16)
                sp.dma_start(lora[64:128, :], a2[:, 0:P]).then_inc(lora_in, 16)
                for m in range(1, 4):
                    sp.dma_start(W[m][:, :, :], w_block(w_in, B0 + m * BW, P)).then_inc(w_ld[m], 16)
                sp.wait_ge(low[0], 1)
                sp.dma_start(W[0][:, :, :], w_block(w_in, B0, P)).then_inc(w_ld[0], 16)

                def body(j, more):
                    for m in range(4):
                        if more:
                            sp.wait_ge(low[m], j + 1 + (1 if m == 0 else 0))
                            alone(sp, K)
                            sp.dma_start(W[m][:, :, :], w_block(w_in, B0 + m * BW + (j + 1) * P, P)).then_inc(w_ld[m], 16)
                    if more:
                        sp.wait_ge(gate_mm, 2 * (j + 1))
                        alone(sp, K)
                        sp.dma_start(lora[0:64, :], w2[:, bass.ds((j + 1) * P, P)]).then_inc(lora_in, 16)
                        sp.dma_start(lora[64:128, :], a2[:, bass.ds((j + 1) * P, P)]).then_inc(lora_in, 16)
                    for m, t in ((4, X[2]), (5, X[3]), (0, X[0]), (1, E2), (2, kk), (3, X[1])):
                        sp.wait_ge(outs[m], j + 1)
                        alone(sp, K)
                        sp.dma_start(S.rw[m, bass.ds(j * P, P), :], t[:, :]).then_inc(stored[m], 16)
                over(sp, NP, body)
                for s in stored:
                    sp.wait_ge(s, 16 * NP)

            @block.gpsimd
            def _(pool):
                done = Seq(pseq, pool, 5)
                done.start(0)
                for m in range(4):
                    done(pool.memset(U[m][:, 0:1], 0.0))
                done(pool.memset(T1[:, TOK:XW], 0.0))
                done.end()
                pool.sem_inc(zeroed, 1)

                def split(m, k):
                    pool.wait_ge(high[m], k + 1)
                    pool.tensor_tensor(WP[m][1][:, :, :], W[m][:, :, :], WP[m][0][:, :, :].bitcast(F32), ALU.subtract
                                       ).then_inc(low[m], 1)
                for m, k in ((0, 0), (1, 0), (2, 0), (3, 0), (0, 1)):
                    split(m, k)

                def body(j, more):
                    if more:
                        split(0, j + 2)
                        for m in range(1, 4):
                            split(m, j + 1)
                over(pool, NP, body)

            @block.scalar
            def _(act):
                act.wait_ge(zeroed, 1)

                def keep(m, j, base):
                    act.wait_ge(mixed[m], j + (1 if base else 0))
                    b0 = 3 * (m % 2)
                    for g, (c, n) in enumerate(THIRDS):
                        act.wait_ge(proj[m], 3 * j + base + g + 1)
                        n = min(n, SEQ - c)
                        ins = act.activation(U[m][:, 1 + c:1 + c + n], bank[b0 + g][:, 0:n], ACT.Copy)
                        if g == 2:
                            act.activation(US[m][:, :, 1:1 + DS], bank[b0 + 2][:, n:n + SR].rearrange("p (b t) -> p b t", b=DB), ACT.Copy)
                            ins = act.activation(US[m][:, :, 0], bank[b0 + 2][:, n + SR:n + SR + DB], ACT.Copy)
                        ins.then_inc(evac[m], 1)

                def split(m, k):
                    act.wait_ge(w_ld[m], 16 * (k + 1))
                    act.wait_ge(low[m], k)
                    act.wait_ge(proj[m], 3 * k)
                    act.activation(WP[m][0][:, :, :], W[m][:, :, :], ACT.Copy).then_inc(high[m], 1)
                for m in range(4):
                    split(m, 0)
                keep(0, 0, 0)
                split(0, 1)
                act.wait_ge(mixed[0], 1)
                act.activation(LO[0:64, :], LO[0:64, :], ACT.Tanh).then_inc(lo_a, 1)

                def body(j, more):
                    act.wait_ge(expo, 3 * j)
                    act.wait_ge(gsub, j)
                    act.wait_ge(outs[3], j)
                    act.wait_ge(outs[2], j)
                    keep(0, j, 3)
                    act.wait_ge(gate_mm, 2 * j + 1)
                    act.wait_ge(par_kept, 2)
                    for g, (c, n) in enumerate(GROUPS):
                        src = bank[6 + g][:, 0:n] if g < 2 else bank[5][:, SUM:SUM + n]
                        act.activation(lw[:, c:c + n], src, ACT.Tanh, scale=0.5, bias=par[:, bass.ds(W0 + j, 1)]).then_inc(gate_t, 1)
                    keep(1, j, 0)
                    if more:
                        split(0, j + 2)
                    act.wait_ge(mixed[1], j + 1)
                    act.wait_ge(outs[0], j)
                    act.activation(E1[:, :], X[1][:, :], ACT.Square, scale=par[:, bass.ds(KK + j, 1)]).then_inc(sq, 1)
                    keep(2, j, 0)
                    if more:
                        split(1, j + 1)
                    act.wait_ge(gate_mm, 2 * j + 2)
                    for g, (c, n) in enumerate(GROUPS):
                        src = bank[6 + g][:, 0:n] if g < 2 else bank[5][:, SUM:SUM + n]
                        act.activation(A[:, c:c + n], src, ACT.Tanh, scale=0.5, bias=par[:, bass.ds(A0 + j, 1)]).then_inc(gate_t, 1)
                    keep(3, j, 0)
                    if more:
                        split(2, j + 1)
                    act.wait_ge(mixed[3], j + 1)
                    act.wait_ge(stored[1], 16 * j)
                    act.activation(E2[:, :], X[3][:, :], ACT.Tanh, scale=0.5).then_inc(gt, 1)
                    act.wait_ge(ssq, j + 1)
                    for g, (c, n) in enumerate(GROUPS):
                        src = bank[6 + g][:, 0:n] if g < 2 else bank[5][:, SUM:SUM + n]
                        act.activation(E3[:, c:c + n], src, ACT.Ln, bias=EPS).then_inc(ssq_free, 1)
                    act.wait_ge(ssq_free, 3 * (j + 1))
                    act.activation(E3[:, :], E3[:, :], ACT.Exp, scale=-0.5).then_inc(rs, 1)
                    act.wait_ge(gc, j + 1)
                    act.wait_ge(ssq, j + 1)
                    act.activation(E1[:, :], G[:, :], ACT.Exp).then_inc(expo, 1)
                    act.wait_ge(gsub, j + 1)
                    act.wait_ge(outs[5], j + 1)
                    act.activation(E2[:, :], lw[:, :], ACT.Exp).then_inc(expo, 1)
                    act.wait_ge(kk_ready, j + 1)
                    act.activation(E3[:, :], G[:, :], ACT.Exp, scale=-1.0).then_inc(expo, 1)
                    act.activation(K.rw_in[:, bass.ds(j, 1), :], K.rw_mid[:, bass.ds(j, 1), :], ACT.Exp).then_inc(ends, 1)
                    act.activation(K.rw_out[:, bass.ds(j, 1), 0:TILES], G[:, P - 1:SEQ:P], ACT.Exp).then_inc(ends, 1)
                    act.activation(K.rw_out[:, bass.ds(j, 1), TILES:TILES + DB], G[:, SEQ + DS - 1:TOK:DS], ACT.Exp).then_inc(ends, 1)
                    if more:
                        split(3, j + 1)
                over(act, NP, body)

            @block.vector
            def _(dve):
                dve.wait_ge(turned, 2)
                dve.tensor_copy(mus[:, :], bank[6][:, 0:17]).then_inc(par_kept, 1)
                dve.tensor_copy(par[:, 0:12], bank[6][:, 32:44]).then_inc(dseq, 1)
                dve.tensor_scalar(par[:, 12:20], bank[6][:, 44:52], 0.5, None, ALU.mult).then_inc(par_kept, 1)
                dve.wait_ge(dseq, 1)
                dve.tensor_scalar(par[:, 4:8], par[:, 4:8], 0.5, None, ALU.mult).then_inc(dseq, 1)
                dve.wait_ge(dseq, 2)
                dve.tensor_scalar(par[:, 20:24], par[:, 4:8], -1.0, 1.0, ALU.mult, ALU.add).then_inc(dseq, 1)
                dve.wait_ge(dseq, 3)
                dve.wait_ge(par_kept, 2)

                one = Seq(dseq, dve, 19)

                def blend(m, dst, col, n):
                    dve.wait_ge(evac[m], n)
                    now_s, now_d = shifted(m)
                    ds_, dd_ = halves(dst)
                    one(dve.tensor_tensor(ds_, now_s[1], now_s[0], ALU.subtract))
                    one(dve.tensor_tensor(dd_, now_d[1], now_d[0], ALU.subtract))
                    one(dve.scalar_tensor_tensor(out=ds_, in0=ds_, scalar=mus[:, col], in1=now_s[0], op0=ALU.mult, op1=ALU.add))
                    dve.scalar_tensor_tensor(out=dd_, in0=dd_, scalar=mus[:, col], in1=now_d[0],
                                             op0=ALU.mult, op1=ALU.add).then_inc(mixed[m], 1)
                one.start(0)
                one.n = 3
                blend(0, LO, slice(16, 17), 3)

                def keep_bonus(j):
                    dve.wait_ge(bonus_mm, j + 1)
                    dve.tensor_copy(K.bonus[:, :, bass.ds(2 * j, 2)], bank[2][:, BONUS:BONUS + 18].rearrange("p (n h) -> p n h", h=2)
                                    ).then_inc(bonus_kept, 1)

                def body(j, more):
                    one.start(j)
                    one.base = one.base + 6
                    dve.wait_ge(stored[0], 16 * j)
                    blend(0, X[0], bass.ds(0 + j, 1), 3 * j + 6)
                    dve.wait_ge(gate_t, 6 * j + 3)
                    one(dve.tensor_scalar(lw[:, :], lw[:, :], 1.0, -0.5 * DECAY, ALU.add, ALU.mult))
                    dve.wait_ge(ends, 3 * j)
                    one(dve.tensor_tensor_scan(G[:, :], K.restart[:, :], lw[:, :], 0.0, ALU.mult, ALU.add))
                    one(dve.tensor_copy(K.rw_mid[:, bass.ds(j, 1), :], G[:, P // 2 - 1:SEQ:P]))
                    g3 = G[:, 0:SEQ].rearrange("p (n t) -> p n t", n=TILES)
                    mid = K.rw_mid[:, bass.ds(j, 1), :].rearrange("p a n -> p (a n)")
                    one(dve.tensor_tensor(g3, g3, mid.rearrange("p (n a) -> p n a", a=1).broadcast_to([P, TILES, P]), ALU.subtract))
                    dve.sem_inc(gc, 1)
                    dve.tensor_tensor(lw[:, :], G[:, :], lw[:, :], ALU.subtract).then_inc(gsub, 1)
                    dve.wait_ge(stored[3], 16 * j)
                    blend(1, X[1], bass.ds(4 + j, 1), 3 * j + 3)
                    if not isinstance(j, int) or j > 0:
                        keep_bonus(j - 1)
                    dve.wait_ge(stored[4], 16 * j)
                    blend(2, X[2], bass.ds(8 + j, 1), 3 * j + 3)
                    dve.wait_ge(mixed[2], j + 1)
                    dve.sem_inc(outs[4], 1)
                    dve.wait_ge(stored[5], 16 * j)
                    blend(3, X[3], bass.ds(12 + j, 1), 3 * j + 3)
                    dve.wait_ge(gt, j + 1)
                    dve.wait_ge(mixed[3], j + 1)
                    dve.scalar_tensor_tensor(out=X[3][:, :], in0=E2[:, :], scalar=1.0, in1=X[3][:, :],
                                             op0=ALU.add, op1=ALU.mult).then_inc(outs[5], 1)
                    dve.wait_ge(rs, j + 1)
                    dve.wait_ge(mixed[1], j + 1)
                    dve.wait_ge(stored[2], 16 * j)
                    dve.scalar_tensor_tensor(out=kk[:, :], in0=X[1][:, :], scalar=par[:, bass.ds(KK + j, 1)], in1=E3[:, :],
                                             op0=ALU.mult, op1=ALU.mult).then_inc(kk_ready, 1)
                    dve.wait_ge(gate_t, 6 * j + 6)
                    dve.wait_ge(bonus_kept, j)
                    one(dve.tensor_scalar(T1[:, 0:TOK], A[:, :], par[:, bass.ds(KA + j, 1)],
                                          par[:, bass.ds(20 + j, 1)], ALU.mult, ALU.add))
                    one(dve.tensor_tensor(X[1][:, :], X[1][:, :], T1[:, 0:TOK], ALU.mult))
                    dve.wait_ge(mixed[0], j + 2)
                    dve.scalar_tensor_tensor(out=T1[:, 0:TOK], in0=X[1][:, :], scalar=par[:, bass.ds(RK + j, 1)], in1=X[0][:, :],
                                             op0=ALU.mult, op1=ALU.mult).then_inc(rk_ready, 1)
                    dve.wait_ge(expo, 3 * j + 1)
                    dve.wait_ge(rk_ready, j + 1)
                    dve.tensor_tensor(X[0][:, :], X[0][:, :], E1[:, :], ALU.mult).then_inc(outs[0], 1)
                    dve.wait_ge(expo, 3 * j + 3)
                    dve.wait_ge(kk_ready, j + 1)
                    dve.wait_ge(stored[1], 16 * j)
                    dve.tensor_tensor(E2[:, :], kk[:, :], E2[:, :], ALU.mult).then_inc(outs[1], 1)
                    one(dve.scalar_tensor_tensor(out=A[:, :], in0=A[:, :], scalar=1.0, in1=kk[:, :], op0=ALU.add, op1=ALU.mult))
                    dve.wait_ge(outs[1], j + 1)
                    dve.scalar_tensor_tensor(out=kk[:, :], in0=A[:, :], scalar=0.5, in1=E3[:, :],
                                             op0=ALU.mult, op1=ALU.mult).then_inc(outs[2], 1)
                    dve.tensor_tensor(X[1][:, :], X[1][:, :], E3[:, :], ALU.mult).then_inc(outs[3], 1)
                    one.end()
                over(dve, NP, body)
                keep_bonus(NP - 1)

            @block.tensor
            def _(pe):
                pe.wait_ge(par_in, 96)
                pe.transpose(bank[6][:, 0:17], mu_rows[:, :], K.ident[0:17, 0:17]).then_inc(turned, 1)
                pe.transpose(bank[6][:, 32:52], par_rows[0:20, :], K.ident[0:20, 0:20]).then_inc(turned, 1)

                def project(m, k, before_last):
                    b0 = 3 * (m % 2)
                    pe.wait_ge(high[m], k + 1)
                    pe.wait_ge(low[m], k + 1)
                    for g, (c, n) in enumerate(THIRDS):
                        if g == 2:
                            n = XC - c
                            before_last()
                        for kt in range(KT):
                            w = WP[m][0][:, kt, :], WP[m][1][:, kt, :]
                            x = K.xh[:, kt, c:c + n], K.xl[:, kt, c:c + n]
                            mm = products(pe, bank[b0 + g][:, 0:n], w, x, kt == 0, kt == KT - 1)
                        mm.then_inc(proj[m], 1)

                def gate(half, j):
                    r = slice(64 * half, 64 * half + 64)
                    for g, (c, n) in enumerate(GROUPS):
                        dst = bank[6 + g][:, 0:n] if g < 2 else bank[5][:, SUM:SUM + n]
                        mm = pe.matmul(dst, lora[r, :], LO[r, c:c + n], start=True, stop=True)
                    mm.then_inc(gate_mm, 1)

                def bonus(j):
                    pe.wait_ge(rk_ready, j + 1)
                    for n in range(TILES + 1):
                        mm = pe.matmul(bank[2][:, BONUS + 2 * n:BONUS + 2 * n + 2], T1[:, n * P:(n + 1) * P], K.head_cols[:, :],
                                       start=True, stop=True)
                    mm.then_inc(bonus_mm, 1)

                def nothing():
                    pass
                project(0, 0, nothing)
                pe.wait_ge(lora_in, 32)
                pe.wait_ge(lo_a, 1)
                pe.wait_ge(par_kept, 2)
                pe.wait_ge(evac[0], 3)

                def body(j, more):
                    later = not isinstance(j, int) or j > 0

                    def read_w():
                        pe.wait_ge(gate_t, 6 * j + 3)

                    def read_a():
                        pe.wait_ge(gate_t, 6 * j + 6)

                    def read_bonus():
                        if later:
                            pe.wait_ge(bonus_kept, j)
                    pe.wait_ge(evac[2], 3 * j)
                    project(0, j + 1, nothing)
                    pe.wait_ge(ssq_free, 3 * j)
                    pe.wait_ge(evac[3], 3 * j)
                    pe.wait_ge(lora_in, 32 * (j + 1))
                    gate(0, j)
                    project(1, j, read_w)
                    pe.wait_ge(evac[0], 3 * j + 6)
                    if later:
                        bonus(j - 1)
                    project(2, j, read_bonus)
                    pe.wait_ge(gate_t, 6 * j + 3)
                    pe.wait_ge(evac[1], 3 * j + 3)
                    gate(1, j)
                    project(3, j, read_a)
                    pe.wait_ge(evac[3], 3 * j + 3)
                    pe.wait_ge(sq, j + 1)
                    for g, (c, n) in enumerate(GROUPS):
                        dst = bank[6 + g][:, 0:n] if g < 2 else bank[5][:, SUM:SUM + n]
                        mm = pe.matmul(dst, K.pair_ones[:, :], E1[:, c:c + n], start=True, stop=True)
                    mm.then_inc(ssq, 1)
                over(pe, NP, body)
                pe.wait_ge(evac[2], 3 * NP)
                bonus(NP - 1)


LEVELS = 7
LEVELS_S = 3


def phase_mix0(nc, K, w_out, norm_w, gdn_norm, ln_w, ln_b, x_prompt, x_sample, gdn0, rwkv0, S,
               p_gdn, p_rwkv, s_gdn, s_rwkv):
    with ExitStack() as ctx:
        sb = lambda n, s: ctx.enter_context(nc.sbuf_tensor("c_" + n, s, F32))
        ev = Events(nc, ctx, "c_")

        QK = sb("qk", [P, 2, AH, P])
        V = sb("v", [P, AH, P])
        RW = sb("rw", [P, 4, NP, P])
        VG = sb("vg", [P, 2, NP, P])
        Z = sb("z", [P, AKEY])
        XR = sb("xr", [P, D])
        wo = sb("wo", [P, KT, D])
        nw = sb("nw", [P, D])
        gnw = sb("gnw", [P, P])
        lnw = sb("lnw", [P, BW])
        lnb = sb("lnb", [P, BW])
        ld, bt, nbt, bo = sb("ld", [P, AH]), sb("bt", [P, AH]), sb("nbt", [P, AH]), sb("bo", [P, BH])
        g, eg = sb("g", [P, AH]), sb("eg", [P, AH])
        dend = sb("dend", [P, AH])
        dec = sb("dec", [P, AH, P])
        eGB = sb("egb", [P, AH, P])
        attn = sb("attn", [P, AH, P])
        NT = sb("nt", [P, AH, P])
        SC = sb("sc", [P, BH, 4, P])
        mask4 = sb("mask4", [P, 4, P])
        mask4s = sb("mask4s", [SR, 4, SR])
        lev = sb("lev", [P, LEVELS, P])
        kr, vr = sb("kr", [P, AH, P]), sb("vr", [P, AH, P])
        Br, Kr, Vr, Gr = [sb(n, [P, BW]) for n in ("br", "krr", "vrr", "grr")]
        X = [sb(f"inv{u}", [P, 4, P]) for u in range(3)]
        XT = [sb(f"invt{u}", [P, 4, P]) for u in range(3)]
        Yall = sb("y", [P, 3, 4, P])
        Y = [Yall[:, u, :, :] for u in range(3)]
        M = [sb(f"m{u}", [P, 4, P]) for u in range(3)]
        Wr = sb("wr", [P, AH, P])
        NV = sb("nv", [P, AH, P])
        NVd = sb("nvd", [P, AH, P])
        RH = sb("rh", [P, BW])
        SA = sb("sa", [P, BW])
        St = sb("st", [P, AH, P])
        Tt = sb("tt", [P, NP, P])
        Th = sb("th", [P, NP, P])
        sqa, sqb = sb("sqa", [P, BW]), sb("sqb", [P, BW])
        st = sb("stats", [P, 12])
        rstd = sb("rstd", [P, 12])
        mean = sb("mean", [P, BH])
        OR = sb("or", [P, D])
        bv = sb("bv", [P, BW])
        gw = sb("gw", [P, BW])
        OT = sb("ot", [P, KT, P])
        x1 = XR
        n1 = sb("n1", [P, 4])
        xn = sb("xn", [P, D])
        QG = sb("qg", [P, AH, P])
        tr = Wr
        bank = [ctx.enter_context(nc.psum_tensor(f"c_bank{i}", [P, 512], F32)) for i in range(8)]
        Sb = sb("sb", [P, DB, AH, P])
        Tb = sb("tb", [P, DB, NP, 64])
        Rb = Yall[0:64, 0:2, :, :]
        Q1 = sb("q1", [P, DB, SR])

        def v4(b, r=P, c=P):
            return bank[b][0:r, 0:4 * P].rearrange("p (h c) -> p h c", h=4)[:, :, 0:c]

        def half(t, l, T, s):
            if len(t.shape) == 2:
                return t[:, 0:T].rearrange("p (b u h) -> p b u h", u=2, h=1 << l)[:, :, s, :]
            return t[:, :, 0:T].rearrange("p k (b u h) -> p k b u h", u=2, h=1 << l)[:, :, :, s, :]

        def packed(b, l, T, r):
            return bank[b][0:r, :].rearrange("p (k c) -> p k c", k=4)[:, :, 0:T // 2].rearrange("p k (b h) -> p k b h", h=1 << l)

        def bc(t, shape):
            return t.broadcast_to(shape)

        with nc.Block() as block:
            @block.sync
            def _(sp):
                sp.dma_start(wo[:, :, :], w_block(w_out, 0, D)).then_inc(ev("ld_wo"), 16)
                for t, v in ((nw, norm_w), (gnw, gdn_norm), (lnw, ln_w), (lnb, ln_b)):
                    sp.dma_start(t[:, :], as_row(v)).then_inc(ev("ld_par"), 16)

                col = lambda t, c, T: t.rearrange("(h p) t -> p h t", p=P)[:, :, bass.ds(c, T)]

                def load_qkv(c, T):
                    for m in range(2):
                        sp.dma_start(QK[:, m, :, 0:T], col(S.qkv[m], c, T)).then_inc(ev("ld_qk"), 16)
                    sp.dma_start(V[:, :, 0:T], col(S.qkv[2], c, T)).then_inc(ev("ld_v"), 16)

                def load_abk(c, T):
                    for m in range(1, 4):
                        sp.dma_start(RW[:, m, :, 0:T], col(S.rw[m], c, T)).then_inc(ev("ld_rw"), 16)
                    for m in range(2):
                        sp.dma_start(VG[:, m, :, 0:T], col(S.rw[4 + m], c, T)).then_inc(ev("ld_vg"), 16)

                def load_r(c, T):
                    sp.dma_start(RW[:, 0, :, 0:T], col(S.rw[0], c, T)).then_inc(ev("ld_r"), 16)

                def load_z(c, T):
                    sp.dma_start(Z[0:T, :], S.z[bass.ds(c, T), :]).then_inc(ev("ld_z"), 16)

                def load_x(c, T):
                    x = x_prompt[0, bass.ds(c, T), :] if T == P else x_sample.rearrange("b t d -> (b t) d")
                    sp.dma_start(XR[0:T, :], x).then_inc(ev("ld_x"), 16)

                def during(i, ahead):
                    n, c = i + 1, i * P
                    sp.wait_ge(ev("rows_a"), n)
                    sp.wait_ge(ev("rhs_a"), n)
                    sp.wait_ge(ev("qg"), n)
                    alone(sp, K)
                    load_qkv(c + P, ahead)
                    sp.wait_ge(ev("rows_vg"), n)
                    sp.wait_ge(ev("rows_b"), n)
                    sp.wait_ge(ev("rhs_b"), n)
                    alone(sp, K)
                    load_abk(c + P, ahead)
                    if not (isinstance(i, int) and i == 0):
                        sp.wait_ge(ev("oa"), i)
                        alone(sp, K)
                        load_z(c, P)
                        sp.wait_ge(ev("x1"), i)
                        alone(sp, K)
                        sp.dma_start(S.x1[bass.ds(c - P, P), :], x1[:, :]).then_inc(ev("stored"), 16)
                    sp.wait_ge(ev("out_b"), n)
                    alone(sp, K)
                    load_r(c + P, ahead)
                    if not (isinstance(i, int) and i == 0):
                        sp.wait_ge(ev("xn1"), i)
                        alone(sp, K)
                        sp.wait_ge(ev("stored"), 16 * i)
                        alone(sp, K)
                        load_x(c, P)
                        sp.wait_ge(ev("xk_a"), i)
                        sp.wait_ge(ev("xk_b"), i)
                        alone(sp, K)
                        sp.dma_start(S.xnT[:, :, bass.ds(c - P, P)], OT[:, :, :]).then_inc(ev("xn_out"), 16)

                def after(i, T):
                    c = i * P
                    if i < TILES:
                        sp.wait_ge(ev("oa"), i + 1)
                        load_z(SEQ, SR)
                    sp.wait_ge(ev("x1"), i + 1)
                    sp.dma_start(S.x1[c:c + T, :], x1[0:T, :]).then_inc(ev("stored"), 16)
                    if i < TILES:
                        sp.wait_ge(ev("xn1"), i + 1)
                        sp.wait_ge(ev("stored"), 16 * (i + 1))
                        load_x(SEQ, SR)
                    sp.wait_ge(ev("xk_a"), i + 1)
                    sp.wait_ge(ev("xk_b"), i + 1)
                    sp.dma_start(S.xnT[:, :, c:c + T], OT[:, :, 0:T]).then_inc(ev("xn_out"), 16)
                load_qkv(0, P)
                load_abk(0, P)
                load_r(0, P)
                load_z(0, P)
                load_x(0, P)
                for i in range(2):
                    during(i, P)
                with sp.Fori(2, TILES - 1) as i:
                    during(i, P)
                during(TILES - 1, SR)
                after(TILES - 1, P)
                sp.wait_ge(ev("state_a"), TILES)
                sp.dma_start(p_gdn[0].rearrange("h d v -> d h v"), St[:, :, :]).then_inc(ev("st_out"), 16)
                sp.dma_start(Sb[:, :, :, :], gdn0.rearrange("b h d v -> d b h v")).then_inc(ev("ld_sb"), 16)
                for b in range(DB):
                    if b >= 2:
                        sp.wait_ge(ev("tb_mm"), b // 2)
                    sp.dma_start(Rb[:, b % 2, :, :].rearrange("v j (h k) -> v (j h) k", h=2),
                                 rwkv0[b].rearrange("h v k -> v h k")).then_inc(ev("ld_rb"), 16)
                sp.wait_ge(ev("tr"), 1)
                for h in range(2):
                    r = slice(64 * h, 64 * h + 64)
                    sp.dma_start(p_rwkv[0].rearrange("(j h) v k -> h v j k", h=2)[h], tr[r, :, r]).then_inc(ev("tr_out"), 16)
                after(TILES, SR)
                for b in range(DB):
                    sp.wait_ge(ev("rb_new"), b + 1)
                    sp.dma_start(s_rwkv[b].rearrange("h v k -> v h k"),
                                 Rb[:, b % 2, :, :].rearrange("v j (h k) -> v (j h) k", h=2)).then_inc(ev(f"rb_out{b % 2}"), 16)
                sp.wait_ge(ev("sb_new"), DB)
                sp.dma_start(s_gdn.rearrange("b h d v -> d b h v"), Sb[:, :, :, :]).then_inc(ev("st_out"), 16)
                sp.wait_ge(ev("st_out"), 16 * 2)
                sp.wait_ge(ev("tr_out"), 16 * 2)
                for m in range(2):
                    sp.wait_ge(ev(f"rb_out{m}"), 16 * DB // 2)
                sp.wait_ge(ev("stored"), 16 * (TILES + 1))
                sp.wait_ge(ev("xn_out"), 16 * (TILES + 1))

            @block.gpsimd
            def _(pool):
                done = Seq(ev("pool_seq"), pool, 8 + 4 * LEVELS)
                done.start(0)
                m4 = ((K.causal, -1.0), (K.strict, 1.0), (K.causal, 1.0), (K.strict, 1.0))
                for n, (m, f) in enumerate(m4):
                    done(pool.tensor_scalar(mask4[:, n, :], m[:, :], f, None, ALU.mult))
                for n, (m, f) in enumerate(((K.causal_s, -1.0), (K.strict_s, 1.0), (K.causal_s, 1.0), (K.strict_s, 1.0))):
                    done(pool.tensor_scalar(mask4s[:, n, :], m[:, :], f, None, ALU.mult))
                for l in range(LEVELS):
                    h = 1 << l
                    nb = P // (2 * h)
                    done(pool.memset(lev[:, l, :], 0.0))
                    v = lev[:, l, :].rearrange("s (b u t) -> s b u t", u=2, t=h)[:, :, 1, :]
                    done(pool.memset(v, 1.0))
                    done(pool.affine_select(out=v, in_=v, compare_op=ALU.is_ge, fill=0.0, base=0,
                                            pattern=[[-2 * h, nb], [0, h]], channel_multiplier=1))
                    done(pool.affine_select(out=v, in_=v, compare_op=ALU.is_ge, fill=0.0, base=h - 1,
                                            pattern=[[2 * h, nb], [0, h]], channel_multiplier=-1))
                done.end()
                pool.sem_inc(ev("masks"), 1)

                def norms(f, T):
                    pool.wait_ge(ev("stats"), f + 1)
                    pool.wait_ge(ev("ob1"), f)
                    pool.tensor_tensor(rstd[0:T, :], st[0:T, :], K.half_neg[0:T, 0:12], ALU.pow).then_inc(ev("rstd"), 1)

                def norm(f, T):
                    pool.wait_ge(ev("n1"), f + 1)
                    pool.tensor_tensor(n1[0:T, 2:3], n1[0:T, 1:2], K.half_neg[0:T, 0:1], ALU.pow).then_inc(ev("n1r"), 1)

                def tile(i, T, levels, last):
                    n = i + 1
                    for l in range(levels):
                        if l == 3 and last is not None:
                            norms(last, P)
                        for u in range(3):
                            if l == 0:
                                pool.wait_ge(ev("nt_a") if u == 0 else ev("sc"), n if u == 0 else 8 * i + 4 * u)
                                pool.wait_ge(ev(f"ymm{u}"), (LEVELS - 1) * i)
                                pool.wait_ge(ev(f"xt1_{u}"), i)
                            elif l == 1:
                                pool.wait_ge(ev(f"xt1_{u}"), n)
                            else:
                                pool.wait_ge(ev(f"ymm{u}"), (LEVELS - 1) * i + l - 1)
                            src = NT[0:T, :, 0:T] if u == 0 else SC[0:T, 4 * (u - 1):4 * u, 1, 0:T]
                            pool.tensor_tensor(M[u][0:T, :, 0:T], src, bc(lev[0:T, l:l + 1, 0:T], [T, 4, T]),
                                               ALU.mult).then_inc(ev(f"m{u}"), 1)
                    pool.wait_ge(ev("ld_z"), 16 * n)
                    z = Z[0:T, :].rearrange("p (h c) -> p h c", h=AH)
                    pool.wait_ge(ev("gnw"), 1)
                    pool.tensor_tensor(z, z, bc(gnw[0:T, :].rearrange("p (a c) -> p a c", a=1), [T, AH, P]),
                                       ALU.mult).then_inc(ev("zw"), 1)
                    pool.wait_ge(ev("vr_b"), n)
                    pool.wait_ge(ev("bo"), n)
                    pool.wait_ge(ev("ob"), i)
                    v8 = lambda t: t[0:T, :].rearrange("p (h c) -> p h c", h=BH)
                    pool.tensor_tensor(v8(bv), v8(Vr), bc(bo[0:T, :].rearrange("p (h a) -> p h a", a=1), [T, BH, 64]),
                                       ALU.mult).then_inc(ev("bv1"), 1)
                    pool.wait_ge(ev("bv1"), n)
                    pool.tensor_tensor(bv[0:T, :], bv[0:T, :], lnb[0:T, :], ALU.add).then_inc(ev("bv2"), 1)
                    pool.wait_ge(ev("bv2"), n)
                    pool.wait_ge(ev("gr"), n)
                    pool.tensor_tensor(bv[0:T, :], bv[0:T, :], Gr[0:T, :], ALU.mult).then_inc(ev("bv"), 1)
                    pool.tensor_tensor(gw[0:T, :], lnw[0:T, :], Gr[0:T, :], ALU.mult).then_inc(ev("gw"), 1)
                    if last is not None:
                        norm(last, P)
                pool.wait_ge(ev("ld_par"), 64)
                for i in range(2):
                    tile(i, P, LEVELS, i - 1 if i else None)
                with pool.Fori(2, TILES) as i:
                    tile(i, P, LEVELS, i - 1)
                norms(TILES - 1, P)
                norm(TILES - 1, P)
                tile(TILES, SR, LEVELS_S, None)
                norms(TILES, SR)
                norm(TILES, SR)

            @block.scalar
            def _(act):
                def end_rows(f, T):
                    act.wait_ge(ev("ot_mm"), f + 1)
                    act.wait_ge(ev("prj"), 2 * f)
                    act.wait_ge(ev("xn_out"), 16 * f)
                    act.activation(OT[:, 0:4, 0:T], v4(6, P, T), ACT.Copy).then_inc(ev("ot"), 1)

                def end_square(f, T):
                    act.wait_ge(ev("x1"), f + 1)
                    act.wait_ge(ev("nt_mm"), f)
                    act.activation(xn[0:T, :], x1[0:T, :], ACT.Square, accum_out=n1[0:T, 0:1]).then_inc(ev("n1s"), 1)

                def end_keep(f, T):
                    act.wait_ge(ev("nt_mm"), f + 1)
                    act.activation(OT[:, 4:8, 0:T], v4(7, P, T), ACT.Copy).then_inc(ev("xk_b"), 1)

                def tile(i, T, levels, last):
                    n = i + 1
                    act.wait_ge(ev("gB"), i)
                    act.wait_ge(ev("gcol_mm"), i)
                    act.activation(ld[:, :], K.logd[:, bass.ds(i, 1), :].rearrange("p a h -> p (a h)"), ACT.Copy).then_inc(ev("ldc"), 1)
                    act.wait_ge(ev("nv"), i)
                    act.wait_ge(ev("nt_a"), i)
                    act.activation(bt[:, :], K.beta[:, bass.ds(i, 1), :].rearrange("p a h -> p (a h)"), ACT.Copy).then_inc(ev("bt"), 1)
                    act.activation(nbt[:, :], K.beta[:, bass.ds(i, 1), :].rearrange("p a h -> p (a h)"), ACT.Copy,
                                   scale=-1.0).then_inc(ev("bt"), 1)
                    act.wait_ge(ev("bv1"), i)
                    act.activation(bo[:, :], K.bonus[:, bass.ds(i, 1), :].rearrange("p a h -> p (a h)"), ACT.Copy).then_inc(ev("bo"), 1)
                    act.wait_ge(ev("gcol_mm"), n)
                    act.wait_ge(ev("dm"), i)
                    act.activation(g[0:T, :], bank[1][0:T, 0:AH], ACT.Copy).then_inc(ev("g"), 1)
                    act.wait_ge(ev("wr"), i)
                    act.activation(eg[0:T, :], bank[1][0:T, 0:AH], ACT.Exp).then_inc(ev("eg"), 1)
                    act.wait_ge(ev("dm"), n)
                    act.wait_ge(ev("attn"), i)
                    act.activation(dec[0:T, :, 0:T], dec[0:T, :, 0:T], ACT.Exp).then_inc(ev("dec"), 1)
                    act.wait_ge(ev("state_a"), i)
                    act.activation(eGB[:, :, 0:T], v4(0, P, T), ACT.Exp).then_inc(ev("egb"), 1)
                    act.wait_ge(ev("rows_a"), n)
                    act.wait_ge(ev("upd_a"), i)
                    act.activation(kr[0:T, :, :], v4(4, T), ACT.Copy).then_inc(ev("kr"), 1)
                    act.wait_ge(ev("rows_b"), n)
                    act.wait_ge(ev("upd_b"), i)
                    act.activation(Br[0:T, :], bank[6][0:T, :], ACT.Copy, scale=-1.0).then_inc(ev("br"), 1)
                    act.wait_ge(ev("rows_vg"), n)
                    act.wait_ge(ev("bv1"), i)
                    act.activation(Vr[0:T, :], bank[0][0:T, :], ACT.Copy).then_inc(ev("vr_b"), 1)
                    for l in range(levels):
                        for u in range(3):
                            b = 2 * u
                            if l == 0:
                                act.wait_ge(ev(f"x1mm{u}"), n)
                                act.activation(X[u][0:T, :, 0:T], v4(b, T, T), ACT.Copy).then_inc(ev(f"xk{u}"), 1)
                            else:
                                act.wait_ge(ev(f"ymm{u}"), (LEVELS - 1) * i + l)
                                w = P // 2 if l == LEVELS - 1 else T
                                act.activation(Y[u][0:T, :, 0:w], v4(b, T, w), ACT.Copy).then_inc(ev(f"y{u}"), 1)
                        if last is not None and l == 3:
                            end_rows(last, P)
                        if last is not None and l == 6:
                            end_square(last, P)
                    act.wait_ge(ev("sa_mm"), n)
                    act.activation(SA[0:T, :], bank[2][0:T, :], ACT.Copy).then_inc(ev("sa"), 1)
                    act.wait_ge(ev("out_a"), n)
                    act.wait_ge(ev("suma"), i)
                    act.wait_ge(ev("ot_mm"), i)
                    act.activation(sqa[0:T, :], bank[1][0:T, :], ACT.Square).then_inc(ev("sqa"), 1)
                    act.activation(OR[0:T, 0:AKEY], bank[1][0:T, :], ACT.Copy).then_inc(ev("raw"), 1)
                    act.wait_ge(ev("cent"), n)
                    act.wait_ge(ev("sumb"), i)
                    act.activation(sqb[0:T, :], OR[0:T, AKEY:D], ACT.Square).then_inc(ev("sqb"), 1)
                    if last is not None:
                        end_keep(last, P)
                for i in range(2):
                    tile(i, P, LEVELS, i - 1 if i else None)
                with act.Fori(2, TILES) as i:
                    tile(i, P, LEVELS, i - 1)
                for i, T in ((TILES - 1, P), (TILES, SR)):
                    if i == TILES:
                        tile(i, T, LEVELS_S, None)
                    end_rows(i, T)
                    end_square(i, T)
                    end_keep(i, T)
                for b in range(DB):
                    if b == 0:
                        act.wait_ge(ev("xk_b"), TILES + 1)
                    act.wait_ge(ev("upd_s"), b)
                    row = K.same[:, b * DS:b * DS + 1]
                    act.activation(Wr[0:SR, :, :], NVd[0:SR, :, :], ACT.Copy, scale=row).then_inc(ev("pick"), 1)
                    act.activation(RH[0:SR, :], SA[0:SR, :], ACT.Copy, scale=row).then_inc(ev("pick"), 1)
                    act.activation(sqa[0:SR, :], Vr[0:SR, :], ACT.Copy, scale=row).then_inc(ev("pick"), 1)
                    act.wait_ge(ev("rb_mm"), b + 1)
                    if b >= 2:
                        act.wait_ge(ev(f"rb_out{b % 2}"), 16 * (b // 2))
                    act.activation(Rb[:, b % 2, :, :], bank[6][0:64, :].rearrange("v (j c) -> v j c", j=NP), ACT.Copy).then_inc(ev("rb_new"), 1)

            @block.vector
            def _(dve):
                def spread(half):
                    for r in range(AH + BH):
                        k = (AH + BH) * half + r
                        j = (r - AH) // 2
                        if half == 0:
                            src = QK[:, 1, r, 0:SR] if r < AH else RW[:, 1, j, 0:SR]
                        else:
                            src = QG[:, r, 0:SR] if r < AH else RW[:, 0, j, 0:SR]
                        if k > 0:
                            dve.wait_ge(ev("q1_used"), k)
                        keep = K.ones[:, 0:1] if r < AH else K.head_cols[:, (r - AH) % 2:(r - AH) % 2 + 1]
                        dve.scalar_tensor_tensor(out=Q1[:, :, :], in0=bc(src.rearrange("p (a t) -> p a t", a=1), [P, DB, SR]),
                                                 scalar=keep, in1=K.batch_cols[:, :, :], op0=ALU.mult,
                                                 op1=ALU.mult).then_inc(ev("q1"), 1)

                dve.memset(St[:, :, :], 0.0).then_inc(ev("init"), 1)
                dve.memset(Tt[:, :, :], 0.0).then_inc(ev("init"), 1)
                dve.wait_ge(ev("ld_par"), 64)
                dve.tensor_scalar(gnw[:, :], gnw[:, :], 0.5, None, ALU.mult).then_inc(ev("gnw"), 1)
                dve.wait_ge(ev("init"), 2)
                dve.wait_ge(ev("masks"), 1)

                v8 = lambda t: t.rearrange("p (h c) -> p h c", h=BH)
                wide = lambda t, T, w: bc(t.rearrange("p (h a) -> p h a", a=1), [T, t.shape[1], w])

                def end_sums(f, T):
                    n = f + 1
                    dve.wait_ge(ev("sqa"), n)
                    dve.tensor_reduce(st[0:T, 0:4], sqa[0:T, :].rearrange("p (h c) -> p h c", h=AH), AX_X, ALU.add).then_inc(ev("suma"), 1)
                    dve.wait_ge(ev("sqb"), n)
                    dve.tensor_reduce(st[0:T, 4:12], v8(sqb[0:T, :]), AX_X, ALU.add).then_inc(ev("sumb"), 1)
                    dve.wait_ge(ev("suma"), n)
                    dve.tensor_scalar(st[0:T, 0:4], st[0:T, 0:4], 1.0 / P, EPS, ALU.mult, ALU.add).then_inc(ev("st1"), 1)
                    dve.wait_ge(ev("sumb"), n)
                    dve.tensor_scalar(st[0:T, 4:12], st[0:T, 4:12], 1.0 / 64, B_GN_EPS, ALU.mult, ALU.add).then_inc(ev("stats"), 1)

                def end_gate(f, T):
                    n = f + 1
                    dve.wait_ge(ev("rstd"), n)
                    dve.wait_ge(ev("raw"), n)
                    oa = OR[0:T, 0:AKEY].rearrange("p (h c) -> p h c", h=AH)
                    dve.tensor_tensor(oa, oa, wide(rstd[0:T, 0:4], T, P), ALU.mult).then_inc(ev("oa1"), 1)
                    ob = v8(OR[0:T, AKEY:D])
                    dve.tensor_tensor(ob, ob, wide(rstd[0:T, 4:12], T, 64), ALU.mult).then_inc(ev("ob1"), 1)
                    dve.wait_ge(ev("oa1"), n)
                    dve.wait_ge(ev("zw"), n)
                    dve.tensor_tensor(OR[0:T, 0:AKEY], OR[0:T, 0:AKEY], Z[0:T, :], ALU.mult).then_inc(ev("oa"), 1)
                    o = OR[0:T, AKEY:D]
                    dve.wait_ge(ev("ob1"), n)
                    dve.wait_ge(ev("gw"), n)
                    dve.tensor_tensor(o, o, gw[0:T, :], ALU.mult).then_inc(ev("ob2"), 1)
                    dve.wait_ge(ev("ob2"), n)
                    dve.wait_ge(ev("bv"), n)
                    dve.tensor_tensor(o, o, bv[0:T, :], ALU.add).then_inc(ev("ob"), 1)

                def end_rows(f, T):
                    dve.wait_ge(ev("ot_mm"), f + 1)
                    dve.wait_ge(ev("prj"), 2 * f)
                    dve.wait_ge(ev("xn_out"), 16 * f)
                    dve.tensor_copy(OT[:, 4:8, 0:T], v4(7, P, T)).then_inc(ev("ot2"), 1)

                def end_add(f, T):
                    for c in range(2):
                        dve.wait_ge(ev("prj"), 2 * f + c + 1)
                        if c == 0:
                            dve.wait_ge(ev("ld_x"), 16 * (f + 1))
                        ins = dve.tensor_tensor(x1[0:T, 512 * c:512 * c + 512], bank[6 + c][0:T, :], XR[0:T, 512 * c:512 * c + 512], ALU.add)
                    ins.then_inc(ev("x1"), 1)

                def end_norm(f, T):
                    dve.wait_ge(ev("n1s"), f + 1)
                    dve.tensor_scalar(n1[0:T, 1:2], n1[0:T, 0:1], 1.0 / D, EPS, ALU.mult, ALU.add).then_inc(ev("n1"), 1)
                    dve.wait_ge(ev("n1r"), f + 1)
                    dve.wait_ge(ev("nt_mm"), f)
                    dve.scalar_tensor_tensor(out=xn[0:T, :], in0=x1[0:T, :], scalar=n1[0:T, 2:3], in1=nw[0:T, :],
                                             op0=ALU.mult, op1=ALU.mult).then_inc(ev("xn1"), 1)

                def end_keep(f, T):
                    dve.wait_ge(ev("nt_mm"), f + 1)
                    dve.tensor_copy(OT[:, 0:4, 0:T], v4(6, P, T)).then_inc(ev("xk_a"), 1)

                def center(i, T):
                    n = i + 1
                    dve.wait_ge(ev("out_b"), n)
                    dve.tensor_reduce(mean[0:T, :], v8(bank[3][0:T, :]), AX_X, ALU.add).then_inc(ev("mean"), 1)
                    dve.wait_ge(ev("mean"), n)
                    dve.wait_ge(ev("ot_mm"), i)
                    dve.scalar_tensor_tensor(out=v8(OR[0:T, AKEY:D]), in0=wide(mean[0:T, :], T, 64), scalar=-1.0 / 64,
                                             in1=v8(bank[3][0:T, :]), op0=ALU.mult, op1=ALU.add).then_inc(ev("cent"), 1)

                def tile(i, T, levels, mask, lmask, last):
                    n = i + 1
                    dve.wait_ge(ev("gB"), n)
                    dve.wait_ge(ev("g"), n)
                    dve.wait_ge(ev("attn"), i)
                    for h in range(AH):
                        ins = dve.scalar_tensor_tensor(out=dec[0:T, h, 0:T], in0=v4(0, T, T)[:, h, :], scalar=g[0:T, h:h + 1],
                                                       in1=lmask[0:T, 0:T], op0=ALU.subtract, op1=ALU.min)
                    ins.then_inc(ev("dm"), 1)
                    if T == P:
                        dve.wait_ge(ev("out_b"), i)
                        dve.wait_ge(ev("rhs_b"), i)
                        dve.wait_ge(ev("state_b"), i)
                        dve.tensor_tensor(Th[:, :, :], Tt[:, :, :], bc(K.rw_in[:, :, bass.ds(i, 1)], [P, NP, P]),
                                          ALU.mult).then_inc(ev("th"), 1)
                    dve.wait_ge(ev("dec"), n)
                    dve.wait_ge(ev("kkqk"), n)
                    dve.wait_ge(ev("bt"), 2 * n)
                    dve.wait_ge(ev("m0"), LEVELS * i)
                    dve.wait_ge(ev("out_a"), i)
                    for h in range(AH):
                        b = v4(2 + h // 2, T, T)
                        ins = dve.scalar_tensor_tensor(out=NT[0:T, h, 0:T], in0=b[:, 2 * (h % 2) + 1, :], scalar=bt[0:T, h:h + 1],
                                                       in1=dec[0:T, h, 0:T], op0=ALU.mult, op1=ALU.mult)
                    ins.then_inc(ev("nt_a"), 1)
                    for h in range(0, AH, 2):
                        b = v4(2 + h // 2, T, T)
                        ins = dve.tensor_tensor(attn[0:T, h:h + 2, 0:T], b[:, 0::2, :], dec[0:T, h:h + 2, 0:T], ALU.mult)
                    ins.then_inc(ev("attn"), 1)
                    dve.wait_ge(ev("egb"), n)
                    dve.tensor_tensor(QG[:, :, 0:T], QK[:, 0, :, 0:T], eGB[:, :, 0:T], ALU.mult).then_inc(ev("qg"), 1)
                    if T == P:
                        dve.wait_ge(ev("nvd"), i)
                        dve.tensor_copy(dend[:, :], dec[:, :, P - 1]).then_inc(ev("dend"), 1)
                    else:
                        dve.wait_ge(ev("w_mm"), i)
                        dve.tensor_tensor(Wr[0:T, :, 0:T], dec[0:T, :, 0:T], bc(K.last[:, :].rearrange("s (a t) -> s a t", a=1),
                                                                                [T, AH, T]), ALU.mult).then_inc(ev("dend_m"), 1)
                        dve.wait_ge(ev("dend_m"), 1)
                        dve.tensor_reduce(dend[0:T, :], Wr[0:T, :, 0:T], AX_X, ALU.add).then_inc(ev("dend"), 1)
                    dve.wait_ge(ev("rows_a"), n)
                    dve.wait_ge(ev("wr"), i)
                    dve.tensor_copy(vr[0:T, :, :], v4(5, T)).then_inc(ev("vr_a"), 1)
                    dve.wait_ge(ev("rows_b"), n)
                    dve.wait_ge(ev("upd_b"), i)
                    dve.tensor_copy(Kr[0:T, :], bank[7][0:T, :]).then_inc(ev("krr"), 1)
                    for h in range(BH):
                        dve.wait_ge(ev("score"), 8 * i + h + 1)
                        if h == 0:
                            dve.wait_ge(ev("m1"), LEVELS * i)
                            dve.wait_ge(ev("m2"), LEVELS * i)
                            dve.wait_ge(ev("out_b"), i)
                        dve.tensor_tensor(SC[0:T, h, :, 0:T], v4(2 + h % 6, T, T), mask[0:T, :, 0:T],
                                          ALU.mult).then_inc(ev("sc"), 1)
                    dve.wait_ge(ev("rows_vg"), n)
                    dve.wait_ge(ev("gw"), i)
                    dve.wait_ge(ev("bv"), i)
                    dve.tensor_scalar(Gr[0:T, :], bank[1][0:T, :], 0.5, None, ALU.mult).then_inc(ev("gr"), 1)
                    for u in range(3):
                        dve.wait_ge(ev(f"m{u}"), LEVELS * i + 1)
                        dve.wait_ge(ev("w_mm" if u == 0 else "sa_mm"), i)
                        dve.tensor_tensor(XT[u][0:T, :, 0:T], bc(K.ident[0:T, 0:T].rearrange("p (a c) -> p a c", a=1), [T, 4, T]),
                                          M[u][0:T, :, 0:T], ALU.subtract).then_inc(ev(f"xt1_{u}"), 1)
                    if T != P:
                        spread(0)
                    dve.wait_ge(ev("rhs_a"), n)
                    dve.wait_ge(ev("eg"), n)
                    dve.wait_ge(ev("w_mm"), i)
                    dve.wait_ge(ev("vr_a"), n)
                    for h in range(AH):
                        ins = dve.scalar_tensor_tensor(out=Wr[0:T, h, :], in0=v4(6, T)[:, h, :], scalar=eg[0:T, h:h + 1],
                                                       in1=vr[0:T, h, :], op0=ALU.mult, op1=ALU.subtract)
                    ins.then_inc(ev("wr"), 1)
                    dve.wait_ge(ev("rhs_b"), n)
                    dve.wait_ge(ev("sa_mm"), i)
                    dve.tensor_copy(RH[0:T, :], bank[7][0:T, :]).then_inc(ev("rh"), 1)
                    for l in range(1, levels):
                        for u in range(3):
                            if l < levels - 1:
                                dve.wait_ge(ev(f"zmm{u}"), (2 * LEVELS - 3) * i + 2 * l - 1)
                                if l == 1:
                                    dve.wait_ge(ev(f"xk{u}"), n)
                                dve.wait_ge(ev(f"xd{u}"), (2 * LEVELS - 3) * i + 2 * l - 2)
                                x = half(X[u][0:T, :, :], l, T, 0)
                                dve.tensor_tensor(x, x, packed(2 * u + 1, l, T, T), ALU.subtract).then_inc(ev(f"xd{u}"), 1)
                                dve.wait_ge(ev(f"zmm{u}"), (2 * LEVELS - 3) * i + 2 * l)
                                xt = half(XT[u][0:T, :, :], l, T, 1)
                                dve.tensor_tensor(xt, xt, packed(2 * u, l, T, T), ALU.subtract).then_inc(ev(f"xd{u}"), 1)
                            else:
                                dve.wait_ge(ev(f"zmm{u}"), (2 * LEVELS - 3) * i + 2 * l - 1)
                                dve.wait_ge(ev(f"xd{u}"), (2 * LEVELS - 3) * i + 2 * l - 2)
                                r = P // 2 if l == LEVELS - 1 else T
                                xt = half(XT[u][0:r, :, :], l, T, 1)
                                dve.tensor_tensor(xt, xt, packed(2 * u, l, T, r), ALU.subtract).then_inc(ev(f"xd{u}"), 1)
                        if last is not None:
                            if l == 1:
                                end_sums(last, P)
                            if l == 2:
                                end_gate(last, P)
                            if l == 3:
                                end_rows(last, P)
                            if l == 5:
                                end_add(last, P)
                    dve.wait_ge(ev("w_mm"), n)
                    dve.wait_ge(ev("out_a"), i)
                    dve.tensor_tensor(NV[0:T, :, :], v4(0, T), bc(nbt[0:T, :].rearrange("p (h a) -> p h a", a=1), [T, AH, P]),
                                      ALU.mult).then_inc(ev("nv"), 1)
                    dve.wait_ge(ev("nv"), n)
                    dve.wait_ge(ev("dend"), n)
                    dve.wait_ge(ev("upd_a"), i)
                    dve.tensor_tensor(NVd[0:T, :, :], NV[0:T, :, :], bc(dend[0:T, :].rearrange("p (h a) -> p h a", a=1),
                                                                        [T, AH, P]), ALU.mult).then_inc(ev("nvd"), 1)
                    if last is not None:
                        end_norm(last, P)
                    if T != P:
                        spread(1)
                    center(i, T)

                def whole_tile(i, last):
                    n = i + 1
                    tile(i, P, LEVELS, mask4, K.lcausal, last)
                    dve.wait_ge(ev("upd_a"), n)
                    for h in range(AH):
                        ins = dve.scalar_tensor_tensor(out=St[:, h, :], in0=St[:, h, :], scalar=eGB[:, h, P - 1:P],
                                                       in1=v4(4)[:, h, :], op0=ALU.mult, op1=ALU.add)
                    ins.then_inc(ev("state_a"), 1)
                    dve.wait_ge(ev("upd_b"), n)
                    for h in range(2):
                        r = slice(64 * h, 64 * h + 64)
                        ins = dve.tensor_tensor(Tt[r, :, r], Th[r, :, r], v4(5)[r, :, r], ALU.add)
                    ins.then_inc(ev("tt1"), 1)
                    dve.wait_ge(ev("tt1"), n)
                    dve.tensor_tensor(Tt[:, :, :], Tt[:, :, :], bc(K.rw_out[:, :, bass.ds(i, 1)], [P, NP, P]),
                                      ALU.mult).then_inc(ev("state_b"), 1)
                    if last is not None:
                        end_keep(last, P)

                def end(f, T):
                    end_sums(f, T)
                    end_gate(f, T)
                    end_rows(f, T)
                    end_add(f, T)
                    end_norm(f, T)
                    end_keep(f, T)
                for i in range(2):
                    whole_tile(i, i - 1 if i else None)
                with dve.Fori(2, TILES) as i:
                    whole_tile(i, i - 1)
                end(TILES - 1, P)
                dve.wait_ge(ev("tr_mm"), 1)
                dve.tensor_copy(tr[:, :, :], v4(4)).then_inc(ev("tr"), 1)
                for r in range(4):
                    dve.wait_ge(ev("tb_mm"), r + 1)
                    dve.tensor_copy(Tb[:, 2 * r:2 * r + 2, :, :], bank[6 + r % 2][:, :].rearrange("p (b j v) -> p b j v", b=2, j=NP)
                                    ).then_inc(ev("tb"), 1)
                dve.wait_ge(ev("ld_sb"), 16)
                dve.wait_ge(ev("tr_out"), 32)
                tile(TILES, SR, LEVELS_S, mask4s, K.lcausal_s, None)
                end(TILES, SR)
                for b in range(DB):
                    dve.wait_ge(ev("upd_s"), b + 1)
                    for h in range(AH):
                        dve.scalar_tensor_tensor(out=Sb[:, b, h, :], in0=Sb[:, b, h, :], scalar=eGB[:, h, b * DS + DS - 1:(b + 1) * DS],
                                                 in1=v4(4)[:, h, :], op0=ALU.mult, op1=ALU.add).then_inc(ev("sb_step"), 1)
                    dve.wait_ge(ev("sb_step"), AH * (b + 1))
                    dve.tensor_tensor(Tb[:, b, :, :], Tb[:, b, :, :], bank[5][:, 0:256].rearrange("p (j v) -> p j v", j=NP),
                                      ALU.add).then_inc(ev("tb1"), 1)
                    dve.wait_ge(ev("tb1"), b + 1)
                    dve.sem_inc(ev("sb_new"), 1)
                    dve.tensor_tensor(Tb[:, b, :, :], Tb[:, b, :, :], bc(K.rw_out[:, :, TILES + b:TILES + b + 1], [P, NP, 64]),
                                      ALU.mult).then_inc(ev("tb_new"), 1)

            @block.tensor
            def _(pe):
                def end_rows(f, T, used):
                    pe.wait_ge(ev("oa"), f + 1)
                    pe.wait_ge(ev("ob"), f + 1)
                    pe.wait_ge(ev("wr"), used)
                    pe.wait_ge(ev("rh"), used)
                    for c in range(KT):
                        mm = pe.transpose(v4(6 + c // 4, P, T)[:, c % 4, :], OR[0:T, c * P:(c + 1) * P], K.ident[0:T, 0:T])
                    mm.then_inc(ev("ot_mm"), 1)

                def end_project(f, T, c):
                    if c == 0:
                        pe.wait_ge(ev("ot"), f + 1)
                        pe.wait_ge(ev("ot2"), f + 1)
                    for kt in range(KT):
                        mm = pe.matmul(bank[6 + c][0:T, :], OT[:, kt, 0:T], wo[:, kt, 512 * c:512 * c + 512],
                                       start=(kt == 0), stop=(kt == KT - 1))
                    mm.then_inc(ev("prj"), 1)

                def end_norm(f, T):
                    pe.wait_ge(ev("xn1"), f + 1)
                    for c in range(KT):
                        mm = pe.transpose(v4(6 + c // 4, P, T)[:, c % 4, :], xn[0:T, c * P:(c + 1) * P], K.ident[0:T, 0:T])
                    mm.then_inc(ev("nt_mm"), 1)

                def tile(i, T, levels, ks, kd, last):
                    n = i + 1
                    pe.wait_ge(ev("ldc"), n)
                    pe.wait_ge(ev("nv"), i)
                    pe.wait_ge(ev("sqa"), i)
                    pe.wait_ge(ev("raw"), i)
                    pe.wait_ge(ev("cent"), i)
                    caus = K.causal if T == P else K.causal_s
                    for h in range(AH):
                        mm = pe.matmul(v4(0, P, T)[:, h, :], ld[0:T, h:h + 1].broadcast_to([T, P]), caus[0:T, 0:T], start=True, stop=True)
                    mm.then_inc(ev("gB"), 1)
                    pe.matmul(bank[1][0:T, 0:AH], caus[0:T, 0:T], ld[0:T, :], start=True, stop=True).then_inc(ev("gcol_mm"), 1)
                    pe.wait_ge(ev("ld_qk"), 32 * n)
                    for h in range(AH):
                        o = v4(2 + h // 2, T, T)[:, 2 * (h % 2):2 * (h % 2) + 2, :]
                        mm = pe.matmul(o, QK[:, 1, h, 0:T], QK[:, :, h, 0:T], start=True, stop=True)
                    mm.then_inc(ev("kkqk"), 1)
                    pe.wait_ge(ev("state_a"), i)
                    pe.wait_ge(ev("state_b"), i)
                    pe.wait_ge(ev("ld_v"), 16 * n)
                    for h in range(AH):
                        pe.transpose(v4(4, T)[:, h, :], QK[:, 1, h, 0:T], K.ident[:, :])
                        mm = pe.transpose(v4(5, T)[:, h, :], V[:, h, 0:T], K.ident[:, :])
                    mm.then_inc(ev("rows_a"), 1)
                    kept = i if T != P else 0 if isinstance(i, int) and i == 0 else i - 1
                    pe.wait_ge(ev("xk_a"), kept)
                    pe.wait_ge(ev("xk_b"), kept)
                    pe.wait_ge(ev("ld_rw"), 48 * n)
                    pe.wait_ge(ev("ld_r"), 16 * n)
                    for j in range(NP):
                        pe.transpose(v4(6, T)[:, j, :], RW[:, 2, j, 0:T], K.ident[:, :])
                        mm = pe.transpose(v4(7, T)[:, j, :], RW[:, 3, j, 0:T], K.ident[:, :])
                    mm.then_inc(ev("rows_b"), 1)
                    for h in range(BH):
                        if h == 0:
                            pe.wait_ge(ev("attn"), n)
                        if h == 2:
                            pe.wait_ge(ev("kr"), n)
                        if h == 3:
                            pe.wait_ge(ev("vr_a"), n)
                        if h == 4:
                            pe.wait_ge(ev("br"), n)
                        if h == 5:
                            pe.wait_ge(ev("krr"), n)
                        if h >= 6:
                            pe.wait_ge(ev("sc"), 8 * i + h - 5)
                        r = slice(64 * (h % 2), 64 * (h % 2) + 64)
                        o = v4(2 + h % 6, T, T)
                        pe.matmul(o[:, 0:2, :], RW[r, 2, h // 2, 0:T], RW[r, 0:2, h // 2, 0:T], start=True, stop=True)
                        pe.matmul(o[:, 2:4, :], RW[r, 3, h // 2, 0:T], RW[r, 0:2, h // 2, 0:T], start=True, stop=True
                                  ).then_inc(ev("score"), 1)
                    pe.wait_ge(ev("egb"), n)
                    pe.wait_ge(ev("eg"), n)
                    pe.wait_ge(ev("ld_vg"), 32 * n)
                    for j in range(NP):
                        pe.transpose(v4(0, T)[:, j, :], VG[:, 0, j, 0:T], K.ident[:, :])
                        mm = pe.transpose(v4(1, T)[:, j, :], VG[:, 1, j, 0:T], K.ident[:, :])
                    mm.then_inc(ev("rows_vg"), 1)
                    pe.wait_ge(ev("sc"), 8 * i + 5)
                    ks(6)
                    pe.wait_ge(ev("vr_b"), n)
                    if T == P:
                        pe.wait_ge(ev("th"), n)
                    pe.wait_ge(ev("sc"), 8 * n)
                    kd(7)
                    pe.wait_ge(ev("gr"), n)
                    for u in range(3):
                        pe.wait_ge(ev(f"xt1_{u}"), n)
                        for k in range(4):
                            mm = pe.transpose(v4(2 * u, T, T)[:, k, :], XT[u][0:T, k, 0:T], K.ident[0:T, 0:T])
                        mm.then_inc(ev(f"x1mm{u}"), 1)
                    for l in range(1, levels):
                        for u in range(3):
                            if l == 1:
                                pe.wait_ge(ev(f"xk{u}"), n)
                            else:
                                pe.wait_ge(ev(f"xd{u}"), (2 * LEVELS - 3) * i + 2 * l - 2)
                            pe.wait_ge(ev(f"m{u}"), LEVELS * i + l + 1)
                            for k in range(4):
                                w = P // 2 if l == LEVELS - 1 else T
                                mm = pe.matmul(v4(2 * u, T, w)[:, k, :], M[u][0:T, k, 0:T], X[u][0:T, k, 0:w], start=True, stop=True)
                            mm.then_inc(ev(f"ymm{u}"), 1)
                        for u in range(3):
                            pe.wait_ge(ev(f"y{u}"), (LEVELS - 1) * i + l)
                            if l < levels - 1:
                                for k in range(4):
                                    mm = pe.matmul(packed(2 * u + 1, l, T, T)[:, k], XT[u][0:T, k, 0:T], half(Y[u][0:T, k, :], l, T, 0), start=True, stop=True)
                                mm.then_inc(ev(f"zmm{u}"), 1)
                            r = P // 2 if l == LEVELS - 1 else T
                            for k in range(4):
                                mm = pe.matmul(packed(2 * u, l, T, r)[:, k], Y[u][0:T, k, 0:r], half(XT[u][0:T, k, :], l, T, 1), start=True, stop=True)
                            mm.then_inc(ev(f"zmm{u}"), 1)
                        if last is not None and l == 3:
                            end_rows(last, P, n)
                        if last is not None and l in (4, 5):
                            end_project(last, P, l - 4)
                    pe.wait_ge(ev("xd0"), (2 * LEVELS - 3) * i + 2 * levels - 3)
                    pe.wait_ge(ev("wr"), n)
                    for h in range(AH):
                        mm = pe.matmul(v4(0, T)[:, h, :], XT[0][0:T, h, 0:T], Wr[0:T, h, :], start=True, stop=True)
                    mm.then_inc(ev("w_mm"), 1)
                    pe.wait_ge(ev("xd1"), (2 * LEVELS - 3) * i + 2 * levels - 3)
                    pe.wait_ge(ev("xd2"), (2 * LEVELS - 3) * i + 2 * levels - 3)
                    pe.wait_ge(ev("rh"), n)
                    for h in range(BH):
                        mm = pe.matmul(bank[2][0:T, 64 * h:64 * h + 64], XT[1 + h // 4][0:T, h % 4, 0:T],
                                       RH[0:T, 64 * h:64 * h + 64], start=True, stop=True)
                    mm.then_inc(ev("sa_mm"), 1)

                def end(f, T):
                    pe.wait_ge(ev("xk_a"), f)
                    pe.wait_ge(ev("xk_b"), f)
                    end_rows(f, T, f + 1)
                    end_project(f, T, 0)
                    end_project(f, T, 1)
                    end_norm(f, T)

                pe.wait_ge(ev("ld_wo"), 16)
                pe.wait_ge(ev("init"), 2)

                def whole_tile(i, last):
                    n = i + 1

                    def ks(b):
                        for h in range(AH):
                            mm = pe.matmul(v4(b)[:, h, :], QK[:, 1, h, :], St[:, h, :], start=True, stop=True)
                        mm.then_inc(ev("rhs_a"), 1)

                    def kd(b):
                        for j in range(NP):
                            pe.matmul(v4(b)[:, j, :], RW[:, 1, j, :], Th[:, j, :], start=(j == 0), stop=False, skip_group_check=True)
                            for h in (2 * j, 2 * j + 1):
                                mm = pe.matmul(bank[b][:, 64 * h:64 * h + 64], SC[:, h, 3, :], Vr[:, 64 * h:64 * h + 64],
                                               start=False, stop=(h == BH - 1), skip_group_check=True)
                        mm.then_inc(ev("rhs_b"), 1)
                    tile(i, P, LEVELS, ks, kd, last)
                    pe.wait_ge(ev("nv"), n)
                    pe.wait_ge(ev("qg"), n)
                    for h in range(AH):
                        pe.matmul(v4(1)[:, h, :], QG[:, h, :], St[:, h, :], start=True, stop=False)
                        mm = pe.matmul(v4(1)[:, h, :], attn[:, h, :], NV[:, h, :], start=False, stop=True)
                    mm.then_inc(ev("out_a"), 1)
                    pe.wait_ge(ev("sa"), n)
                    for j in range(NP):
                        pe.matmul(v4(3)[:, j, :], RW[:, 0, j, :], Th[:, j, :], start=(j == 0), stop=False, skip_group_check=True)
                        for h in (2 * j, 2 * j + 1):
                            o = bank[3][:, 64 * h:64 * h + 64]
                            pe.matmul(o, SC[:, h, 0, :], SA[:, 64 * h:64 * h + 64], start=False, stop=False, skip_group_check=True)
                            mm = pe.matmul(o, SC[:, h, 2, :], Vr[:, 64 * h:64 * h + 64], start=False, stop=(h == BH - 1), skip_group_check=True)
                    mm.then_inc(ev("out_b"), 1)
                    pe.wait_ge(ev("nvd"), n)
                    pe.wait_ge(ev("kr"), n)
                    for h in range(AH):
                        mm = pe.matmul(v4(4)[:, h, :], kr[:, h, :], NVd[:, h, :], start=True, stop=True)
                    mm.then_inc(ev("upd_a"), 1)
                    for j in range(NP):
                        c = slice(j * P, (j + 1) * P)
                        pe.matmul(v4(5)[:, j, :], Br[:, c], SA[:, c], start=True, stop=False)
                        mm = pe.matmul(v4(5)[:, j, :], Kr[:, c], Vr[:, c], start=False, stop=True)
                    mm.then_inc(ev("upd_b"), 1)
                    if last is not None:
                        end_norm(last, P)
                for i in range(2):
                    whole_tile(i, i - 1 if i else None)
                with pe.Fori(2, TILES) as i:
                    whole_tile(i, i - 1)
                end(TILES - 1, P)
                pe.wait_ge(ev("state_b"), TILES)
                for j in range(NP):
                    mm = pe.transpose(v4(4)[:, j, :], Tt[:, j, :], K.ident[:, :])
                mm.then_inc(ev("tr_mm"), 1)
                pe.wait_ge(ev("xk_a"), TILES)
                pe.wait_ge(ev("xk_b"), TILES)
                for r in range(4):
                    pe.wait_ge(ev("ld_rb"), 32 * (r + 1))
                    if r >= 2:
                        pe.wait_ge(ev("tb"), r - 1)
                    for b in range(2):
                        for j in range(NP):
                            o = bank[6 + r % 2][:, b * 256 + j * 64:b * 256 + j * 64 + 64]
                            mm = pe.transpose(o, Rb[:, b, j, :], K.ident[0:64, 0:64])
                    mm.then_inc(ev("tb_mm"), 1)
                pe.wait_ge(ev("tb"), 4)
                pe.wait_ge(ev("tr"), 1)

                def ks_s(bk):
                    for h in range(AH):
                        pe.wait_ge(ev("q1"), h + 1)
                        for b in range(DB):
                            mm = pe.matmul(v4(bk, SR)[:, h, :], Q1[:, b, :], Sb[:, b, h, :], start=(b == 0), stop=(b == DB - 1))
                        mm.then_inc(ev("q1_used"), 1)
                        pe.wait_ge(ev("q1_used"), h + 1)
                    pe.sem_inc(ev("rhs_a"), 1)

                def kd_s(bk):
                    for h in range(BH):
                        pe.wait_ge(ev("q1"), AH + h + 1)
                        o = bank[bk][0:SR, 64 * h:64 * h + 64]
                        pe.matmul(o, SC[0:SR, h, 3, 0:SR], Vr[0:SR, 64 * h:64 * h + 64], start=True, stop=False)
                        for b in range(DB):
                            mm = pe.matmul(o, Q1[:, b, :], Tb[:, b, h // 2, :], start=False, stop=(b == DB - 1))
                        mm.then_inc(ev("q1_used"), 1)
                        pe.wait_ge(ev("q1_used"), AH + h + 1)
                    pe.sem_inc(ev("rhs_b"), 1)
                tile(TILES, SR, LEVELS_S, ks_s, kd_s, None)
                pe.wait_ge(ev("nv"), TILES + 1)
                for h in range(AH):
                    pe.matmul(v4(1, SR)[:, h, :], attn[0:SR, h, 0:SR], NV[0:SR, h, :], start=True, stop=False)
                    pe.wait_ge(ev("q1"), AH + BH + h + 1)
                    for b in range(DB):
                        mm = pe.matmul(v4(1, SR)[:, h, :], Q1[:, b, :], Sb[:, b, h, :], start=False, stop=(b == DB - 1))
                    mm.then_inc(ev("q1_used"), 1)
                    pe.wait_ge(ev("q1_used"), AH + BH + h + 1)
                pe.sem_inc(ev("out_a"), 1)
                pe.wait_ge(ev("sa"), TILES + 1)
                for h in range(BH):
                    pe.wait_ge(ev("q1"), 2 * AH + BH + h + 1)
                    o = bank[3][0:SR, 64 * h:64 * h + 64]
                    pe.matmul(o, SC[0:SR, h, 0, 0:SR], SA[0:SR, 64 * h:64 * h + 64], start=True, stop=False)
                    pe.matmul(o, SC[0:SR, h, 2, 0:SR], Vr[0:SR, 64 * h:64 * h + 64], start=False, stop=False)
                    for b in range(DB):
                        mm = pe.matmul(o, Q1[:, b, :], Tb[:, b, h // 2, :], start=False, stop=(b == DB - 1))
                    mm.then_inc(ev("q1_used"), 1)
                    pe.wait_ge(ev("q1_used"), 2 * AH + BH + h + 1)
                pe.sem_inc(ev("out_b"), 1)
                end(TILES, SR)
                for b in range(DB):
                    pe.wait_ge(ev("pick"), 3 * (b + 1))
                    if b > 0:
                        pe.wait_ge(ev("tb_new"), b)
                    for h in range(AH):
                        pe.matmul(v4(4)[:, h, :], kr[0:SR, h, :], Wr[0:SR, h, :], start=True, stop=True)
                    for h in range(BH):
                        r = slice(64 * (h % 2), 64 * (h % 2) + 64)
                        o = bank[5][r, 64 * (h // 2):64 * (h // 2) + 64]
                        c = slice(64 * h, 64 * h + 64)
                        pe.matmul(o, Br[0:SR, c], RH[0:SR, c], start=True, stop=False)
                        mm = pe.matmul(o, Kr[0:SR, c], sqa[0:SR, c], start=False, stop=True)
                    mm.then_inc(ev("upd_s"), 1)
                    pe.wait_ge(ev("tb_new"), b + 1)
                    if b > 0:
                        pe.wait_ge(ev("rb_new"), b)
                    for j in range(NP):
                        mm = pe.transpose(bank[6][0:64, j * P:(j + 1) * P], Tb[:, b, j, :], K.ident[:, :])
                    mm.then_inc(ev("rb_mm"), 1)


QKC, VC = CH * CQK, CH * CV
OG, ZG, IG = 2 * QKC + VC, 2 * QKC + 2 * VC, 2 * QKC + 3 * VC
VA1 = CV + 1
BLK = 256
GF = 32


def phase_mlstm_in(nc, K, w_in, b_i, b_f, m0, S, p_m, s_m):
    with ExitStack() as ctx:
        sb = lambda n, s: ctx.enter_context(nc.sbuf_tensor("e_" + n, s, F32))
        parts = lambda n, s: [ctx.enter_context(nc.sbuf_tensor(f"e_{n}{h}", s, F32R)) for h in "hl"]
        ev = Events(nc, ctx, "e_")
        X = parts("x", [P, KT, XW])
        xs = sb("xs", [P, 2, TOK])
        W = [sb(f"w{b}", [P, KT, BLK]) for b in range(2)]
        WP = [parts(f"wp{b}", [P, KT, BLK]) for b in range(2)]
        wg = sb("wg", [P, KT, GF + CH])
        wgp = parts("wgp", [P, KT, GF + CH])
        QB = [sb(f"qb{t}", [P, TOK]) for t in range(2)]
        VB = sb("vb", [P, TILES + 1, BLK])
        GO = sb("go", [P, TILES + 1, BLK])
        T2 = sb("t2", [P, 2, 2, BLK])
        bias = sb("bias", [CH, 2])
        li, lf, bc_, m = [sb(n, [CH, TOK]) for n in ("li", "lf", "b", "m")]
        pad = sb("pad", [CH, 2, DB, DS + 1])
        ms = sb("ms", [CH, DB, DS + 1])
        m0t = sb("m0t", [CH, DB])
        mp = sb("mp", [CH, TILES])
        bank = [ctx.enter_context(nc.psum_tensor(f"e_bank{i}", [P, 512], F32)) for i in range(8)]
        NB = TILES + 1
        PAIRS = ((0, 2, P), (2, 2, P), (4, 2, P), (6, 2, P), (8, 1, SR))
        PLACES = ((0, 1, 2, 3, 4), (5, 6, 7, 2, 3))
        QK_BLOCKS, ROUNDS = 4, CH * CV // BLK // 2
        BEFORE = (5, 5, 5, 4, 4, 4, 1, 1)
        PER = (3, 3, 6, 6, 3, 3, 3, 3)

        def cols(b, r, n):
            return bank[b][0:r, 0:8 * NB].rearrange("p (n h) -> p n h", h=CH)[:, n, :]

        def two(b, c):
            return bank[b][0:c[2], 0:c[1] * BLK].rearrange("p (n c) -> p n c", c=BLK)

        def column(k):
            if k < QK_BLOCKS:
                return k * BLK
            k -= QK_BLOCKS
            return 2 * QKC + (k % 3) * VC + (k // 3) * BLK
        BLOCKS = QK_BLOCKS + 6 * ROUNDS

        def done_at(k, i):
            return 6 * k + i + 1 if k < QK_BLOCKS else 6 * QK_BLOCKS + 5 * (k - QK_BLOCKS) + i + 1

        def last_of(k):
            return done_at(k, 5 if k < QK_BLOCKS else 4)

        def free_at(k, i):
            if k < QK_BLOCKS:
                return i, k + 1 + (1 if i < 3 else 0)
            g, p = divmod(k - QK_BLOCKS, 6)
            b = PLACES[k % 2][i]
            return b, BEFORE[b] + PER[b] * g + (p if b in (2, 3) else p // 2) + 1

        def read(eng, k, i):
            b, n = free_at(k, i)
            eng.wait_ge(ev(f"free{b}"), n)

        with nc.Block() as block:
            @block.sync
            def _(sp):
                def load(k):
                    sp.wait_ge(ev(f"low{k % 2}"), k // 2)
                    sp.dma_start(W[k % 2][:, :, :], w_block(w_in, column(k), BLK)).then_inc(ev(f"ld_w{k % 2}"), 16)
                sp.wait_ge(ev("pad"), 3)
                sp.dma_start(wg[:, :, 0:CH], w_block(w_in, IG, CH)).then_inc(ev("ld_g"), 16)
                sp.dma_start(wg[:, :, GF:GF + CH], w_block(w_in, IG + CH, CH)).then_inc(ev("ld_g"), 16)
                sp.dma_start(bias[:, 0:1], b_i.rearrange("(h a) -> h a", a=1)).then_inc(ev("ld_b"), 16)
                sp.dma_start(bias[:, 1:2], b_f.rearrange("(h a) -> h a", a=1)).then_inc(ev("ld_b"), 16)
                sp.dma_start(m0t[:, :], m0.rearrange("b h -> h b"), allow_slow_non_contiguous=True).then_inc(ev("ld_b"), 16)
                for kt in range(KT):
                    if kt >= 2:
                        sp.wait_ge(ev("x_low"), kt - 1)
                    sp.dma_start(xs[:, kt % 2, :], S.xnT[:, kt, :]).then_inc(ev(f"ld_x{kt % 2}"), 16)
                    if kt == KT - 3:
                        load(0)
                load(1)
                for k in range(QK_BLOCKS):
                    load(k + 2)
                    for t in range(2):
                        read(sp, k, 3 * t + 2)
                        r = (k % 2) * BLK + t * P
                        sp.dma_start(S.ql[k // 2, r:r + P, :], QB[t][:, :]).then_inc(ev(f"out_q{t}"), 16)

                def store(c, dram, t, done):
                    sp.dma_start(dram[0:SEQ, c * BLK:c * BLK + BLK].rearrange("(n p) c -> p n c", p=P), t[:, 0:TILES, :]).then_inc(done, 16)
                    sp.dma_start(dram[SEQ:TOK, c * BLK:c * BLK + BLK], t[0:SR, TILES, :]).then_inc(done, 16)
                for c in range(2 * ROUNDS):
                    for q in range(3):
                        k = QK_BLOCKS + 3 * c + q + 2
                        if k < BLOCKS:
                            load(k)
                        if q == 0:
                            read(sp, QK_BLOCKS + 3 * c, 4)
                            store(c, S.v, VB, ev("out_v"))
                    sp.wait_ge(ev("gated"), 5 * (c + 1))
                    store(c, S.g, GO, ev("out_g"))
                sp.wait_ge(ev("m_end"), 1)
                sp.dma_start(p_m.rearrange("b h -> h b"), m[:, SEQ - 1:SEQ], allow_slow_non_contiguous=True).then_inc(ev("out_m"), 16)
                sp.dma_start(s_m.rearrange("b h -> h b"), ms[:, :, DS], allow_slow_non_contiguous=True).then_inc(ev("out_m"), 16)
                for n, k in (("out_q0", QK_BLOCKS), ("out_q1", QK_BLOCKS), ("out_v", 4 * ROUNDS), ("out_g", 4 * ROUNDS), ("out_m", 2)):
                    sp.wait_ge(ev(n), 16 * k)

            @block.gpsimd
            def _(pool):
                pool.memset(wg[:, :, :], 0.0).then_inc(ev("pad"), 1)
                for x in X:
                    pool.memset(x[:, :, TOK:XW].bitcast(F32), 0.0).then_inc(ev("pad"), 1)
                done = Seq(ev("pseq"), pool, 4)
                done.start(0)
                done(pool.memset(K.sel[:, :, :], 1.0))
                done(pool.affine_select(out=K.sel[:, :, :], in_=K.sel[:, :, :], compare_op=ALU.is_equal, fill=0.0, base=0,
                                        pattern=[[-1, CH], [0, P]], channel_multiplier=1))
                done(pool.memset(K.sel2[:, :, :], 1.0))
                done(pool.affine_select(out=K.sel2[:, :, :].rearrange("g j (u c) -> g (j u) c", u=2),
                                        in_=K.sel2[:, :, :].rearrange("g j (u c) -> g (j u) c", u=2),
                                        compare_op=ALU.is_equal, fill=0.0, base=0,
                                        pattern=[[-1, CH], [0, 64]], channel_multiplier=1))
                done.end()
                pool.wait_ge(ev("g_high"), 1)
                pool.tensor_tensor(wgp[1][:, :, :], wg[:, :, :], wgp[0][:, :, :].bitcast(F32), ALU.subtract).then_inc(ev("g_low"), 1)
                for k in range(BLOCKS):
                    b = k % 2
                    pool.wait_ge(ev(f"high{b}"), k // 2 + 1)
                    pool.tensor_tensor(WP[b][1][:, :, :], W[b][:, :, :], WP[b][0][:, :, :].bitcast(F32), ALU.subtract
                                       ).then_inc(ev(f"low{b}"), 1)

            @block.scalar
            def _(act):
                def high(k):
                    if k < BLOCKS:
                        b = k % 2
                        act.wait_ge(ev(f"ld_w{b}"), 16 * (k // 2 + 1))
                        act.wait_ge(ev(f"low{b}"), k // 2)
                        if k >= 2:
                            act.wait_ge(ev("bank_full"), last_of(k - 2))
                        act.activation(WP[b][0][:, :, :], W[b][:, :, :], ACT.Copy).then_inc(ev(f"high{b}"), 1)
                act.wait_ge(ev("ld_g"), 32)
                act.activation(wgp[0][:, :, :], wg[:, :, :], ACT.Copy).then_inc(ev("g_high"), 1)
                for kt in range(KT):
                    act.wait_ge(ev(f"ld_x{kt % 2}"), 16 * (kt // 2 + 1))
                    act.activation(X[0][:, kt, 0:TOK], xs[:, kt % 2, :], ACT.Copy).then_inc(ev("x_high"), 1)
                high(0)
                act.wait_ge(ev("bias"), 1)
                for g, (c, n) in enumerate(THIRDS):
                    act.wait_ge(ev("gate_mm"), g + 1)
                    act.activation(li[:, c:c + n], bank[g][0:CH, 0:n], ACT.Tanh, scale=1.0 / CAP, bias=bias[:, 0:1])
                    act.activation(lf[:, c:c + n], bank[g][GF:GF + CH, 0:n], ACT.Tanh, scale=1.0 / CAP,
                                   bias=bias[:, 1:2]).then_inc(ev(f"free{g}"), 1)
                act.wait_ge(ev("free2"), 1)
                act.activation(lf[:, :], lf[:, :], ACT.Exp, scale=-CAP).then_inc(ev("gate_e"), 1)
                act.wait_ge(ev("gate_e"), 1)
                act.activation(lf[:, :], lf[:, :], ACT.Ln, bias=1.0).then_inc(ev("gate_e"), 1)
                for k in range(QK_BLOCKS):
                    high(k + 1)
                    for t in range(2):
                        act.wait_ge(ev(f"out_q{t}"), 16 * k)
                        for g, (c, n) in enumerate(THIRDS):
                            i = 3 * t + g
                            act.wait_ge(ev("bank_full"), done_at(k, i))
                            act.activation(QB[t][:, c:c + n], bank[i][:, 0:n], ACT.Copy,
                                           scale=CQK ** -0.5 if k < 2 else 1.0).then_inc(ev(f"free{i}"), 1)
                    if k == 1:
                        act.wait_ge(ev("e_log"), 2)
                        act.activation(K.e[:, :], K.e[:, :], ACT.Exp).then_inc(ev("e_kept"), 1)
                act.wait_ge(ev("turned"), 1)
                for r, n in ((P, slice(0, TILES)), (SR, slice(TILES, NB))):
                    ins = act.activation(K.em[0:r, n, :], cols(6, r, n), ACT.Exp, scale=-1.0)
                ins.then_inc(ev("free6"), 1)
                for c in range(2 * ROUNDS):
                    for q in range(3):
                        k = QK_BLOCKS + 3 * c + q
                        high(k + 1)
                        for i, at in enumerate(PAIRS):
                            b = PLACES[k % 2][i]
                            r, n = at[2], slice(at[0], at[0] + at[1])
                            act.wait_ge(ev("bank_full"), done_at(k, i))
                            if q == 0:
                                if i == 0:
                                    act.wait_ge(ev("out_v"), 32 * c)
                                act.activation(VB[0:r, n, :], two(b, at), ACT.Copy).then_inc(ev(f"free{b}"), 1)
                            elif q == 1:
                                if i == 0:
                                    act.wait_ge(ev("out_g"), 32 * c)
                                act.activation(GO[0:r, n, :], two(b, at), ACT.Tanh, scale=0.5).then_inc(ev(f"free{b}"), 1)
                            else:
                                z = 5 * c + i
                                if z >= 2:
                                    act.wait_ge(ev("gated"), z - 1)
                                act.activation(T2[0:r, z % 2, 0:at[1], :], two(b, at), ACT.Tanh, scale=0.5).then_inc(ev("tz"), 1)

            @block.vector
            def _(dve):
                dve.wait_ge(ev("ld_b"), 48)
                dve.tensor_scalar(bias[:, :], bias[:, :], 1.0 / CAP, None, ALU.mult).then_inc(ev("bias"), 1)
                for kt in range(KT):
                    dve.wait_ge(ev("x_high"), kt + 1)
                    dve.tensor_tensor(X[1][:, kt, 0:TOK], xs[:, kt % 2, :], X[0][:, kt, 0:TOK].bitcast(F32), ALU.subtract).then_inc(ev("x_low"), 1)
                done = Seq(ev("dseq"), dve, 14)
                done.start(0)
                dve.wait_ge(ev("gate_e"), 2)
                done(dve.tensor_scalar(li[:, :], li[:, :], CAP, None, ALU.mult))
                done(dve.tensor_scalar(lf[:, :], lf[:, :], -1.0, None, ALU.mult))
                done(dve.tensor_tensor_scan(bc_[:, :], K.restart[0:CH, :], lf[:, :], 0.0, ALU.mult, ALU.add))
                done(dve.tensor_tensor_scan(m[:, 0:SEQ], lf[:, 0:SEQ], li[:, 0:SEQ], 0.0, ALU.add, ALU.max))
                done(dve.memset(pad[:, 0, :, 0], -1e30))
                done(dve.tensor_copy(pad[:, 1, :, 0], m0t[:, :]))
                done(dve.tensor_copy(pad[:, 0, :, 1:DS + 1], lf[:, SEQ:TOK].rearrange("h (b t) -> h b t", b=DB)))
                done(dve.tensor_copy(pad[:, 1, :, 1:DS + 1], li[:, SEQ:TOK].rearrange("h (b t) -> h b t", b=DB)))
                done(dve.tensor_tensor_scan(ms[:, :, :].rearrange("h b t -> h (b t)"), pad[:, 0, :, :].rearrange("h b t -> h (b t)"),
                                            pad[:, 1, :, :].rearrange("h b t -> h (b t)"), 0.0, ALU.add, ALU.max))
                done(dve.tensor_copy(m[:, SEQ:TOK].rearrange("h (b t) -> h b t", b=DB), ms[:, :, 1:DS + 1]))
                dve.sem_inc(ev("m_end"), 1)
                done(dve.tensor_tensor(K.u[:, :], bc_[:, :], m[:, :], ALU.subtract))
                done(dve.tensor_tensor(li[:, :], li[:, :], bc_[:, :], ALU.subtract))
                done(dve.memset(mp[:, 0:1], 0.0))
                done(dve.tensor_copy(mp[:, 1:TILES], m[:, P - 1:SEQ - P:P]))
                done.end()
                dve.sem_inc(ev("w"), 1)
                dve.tensor_tensor(K.e[:, 0:SEQ].rearrange("h (n t) -> h n t", n=TILES), K.u[:, 0:SEQ].rearrange("h (n t) -> h n t", n=TILES),
                                  mp[:, :].rearrange("h (n a) -> h n a", a=1).broadcast_to([CH, TILES, P]), ALU.add).then_inc(ev("e_log"), 1)
                dve.tensor_tensor(K.e[:, SEQ:TOK].rearrange("h (b t) -> h b t", b=DB), K.u[:, SEQ:TOK].rearrange("h (b t) -> h b t", b=DB),
                                  m0t[:, :].rearrange("h (b a) -> h b a", a=1).broadcast_to([CH, DB, DS]), ALU.add).then_inc(ev("e_log"), 1)
                dve.wait_ge(ev("turned"), 2)
                for r, n in ((P, slice(0, TILES)), (SR, slice(TILES, NB))):
                    ins = dve.tensor_copy(K.w[0:r, n, :], cols(7, r, n))
                ins.then_inc(ev("free7"), 1)
                for c in range(2 * ROUNDS):
                    k = QK_BLOCKS + 3 * c + 2
                    for i, at in enumerate(PAIRS):
                        b, z = PLACES[k % 2][i], 5 * c + i
                        r, n = at[2], slice(at[0], at[0] + at[1])
                        t2 = T2[0:r, z % 2, 0:at[1], :]
                        dve.wait_ge(ev("tz"), z + 1)
                        dve.scalar_tensor_tensor(out=t2, in0=t2, scalar=1.0, in1=two(b, at), op0=ALU.add, op1=ALU.mult).then_inc(ev(f"free{b}"), 1)
                        read(dve, k, i)
                        read(dve, k - 1, i)
                        dve.scalar_tensor_tensor(out=GO[0:r, n, :], in0=GO[0:r, n, :], scalar=1.0, in1=t2,
                                                 op0=ALU.add, op1=ALU.mult).then_inc(ev("gated"), 1)

            @block.tensor
            def _(pe):
                pe.wait_ge(ev("g_high"), 1)
                pe.wait_ge(ev("g_low"), 1)
                for kt in range(KT):
                    pe.wait_ge(ev("x_low"), kt + 1)
                    for g, (c, n) in enumerate(THIRDS):
                        mm = products(pe, bank[g][0:GF + CH, 0:n], (wgp[0][:, kt, :], wgp[1][:, kt, :]),
                                      (X[0][:, kt, c:c + n], X[1][:, kt, c:c + n]), kt == 0, kt == KT - 1)
                        if kt == KT - 1:
                            mm.then_inc(ev("gate_mm"), 1)
                pe.wait_ge(ev("pad"), 3)
                for k in range(QK_BLOCKS):
                    b = k % 2
                    pe.wait_ge(ev(f"high{b}"), k // 2 + 1)
                    pe.wait_ge(ev(f"low{b}"), k // 2 + 1)
                    for t in range(2):
                        for g, (c, n) in enumerate(THIRDS):
                            i = 3 * t + g
                            pe.wait_ge(ev(f"free{i}"), k + (1 if i < 3 else 0))
                            for kt in range(KT):
                                w = [x[:, kt, t * P:(t + 1) * P] for x in WP[b]]
                                mm = products(pe, bank[i][:, 0:n], w, [x[:, kt, c:c + n] for x in X], kt == 0, kt == KT - 1)
                            mm.then_inc(ev("bank_full"), 1)
                pe.wait_ge(ev("w"), 1)
                for src, b in ((m, 6), (li, 7)):
                    for n in range(NB):
                        r = P if n < TILES else SR
                        mm = pe.transpose(bank[b][0:r, 8 * n:8 * n + 8], src[:, n * P:n * P + r], K.ident[0:CH, 0:CH])
                    mm.then_inc(ev("turned"), 1)
                with pe.Fori(0, ROUNDS) as g:
                    for p in range(6):
                        b = p % 2
                        n = QK_BLOCKS // 2 + p // 2 + 1
                        pe.wait_ge(ev(f"high{b}"), 3 * g + n)
                        pe.wait_ge(ev(f"low{b}"), 3 * g + n)
                        for i, at in enumerate(PAIRS):
                            o = PLACES[b][i]
                            used = p // 2 if o not in (2, 3) else p
                            pe.wait_ge(ev(f"free{o}"), PER[o] * g + BEFORE[o] + used)
                            for t in range(at[1]):
                                tok = slice((at[0] + t) * P, (at[0] + t + 1) * P)
                                for kt in range(KT):
                                    mm = products(pe, bank[o][:, t * BLK:(t + 1) * BLK], [x[:, kt, tok] for x in X],
                                                  [w[:, kt, :] for w in WP[b]], kt == 0, kt == KT - 1)
                            mm.then_inc(ev("bank_full"), 1)
    

def phase_mix1(nc, K, w_out, norm_w, c0, n0, S, y_p, y_s, p_c, p_n, s_c, s_n):
    with ExitStack() as ctx:
        sb = lambda n, s: ctx.enter_context(nc.sbuf_tensor("f_" + n, s, F32))
        ev = Events(nc, ctx, "f_")
        QL = sb("ql", [P, 2, NP, P])
        VA = sb("va", [P, CH, VA1])
        GR = sb("gr", [P, D])
        XR = sb("xr", [P, D])
        wo = sb("wo", [P, KT, D])
        nw = sb("nw", [P, D])
        ut, et = sb("ut", [CH, P]), sb("et", [CH, P])
        wt, emt = sb("wt", [P, CH]), sb("emt", [P, CH])
        Dm = sb("dm", [P, CH, P])
        PM = sb("pm", [P, CH, P])
        qe = sb("qe", [P, NP, P])
        ec = sb("ec", [P, NP, DB])
        wk = sb("wk", [P, CH])
        KW = sb("kw", [P, QKC])
        den = sb("den", [P, 2, CH])
        H = sb("h", [P, D])
        OT = sb("ot", [P, KT, P])
        C = sb("c", [P, NP, VA1])
        n1 = sb("n1", [P, 4])
        yo = sb("yo", [P, D])
        Cb = sb("cb", [P, DB, NP, VA1])
        Q1 = sb("q1", [P, DB, SR])
        KM = sb("km", [P, QKC])
        bank = [ctx.enter_context(nc.psum_tensor(f"f_bank{i}", [P, 512], F32)) for i in range(8)]
        place = {h: (6 + h % 2, VA1 * (h // 2)) if h < 6 else (3 + h % 2, 0) for h in range(CH)}

        def v4(b, r=P, c=P):
            return bank[b][0:r, :].rearrange("p (h c) -> p h c", h=4)[:, :, 0:c]

        def split(b, r):
            if b >= 6:
                t = bank[b][0:r, 0:3 * VA1].rearrange("p (h c) -> p h c", h=3)
                return slice(b % 2, 6, 2), t[:, :, 0:CV], t[:, :, CV]
            t = bank[b][0:r, 0:VA1].rearrange("p (h c) -> p h c", h=1)
            return slice(3 + b, 4 + b), t[:, :, 0:CV], t[:, :, CV]

        with nc.Block() as block:
            @block.sync
            def _(sp):
                sp.dma_start(wo[:, :, :], w_block(w_out, 0, D)).then_inc(ev("ld_wo"), 16)
                sp.dma_start(nw[:, :], as_row(norm_w)).then_inc(ev("ld_nw"), 16)

                def load(i, c, T):
                    sp.wait_ge(ev("qk"), i)
                    sp.wait_ge(ev("rows"), i)
                    sp.wait_ge(ev("qe"), i)
                    alone(sp, K)
                    for m in range(2):
                        sp.dma_start(QL[:, m, :, 0:T], S.ql[m].rearrange("(j p) t -> p j t", p=P)[:, :, bass.ds(c, T)]).then_inc(ev("ld_q"), 16)
                    sp.wait_ge(ev("num"), i)
                    sp.wait_ge(ev("upd"), i)
                    alone(sp, K)
                    sp.dma_start(VA[0:T, :, 0:CV], S.v[bass.ds(c, T), :].rearrange("t (h v) -> t h v", h=CH)).then_inc(ev("ld_v"), 16)
                    sp.wait_ge(ev("gate"), i)
                    alone(sp, K)
                    sp.dma_start(GR[0:T, :], S.g[bass.ds(c, T), :]).then_inc(ev("ld_gr"), 16)
                    sp.wait_ge(ev("y"), i)
                    alone(sp, K)
                    sp.dma_start(XR[0:T, :], S.x1[bass.ds(c, T), :]).then_inc(ev("ld_x"), 16)

                def store(i, c, T):
                    sp.wait_ge(ev("y"), i + 1)
                    alone(sp, K)
                    y = y_p[0, bass.ds(c, T), :] if T == P else y_s.rearrange("b t d -> (b t) d")
                    sp.dma_start(y, yo[0:T, :]).then_inc(ev("stored"), 16)
                with sp.Fori(0, TILES) as i:
                    load(i, i * P, P)
                    store(i, i * P, P)
                sp.wait_ge(ev("state"), TILES)
                pair = lambda t: t.rearrange("(j h) k v -> (h k) j v", h=2)
                pair2 = lambda t: t.rearrange("(j h) k -> (h k) j", h=2)
                for h in range(2):
                    r = slice(64 * h, 64 * h + 64)
                    sp.dma_start(p_c[0].rearrange("(j h) k v -> h k j v", h=2)[h], C[r, :, 0:CV], allow_slow_non_contiguous=True).then_inc(ev("c_out"), 16)
                    sp.dma_start(p_n[0].rearrange("(j h) k -> h k j", h=2)[h], C[r, :, CV], allow_slow_non_contiguous=True).then_inc(ev("c_out"), 16)
                    for b in range(DB):
                        sp.dma_start(Cb[r, b, :, 0:CV], c0[b].rearrange("(j h) k v -> h k j v", h=2)[h]).then_inc(ev("ld_c"), 16)
                        sp.dma_start(Cb[r, b, :, CV], n0[b].rearrange("(j h) k -> h k j", h=2)[h], allow_slow_non_contiguous=True).then_inc(ev("ld_c"), 16)
                load(TILES, SEQ, SR)
                store(TILES, SEQ, SR)
                for b in range(DB):
                    sp.wait_ge(ev("cb"), b + 1)
                    for h in range(2):
                        r = slice(64 * h, 64 * h + 64)
                        sp.dma_start(s_c[b].rearrange("(j h) k v -> h k j v", h=2)[h], Cb[r, b, :, 0:CV], allow_slow_non_contiguous=True).then_inc(ev("cb_out"), 16)
                        sp.dma_start(s_n[b].rearrange("(j h) k -> h k j", h=2)[h], Cb[r, b, :, CV], allow_slow_non_contiguous=True).then_inc(ev("cb_out"), 16)
                sp.wait_ge(ev("stored"), 16 * (TILES + 1))
                sp.wait_ge(ev("c_out"), 64)
                sp.wait_ge(ev("cb_out"), 64 * DB)

            @block.gpsimd
            def _(pool):
                pool.memset(VA[:, :, CV:VA1], 1.0).then_inc(ev("va1"), 1)
                pool.memset(C[:, :, :], 0.0).then_inc(ev("init"), 1)

                def tile(i, T):
                    n = i + 1
                    pool.wait_ge(ev("n1"), n)
                    pool.tensor_tensor(n1[0:T, 2:3], n1[0:T, 1:2], K.half_neg[0:T, 0:1], ALU.pow).then_inc(ev("n1r"), 1)
                with pool.Fori(0, TILES) as i:
                    tile(i, P)
                tile(TILES, SR)

            @block.scalar
            def _(act):
                def tile(i, c, T):
                    n = i + 1
                    act.wait_ge(ev("ub"), i)
                    act.activation(ut[:, 0:T], K.u[:, bass.ds(c, T)], ACT.Copy).then_inc(ev("ut"), 1)
                    act.wait_ge(ev("eb"), i)
                    act.activation(et[:, 0:T], K.e[:, bass.ds(c, T)], ACT.Copy).then_inc(ev("et"), 1)
                    act.wait_ge(ev("dmin"), i)
                    act.activation(wt[0:T, :], K.w[0:T, bass.ds(i, 1), :].rearrange("p a h -> p (a h)"), ACT.Copy).then_inc(ev("wt"), 1)
                    act.wait_ge(ev("rden"), i)
                    act.activation(emt[0:T, :], K.em[0:T, bass.ds(i, 1), :].rearrange("p a h -> p (a h)"), ACT.Copy).then_inc(ev("emt"), 1)
                    act.wait_ge(ev("dmin"), n)
                    act.activation(Dm[0:T, :, 0:T], Dm[0:T, :, 0:T], ACT.Exp).then_inc(ev("dexp"), 1)
                    act.wait_ge(ev("num"), n)
                    for b in (6, 7, 3, 4):
                        hs, _, dn = split(b, T)
                        ins = act.activation(den[0:T, 0, hs], dn, ACT.Abs)
                    ins.then_inc(ev("den"), 1)
                    act.wait_ge(ev("ot_mm"), n)
                    act.wait_ge(ev("prj"), i)
                    act.activation(OT[:, 0:4, 0:T], v4(0, P, T), ACT.Copy).then_inc(ev("ot"), 1)
                    act.wait_ge(ev("x2"), n)
                    act.wait_ge(ev("stored"), 16 * i)
                    act.activation(yo[0:T, :], XR[0:T, :], ACT.Square, accum_out=n1[0:T, 0:1]).then_inc(ev("n1s"), 1)
                with act.Fori(0, TILES) as i:
                    tile(i, i * P, P)
                tile(TILES, SEQ, SR)
                for b in range(DB):
                    act.wait_ge(ev("upd_s"), b)
                    act.activation(KM[0:SR, :], KW[0:SR, :], ACT.Copy, scale=K.same[:, b * DS:b * DS + 1]).then_inc(ev("pick"), 1)

            @block.vector
            def _(dve):
                bc = lambda t, s: t.broadcast_to(s)

                def tile(i, T, lmask):
                    n = i + 1
                    dve.wait_ge(ev("ub"), n)
                    dve.wait_ge(ev("wt"), n)
                    dve.wait_ge(ev("kw"), i)
                    dve.wait_ge(ev("pm"), 2 * i)
                    for h in range(CH):
                        ins = dve.scalar_tensor_tensor(out=Dm[0:T, h, 0:T], in0=v4(h // 4, T, T)[:, h % 4, :], scalar=wt[0:T, h:h + 1],
                                                       in1=lmask[0:T, 0:T], op0=ALU.add, op1=ALU.min)
                    ins.then_inc(ev("dmin"), 1)
                    dve.wait_ge(ev("eb"), n)
                    dve.wait_ge(ev("ld_q"), 32 * n)
                    dve.wait_ge(ev("num"), i)
                    dve.wait_ge(ev("state"), i)
                    dve.tensor_tensor(qe[:, :, 0:T], QL[:, 0, :, 0:T], v4(2, P, T), ALU.mult).then_inc(ev("qe"), 1)
                    if T == P:
                        dve.tensor_copy(ec[:, :, 0], v4(2)[:, :, P - 1]).then_inc(ev("ec"), 1)
                    else:
                        dve.tensor_copy(ec[:, :, :], v4(2, P, T)[:, :, DS - 1:SR:DS]).then_inc(ev("ec"), 1)
                    dve.wait_ge(ev("dexp"), n)
                    dve.wait_ge(ev("qk"), n)
                    for k in range(2):
                        dve.tensor_tensor(PM[0:T, k::2, 0:T], Dm[0:T, k::2, 0:T], v4(3 + k, T, T), ALU.mult).then_inc(ev("pm"), 1)
                    dve.wait_ge(ev("rows"), n)
                    dve.wait_ge(ev("upd"), i)
                    if T == P:
                        w = Dm[:, :, P - 1]
                    else:
                        dve.wait_ge(ev("pm"), 2 * n)
                        dve.tensor_tensor(Dm[0:T, :, 0:T], Dm[0:T, :, 0:T], bc(K.last[:, :].rearrange("s (a t) -> s a t", a=1),
                                                                            [T, CH, T]), ALU.mult).then_inc(ev("wk"), 1)
                        dve.wait_ge(ev("wk"), 1)
                        dve.tensor_reduce(wk[0:T, :], Dm[0:T, :, 0:T], AX_X, ALU.add).then_inc(ev("wk"), 1)
                        dve.wait_ge(ev("wk"), 2)
                        w = wk[0:T, :]
                    dve.tensor_tensor(KW[0:T, :].rearrange("p (h k) -> p h k", h=CH), bank[5][0:T, :].rearrange("p (h k) -> p h k", h=CH),
                                      bc(w.rearrange("p (h a) -> p h a", a=1), [T, CH, 64]), ALU.mult).then_inc(ev("kw"), 1)
                    if T != P:
                        for h in range(CH):
                            if h:
                                dve.wait_ge(ev("q1_used"), h)
                            dve.wait_ge(ev("qe"), n)
                            dve.scalar_tensor_tensor(out=Q1[:, :, :], in0=bc(qe[:, h // 2, 0:T].rearrange("p (a t) -> p a t", a=1), [P, DB, SR]),
                                                     scalar=K.head_cols[:, h % 2:h % 2 + 1], in1=K.batch_cols[:, :, :],
                                                     op0=ALU.mult, op1=ALU.mult).then_inc(ev("q1"), 1)
                    dve.wait_ge(ev("den"), n)
                    dve.wait_ge(ev("emt"), n)
                    dve.tensor_tensor(den[0:T, 0, :], den[0:T, 0, :], emt[0:T, :], ALU.max).then_inc(ev("den2"), 1)
                    dve.wait_ge(ev("den2"), n)
                    dve.tensor_scalar(den[0:T, 0, :], den[0:T, 0, :], 4.0, None, ALU.mult).then_inc(ev("den3"), 1)
                    dve.wait_ge(ev("den3"), n)
                    dve.wait_ge(ev("ot_mm"), i)
                    dve.reciprocal(den[0:T, 1, :], den[0:T, 0, :]).then_inc(ev("rden"), 1)
                    dve.wait_ge(ev("rden"), n)
                    h3 = H[0:T, :].rearrange("p (h c) -> p h c", h=CH)
                    for b in (6, 7, 3, 4):
                        hs, nm, _ = split(b, T)
                        w = nm.shape[1]
                        ins = dve.tensor_tensor(h3[:, hs, :], nm, bc(den[0:T, 1, hs].rearrange("p (h a) -> p h a", a=1), [T, w, CV]), ALU.mult)
                    ins.then_inc(ev("hr"), 1)
                    dve.wait_ge(ev("hr"), n)
                    dve.wait_ge(ev("ld_gr"), 16 * n)
                    dve.tensor_tensor(H[0:T, :], H[0:T, :], GR[0:T, :], ALU.mult).then_inc(ev("gate"), 1)
                    if T == P:
                        dve.wait_ge(ev("upd"), n)
                        dve.wait_ge(ev("ec"), n)
                        for j in range(NP):
                            src = bank[2][:, VA1 * j:VA1 * (j + 1)] if j < 3 else bank[5][:, 0:VA1]
                            ins = dve.scalar_tensor_tensor(out=C[:, j, :], in0=C[:, j, :], scalar=ec[:, j, 0:1], in1=src,
                                                           op0=ALU.mult, op1=ALU.add)
                        ins.then_inc(ev("state"), 1)
                    dve.wait_ge(ev("ot_mm"), n)
                    dve.wait_ge(ev("prj"), i)
                    dve.tensor_copy(OT[:, 4:8, 0:T], v4(1, P, T)).then_inc(ev("ot2"), 1)
                    dve.wait_ge(ev("prj"), n)
                    dve.wait_ge(ev("ld_x"), 16 * n)
                    for c in range(2):
                        ins = dve.tensor_tensor(XR[0:T, 512 * c:512 * c + 512], bank[6 + c][0:T, :], XR[0:T, 512 * c:512 * c + 512], ALU.add)
                    ins.then_inc(ev("x2"), 1)
                    dve.wait_ge(ev("n1s"), n)
                    dve.tensor_scalar(n1[0:T, 1:2], n1[0:T, 0:1], 1.0 / D, EPS, ALU.mult, ALU.add).then_inc(ev("n1"), 1)
                    dve.wait_ge(ev("n1r"), n)
                    dve.scalar_tensor_tensor(out=yo[0:T, :], in0=XR[0:T, :], scalar=n1[0:T, 2:3], in1=nw[0:T, :],
                                             op0=ALU.mult, op1=ALU.mult).then_inc(ev("y"), 1)
                dve.wait_ge(ev("ld_nw"), 16)
                with dve.Fori(0, TILES) as i:
                    tile(i, P, K.lcausal)
                tile(TILES, SR, K.lcausal_s)
                for b in range(DB):
                    dve.wait_ge(ev("upd_s"), b + 1)
                    for j in range(NP):
                        src = bank[2][:, VA1 * j:VA1 * (j + 1)] if j < 3 else bank[5][:, 0:VA1]
                        ins = dve.scalar_tensor_tensor(out=Cb[:, b, j, :], in0=Cb[:, b, j, :], scalar=ec[:, j, b:b + 1], in1=src,
                                                       op0=ALU.mult, op1=ALU.add)
                    ins.then_inc(ev("cb"), 1)

            @block.tensor
            def _(pe):
                def update(T, keys, name):
                    for h in range(CH):
                        r = slice(64 * (h % 2), 64 * (h % 2) + 64)
                        j = h // 2
                        o = bank[2][r, VA1 * j:VA1 * (j + 1)] if j < 3 else bank[5][r, 0:VA1]
                        mm = pe.matmul(o, keys[0:T, 64 * h:64 * h + 64], VA[0:T, h, :], start=True, stop=True)
                    mm.then_inc(ev(name), 1)

                def tile(i, T):
                    n = i + 1
                    pe.wait_ge(ev("ut"), n)
                    pe.wait_ge(ev("ot"), i)
                    pe.wait_ge(ev("ot2"), i)
                    for h in range(CH):
                        mm = pe.matmul(v4(h // 4, T, T)[:, h % 4, :], K.sel[:, h, 0:T], ut[:, 0:T], start=True, stop=True)
                    mm.then_inc(ev("ub"), 1)
                    pe.wait_ge(ev("et"), n)
                    pe.wait_ge(ev("state"), i)
                    for j in range(NP):
                        mm = pe.matmul(v4(2, P, T)[:, j, :], K.sel2[:, j, :], et[:, 0:T], start=True, stop=True)
                    mm.then_inc(ev("eb"), 1)
                    pe.wait_ge(ev("hr"), i)
                    pe.wait_ge(ev("ld_q"), 32 * n)
                    for h in range(CH):
                        r = slice(64 * (h % 2), 64 * (h % 2) + 64)
                        mm = pe.matmul(v4(3 + h % 2, T, T)[:, h // 2, :], QL[r, 1, h // 2, 0:T], QL[r, 0, h // 2, 0:T], start=True, stop=True)
                    mm.then_inc(ev("qk"), 1)
                    for j in range(NP):
                        mm = pe.transpose(v4(5, T)[:, j, :], QL[:, 1, j, 0:T], K.ident[:, :])
                    mm.then_inc(ev("rows"), 1)
                    pe.wait_ge(ev("ld_v"), 16 * n)
                    pe.wait_ge(ev("qe"), n)
                    pe.wait_ge(ev("x2"), i)
                    pe.wait_ge(ev("pm"), 2 * n)
                    for h in range(CH):
                        r = slice(64 * (h % 2), 64 * (h % 2) + 64)
                        b, c = place[h]
                        o = bank[b][0:T, c:c + VA1]
                        pe.matmul(o, PM[0:T, h, 0:T], VA[0:T, h, :], start=True, stop=False)
                        if T == P:
                            mm = pe.matmul(o, qe[r, h // 2, :], C[r, h // 2, :], start=False, stop=True)
                        else:
                            pe.wait_ge(ev("q1"), h + 1)
                            for b in range(DB):
                                mm = pe.matmul(o, Q1[:, b, :], Cb[:, b, h // 2, :], start=False, stop=(b == DB - 1))
                            mm.then_inc(ev("q1_used"), 1)
                            pe.wait_ge(ev("q1_used"), h + 1)
                    if T == P:
                        mm.then_inc(ev("num"), 1)
                        pe.wait_ge(ev("kw"), n)
                        pe.wait_ge(ev("ec"), n)
                        update(T, KW, "upd")
                    else:
                        pe.sem_inc(ev("num"), 1)
                    pe.wait_ge(ev("gate"), n)
                    pe.wait_ge(ev("dmin"), n)
                    for c in range(KT):
                        mm = pe.transpose(v4(c // 4, P, T)[:, c % 4, :], H[0:T, c * P:(c + 1) * P], K.ident[0:T, 0:T])
                    mm.then_inc(ev("ot_mm"), 1)
                    pe.wait_ge(ev("ot"), n)
                    pe.wait_ge(ev("ot2"), n)
                    for c in range(2):
                        for kt in range(KT):
                            mm = pe.matmul(bank[6 + c][0:T, :], OT[:, kt, 0:T], wo[:, kt, 512 * c:512 * c + 512],
                                           start=(kt == 0), stop=(kt == KT - 1))
                    mm.then_inc(ev("prj"), 1)
                pe.wait_ge(ev("ld_wo"), 16)
                pe.wait_ge(ev("va1"), 1)
                pe.wait_ge(ev("init"), 1)
                with pe.Fori(0, TILES) as i:
                    tile(i, P)
                pe.wait_ge(ev("ld_c"), 32 * DB * 2)
                tile(TILES, SR)
                for b in range(DB):
                    pe.wait_ge(ev("pick"), b + 1)
                    pe.wait_ge(ev("cb"), b)
                    pe.wait_ge(ev("kw"), TILES + 1)
                    pe.wait_ge(ev("ec"), TILES + 1)
                    update(SR, KM, "upd_s")


_INS = ("x_prompt", "x_sample", "state_gdn_conv", "state_gdn", "state_rwkv_shift", "state_rwkv",
        "state_mlstm_c", "state_mlstm_n", "state_mlstm_m",
        "norm0_w", "w_in0", "w_out0", "gdn_conv_w", "gdn_a_log", "gdn_dt_bias", "gdn_norm_w",
        "rwkv_mu", "rwkv_w0", "rwkv_w2", "rwkv_a0", "rwkv_a2", "rwkv_k_k", "rwkv_k_a", "rwkv_r_k",
        "rwkv_ln_w", "rwkv_ln_b", "norm1_w", "w_in1", "w_out1", "mlstm_b_i", "mlstm_b_f", "norm_f_w")
_OUTS = (("y_prompt", (1, SEQ, D)), ("y_sample", (DB, DS, D)),
         ("p_conv", (1, CONV - 1, AQKV)), ("p_gdn", (1, AH, P, P)), ("p_shift", (1, D)), ("p_rwkv", (1, BH, 64, 64)),
         ("p_c", (1, CH, CQK, CV)), ("p_n", (1, CH, CQK)), ("p_m", (1, CH)),
         ("s_conv", (DB, CONV - 1, AQKV)), ("s_gdn", (DB, AH, P, P)), ("s_shift", (DB, D)), ("s_rwkv", (DB, BH, 64, 64)),
         ("s_c", (DB, CH, CQK, CV)), ("s_n", (DB, CH, CQK)), ("s_m", (DB, CH)))


class Scope:
    pass


def build(nc, A, O):
    K, S = Scope(), Scope()
    dram = lambda name, shape: nc.dram_tensor("scratch_" + name, shape, F32, kind="Internal").ap()
    S.qkv, S.z, S.rw = dram("qkv", [3, AKEY, TOK]), dram("z", [TOK, AKEY]), dram("rw", [6, BW, TOK])
    S.x1, S.xnT = dram("x1", [TOK, D]), dram("xnT", [P, KT, TOK])
    S.ql, S.v, S.g = dram("ql", [2, CH * CQK, TOK]), dram("v", [TOK, D]), dram("g", [TOK, D])
    chip = lambda ctx, name, shape: ctx.enter_context(nc.sbuf_tensor("k_" + name, shape, F32))
    NB = TILES + 1

    with ExitStack() as kept:
        (K.ident, K.ones, K.half_neg, K.pair_ones, K.causal, K.strict, K.same, K.causal_s, K.strict_s, K.last, K.restart,
         K.batch_cols, K.head_cols, K.lcausal, K.lcausal_s) = [chip(kept, name, shape) for name, shape in CONSTS]
        K.idle = {n: kept.enter_context(nc.semaphore("idle_" + n)) for n in ("SP", "Pool", "PE", "DVE", "Activation")}
        with ExitStack() as layer:
            K.beta, K.logd, K.bonus = [chip(layer, n, [P, NB, h]) for n, h in (("beta", AH), ("logd", AH), ("bonus", BH))]
            K.rw_mid, K.rw_in, K.rw_out = [chip(layer, n, [P, NP, h]) for n, h in (("rw_mid", TILES), ("rw_in", TILES), ("rw_out", TILES + DB))]
            with ExitStack() as rows:
                K.xh, K.xl = [rows.enter_context(nc.sbuf_tensor(n, [P, KT, XW], F32R)) for n in ("k_xh", "k_xl")]
                phase_norm(nc, K, A["x_prompt"], A["x_sample"], A["state_rwkv_shift"], A["norm0_w"], O["p_shift"], O["s_shift"])
                phase_gdn_in(nc, K, A["w_in0"], A["gdn_conv_w"], A["state_gdn_conv"], A["gdn_a_log"], A["gdn_dt_bias"], S,
                             O["p_conv"], O["s_conv"])
                phase_rwkv_in(nc, K, A["w_in0"], A["rwkv_mu"], A["rwkv_w0"], A["rwkv_w2"], A["rwkv_a0"], A["rwkv_a2"],
                              A["rwkv_k_k"], A["rwkv_k_a"], A["rwkv_r_k"], S)
            phase_mix0(nc, K, A["w_out0"], A["norm1_w"], A["gdn_norm_w"], A["rwkv_ln_w"], A["rwkv_ln_b"],
                       A["x_prompt"], A["x_sample"], A["state_gdn"], A["state_rwkv"], S,
                       O["p_gdn"], O["p_rwkv"], O["s_gdn"], O["s_rwkv"])
        with ExitStack() as layer:
            K.sel, K.sel2 = chip(layer, "sel", [CH, CH, P]), chip(layer, "sel2", [CH, NP, P])
            K.w, K.em = chip(layer, "w", [P, NB, CH]), chip(layer, "em", [P, NB, CH])
            K.u, K.e = chip(layer, "u", [CH, TOK]), chip(layer, "e", [CH, TOK])
            phase_mlstm_in(nc, K, A["w_in1"], A["mlstm_b_i"], A["mlstm_b_f"], A["state_mlstm_m"], S, O["p_m"], O["s_m"])
            phase_mix1(nc, K, A["w_out1"], A["norm_f_w"], A["state_mlstm_c"], A["state_mlstm_n"], S,
                       O["y_prompt"], O["y_sample"], O["p_c"], O["p_n"], O["s_c"], O["s_n"])


def kernel(**inputs):
    import numpy as _np
    import concourse.bacc as _bacc
    from concourse import mybir as _mybir
    from concourse.bass_utils import run_bass_kernel_spmd as _run

    nc = _bacc.Bacc("TRN2", target_bir_lowering=False, num_devices=1)
    arrays, A, O = {}, {}, {}
    for name in _INS:
        arrays[f"in_{name}_dram"] = a = _np.ascontiguousarray(inputs[name])
        A[name] = nc.dram_tensor(f"in_{name}_dram", a.shape, _mybir.dt.from_np(a.dtype), kind="ExternalInput").ap()
    for name, shape in _OUTS:
        O[name] = nc.dram_tensor(f"out_{name}_dram", shape, _mybir.dt.float32, kind="ExternalOutput").ap()
    build(nc, A, O)
    r = _run(nc, [arrays], core_ids=[0])
    return tuple(r.results[0][f"out_{name}_dram"] for name, _ in _OUTS)
```

```python
import math
from contextlib import ExitStack

import concourse.bass as bass
from concourse import mybir

F32 = mybir.dt.float32
F32R = mybir.dt.float32r
ALU = mybir.AluOpType
ACT = mybir.ActivationFunctionType
AX_X = mybir.AxisListType.X

P = 128
D = 1024
KT = D // P
SEQ = 1024
TILES = SEQ // P
DB, DS = 8, 8
SR = DB * DS
TOK = SEQ + SR
XC = TOK + DB
XW = (TILES + 1) * P
EPS = 1e-6
AH, AKEY = 4, 512
AQKV = 3 * AKEY
AGATE = AQKV + AKEY
ACOLS = AGATE + 2 * AH
BW, BH = 512, 8
NP = BW // P
B_GN_EPS = 64e-5
DECAY = math.exp(-0.5)
CH, CQK, CV = 8, 64, 128
CAP = 15.0
NEG = -30000.0
CONV = 4
GROUPS = ((0, 512), (512, 512), (SEQ, SR))
THIRDS = ((0, 364), (364, 364), (728, TOK - 728))


def alone(eng, K):
    eng.sem_inc(K.idle[eng.engine.name], 1)


class Events:

    def __init__(self, nc, ctx, prefix):
        self.nc, self.prefix, self.sems = nc, prefix, {}
        ctx.callback(self.close)

    def __call__(self, name):
        if name not in self.sems:
            self.sems[name] = self.nc.alloc_semaphore(self.prefix + name)
        return self.sems[name]

    def close(self):
        self.nc.clear_and_free_semaphores(list(self.sems.values()))
        self.nc.all_engine_barrier()


class Seq:

    def __init__(self, sem, eng, per):
        self.sem, self.eng, self.per, self.n, self.base = sem, eng, per, 0, 0

    def start(self, i):
        self.base, self.n = i * self.per, 0

    def __call__(self, ins):
        self.n += 1
        ins.then_inc(self.sem, 1)
        self.eng.wait_ge(self.sem, self.base + self.n)

    def end(self):
        pass


def products(pe, out, w, x, first, last):
    pe.matmul(out, w[0], x[0], start=first, stop=False)
    pe.matmul(out, w[0], x[1], start=False, stop=False)
    return pe.matmul(out, w[1], x[0], start=False, stop=last)


def as_row(v):
    n = v.shape[0]
    return v.rearrange("(a n) -> a n", a=1).broadcast_to([P, n])


def phase_norm(nc, K, x_prompt, x_sample, shift, norm_w, p_shift, s_shift):
    with ExitStack() as ctx:
        sb = lambda n, s: ctx.enter_context(nc.sbuf_tensor(n, s, F32))
        ev = Events(nc, ctx, "n_")
        x = sb("n_x", [P, 2, D])
        xn = sb("n_xn", [P, 2, D])
        sq = sb("n_sq", [P, D])
        st = sb("n_st", [P, 2, 4])
        wb = sb("n_wb", [P, D])
        pt = [ctx.enter_context(nc.psum_tensor(f"n_pt{i}", [P, 4, P], F32)) for i in range(4)]
        x_in0, x_in1, w_in, ssq, mean, rstd, norm, turned, high, low, shifts, consts, tmp, prev_rows = [ev(n) for n in (
            "x_in0", "x_in1", "w_in", "ssq", "mean", "rstd", "norm", "turned", "high", "low", "shifts", "consts", "tmp", "prev_rows")]

        x_in = (x_in0, x_in1)

        with nc.Block() as block:
            @block.sync
            def _(sp):
                sp.dma_start(wb[:, :], as_row(norm_w)).then_inc(w_in, 16)
                for b in range(2):
                    sp.dma_start(x[:, b, :], x_prompt[0, b * P:(b + 1) * P, :]).then_inc(x_in[b], 16)
                with sp.Fori(0, TILES // 2 - 1) as g:
                    for b in range(2):
                        sp.wait_ge(norm, 2 * g + b + 1)
                        sp.dma_start(x[:, b, :], x_prompt[0, bass.ds((2 * g + b + 2) * P, P), :]).then_inc(x_in[b], 16)
                sp.wait_ge(norm, TILES - 1)
                sp.dma_start(x[0:SR, 0, :], x_sample.rearrange("b t d -> (b t) d")).then_inc(x_in[0], 16)
                sp.dma_start(x[SR:SR + DB, 0, :], shift).then_inc(x_in[0], 16)
                sp.wait_ge(norm, TILES)
                sp.dma_start(p_shift, xn[P - 1:P, 1, :]).then_inc(shifts, 16)
                sp.wait_ge(norm, TILES + 1)
                for b in range(DB):
                    r = b * DS + DS - 1
                    sp.dma_start(s_shift[b:b + 1, :], xn[r:r + 1, 0, :]).then_inc(shifts, 16)
                sp.wait_ge(shifts, 16 * (DB + 1))

            @block.gpsimd
            def _(pool):
                done = Seq(tmp, pool, 34)
                done.start(0)
                done(pool.memset(K.ident[:, :], 0.0))
                done(pool.affine_select(out=K.ident[:, :], in_=K.ident[:, :], compare_op=ALU.not_equal, fill=1.0,
                                        base=0, pattern=[[-1, P]], channel_multiplier=1))
                pool.sem_inc(consts, 1)
                done(pool.memset(K.half_neg[:, :], -0.5))
                done(pool.memset(K.ones[:, :], 1.0))
                done(pool.memset(K.pair_ones[:, :], 0.0))
                done(pool.memset(K.pair_ones[0:64, 0:64], 1.0))
                done(pool.memset(K.pair_ones[64:128, 64:128], 1.0))
                for out, cmp in ((K.causal, ALU.is_ge), (K.strict, ALU.is_gt)):
                    done(pool.affine_select(out=out[:, :], in_=K.ones[:, :], compare_op=cmp, fill=0.0,
                                            base=0, pattern=[[1, P]], channel_multiplier=-1))
                v = K.same[0:SR, 0:SR].rearrange("s (b t) -> s b t", b=DB)
                done(pool.affine_select(out=v, in_=K.ones[0:SR, 0:SR].rearrange("s (b t) -> s b t", b=DB),
                                        compare_op=ALU.is_ge, fill=0.0, base=0, pattern=[[-DS, DB], [0, DS]],
                                        channel_multiplier=1))
                done(pool.affine_select(out=v, in_=v, compare_op=ALU.is_ge, fill=0.0, base=DS - 1,
                                        pattern=[[DS, DB], [0, DS]], channel_multiplier=-1))
                for out, m in ((K.causal_s, K.causal), (K.strict_s, K.strict)):
                    done(pool.tensor_tensor(out[:, :], K.same[0:SR, 0:SR], m[0:SR, 0:SR], ALU.mult))
                done(pool.memset(K.last[:, :], 0.0))
                done(pool.tensor_copy(K.last[:, DS - 1:SR:DS], K.same[0:SR, DS - 1:SR:DS]))
                done(pool.memset(K.restart[:, :], 1.0))
                done(pool.memset(K.restart[:, 0:SEQ:P], 0.0))
                done(pool.memset(K.restart[:, SEQ:TOK:DS], 0.0))
                done(pool.memset(K.batch_cols[:, :, :], 0.0))
                for b in range(DB):
                    done(pool.memset(K.batch_cols[:, b, b * DS:(b + 1) * DS], 1.0))
                done(pool.memset(K.head_cols[:, :], 0.0))
                done(pool.memset(K.head_cols[0:64, 0:1], 1.0))
                done(pool.memset(K.head_cols[64:128, 1:2], 1.0))
                done(pool.tensor_scalar(K.lcausal[:, :], K.causal[:, :], -NEG, NEG, ALU.mult, ALU.add))
                done(pool.tensor_scalar(K.lcausal_s[:, :], K.causal_s[:, :], -NEG, NEG, ALU.mult, ALU.add))
                for t in (K.xh, K.xl):
                    done(pool.memset(t[:, :, XC:XW].bitcast(F32), 0.0))
                done.end()

                def one(i, n, k):
                    pool.wait_ge(mean, n)
                    pool.tensor_tensor(st[:, k, 2:3], st[:, k, 1:2], K.half_neg[:, 0:1], ALU.pow).then_inc(rstd, 1)
                with pool.Fori(0, TILES // 2) as g:
                    for b in range(2):
                        one(g, 2 * g + b + 1, b)
                pool.wait_ge(mean, TILES + 1)
                pool.tensor_tensor(st[0:SR, 0, 2:3], st[0:SR, 0, 1:2], K.half_neg[0:SR, 0:1], ALU.pow).then_inc(rstd, 1)

            @block.scalar
            def _(act):
                def square(n, k, r):
                    act.wait_ge(mean, n)
                    act.activation(sq[0:r, :], x[0:r, k, :], ACT.Square, accum_out=st[0:r, k, 0:1]).then_inc(ssq, 1)

                def keep(n, k, cols, r):
                    act.wait_ge(turned, n + 1)
                    for h in range(2):
                        act.activation(K.xh[:, 4 * h:4 * h + 4, cols], pt[2 * k + h][:, :, 0:r], ACT.Copy).then_inc(high, 1)
                act.wait_ge(x_in[0], 16)
                square(0, 0, P)
                act.wait_ge(x_in[1], 16)
                square(1, 1, P)
                keep(0, 0, slice(0, P), P)
                with act.Fori(1, TILES // 2) as g:
                    for b in range(2):
                        act.wait_ge(x_in[b], 16 * (g + 1))
                        square(2 * g + b, b, P)
                        keep(2 * g + b - 1, 1 - b, bass.ds((2 * g + b - 1) * P, P), P)
                act.wait_ge(x_in[0], 16 * (TILES // 2 + 2))
                square(TILES, 0, SR)
                keep(TILES - 1, 1, slice(SEQ - P, SEQ), P)
                keep(TILES, 0, slice(SEQ, XC), SR + DB)

            @block.vector
            def _(dve):
                dve.wait_ge(w_in, 16)

                def one(n, k, r):
                    m = SR if r != P else P
                    dve.wait_ge(ssq, n + 1)
                    dve.tensor_scalar(st[0:m, k, 1:2], st[0:m, k, 0:1], 1.0 / D, EPS, ALU.mult, ALU.add).then_inc(mean, 1)
                    if isinstance(n, int) and n < 2:
                        pass
                    else:
                        dve.wait_ge(turned, n - 1)
                    if r != P:
                        dve.tensor_copy(xn[SR:SR + DB, k, :], x[SR:SR + DB, k, :]).then_inc(prev_rows, 1)
                    dve.wait_ge(rstd, n + 1)
                    dve.scalar_tensor_tensor(out=xn[0:m, k, :], in0=x[0:m, k, :], scalar=st[0:m, k, 2:3],
                                             in1=wb[0:m, :], op0=ALU.mult, op1=ALU.mult).then_inc(norm, 1)

                def rest(n, k, cols, r):
                    for h in range(2):
                        dve.wait_ge(high, 2 * n + h + 1)
                        dve.tensor_tensor(K.xl[:, 4 * h:4 * h + 4, cols], pt[2 * k + h][:, :, 0:r],
                                          K.xh[:, 4 * h:4 * h + 4, cols].bitcast(F32), ALU.subtract).then_inc(low, 1)
                one(0, 0, P)
                one(1, 1, P)
                rest(0, 0, slice(0, P), P)
                with dve.Fori(1, TILES // 2) as g:
                    for b in range(2):
                        one(2 * g + b, b, P)
                        rest(2 * g + b - 1, 1 - b, bass.ds((2 * g + b - 1) * P, P), P)
                one(TILES, 0, SR + DB)
                rest(TILES - 1, 1, slice(SEQ - P, SEQ), P)
                rest(TILES, 0, slice(SEQ, XC), SR + DB)

            @block.tensor
            def _(pe):
                pe.wait_ge(consts, 1)

                def one(n, k, r):
                    pe.wait_ge(norm, n + 1)
                    if r != P:
                        pe.wait_ge(prev_rows, 1)
                    if not isinstance(n, int) or n >= 2:
                        pe.wait_ge(low, 2 * n - 2)
                    for kt in range(KT):
                        mm = pe.transpose(pt[2 * k + kt // 4][:, kt % 4, 0:r], xn[0:r, k, kt * P:(kt + 1) * P],
                                          K.ident[0:r, 0:r])
                    mm.then_inc(turned, 1)
                one(0, 0, P)
                one(1, 1, P)
                with pe.Fori(1, TILES // 2) as g:
                    for b in range(2):
                        one(2 * g + b, b, P)
                one(TILES, 0, SR + DB)


CONSTS = (("ident", [P, P]), ("ones", [P, P]), ("half_neg", [P, 16]), ("pair_ones", [P, P]), 
          ("causal", [P, P]), ("strict", [P, P]), ("same", [SR, SR]), ("causal_s", [SR, SR]), ("strict_s", [SR, SR]),
          ("last", [SR, SR]), ("restart", [P, TOK]), ("batch_cols", [P, DB, SR]),
          ("head_cols", [P, 2]), ("lcausal", [P, P]), ("lcausal_s", [SR, SR]))


def w_block(w, col, n):
    return w.rearrange("(kt p) c -> p kt c", p=P)[:, :, bass.ds(col, n)]


def over(eng, count, body):
    body(0, True)
    with eng.Fori(1, count - 1) as j:
        body(j, True)
    body(count - 1, False)


def phase_gdn_in(nc, K, w_in, conv_w, conv_state, a_log, dt_bias, S, p_conv, s_conv):
    with ExitStack() as ctx:
        sb = lambda n, s: ctx.enter_context(nc.sbuf_tensor("a_" + n, s, F32))
        sem = Events(nc, ctx, "a_")
        W = [sb(f"w{m}", [P, KT, P]) for m in range(4)]
        parts = lambda n, s: [ctx.enter_context(nc.sbuf_tensor(f"a_{n}{h}", s, F32R)) for h in "hl"]
        WP = [parts(f"wp{m}", [P, KT, P]) for m in range(4)]
        wg = sb("wg", [P, KT, 2 * AH])
        wgp = parts("wgp", [P, KT, 2 * AH])
        gT = sb("gt", [2 * AH, XW])
        U = [sb(f"u{m}", [P, CONV - 1 + SEQ]) for m in range(3)]
        US = [sb(f"us{m}", [P, DB, CONV - 1 + DS]) for m in range(3)]
        Y = [sb(f"y{m}", [P, TOK]) for m in range(3)]
        T = [sb(f"t{m}", [P, TOK]) for m in range(3)]
        O = [sb(f"o{m}", [P, TOK]) for m in range(3)]
        TZ = sb("tz", [P, TOK])
        Z = sb("z", [P, TILES + 1, P])
        rows = sb("rows", [64, AQKV])
        cw_rows, cs_rows = rows[0:CONV, :], rows[32:32 + DB * (CONV - 1), :]
        cw = sb("cw", [P, 3 * AH, CONV])
        cs = sb("cs", [P, 3 * AH, DB, CONV - 1])
        tail = sb("tail", [P, 3, 27])
        tails = sb("tails", [27, 3, P])
        gp = sb("gp", [P, 2, AH])
        g1 = sb("g1", [P, TILES + 1, AH])
        g2 = sb("g2", [P, TILES + 1, AH])
        g3 = sb("g3", [P, TILES + 1, AH])
        bank = [ctx.enter_context(nc.psum_tensor(f"a_bank{i}", [P, 512], F32)) for i in range(8)]
        w_ld = [sem(f"w_ld{m}") for m in range(4)]
        proj = [sem(f"proj{m}") for m in range(4)]
        evac = [sem(f"evac{m}") for m in range(3)]
        conv = [sem(f"conv{m}") for m in range(3)]
        tanh = [sem(f"tanh{m}") for m in range(4)]
        silu = [sem(f"silu{m}") for m in range(4)]
        square = [sem(f"square{m}") for m in range(2)]
        ssq = [sem(f"ssq{m}") for m in range(2)]
        logn = [sem(f"logn{m}") for m in range(2)]
        rs = [sem(f"rs{m}") for m in range(2)]
        normed = [sem(f"normed{m}") for m in range(2)]
        stored = [sem(f"stored{m}") for m in range(4)]
        high = [sem(f"high{m}") for m in range(4)]
        low = [sem(f"low{m}") for m in range(4)]
        z_t, z_kept, z_last = sem("z_t"), sem("z_kept"), sem("z_last")
        g_high, g_low, g_rows = sem("g_high"), sem("g_low"), sem("g_rows")
        halo, tailed, tails_t, tails_kept, tails_out, par, par2, pre_t, pre_k, gates, gate_a, gate_v, padded, dseq, pseq = [sem(n) for n in (
            "halo", "tailed", "tails_t", "tails_kept", "tails_out", "par", "par2", "pre_t", "pre_k", "gates", "gate_a",
            "gate_v", "padded", "dseq", "pseq")]

        with nc.Block() as block:
            @block.sync
            def _(sp):
                sp.dma_start(W[0][:, :, :], w_block(w_in, 0, P)).then_inc(w_ld[0], 16)
                sp.dma_start(cw_rows[:, :], conv_w).then_inc(par, 16)
                sp.dma_start(cs_rows[:, :], conv_state.rearrange("b r c -> (b r) c")).then_inc(par, 16)
                sp.dma_start(wg[:, :, :], w_block(w_in, AGATE, 2 * AH)).then_inc(par, 16)
                sp.dma_start(gp[:, 0, :], as_row(a_log)).then_inc(par2, 16)
                sp.dma_start(gp[:, 1, :], as_row(dt_bias)).then_inc(par2, 16)
                for m in range(1, 4):
                    sp.dma_start(W[m][:, :, :], w_block(w_in, m * AKEY, P)).then_inc(w_ld[m], 16)

                def load(m, j):
                    sp.wait_ge(low[m], j + 1)
                    alone(sp, K)
                    sp.dma_start(W[m][:, :, :], w_block(w_in, m * AKEY + (j + 1) * P, P)).then_inc(w_ld[m], 16)

                def body(j, more):
                    for m in range(3):
                        if more:
                            load(m, j)
                    sp.wait_ge(silu[2], j + 1)
                    alone(sp, K)
                    sp.dma_start(S.qkv[2, bass.ds(j * P, P), :], O[2][:, :]).then_inc(stored[2], 16)
                    sp.wait_ge(z_last, j + 1)
                    alone(sp, K)
                    sp.wait_ge(z_kept, 2 * (j + 1))
                    alone(sp, K)
                    sp.dma_start(S.z[0:SEQ, bass.ds(j * P, P)].rearrange("(n p) c -> p n c", p=P),
                                 Z[:, 0:TILES, :]).then_inc(stored[3], 16)
                    alone(sp, K)
                    sp.dma_start(S.z[SEQ:TOK, bass.ds(j * P, P)], Z[0:SR, TILES, :]).then_inc(stored[3], 16)
                    if more:
                        load(3, j)
                    for m in range(2):
                        sp.wait_ge(normed[m], j + 1)
                        alone(sp, K)
                        sp.dma_start(S.qkv[m, bass.ds(j * P, P), :], O[m][:, :]).then_inc(stored[m], 16)
                    sp.wait_ge(tails_kept, j + 1)
                    col = lambda t: t.rearrange("r (m c) -> r m c", m=3)[:, :, bass.ds(j * P, P)]
                    alone(sp, K)
                    sp.dma_start(col(p_conv[0]), tails[0:3, :, :]).then_inc(tails_out, 16)
                    alone(sp, K)
                    sp.dma_start(col(s_conv.rearrange("b r c -> (b r) c")), tails[3:27, :, :]).then_inc(tails_out, 16)
                over(sp, AH, body)
                for s, n in ((stored[0], 1), (stored[1], 1), (stored[2], 1), (stored[3], 2), (tails_out, 2)):
                    sp.wait_ge(s, 16 * n * AH)

            @block.gpsimd
            def _(pool):
                done = Seq(pseq, pool, 7)
                done.start(0)
                for m in range(3):
                    done(pool.memset(U[m][:, 0:CONV - 1], 0.0))
                for m in range(3):
                    done(pool.memset(US[m][:, :, :], 0.0))
                done(pool.memset(tail[:, :, :], 0.0))
                done.end()
                pool.sem_inc(padded, 1)
                pool.wait_ge(pre_k, 2)
                pool.wait_ge(g_high, 1)
                pool.tensor_tensor(wgp[1][:, :, :], wg[:, :, :], wgp[0][:, :, :].bitcast(F32), ALU.subtract).then_inc(g_low, 1)

                def split(m, j):
                    pool.wait_ge(high[m], j + 1)
                    pool.tensor_tensor(WP[m][1][:, :, :], W[m][:, :, :], WP[m][0][:, :, :].bitcast(F32), ALU.subtract
                                       ).then_inc(low[m], 1)
                for m in range(4):
                    split(m, 0)

                def body(j, more):
                    for m in range(3):
                        pool.wait_ge(conv[m], j)
                        alone(pool, K)
                        pool.tensor_copy(US[m][:, :, 0:CONV - 1], cs[:, bass.ds(m * AH + j, 1), :, :].rearrange(
                            "p a b r -> p (a b) r")).then_inc(halo, 1)
                        pool.wait_ge(halo, 3 * j + m + 1)
                    pool.wait_ge(tails_t, j)
                    for m in range(3):
                        pool.wait_ge(evac[m], 3 * (j + 1))
                        alone(pool, K)
                        pool.tensor_copy(tail[:, m, 0:3], U[m][:, SEQ:SEQ + 3]).then_inc(tailed, 1)
                        pool.wait_ge(tailed, 6 * j + 2 * m + 1)
                        alone(pool, K)
                        pool.tensor_copy(tail[:, m, 3:27].rearrange("p (b r) -> p b r", b=DB),
                                         US[m][:, :, DS:DS + CONV - 1]).then_inc(tailed, 1)
                        pool.wait_ge(tailed, 6 * j + 2 * m + 2)
                        if more:
                            split(m, j + 1)
                    if more:
                        split(3, j + 1)
                over(pool, AH, body)

            @block.scalar
            def _(act):
                def split(m, j):
                    act.wait_ge(w_ld[m], 16 * (j + 1))
                    act.wait_ge(low[m], j)
                    act.wait_ge(proj[m], 3 * j)
                    act.activation(WP[m][0][:, :, :], W[m][:, :, :], ACT.Copy).then_inc(high[m], 1)
                act.wait_ge(par, 48)
                act.activation(wgp[0][:, :, :], wg[:, :, :], ACT.Copy).then_inc(g_high, 1)
                for m in range(4):
                    split(m, 0)
                for g in range(3):
                    act.wait_ge(pre_t, g + 3)
                    n = 512 if g < 2 else P
                    act.activation(gT[:, 512 * g:512 * g + n], bank[g][0:2 * AH, 0:n], ACT.Copy).then_inc(g_rows, 1)
                act.wait_ge(padded, 1)
                act.wait_ge(gate_v, 1)
                x = bank[3][:, 0:72].rearrange("p (n h) -> p n h", h=2 * AH)
                act.activation(K.beta[:, :, :], x[:, :, 0:AH], ACT.Tanh, scale=0.5).then_inc(gate_a, 1)
                act.wait_ge(par2, 32)
                act.activation(gp[:, 0, :], gp[:, 0, :], ACT.Exp).then_inc(gate_a, 1)
                act.wait_ge(gate_v, 1)
                act.activation(g2[:, :, :], g1[:, :, :], ACT.Abs).then_inc(gate_a, 1)
                act.wait_ge(gate_a, 3)
                act.activation(g2[:, :, :], g2[:, :, :], ACT.Exp, scale=-1.0).then_inc(gate_a, 1)
                act.wait_ge(gate_a, 4)
                act.activation(g2[:, :, :], g2[:, :, :], ACT.Ln, bias=1.0).then_inc(gate_a, 1)

                def keep(m, j):
                    b0 = 3 * (m % 2)
                    act.wait_ge(conv[m], j)
                    act.wait_ge(tailed, 6 * j)
                    if m < 3:
                        act.wait_ge(halo, 3 * j + m + 1)
                    for g, (c, n) in enumerate(THIRDS):
                        act.wait_ge(proj[m], 3 * j + g + 1)
                        n = min(n, SEQ - c)
                        ins = act.activation(U[m][:, 3 + c:3 + c + n], bank[b0 + g][:, 0:n], ACT.Copy)
                        if g == 2:
                            ins = act.activation(US[m][:, :, 3:11], bank[b0 + 2][:, n:n + SR].rearrange("p (b t) -> p b t", b=DB), ACT.Copy)
                        ins.then_inc(evac[m], 1)

                def tanhs(m, j):
                    act.wait_ge(conv[m], j + 1)
                    act.wait_ge(silu[m], j)
                    if m < 2:
                        act.wait_ge(normed[m], j)
                    act.activation(T[m][:, :], Y[m][:, :], ACT.Tanh).then_inc(tanh[m], 1)

                def squares(m, j):
                    act.wait_ge(silu[m], j + 1)
                    act.activation(T[m][:, :], O[m][:, :], ACT.Square).then_inc(square[m], 1)

                def logs(m, j):
                    act.wait_ge(ssq[m], j + 1)
                    for g, (c, n) in enumerate(GROUPS):
                        src = bank[6 + g][:, 0:n] if g < 2 else bank[2][:, 128:128 + n]
                        act.activation(T[m][:, c:c + n], src, ACT.Ln, bias=EPS).then_inc(logn[m], 1)

                def body(j, more):
                    keep(0, j)
                    if more:
                        split(0, j + 1)
                    keep(1, j)
                    if more:
                        split(1, j + 1)
                    tanhs(0, j)
                    squares(0, j)
                    keep(2, j)
                    if more:
                        split(2, j + 1)
                    tanhs(1, j)
                    squares(1, j)
                    tanhs(2, j)
                    logs(0, j)
                    act.wait_ge(z_t, j)
                    for g, (c, n) in enumerate(THIRDS):
                        act.wait_ge(proj[3], 3 * j + g + 1)
                        act.activation(TZ[:, c:c + n], bank[3 + g][:, 0:n], ACT.Tanh, scale=0.5).then_inc(tanh[3], 1)
                    logs(1, j)
                    act.wait_ge(z_t, j + 1)
                    act.wait_ge(stored[3], 32 * j)
                    for g in range(2):
                        act.activation(Z[:, 4 * g:4 * g + 4, :], bank[3 + g][:, :].rearrange("p (n c) -> p n c", n=4), ACT.Copy).then_inc(z_kept, 1)
                    for m in range(2):
                        act.wait_ge(logn[m], 3 * (j + 1))
                        act.activation(T[m][:, :], T[m][:, :], ACT.Exp, scale=-0.5,
                                       bias=-0.5 * math.log(P) if m == 0 else 0.0).then_inc(rs[m], 1)
                    if more:
                        split(3, j + 1)
                over(act, AH, body)

            @block.vector
            def _(dve):
                done = Seq(dseq, dve, 4)
                done.start(0)
                dve.wait_ge(pre_t, 1)
                dve.tensor_scalar(cw[:, :, :], bank[6][:, 0:48].rearrange("p (c r) -> p c r", r=CONV), 0.5, None,
                                  ALU.mult).then_inc(pre_k, 1)
                dve.wait_ge(pre_t, 2)
                dve.tensor_copy(cs[:, :, :, :], bank[7][:, 0:288].rearrange("p (c b r) -> p c b r", b=DB, r=3)).then_inc(pre_k, 1)
                dve.wait_ge(pre_t, 6)
                dve.wait_ge(par2, 32)
                dve.tensor_tensor(g1[:, :, :], bank[3][:, 0:72].rearrange("p (n h) -> p n h", h=2 * AH)[:, :, AH:2 * AH],
                                  gp[:, 1:2, :].broadcast_to([P, TILES + 1, AH]), ALU.add).then_inc(gate_v, 1)
                dve.wait_ge(gate_a, 5)
                done(dve.tensor_scalar(K.beta[:, :, :], K.beta[:, :, :], 0.5, 0.5, ALU.mult, ALU.add))
                done(dve.tensor_scalar(g3[:, :, :], g1[:, :, :], 0.0, None, ALU.max))
                done(dve.tensor_tensor(g3[:, :, :], g3[:, :, :], g2[:, :, :], ALU.add))
                done(dve.scalar_tensor_tensor(out=K.logd[:, :, :], in0=g3[:, :, :], scalar=-1.0,
                                              in1=gp[:, 0:1, :].broadcast_to([P, TILES + 1, AH]),
                                              op0=ALU.mult, op1=ALU.mult))
                step = Seq(gates, dve, 21)

                def convolve(m, j):
                    dve.wait_ge(evac[m], 3 * (j + 1))
                    dve.wait_ge(halo, 3 * j + m + 1)
                    y, ys = Y[m][:, 0:SEQ], Y[m][:, SEQ:TOK].rearrange("p (b t) -> p b t", b=DB)
                    for r in range(CONV):
                        w = cw[:, bass.ds(m * AH + j, 1), r]
                        for o, u in ((y, U[m][:, r:r + SEQ]), (ys, US[m][:, :, r:r + DS])):
                            if r == 0:
                                ins = dve.tensor_scalar(o, u, w, None, ALU.mult)
                            else:
                                ins = dve.scalar_tensor_tensor(out=o, in0=u, scalar=w, in1=o, op0=ALU.mult, op1=ALU.add)
                            if r < CONV - 1 or o is y:
                                step(ins)
                    ins.then_inc(conv[m], 1)

                def silus(m, j):
                    dve.wait_ge(tanh[m], j + 1)
                    dve.wait_ge(conv[m], j + 1)
                    dve.wait_ge(stored[m], 16 * j)
                    dve.scalar_tensor_tensor(out=O[m][:, :], in0=T[m][:, :], scalar=1.0, in1=Y[m][:, :],
                                             op0=ALU.add, op1=ALU.mult).then_inc(silu[m], 1)

                def body(j, more):
                    step.start(j)
                    convolve(0, j)
                    silus(0, j)
                    convolve(1, j)
                    silus(1, j)
                    convolve(2, j)
                    silus(2, j)
                    for g, (c, n) in enumerate(THIRDS):
                        dve.wait_ge(tanh[3], 3 * j + g + 1)
                        dve.scalar_tensor_tensor(out=TZ[:, c:c + n], in0=TZ[:, c:c + n], scalar=1.0, in1=bank[3 + g][:, 0:n],
                                                 op0=ALU.add, op1=ALU.mult).then_inc(silu[3], 1)
                    for m in range(2):
                        dve.wait_ge(rs[m], j + 1)
                        dve.tensor_tensor(O[m][:, :], O[m][:, :], T[m][:, :], ALU.mult).then_inc(normed[m], 1)
                    dve.wait_ge(tails_t, j + 1)
                    dve.wait_ge(tails_out, 32 * j)
                    dve.wait_ge(stored[3], 32 * j)
                    dve.tensor_copy(Z[0:SR, TILES, :], bank[5][0:SR, 0:P]).then_inc(z_last, 1)
                    dve.tensor_copy(tails[:, :, :], bank[5][0:27, P:4 * P].rearrange("p (m c) -> p m c", m=3)).then_inc(tails_kept, 1)
                    step.end()
                over(dve, AH, body)

            @block.tensor
            def _(pe):
                pe.wait_ge(par, 48)
                for c in range(3 * AH):
                    mm = pe.transpose(bank[6][:, c * CONV:(c + 1) * CONV], cw_rows[:, c * P:(c + 1) * P], K.ident[0:CONV, 0:CONV])
                mm.then_inc(pre_t, 1)
                for c in range(3 * AH):
                    mm = pe.transpose(bank[7][:, c * 24:(c + 1) * 24], cs_rows[:, c * P:(c + 1) * P], K.ident[32:56, 32:56])
                mm.then_inc(pre_t, 1)
                pe.wait_ge(g_high, 1)
                pe.wait_ge(g_low, 1)
                for g in range(3):
                    n = 512 if g < 2 else P
                    for kt in range(KT):
                        x = K.xh[:, kt, 512 * g:512 * g + n], K.xl[:, kt, 512 * g:512 * g + n]
                        mm = products(pe, bank[g][0:2 * AH, 0:n], (wgp[0][:, kt, :], wgp[1][:, kt, :]), x, kt == 0, kt == KT - 1)
                    mm.then_inc(pre_t, 1)
                pe.wait_ge(g_rows, 3)
                for n in range(TILES + 1):
                    mm = pe.transpose(bank[3][:, n * 8:(n + 1) * 8], gT[:, n * P:(n + 1) * P], K.ident[0:2 * AH, 0:2 * AH])
                mm.then_inc(pre_t, 1)
                pe.wait_ge(gate_v, 1)
                pe.wait_ge(gate_a, 1)
                pe.wait_ge(pre_k, 2)

                def sums(m, j):
                    pe.wait_ge(square[m], j + 1)
                    if m == 0:
                        pe.wait_ge(logn[1], 3 * j)
                    else:
                        pe.wait_ge(logn[0], 3 * (j + 1))
                    for g, (c, n) in enumerate(GROUPS):
                        dst = bank[6 + g][:, 0:n] if g < 2 else bank[2][:, 128:128 + n]
                        mm = pe.matmul(dst, K.ones[:, :], T[m][:, c:c + n], start=True, stop=True)
                    mm.then_inc(ssq[m], 1)

                def body(j, more):
                    for m in range(3):
                        b0 = 3 * (m % 2)
                        if m == 0:
                            pe.wait_ge(evac[2], 3 * j)
                        elif m == 1:
                            pe.wait_ge(z_kept, 2 * j)
                            pe.wait_ge(tails_kept, j)
                        else:
                            pe.wait_ge(evac[0], 3 * (j + 1))
                        pe.wait_ge(high[m], j + 1)
                        pe.wait_ge(low[m], j + 1)
                        for g, (c, n) in enumerate(THIRDS):
                            if m == 0 and g == 2:
                                pe.wait_ge(logn[1], 3 * j)
                            for kt in range(KT):
                                w = WP[m][0][:, kt, :], WP[m][1][:, kt, :]
                                x = K.xh[:, kt, c:c + n], K.xl[:, kt, c:c + n]
                                mm = products(pe, bank[b0 + g][:, 0:n], w, x, kt == 0, kt == KT - 1)
                            mm.then_inc(proj[m], 1)
                    pe.wait_ge(evac[2], 3 * (j + 1))
                    sums(0, j)
                    pe.wait_ge(evac[1], 3 * (j + 1))
                    pe.wait_ge(high[3], j + 1)
                    pe.wait_ge(low[3], j + 1)
                    for g, (c, n) in enumerate(THIRDS):
                        for kt in range(KT):
                            w = WP[3][0][:, kt, :], WP[3][1][:, kt, :]
                            x = K.xh[:, kt, c:c + n], K.xl[:, kt, c:c + n]
                            mm = products(pe, bank[3 + g][:, 0:n], w, x, kt == 0, kt == KT - 1)
                        mm.then_inc(proj[3], 1)
                    sums(1, j)
                    pe.wait_ge(silu[3], 3 * (j + 1))
                    for n in range(TILES + 1):
                        r = P if n < TILES else SR
                        mm = pe.transpose(bank[3 + n // 4][0:r, (n % 4) * P:(n % 4 + 1) * P], TZ[:, n * P:n * P + r], K.ident[:, :])
                    mm.then_inc(z_t, 1)
                    pe.wait_ge(tailed, 6 * (j + 1))
                    for m in range(3):
                        mm = pe.transpose(bank[5][0:27, (m + 1) * P:(m + 2) * P], tail[:, m, :], K.ident[:, :])
                    mm.then_inc(tails_t, 1)
                over(pe, AH, body)


def phase_rwkv_in(nc, K, w_in, mu, w0, w2, a0, a2, k_k, k_a, r_k, S):
    with ExitStack() as ctx:
        sb = lambda n, s: ctx.enter_context(nc.sbuf_tensor("b_" + n, s, F32))
        sem = Events(nc, ctx, "b_")
        W = [sb(f"w{m}", [P, KT, P]) for m in range(4)]
        WP = [[ctx.enter_context(nc.sbuf_tensor(f"b_wp{m}{h}", [P, KT, P], F32R)) for h in "hl"] for m in range(4)]
        U = [sb(f"u{m}", [P, 1 + SEQ]) for m in range(4)]
        US = [sb(f"us{m}", [P, DB, 1 + DS]) for m in range(4)]
        X = [sb(f"x{m}", [P, TOK]) for m in range(4)]
        LO = sb("lo", [P, TOK])
        lora = sb("lora", [P, P])
        T1 = sb("t1", [P, XW])
        par_rows = sb("par_rows", [24, P])
        par = sb("par", [P, 24])
        mu_rows = sb("mu_rows", [17, P])
        mus = sb("mus", [P, 17])
        lw, kk, G, E1, E2, E3, A = [sb(n, [P, TOK]) for n in ("lw", "kk", "g", "e1", "e2", "e3", "a")]
        bank = [ctx.enter_context(nc.psum_tensor(f"b_bank{i}", [P, 512], F32)) for i in range(8)]
        w_ld = [sem(f"w_ld{m}") for m in range(4)]
        proj = [sem(f"proj{m}") for m in range(4)]
        evac = [sem(f"evac{m}") for m in range(4)]
        mixed = [sem(f"mixed{m}") for m in range(4)]
        outs = [sem(f"out{m}") for m in range(6)]
        stored = [sem(f"stored{m}") for m in range(6)]
        high = [sem(f"high{m}") for m in range(4)]
        low = [sem(f"low{m}") for m in range(4)]
        (par_in, lora_in, turned, par_kept, lo_a, gate_mm, gate_t, sq, ssq, ssq_free, rs, gt, expo, gc, gsub,
         rk_ready, bonus_mm, bonus_kept, dseq, pseq, zeroed, ends, kk_ready) = [sem(n) for n in (
             "par_in", "lora_in", "turned", "par_kept", "lo_a", "gate_mm", "gate_t", "sq", "ssq", "ssq_free",
             "rs", "gt", "expo", "gc", "gsub", "rk_ready", "bonus_mm", "bonus_kept", "dseq", "pseq", "zeroed", "ends", "kk_ready")]
        B0 = ACOLS
        SUM, BONUS = 376, 440
        KK, KA, RK, W0, A0 = 0, 4, 8, 12, 16

        def shifted(m):
            return ((U[m][:, 1:1 + SEQ], U[m][:, 0:SEQ]), (US[m][:, :, 1:1 + DS], US[m][:, :, 0:DS]))

        def halves(t):
            return t[:, 0:SEQ], t[:, SEQ:TOK].rearrange("p (b t) -> p b t", b=DB)

        with nc.Block() as block:
            @block.sync
            def _(sp):
                sp.dma_start(W[0][:, :, :], w_block(w_in, B0 + 4 * BW, P)).then_inc(w_ld[0], 16)
                for n, t in enumerate((k_k, k_a, r_k.rearrange("h n -> (h n)"), w0, a0)):
                    sp.dma_start(par_rows[4 * n:4 * n + 4, :], t.rearrange("(j p) -> j p", p=P)).then_inc(par_in, 16)
                sp.dma_start(mu_rows[:, :], mu.rearrange("(j p) -> j p", p=P)).then_inc(par_in, 16)
                sp.dma_start(lora[0:64, :], w2[:, 0:P]).then_inc(lora_in, 16)
                sp.dma_start(lora[64:128, :], a2[:, 0:P]).then_inc(lora_in, 16)
                for m in range(1, 4):
                    sp.dma_start(W[m][:, :, :], w_block(w_in, B0 + m * BW, P)).then_inc(w_ld[m], 16)
                sp.wait_ge(low[0], 1)
                sp.dma_start(W[0][:, :, :], w_block(w_in, B0, P)).then_inc(w_ld[0], 16)

                def body(j, more):
                    for m in range(4):
                        if more:
                            sp.wait_ge(low[m], j + 1 + (1 if m == 0 else 0))
                            alone(sp, K)
                            sp.dma_start(W[m][:, :, :], w_block(w_in, B0 + m * BW + (j + 1) * P, P)).then_inc(w_ld[m], 16)
                    if more:
                        sp.wait_ge(gate_mm, 2 * (j + 1))
                        alone(sp, K)
                        sp.dma_start(lora[0:64, :], w2[:, bass.ds((j + 1) * P, P)]).then_inc(lora_in, 16)
                        sp.dma_start(lora[64:128, :], a2[:, bass.ds((j + 1) * P, P)]).then_inc(lora_in, 16)
                    for m, t in ((4, X[2]), (5, X[3]), (0, X[0]), (1, E2), (2, kk), (3, X[1])):
                        sp.wait_ge(outs[m], j + 1)
                        alone(sp, K)
                        sp.dma_start(S.rw[m, bass.ds(j * P, P), :], t[:, :]).then_inc(stored[m], 16)
                over(sp, NP, body)
                for s in stored:
                    sp.wait_ge(s, 16 * NP)

            @block.gpsimd
            def _(pool):
                done = Seq(pseq, pool, 5)
                done.start(0)
                for m in range(4):
                    done(pool.memset(U[m][:, 0:1], 0.0))
                done(pool.memset(T1[:, TOK:XW], 0.0))
                done.end()
                pool.sem_inc(zeroed, 1)

                def split(m, k):
                    pool.wait_ge(high[m], k + 1)
                    pool.tensor_tensor(WP[m][1][:, :, :], W[m][:, :, :], WP[m][0][:, :, :].bitcast(F32), ALU.subtract
                                       ).then_inc(low[m], 1)
                for m, k in ((0, 0), (1, 0), (2, 0), (3, 0), (0, 1)):
                    split(m, k)

                def body(j, more):
                    if more:
                        split(0, j + 2)
                        for m in range(1, 4):
                            split(m, j + 1)
                over(pool, NP, body)

            @block.scalar
            def _(act):
                act.wait_ge(zeroed, 1)

                def keep(m, j, base):
                    act.wait_ge(mixed[m], j + (1 if base else 0))
                    b0 = 3 * (m % 2)
                    for g, (c, n) in enumerate(THIRDS):
                        act.wait_ge(proj[m], 3 * j + base + g + 1)
                        n = min(n, SEQ - c)
                        ins = act.activation(U[m][:, 1 + c:1 + c + n], bank[b0 + g][:, 0:n], ACT.Copy)
                        if g == 2:
                            act.activation(US[m][:, :, 1:1 + DS], bank[b0 + 2][:, n:n + SR].rearrange("p (b t) -> p b t", b=DB), ACT.Copy)
                            ins = act.activation(US[m][:, :, 0], bank[b0 + 2][:, n + SR:n + SR + DB], ACT.Copy)
                        ins.then_inc(evac[m], 1)

                def split(m, k):
                    act.wait_ge(w_ld[m], 16 * (k + 1))
                    act.wait_ge(low[m], k)
                    act.wait_ge(proj[m], 3 * k)
                    act.activation(WP[m][0][:, :, :], W[m][:, :, :], ACT.Copy).then_inc(high[m], 1)
                for m in range(4):
                    split(m, 0)
                keep(0, 0, 0)
                split(0, 1)
                act.wait_ge(mixed[0], 1)
                act.activation(LO[0:64, :], LO[0:64, :], ACT.Tanh).then_inc(lo_a, 1)

                def body(j, more):
                    act.wait_ge(expo, 3 * j)
                    act.wait_ge(gsub, j)
                    act.wait_ge(outs[3], j)
                    act.wait_ge(outs[2], j)
                    keep(0, j, 3)
                    act.wait_ge(gate_mm, 2 * j + 1)
                    act.wait_ge(par_kept, 2)
                    for g, (c, n) in enumerate(GROUPS):
                        src = bank[6 + g][:, 0:n] if g < 2 else bank[5][:, SUM:SUM + n]
                        act.activation(lw[:, c:c + n], src, ACT.Tanh, scale=0.5, bias=par[:, bass.ds(W0 + j, 1)]).then_inc(gate_t, 1)
                    keep(1, j, 0)
                    if more:
                        split(0, j + 2)
                    act.wait_ge(mixed[1], j + 1)
                    act.wait_ge(outs[0], j)
                    act.activation(E1[:, :], X[1][:, :], ACT.Square, scale=par[:, bass.ds(KK + j, 1)]).then_inc(sq, 1)
                    keep(2, j, 0)
                    if more:
                        split(1, j + 1)
                    act.wait_ge(gate_mm, 2 * j + 2)
                    for g, (c, n) in enumerate(GROUPS):
                        src = bank[6 + g][:, 0:n] if g < 2 else bank[5][:, SUM:SUM + n]
                        act.activation(A[:, c:c + n], src, ACT.Tanh, scale=0.5, bias=par[:, bass.ds(A0 + j, 1)]).then_inc(gate_t, 1)
                    keep(3, j, 0)
                    if more:
                        split(2, j + 1)
                    act.wait_ge(mixed[3], j + 1)
                    act.wait_ge(stored[1], 16 * j)
                    act.activation(E2[:, :], X[3][:, :], ACT.Tanh, scale=0.5).then_inc(gt, 1)
                    act.wait_ge(ssq, j + 1)
                    for g, (c, n) in enumerate(GROUPS):
                        src = bank[6 + g][:, 0:n] if g < 2 else bank[5][:, SUM:SUM + n]
                        act.activation(E3[:, c:c + n], src, ACT.Ln, bias=EPS).then_inc(ssq_free, 1)
                    act.wait_ge(ssq_free, 3 * (j + 1))
                    act.activation(E3[:, :], E3[:, :], ACT.Exp, scale=-0.5).then_inc(rs, 1)
                    act.wait_ge(gc, j + 1)
                    act.wait_ge(ssq, j + 1)
                    act.activation(E1[:, :], G[:, :], ACT.Exp).then_inc(expo, 1)
                    act.wait_ge(gsub, j + 1)
                    act.wait_ge(outs[5], j + 1)
                    act.activation(E2[:, :], lw[:, :], ACT.Exp).then_inc(expo, 1)
                    act.wait_ge(kk_ready, j + 1)
                    act.activation(E3[:, :], G[:, :], ACT.Exp, scale=-1.0).then_inc(expo, 1)
                    act.activation(K.rw_in[:, bass.ds(j, 1), :], K.rw_mid[:, bass.ds(j, 1), :], ACT.Exp).then_inc(ends, 1)
                    act.activation(K.rw_out[:, bass.ds(j, 1), 0:TILES], G[:, P - 1:SEQ:P], ACT.Exp).then_inc(ends, 1)
                    act.activation(K.rw_out[:, bass.ds(j, 1), TILES:TILES + DB], G[:, SEQ + DS - 1:TOK:DS], ACT.Exp).then_inc(ends, 1)
                    if more:
                        split(3, j + 1)
                over(act, NP, body)

            @block.vector
            def _(dve):
                dve.wait_ge(turned, 2)
                dve.tensor_copy(mus[:, :], bank[6][:, 0:17]).then_inc(par_kept, 1)
                dve.tensor_copy(par[:, 0:12], bank[6][:, 32:44]).then_inc(dseq, 1)
                dve.tensor_scalar(par[:, 12:20], bank[6][:, 44:52], 0.5, None, ALU.mult).then_inc(par_kept, 1)
                dve.wait_ge(dseq, 1)
                dve.tensor_scalar(par[:, 4:8], par[:, 4:8], 0.5, None, ALU.mult).then_inc(dseq, 1)
                dve.wait_ge(dseq, 2)
                dve.tensor_scalar(par[:, 20:24], par[:, 4:8], -1.0, 1.0, ALU.mult, ALU.add).then_inc(dseq, 1)
                dve.wait_ge(dseq, 3)
                dve.wait_ge(par_kept, 2)

                one = Seq(dseq, dve, 19)

                def blend(m, dst, col, n):
                    dve.wait_ge(evac[m], n)
                    now_s, now_d = shifted(m)
                    ds_, dd_ = halves(dst)
                    one(dve.tensor_tensor(ds_, now_s[1], now_s[0], ALU.subtract))
                    one(dve.tensor_tensor(dd_, now_d[1], now_d[0], ALU.subtract))
                    one(dve.scalar_tensor_tensor(out=ds_, in0=ds_, scalar=mus[:, col], in1=now_s[0], op0=ALU.mult, op1=ALU.add))
                    dve.scalar_tensor_tensor(out=dd_, in0=dd_, scalar=mus[:, col], in1=now_d[0],
                                             op0=ALU.mult, op1=ALU.add).then_inc(mixed[m], 1)
                one.start(0)
                one.n = 3
                blend(0, LO, slice(16, 17), 3)

                def keep_bonus(j):
                    dve.wait_ge(bonus_mm, j + 1)
                    dve.tensor_copy(K.bonus[:, :, bass.ds(2 * j, 2)], bank[2][:, BONUS:BONUS + 18].rearrange("p (n h) -> p n h", h=2)
                                    ).then_inc(bonus_kept, 1)

                def body(j, more):
                    one.start(j)
                    one.base = one.base + 6
                    dve.wait_ge(stored[0], 16 * j)
                    blend(0, X[0], bass.ds(0 + j, 1), 3 * j + 6)
                    dve.wait_ge(gate_t, 6 * j + 3)
                    one(dve.tensor_scalar(lw[:, :], lw[:, :], 1.0, -0.5 * DECAY, ALU.add, ALU.mult))
                    dve.wait_ge(ends, 3 * j)
                    one(dve.tensor_tensor_scan(G[:, :], K.restart[:, :], lw[:, :], 0.0, ALU.mult, ALU.add))
                    one(dve.tensor_copy(K.rw_mid[:, bass.ds(j, 1), :], G[:, P // 2 - 1:SEQ:P]))
                    g3 = G[:, 0:SEQ].rearrange("p (n t) -> p n t", n=TILES)
                    mid = K.rw_mid[:, bass.ds(j, 1), :].rearrange("p a n -> p (a n)")
                    one(dve.tensor_tensor(g3, g3, mid.rearrange("p (n a) -> p n a", a=1).broadcast_to([P, TILES, P]), ALU.subtract))
                    dve.sem_inc(gc, 1)
                    dve.tensor_tensor(lw[:, :], G[:, :], lw[:, :], ALU.subtract).then_inc(gsub, 1)
                    dve.wait_ge(stored[3], 16 * j)
                    blend(1, X[1], bass.ds(4 + j, 1), 3 * j + 3)
                    if not isinstance(j, int) or j > 0:
                        keep_bonus(j - 1)
                    dve.wait_ge(stored[4], 16 * j)
                    blend(2, X[2], bass.ds(8 + j, 1), 3 * j + 3)
                    dve.wait_ge(mixed[2], j + 1)
                    dve.sem_inc(outs[4], 1)
                    dve.wait_ge(stored[5], 16 * j)
                    blend(3, X[3], bass.ds(12 + j, 1), 3 * j + 3)
                    dve.wait_ge(gt, j + 1)
                    dve.wait_ge(mixed[3], j + 1)
                    dve.scalar_tensor_tensor(out=X[3][:, :], in0=E2[:, :], scalar=1.0, in1=X[3][:, :],
                                             op0=ALU.add, op1=ALU.mult).then_inc(outs[5], 1)
                    dve.wait_ge(rs, j + 1)
                    dve.wait_ge(mixed[1], j + 1)
                    dve.wait_ge(stored[2], 16 * j)
                    dve.scalar_tensor_tensor(out=kk[:, :], in0=X[1][:, :], scalar=par[:, bass.ds(KK + j, 1)], in1=E3[:, :],
                                             op0=ALU.mult, op1=ALU.mult).then_inc(kk_ready, 1)
                    dve.wait_ge(gate_t, 6 * j + 6)
                    dve.wait_ge(bonus_kept, j)
                    one(dve.tensor_scalar(T1[:, 0:TOK], A[:, :], par[:, bass.ds(KA + j, 1)],
                                          par[:, bass.ds(20 + j, 1)], ALU.mult, ALU.add))
                    one(dve.tensor_tensor(X[1][:, :], X[1][:, :], T1[:, 0:TOK], ALU.mult))
                    dve.wait_ge(mixed[0], j + 2)
                    dve.scalar_tensor_tensor(out=T1[:, 0:TOK], in0=X[1][:, :], scalar=par[:, bass.ds(RK + j, 1)], in1=X[0][:, :],
                                             op0=ALU.mult, op1=ALU.mult).then_inc(rk_ready, 1)
                    dve.wait_ge(expo, 3 * j + 1)
                    dve.wait_ge(rk_ready, j + 1)
                    dve.tensor_tensor(X[0][:, :], X[0][:, :], E1[:, :], ALU.mult).then_inc(outs[0], 1)
                    dve.wait_ge(expo, 3 * j + 3)
                    dve.wait_ge(kk_ready, j + 1)
                    dve.wait_ge(stored[1], 16 * j)
                    dve.tensor_tensor(E2[:, :], kk[:, :], E2[:, :], ALU.mult).then_inc(outs[1], 1)
                    one(dve.scalar_tensor_tensor(out=A[:, :], in0=A[:, :], scalar=1.0, in1=kk[:, :], op0=ALU.add, op1=ALU.mult))
                    dve.wait_ge(outs[1], j + 1)
                    dve.scalar_tensor_tensor(out=kk[:, :], in0=A[:, :], scalar=0.5, in1=E3[:, :],
                                             op0=ALU.mult, op1=ALU.mult).then_inc(outs[2], 1)
                    dve.tensor_tensor(X[1][:, :], X[1][:, :], E3[:, :], ALU.mult).then_inc(outs[3], 1)
                    one.end()
                over(dve, NP, body)
                keep_bonus(NP - 1)

            @block.tensor
            def _(pe):
                pe.wait_ge(par_in, 96)
                pe.transpose(bank[6][:, 0:17], mu_rows[:, :], K.ident[0:17, 0:17]).then_inc(turned, 1)
                pe.transpose(bank[6][:, 32:52], par_rows[0:20, :], K.ident[0:20, 0:20]).then_inc(turned, 1)

                def project(m, k, before_last):
                    b0 = 3 * (m % 2)
                    pe.wait_ge(high[m], k + 1)
                    pe.wait_ge(low[m], k + 1)
                    for g, (c, n) in enumerate(THIRDS):
                        if g == 2:
                            n = XC - c
                            before_last()
                        for kt in range(KT):
                            w = WP[m][0][:, kt, :], WP[m][1][:, kt, :]
                            x = K.xh[:, kt, c:c + n], K.xl[:, kt, c:c + n]
                            mm = products(pe, bank[b0 + g][:, 0:n], w, x, kt == 0, kt == KT - 1)
                        mm.then_inc(proj[m], 1)

                def gate(half, j):
                    r = slice(64 * half, 64 * half + 64)
                    for g, (c, n) in enumerate(GROUPS):
                        dst = bank[6 + g][:, 0:n] if g < 2 else bank[5][:, SUM:SUM + n]
                        mm = pe.matmul(dst, lora[r, :], LO[r, c:c + n], start=True, stop=True)
                    mm.then_inc(gate_mm, 1)

                def bonus(j):
                    pe.wait_ge(rk_ready, j + 1)
                    for n in range(TILES + 1):
                        mm = pe.matmul(bank[2][:, BONUS + 2 * n:BONUS + 2 * n + 2], T1[:, n * P:(n + 1) * P], K.head_cols[:, :],
                                       start=True, stop=True)
                    mm.then_inc(bonus_mm, 1)

                def nothing():
                    pass
                project(0, 0, nothing)
                pe.wait_ge(lora_in, 32)
                pe.wait_ge(lo_a, 1)
                pe.wait_ge(par_kept, 2)
                pe.wait_ge(evac[0], 3)

                def body(j, more):
                    later = not isinstance(j, int) or j > 0

                    def read_w():
                        pe.wait_ge(gate_t, 6 * j + 3)

                    def read_a():
                        pe.wait_ge(gate_t, 6 * j + 6)

                    def read_bonus():
                        if later:
                            pe.wait_ge(bonus_kept, j)
                    pe.wait_ge(evac[2], 3 * j)
                    project(0, j + 1, nothing)
                    pe.wait_ge(ssq_free, 3 * j)
                    pe.wait_ge(evac[3], 3 * j)
                    pe.wait_ge(lora_in, 32 * (j + 1))
                    gate(0, j)
                    project(1, j, read_w)
                    pe.wait_ge(evac[0], 3 * j + 6)
                    if later:
                        bonus(j - 1)
                    project(2, j, read_bonus)
                    pe.wait_ge(gate_t, 6 * j + 3)
                    pe.wait_ge(evac[1], 3 * j + 3)
                    gate(1, j)
                    project(3, j, read_a)
                    pe.wait_ge(evac[3], 3 * j + 3)
                    pe.wait_ge(sq, j + 1)
                    for g, (c, n) in enumerate(GROUPS):
                        dst = bank[6 + g][:, 0:n] if g < 2 else bank[5][:, SUM:SUM + n]
                        mm = pe.matmul(dst, K.pair_ones[:, :], E1[:, c:c + n], start=True, stop=True)
                    mm.then_inc(ssq, 1)
                over(pe, NP, body)
                pe.wait_ge(evac[2], 3 * NP)
                bonus(NP - 1)


LEVELS = 7
LEVELS_S = 3
MIDDLE = {LEVELS: 3, LEVELS_S: 1}


def with_batches(batch, steps):
    for b in range(DB):
        if b in steps:
            steps[b]()
        batch(b)


def phase_mix0(nc, K, w_out, norm_w, gdn_norm, ln_w, ln_b, x_prompt, x_sample, gdn0, rwkv0, S,
               p_gdn, p_rwkv, s_gdn, s_rwkv):
    with ExitStack() as ctx:
        sb = lambda n, s: ctx.enter_context(nc.sbuf_tensor("c_" + n, s, F32))
        ev = Events(nc, ctx, "c_")

        QK = sb("qk", [P, 2, AH, P])
        V = sb("v", [P, AH, P])
        RW = sb("rw", [P, 4, NP, P])
        VG = sb("vg", [P, 2, NP, P])
        Z = sb("z", [P, AKEY])
        XR = sb("xr", [P, D])
        wo = sb("wo", [P, KT, D])
        nw = sb("nw", [P, D])
        gnw = sb("gnw", [P, P])
        lnw = sb("lnw", [P, BW])
        lnb = sb("lnb", [P, BW])
        ld, bt, nbt, bo = sb("ld", [P, AH]), sb("bt", [P, AH]), sb("nbt", [P, AH]), sb("bo", [P, BH])
        g, eg = sb("g", [P, AH]), sb("eg", [P, AH])
        dend = sb("dend", [P, AH])
        dec = sb("dec", [P, AH, P])
        eGB = sb("egb", [P, AH, P])
        attn = sb("attn", [P, AH, P])
        NT = sb("nt", [P, AH, P])
        SC = sb("sc", [P, BH, 4, P])
        mask4 = sb("mask4", [P, 4, P])
        mask4s = sb("mask4s", [SR, 4, SR])
        lev = sb("lev", [P, LEVELS, P])
        kr, vr = sb("kr", [P, AH, P]), sb("vr", [P, AH, P])
        Br, Kr, Vr, Gr = [sb(n, [P, BW]) for n in ("br", "krr", "vrr", "grr")]
        X = [sb(f"inv{u}", [P, 4, P]) for u in range(3)]
        XT = [sb(f"invt{u}", [P, 4, P]) for u in range(3)]
        Yall = sb("y", [P, 3, 4, P])
        Y = [Yall[:, u, :, :] for u in range(3)]
        M = [sb(f"m{u}", [P, 4, P]) for u in range(3)]
        Wr = sb("wr", [P, AH, P])
        NV = sb("nv", [P, AH, P])
        NVd = sb("nvd", [P, AH, P])
        RH = sb("rh", [P, BW])
        SA = sb("sa", [P, BW])
        St = sb("st", [P, AH, P])
        Tt = sb("tt", [P, NP, P])
        Th = sb("th", [P, NP, P])
        sqa, sqb = sb("sqa", [P, BW]), sb("sqb", [P, BW])
        st = sb("stats", [P, 12])
        rstd = sb("rstd", [P, 12])
        mean = sb("mean", [P, BH])
        OR = sb("or", [P, D])
        bv = sb("bv", [P, BW])
        gw = sb("gw", [P, BW])
        OT = sb("ot", [P, KT, P])
        x1 = XR
        n1 = sb("n1", [P, 4])
        xn = sb("xn", [P, D])
        QG = sb("qg", [P, AH, P])
        tr = Wr
        bank = [ctx.enter_context(nc.psum_tensor(f"c_bank{i}", [P, 512], F32)) for i in range(8)]
        Sb = sb("sb", [P, DB, AH, P])
        Tb = sb("tb", [P, DB, NP, 64])
        Q1 = [sb("q1", [P, DB, SR]),
              sqb.rearrange("p (b t) -> p b t", b=DB)]
        Rin = [t[0:64, :, :] for t in (*Y, *X, RH.rearrange("p (h c) -> p h c", h=NP), NV)]
        Rout = [t[0:64, :, :] for t in (*Y, *M, XT[1], XT[2])]
        PICK = [(Wr, RH, QG.rearrange("p h c -> p (h c)")),
                (X[0], *(x.rearrange("p h c -> p (h c)") for x in X[1:]))]
        UPD_A, UPD_B, TURN = (4, 1), (5, 2), (3, 0)

        def v4(b, r=P, c=P):
            return bank[b][0:r, 0:4 * P].rearrange("p (h c) -> p h c", h=4)[:, :, 0:c]

        def half(t, l, T, s):
            if len(t.shape) == 2:
                return t[:, 0:T].rearrange("p (b u h) -> p b u h", u=2, h=1 << l)[:, :, s, :]
            return t[:, :, 0:T].rearrange("p k (b u h) -> p k b u h", u=2, h=1 << l)[:, :, :, s, :]

        def packed(b, l, T, r):
            return bank[b][0:r, :].rearrange("p (k c) -> p k c", k=4)[:, :, 0:T // 2].rearrange("p k (b h) -> p k b h", h=1 << l)

        def bc(t, shape):
            return t.broadcast_to(shape)

        with nc.Block() as block:
            @block.sync
            def _(sp):
                col = lambda t, c, T: t.rearrange("(h p) t -> p h t", p=P)[:, :, bass.ds(c, T)]

                def load_qkv(c, T):
                    for m in range(2):
                        sp.dma_start(QK[:, m, :, 0:T], col(S.qkv[m], c, T)).then_inc(ev("ld_qk"), 16)
                    sp.dma_start(V[:, :, 0:T], col(S.qkv[2], c, T)).then_inc(ev("ld_v"), 16)

                def load_abk(c, T):
                    for m in range(1, 4):
                        sp.dma_start(RW[:, m, :, 0:T], col(S.rw[m], c, T)).then_inc(ev("ld_rw"), 16)
                    for m in range(2):
                        sp.dma_start(VG[:, m, :, 0:T], col(S.rw[4 + m], c, T)).then_inc(ev("ld_vg"), 16)

                def load_r(c, T):
                    sp.dma_start(RW[:, 0, :, 0:T], col(S.rw[0], c, T)).then_inc(ev("ld_r"), 16)

                def load_z(c, T):
                    sp.dma_start(Z[0:T, :], S.z[bass.ds(c, T), :]).then_inc(ev("ld_z"), 16)

                def load_x(c, T):
                    x = x_prompt[0, bass.ds(c, T), :] if T == P else x_sample.rearrange("b t d -> (b t) d")
                    sp.dma_start(XR[0:T, :], x).then_inc(ev("ld_x"), 16)

                def during(i, ahead):
                    n, c = i + 1, i * P
                    sp.wait_ge(ev("rows_a"), n)
                    sp.wait_ge(ev("rhs_a"), n)
                    sp.wait_ge(ev("qg"), n)
                    alone(sp, K)
                    load_qkv(c + P, ahead)
                    sp.wait_ge(ev("rows_vg"), n)
                    sp.wait_ge(ev("rows_b"), n)
                    sp.wait_ge(ev("rhs_b"), n)
                    alone(sp, K)
                    load_abk(c + P, ahead)
                    if not (isinstance(i, int) and i == 0):
                        sp.wait_ge(ev("oa"), i)
                        alone(sp, K)
                        load_z(c, P)
                        sp.wait_ge(ev("x1"), i)
                        alone(sp, K)
                        sp.dma_start(S.x1[bass.ds(c - P, P), :], x1[:, :]).then_inc(ev("stored"), 16)
                    sp.wait_ge(ev("out_b"), n)
                    alone(sp, K)
                    load_r(c + P, ahead)
                    if not (isinstance(i, int) and i == 0):
                        sp.wait_ge(ev("xn1"), i)
                        alone(sp, K)
                        sp.wait_ge(ev("stored"), 16 * i)
                        alone(sp, K)
                        load_x(c, P)
                        sp.wait_ge(ev("xk_a"), i)
                        sp.wait_ge(ev("xk_b"), i)
                        alone(sp, K)
                        sp.dma_start(S.xnT[:, :, bass.ds(c - P, P)], OT[:, :, :]).then_inc(ev("xn_out"), 16)

                def after(i, T):
                    c = i * P
                    sp.wait_ge(ev("oa"), i + 1)
                    load_z(SEQ, SR)
                    sp.wait_ge(ev("x1"), i + 1)
                    sp.dma_start(S.x1[c:c + T, :], x1[0:T, :]).then_inc(ev("stored"), 16)
                    sp.wait_ge(ev("xn1"), i + 1)
                    sp.wait_ge(ev("stored"), 16 * (i + 1))
                    load_x(SEQ, SR)
                    sp.wait_ge(ev("xk_a"), i + 1)
                    sp.wait_ge(ev("xk_b"), i + 1)
                    sp.dma_start(S.xnT[:, :, c:c + T], OT[:, :, 0:T]).then_inc(ev("xn_out"), 16)
                load_qkv(0, P)
                load_abk(0, P)
                load_r(0, P)
                for t, v in ((nw, norm_w), (gnw, gdn_norm), (lnw, ln_w), (lnb, ln_b)):
                    sp.dma_start(t[:, :], as_row(v)).then_inc(ev("ld_par"), 16)
                load_z(0, P)
                load_x(0, P)
                sp.dma_start(wo[:, :, :], w_block(w_out, 0, D)).then_inc(ev("ld_wo"), 16)
                for i in range(2):
                    during(i, P)
                with sp.Fori(2, TILES - 1) as i:
                    during(i, P)
                sp.dma_start(Sb[:, :, :, :], gdn0.rearrange("b h d v -> d b h v")).then_inc(ev("ld_sb"), 16)
                during(TILES - 1, SR)
                sp.wait_ge(ev("sa_mm"), TILES)
                for b in range(DB):
                    if b == DB - 1:
                        sp.wait_ge(ev("out_a"), TILES)
                    sp.dma_start(Rin[b].rearrange("v j (h k) -> v (j h) k", h=2),
                                 rwkv0[b].rearrange("h v k -> v h k")).then_inc(ev("ld_rb"), 16)
                sp.wait_ge(ev("state_a"), TILES)
                sp.dma_start(p_gdn[0].rearrange("h d v -> d h v"), St[:, :, :]).then_inc(ev("st_out"), 16)
                sp.wait_ge(ev("tr"), 1)
                for h in range(2):
                    r = slice(64 * h, 64 * h + 64)
                    sp.dma_start(p_rwkv[0].rearrange("(j h) v k -> h v j k", h=2)[h], tr[r, :, r]).then_inc(ev("tr_out"), 16)
                after(TILES - 1, P)

                def store_state(b):
                    sp.wait_ge(ev("sb_new"), b + 1)
                    sp.dma_start(s_gdn[b].rearrange("h d v -> d h v"), Sb[:, b, :, :]).then_inc(ev("st_out"), 16)
                    sp.wait_ge(ev("rb_new"), b + 1)
                    sp.dma_start(s_rwkv[b].rearrange("h v k -> v h k"),
                                 Rout[b].rearrange("v j (h k) -> v (j h) k", h=2)).then_inc(ev("rb_out"), 16)
                for b in range(5):
                    store_state(b)
                sp.wait_ge(ev("x1"), TILES + 1)
                sp.dma_start(S.x1[SEQ:TOK, :], x1[0:SR, :]).then_inc(ev("stored"), 16)
                for b in range(5, DB - 1):
                    store_state(b)
                sp.wait_ge(ev("xk_a"), TILES + 1)
                sp.wait_ge(ev("xk_b"), TILES + 1)
                sp.dma_start(S.xnT[:, :, SEQ:TOK], OT[:, :, 0:SR]).then_inc(ev("xn_out"), 16)
                store_state(DB - 1)
                sp.wait_ge(ev("st_out"), 16 * (1 + DB))
                sp.wait_ge(ev("rb_out"), 16 * DB)
                sp.wait_ge(ev("tr_out"), 16 * 2)
                sp.wait_ge(ev("stored"), 16 * (TILES + 1))
                sp.wait_ge(ev("xn_out"), 16 * (TILES + 1))

            @block.gpsimd
            def _(pool):
                done = Seq(ev("pool_seq"), pool, 8 + 4 * LEVELS)
                done.start(0)
                m4 = ((K.causal, -1.0), (K.strict, 1.0), (K.causal, 1.0), (K.strict, 1.0))
                for n, (m, f) in enumerate(m4):
                    done(pool.tensor_scalar(mask4[:, n, :], m[:, :], f, None, ALU.mult))
                for n, (m, f) in enumerate(((K.causal_s, -1.0), (K.strict_s, 1.0), (K.causal_s, 1.0), (K.strict_s, 1.0))):
                    done(pool.tensor_scalar(mask4s[:, n, :], m[:, :], f, None, ALU.mult))
                pool.wait_ge(ev("pool_seq"), 8)
                pool.sem_inc(ev("masks"), 1)
                for l in range(LEVELS):
                    h = 1 << l
                    nb = P // (2 * h)
                    done(pool.memset(lev[:, l, :], 0.0))
                    v = lev[:, l, :].rearrange("s (b u t) -> s b u t", u=2, t=h)[:, :, 1, :]
                    done(pool.memset(v, 1.0))
                    done(pool.affine_select(out=v, in_=v, compare_op=ALU.is_ge, fill=0.0, base=0,
                                            pattern=[[-2 * h, nb], [0, h]], channel_multiplier=1))
                    done(pool.affine_select(out=v, in_=v, compare_op=ALU.is_ge, fill=0.0, base=h - 1,
                                            pattern=[[2 * h, nb], [0, h]], channel_multiplier=-1))
                done.end()

                def norms(f, T):
                    pool.wait_ge(ev("stats"), f + 1)
                    pool.wait_ge(ev("ob1"), f)
                    pool.tensor_tensor(rstd[0:T, :], st[0:T, :], K.half_neg[0:T, 0:12], ALU.pow).then_inc(ev("rstd"), 1)

                def norm(f, T):
                    pool.wait_ge(ev("n1"), f + 1)
                    pool.tensor_tensor(n1[0:T, 2:3], n1[0:T, 1:2], K.half_neg[0:T, 0:1], ALU.pow).then_inc(ev("n1r"), 1)

                def tile(i, T, levels, last):
                    n = i + 1
                    for l in range(levels):
                        if l == MIDDLE[levels] and last is not None:
                            norms(last, P)
                        for u in range(3):
                            if l == 0:
                                pool.wait_ge(ev("nt_a") if u == 0 else ev("sc"), n if u == 0 else 8 * i + 4 * u)
                                pool.wait_ge(ev(f"ymm{u}"), (LEVELS - 1) * i)
                                pool.wait_ge(ev(f"xt1_{u}"), i)
                            elif l == 1:
                                pool.wait_ge(ev(f"xt1_{u}"), n)
                            else:
                                pool.wait_ge(ev(f"ymm{u}"), (LEVELS - 1) * i + l - 1)
                            src = NT[0:T, :, 0:T] if u == 0 else SC[0:T, 4 * (u - 1):4 * u, 1, 0:T]
                            pool.tensor_tensor(M[u][0:T, :, 0:T], src, bc(lev[0:T, l:l + 1, 0:T], [T, 4, T]),
                                               ALU.mult).then_inc(ev(f"m{u}"), 1)
                    pool.wait_ge(ev("ld_z"), 16 * n)
                    z = Z[0:T, :].rearrange("p (h c) -> p h c", h=AH)
                    pool.wait_ge(ev("gnw"), 1)
                    pool.tensor_tensor(z, z, bc(gnw[0:T, :].rearrange("p (a c) -> p a c", a=1), [T, AH, P]),
                                       ALU.mult).then_inc(ev("zw"), 1)
                    pool.wait_ge(ev("vr_b"), n)
                    pool.wait_ge(ev("bo"), n)
                    pool.wait_ge(ev("ob"), i)
                    v8 = lambda t: t[0:T, :].rearrange("p (h c) -> p h c", h=BH)
                    pool.tensor_tensor(v8(bv), v8(Vr), bc(bo[0:T, :].rearrange("p (h a) -> p h a", a=1), [T, BH, 64]),
                                       ALU.mult).then_inc(ev("bv1"), 1)
                    pool.wait_ge(ev("bv1"), n)
                    pool.tensor_tensor(bv[0:T, :], bv[0:T, :], lnb[0:T, :], ALU.add).then_inc(ev("bv2"), 1)
                    pool.wait_ge(ev("bv2"), n)
                    pool.wait_ge(ev("gr"), n)
                    pool.tensor_tensor(bv[0:T, :], bv[0:T, :], Gr[0:T, :], ALU.mult).then_inc(ev("bv"), 1)
                    pool.tensor_tensor(gw[0:T, :], lnw[0:T, :], Gr[0:T, :], ALU.mult).then_inc(ev("gw"), 1)
                    if last is not None:
                        norm(last, P)
                pool.wait_ge(ev("ld_par"), 64)
                pool.tensor_scalar(gnw[:, :], gnw[:, :], 0.5, None, ALU.mult).then_inc(ev("gnw"), 1)
                for i in range(2):
                    tile(i, P, LEVELS, i - 1 if i else None)
                with pool.Fori(2, TILES) as i:
                    tile(i, P, LEVELS, i - 1)
                tile(TILES, SR, LEVELS_S, TILES - 1)
                norms(TILES, SR)
                norm(TILES, SR)

            @block.scalar
            def _(act):
                def end_rows(f, T):
                    act.wait_ge(ev("ot_mm"), f + 1)
                    act.wait_ge(ev("prj"), 2 * f)
                    act.wait_ge(ev("xn_out"), 16 * f)
                    act.activation(OT[:, 0:4, 0:T], v4(6, P, T), ACT.Copy).then_inc(ev("ot"), 1)

                def end_square(f, T):
                    act.wait_ge(ev("x1"), f + 1)
                    act.wait_ge(ev("nt_mm"), f)
                    act.activation(xn[0:T, :], x1[0:T, :], ACT.Square, accum_out=n1[0:T, 0:1]).then_inc(ev("n1s"), 1)

                def end_keep(f, T):
                    act.wait_ge(ev("nt_mm"), f + 1)
                    act.activation(OT[:, 4:8, 0:T], v4(7, P, T), ACT.Copy).then_inc(ev("xk_b"), 1)

                def turned(i, T, l, u):
                    act.wait_ge(ev(f"xt_mm{u}"), (LEVELS - 2) * i + l)
                    act.activation(XT[u][0:T, :, 0:T], v4(2 * u + 1, T, T), ACT.Copy).then_inc(ev(f"xt{u}"), 1)

                def tile(i, T, levels, last):
                    n = i + 1
                    act.wait_ge(ev("gB"), i)
                    act.wait_ge(ev("gcol_mm"), i)
                    act.activation(ld[:, :], K.logd[:, bass.ds(i, 1), :].rearrange("p a h -> p (a h)"), ACT.Copy).then_inc(ev("ldc"), 1)
                    act.wait_ge(ev("nv"), i)
                    act.wait_ge(ev("nt_a"), i)
                    act.activation(bt[:, :], K.beta[:, bass.ds(i, 1), :].rearrange("p a h -> p (a h)"), ACT.Copy).then_inc(ev("bt"), 1)
                    act.activation(nbt[:, :], K.beta[:, bass.ds(i, 1), :].rearrange("p a h -> p (a h)"), ACT.Copy,
                                   scale=-1.0).then_inc(ev("bt"), 1)
                    act.wait_ge(ev("bv1"), i)
                    act.activation(bo[:, :], K.bonus[:, bass.ds(i, 1), :].rearrange("p a h -> p (a h)"), ACT.Copy).then_inc(ev("bo"), 1)
                    act.wait_ge(ev("gcol_mm"), n)
                    act.wait_ge(ev("dm"), i)
                    act.activation(g[0:T, :], bank[1][0:T, 0:AH], ACT.Copy).then_inc(ev("g"), 1)
                    act.wait_ge(ev("wr"), i)
                    act.activation(eg[0:T, :], bank[1][0:T, 0:AH], ACT.Exp).then_inc(ev("eg"), 1)
                    act.wait_ge(ev("dm"), n)
                    act.wait_ge(ev("attn"), i)
                    act.activation(dec[0:T, :, 0:T], dec[0:T, :, 0:T], ACT.Exp).then_inc(ev("dec"), 1)
                    act.wait_ge(ev("state_a"), i)
                    act.activation(eGB[:, :, 0:T], v4(0, P, T), ACT.Exp).then_inc(ev("egb"), 1)
                    act.wait_ge(ev("rows_a"), n)
                    act.wait_ge(ev("upd_a"), i)
                    act.activation(kr[0:T, :, :], v4(4, T), ACT.Copy).then_inc(ev("kr"), 1)
                    act.wait_ge(ev("rows_b"), n)
                    act.wait_ge(ev("upd_b"), i)
                    act.activation(Br[0:T, :], bank[6][0:T, :], ACT.Copy, scale=-1.0).then_inc(ev("br"), 1)
                    act.wait_ge(ev("rows_vg"), n)
                    act.wait_ge(ev("bv1"), i)
                    act.activation(Vr[0:T, :], bank[0][0:T, :], ACT.Copy).then_inc(ev("vr_b"), 1)
                    for l in range(levels):
                        for u in range(3):
                            b = 2 * u
                            if l == 0:
                                act.wait_ge(ev(f"x1mm{u}"), n)
                                act.activation(X[u][0:T, :, 0:T], v4(b, T, T), ACT.Copy).then_inc(ev(f"xk{u}"), 1)
                            else:
                                act.wait_ge(ev(f"ymm{u}"), (LEVELS - 1) * i + l)
                                act.activation(Y[u][0:T, :, 0:T // 2], v4(b, T, T // 2), ACT.Copy).then_inc(ev(f"y{u}"), 1)
                                if l > 1:
                                    turned(i, T, l - 1, u)
                        if last is not None and l == MIDDLE[levels]:
                            end_rows(last, P)
                        if last is not None and l == 6:
                            end_square(last, P)
                    if levels < LEVELS:
                        for u in range(3):
                            turned(i, T, levels - 1, u)
                        end_square(last, P)
                    act.wait_ge(ev("sa_mm"), n)
                    act.activation(SA[0:T, :], bank[2][0:T, :], ACT.Copy).then_inc(ev("sa"), 1)
                    act.wait_ge(ev("out_a"), n)
                    act.wait_ge(ev("suma"), i)
                    act.wait_ge(ev("ot_mm"), i)
                    act.activation(sqa[0:T, :], bank[1][0:T, :], ACT.Square).then_inc(ev("sqa"), 1)
                    act.activation(OR[0:T, 0:AKEY], bank[1][0:T, :], ACT.Copy).then_inc(ev("raw"), 1)
                    act.wait_ge(ev("cent"), n)
                    act.wait_ge(ev("sumb"), i)
                    act.activation(sqb[0:T, :], OR[0:T, AKEY:D], ACT.Square).then_inc(ev("sqb"), 1)
                    if last is not None:
                        end_keep(last, P)
                for i in range(2):
                    tile(i, P, LEVELS, i - 1 if i else None)
                with act.Fori(2, TILES) as i:
                    tile(i, P, LEVELS, i - 1)
                tile(TILES, SR, LEVELS_S, TILES - 1)

                def turned_state(b):
                    act.wait_ge(ev("rb_mm"), b + 1)
                    act.activation(Rout[b], bank[TURN[b % 2]][0:64, :].rearrange("v (j c) -> v j c", j=NP), ACT.Copy).then_inc(ev("rb_new"), 1)

                def batch(b):
                    if b == 0:
                        act.wait_ge(ev("nvd"), TILES + 1)
                    if b >= 2:
                        act.wait_ge(ev("upd_s"), b - 1)
                    row = K.same[:, b * DS:b * DS + 1]
                    nv, sa, v = PICK[b % 2]
                    act.activation(nv[0:SR, :, :], NVd[0:SR, :, :], ACT.Copy, scale=row).then_inc(ev("pick"), 1)
                    act.activation(sa[0:SR, :], SA[0:SR, :], ACT.Copy, scale=row).then_inc(ev("pick"), 1)
                    act.activation(v[0:SR, :], Vr[0:SR, :], ACT.Copy, scale=row).then_inc(ev("pick"), 1)
                    if b >= 2:
                        turned_state(b - 2)
                with_batches(batch, {2: lambda: end_rows(TILES, SR), 5: lambda: end_square(TILES, SR),
                                     7: lambda: end_keep(TILES, SR)})
                turned_state(DB - 2)
                turned_state(DB - 1)

            @block.vector
            def _(dve):
                def spread(half, heads):
                    for r in heads:
                        k = (AH + BH) * half + r
                        j = (r - AH) // 2
                        if half == 0:
                            src = QK[:, 1, r, 0:SR] if r < AH else RW[:, 1, j, 0:SR]
                        else:
                            src = QG[:, r, 0:SR] if r < AH else RW[:, 0, j, 0:SR]
                        if k >= 2:
                            dve.wait_ge(ev("q1_used"), k - 1)
                        keep = K.ones[:, 0:1] if r < AH else K.head_cols[:, (r - AH) % 2:(r - AH) % 2 + 1]
                        dve.scalar_tensor_tensor(out=Q1[k % 2][:, :, :], in0=bc(src.rearrange("p (a t) -> p a t", a=1), [P, DB, SR]),
                                                 scalar=keep, in1=K.batch_cols[:, :, :], op0=ALU.mult,
                                                 op1=ALU.mult).then_inc(ev("q1"), 1)

                dve.memset(St[:, :, :], 0.0).then_inc(ev("init"), 1)
                dve.memset(Tt[:, :, :], 0.0).then_inc(ev("init"), 1)
                dve.wait_ge(ev("init"), 2)
                dve.wait_ge(ev("masks"), 1)

                v8 = lambda t: t.rearrange("p (h c) -> p h c", h=BH)
                wide = lambda t, T, w: bc(t.rearrange("p (h a) -> p h a", a=1), [T, t.shape[1], w])

                def end_sums(f, T):
                    n = f + 1
                    dve.wait_ge(ev("sqa"), n)
                    dve.tensor_reduce(st[0:T, 0:4], sqa[0:T, :].rearrange("p (h c) -> p h c", h=AH), AX_X, ALU.add).then_inc(ev("suma"), 1)
                    dve.wait_ge(ev("sqb"), n)
                    dve.tensor_reduce(st[0:T, 4:12], v8(sqb[0:T, :]), AX_X, ALU.add).then_inc(ev("sumb"), 1)
                    dve.wait_ge(ev("suma"), n)
                    dve.tensor_scalar(st[0:T, 0:4], st[0:T, 0:4], 1.0 / P, EPS, ALU.mult, ALU.add).then_inc(ev("st1"), 1)
                    dve.wait_ge(ev("sumb"), n)
                    dve.tensor_scalar(st[0:T, 4:12], st[0:T, 4:12], 1.0 / 64, B_GN_EPS, ALU.mult, ALU.add).then_inc(ev("stats"), 1)

                def end_gate(f, T):
                    n = f + 1
                    dve.wait_ge(ev("rstd"), n)
                    dve.wait_ge(ev("raw"), n)
                    oa = OR[0:T, 0:AKEY].rearrange("p (h c) -> p h c", h=AH)
                    dve.tensor_tensor(oa, oa, wide(rstd[0:T, 0:4], T, P), ALU.mult).then_inc(ev("oa1"), 1)
                    ob = v8(OR[0:T, AKEY:D])
                    dve.tensor_tensor(ob, ob, wide(rstd[0:T, 4:12], T, 64), ALU.mult).then_inc(ev("ob1"), 1)
                    dve.wait_ge(ev("oa1"), n)
                    dve.wait_ge(ev("zw"), n)
                    dve.tensor_tensor(OR[0:T, 0:AKEY], OR[0:T, 0:AKEY], Z[0:T, :], ALU.mult).then_inc(ev("oa"), 1)
                    o = OR[0:T, AKEY:D]
                    dve.wait_ge(ev("ob1"), n)
                    dve.wait_ge(ev("gw"), n)
                    dve.tensor_tensor(o, o, gw[0:T, :], ALU.mult).then_inc(ev("ob2"), 1)
                    dve.wait_ge(ev("ob2"), n)
                    dve.wait_ge(ev("bv"), n)
                    dve.tensor_tensor(o, o, bv[0:T, :], ALU.add).then_inc(ev("ob"), 1)

                def end_rows(f, T):
                    dve.wait_ge(ev("ot_mm"), f + 1)
                    dve.wait_ge(ev("prj"), 2 * f)
                    dve.wait_ge(ev("xn_out"), 16 * f)
                    dve.tensor_copy(OT[:, 4:8, 0:T], v4(7, P, T)).then_inc(ev("ot2"), 1)

                def end_add(f, T):
                    for c in range(2):
                        dve.wait_ge(ev("prj"), 2 * f + c + 1)
                        if c == 0:
                            dve.wait_ge(ev("ld_x"), 16 * (f + 1))
                        ins = dve.tensor_tensor(x1[0:T, 512 * c:512 * c + 512], bank[6 + c][0:T, :], XR[0:T, 512 * c:512 * c + 512], ALU.add)
                    ins.then_inc(ev("x1"), 1)

                def end_norm(f, T):
                    dve.wait_ge(ev("n1s"), f + 1)
                    dve.tensor_scalar(n1[0:T, 1:2], n1[0:T, 0:1], 1.0 / D, EPS, ALU.mult, ALU.add).then_inc(ev("n1"), 1)
                    dve.wait_ge(ev("n1r"), f + 1)
                    dve.wait_ge(ev("nt_mm"), f)
                    dve.scalar_tensor_tensor(out=xn[0:T, :], in0=x1[0:T, :], scalar=n1[0:T, 2:3], in1=nw[0:T, :],
                                             op0=ALU.mult, op1=ALU.mult).then_inc(ev("xn1"), 1)

                def end_keep(f, T):
                    dve.wait_ge(ev("nt_mm"), f + 1)
                    dve.tensor_copy(OT[:, 0:4, 0:T], v4(6, P, T)).then_inc(ev("xk_a"), 1)

                def center(i, T):
                    n = i + 1
                    dve.wait_ge(ev("out_b"), n)
                    dve.tensor_reduce(mean[0:T, :], v8(bank[3][0:T, :]), AX_X, ALU.add).then_inc(ev("mean"), 1)
                    dve.wait_ge(ev("mean"), n)
                    dve.wait_ge(ev("ot_mm"), i)
                    dve.scalar_tensor_tensor(out=v8(OR[0:T, AKEY:D]), in0=wide(mean[0:T, :], T, 64), scalar=-1.0 / 64,
                                             in1=v8(bank[3][0:T, :]), op0=ALU.mult, op1=ALU.add).then_inc(ev("cent"), 1)

                def tile(i, T, levels, mask, lmask, last):
                    n = i + 1
                    dve.wait_ge(ev("gB"), n)
                    dve.wait_ge(ev("g"), n)
                    dve.wait_ge(ev("attn"), i)
                    for h in range(AH):
                        ins = dve.scalar_tensor_tensor(out=dec[0:T, h, 0:T], in0=v4(0, T, T)[:, h, :], scalar=g[0:T, h:h + 1],
                                                       in1=lmask[0:T, 0:T], op0=ALU.subtract, op1=ALU.min)
                    ins.then_inc(ev("dm"), 1)
                    if T == P:
                        dve.wait_ge(ev("out_b"), i)
                        dve.wait_ge(ev("rhs_b"), i)
                        dve.wait_ge(ev("state_b"), i)
                        dve.tensor_tensor(Th[:, :, :], Tt[:, :, :], bc(K.rw_in[:, :, bass.ds(i, 1)], [P, NP, P]),
                                          ALU.mult).then_inc(ev("th"), 1)
                    dve.wait_ge(ev("dec"), n)
                    dve.wait_ge(ev("kkqk"), n)
                    dve.wait_ge(ev("bt"), 2 * n)
                    dve.wait_ge(ev("m0"), LEVELS * i)
                    dve.wait_ge(ev("out_a"), i)
                    for h in range(AH):
                        b = v4(2 + h // 2, T, T)
                        ins = dve.scalar_tensor_tensor(out=NT[0:T, h, 0:T], in0=b[:, 2 * (h % 2) + 1, :], scalar=bt[0:T, h:h + 1],
                                                       in1=dec[0:T, h, 0:T], op0=ALU.mult, op1=ALU.mult)
                    ins.then_inc(ev("nt_a"), 1)
                    for h in range(0, AH, 2):
                        b = v4(2 + h // 2, T, T)
                        ins = dve.tensor_tensor(attn[0:T, h:h + 2, 0:T], b[:, 0::2, :], dec[0:T, h:h + 2, 0:T], ALU.mult)
                    ins.then_inc(ev("attn"), 1)
                    dve.wait_ge(ev("egb"), n)
                    dve.tensor_tensor(QG[:, :, 0:T], QK[:, 0, :, 0:T], eGB[:, :, 0:T], ALU.mult).then_inc(ev("qg"), 1)
                    if T == P:
                        dve.wait_ge(ev("nvd"), i)
                        dve.tensor_copy(dend[:, :], dec[:, :, P - 1]).then_inc(ev("dend"), 1)
                    else:
                        dve.wait_ge(ev("upd_a"), i)
                        dve.tensor_tensor(NVd[0:T, :, 0:T], dec[0:T, :, 0:T], bc(K.last[:, :].rearrange("s (a t) -> s a t", a=1),
                                                                                [T, AH, T]), ALU.mult).then_inc(ev("dend_m"), 1)
                        dve.wait_ge(ev("dend_m"), 1)
                        dve.tensor_reduce(dend[0:T, :], NVd[0:T, :, 0:T], AX_X, ALU.add).then_inc(ev("dend"), 1)
                    dve.wait_ge(ev("rows_a"), n)
                    dve.wait_ge(ev("wr"), i)
                    dve.tensor_copy(vr[0:T, :, :], v4(5, T)).then_inc(ev("vr_a"), 1)
                    dve.wait_ge(ev("rows_b"), n)
                    dve.wait_ge(ev("upd_b"), i)
                    dve.tensor_copy(Kr[0:T, :], bank[7][0:T, :]).then_inc(ev("krr"), 1)
                    for h in range(BH):
                        dve.wait_ge(ev("score"), 8 * i + h + 1)
                        if h == 0:
                            dve.wait_ge(ev("m1"), LEVELS * i)
                            dve.wait_ge(ev("m2"), LEVELS * i)
                            dve.wait_ge(ev("out_b"), i)
                        dve.tensor_tensor(SC[0:T, h, :, 0:T], v4(2 + h % 6, T, T), mask[0:T, :, 0:T],
                                          ALU.mult).then_inc(ev("sc"), 1)
                    dve.wait_ge(ev("rows_vg"), n)
                    dve.wait_ge(ev("gw"), i)
                    dve.wait_ge(ev("bv"), i)
                    dve.tensor_scalar(Gr[0:T, :], bank[1][0:T, :], 0.5, None, ALU.mult).then_inc(ev("gr"), 1)
                    for u in range(3):
                        dve.wait_ge(ev(f"m{u}"), LEVELS * i + 1)
                        dve.wait_ge(ev("w_mm" if u == 0 else "sa_mm"), i)
                        dve.tensor_tensor(XT[u][0:T, :, 0:T], bc(K.ident[0:T, 0:T].rearrange("p (a c) -> p a c", a=1), [T, 4, T]),
                                          M[u][0:T, :, 0:T], ALU.subtract).then_inc(ev(f"xt1_{u}"), 1)
                    if T != P:
                        end_sums(last, P)
                        spread(0, range(AH + 2))
                        for r in range(4):
                            dve.wait_ge(ev("tb_mm"), r + 1)
                            dve.tensor_copy(Tb[:, 2 * r:2 * r + 2, :, :], bank[2 + r][:, :].rearrange("p (b j v) -> p b j v", b=2, j=NP)
                                            ).then_inc(ev("tb"), 1)
                        spread(0, range(AH + 2, AH + BH))
                        end_gate(last, P)
                    dve.wait_ge(ev("rhs_a"), n)
                    dve.wait_ge(ev("eg"), n)
                    dve.wait_ge(ev("w_mm"), i)
                    dve.wait_ge(ev("vr_a"), n)
                    if T != P:
                        dve.wait_ge(ev("tr_out"), 32)
                    for h in range(AH):
                        ins = dve.scalar_tensor_tensor(out=Wr[0:T, h, :], in0=v4(6, T)[:, h, :], scalar=eg[0:T, h:h + 1],
                                                       in1=vr[0:T, h, :], op0=ALU.mult, op1=ALU.subtract)
                    ins.then_inc(ev("wr"), 1)
                    dve.wait_ge(ev("rhs_b"), n)
                    dve.wait_ge(ev("sa_mm"), i)
                    dve.tensor_copy(RH[0:T, :], bank[7][0:T, :]).then_inc(ev("rh"), 1)
                    for l in range(1, levels):
                        for u in range(3):
                            dve.wait_ge(ev(f"zmm{u}"), (LEVELS - 1) * i + l)
                            if l < LEVELS - 1:
                                if l == 1:
                                    dve.wait_ge(ev(f"xk{u}"), n)
                                dve.wait_ge(ev(f"xd{u}"), (LEVELS - 1) * i + l - 1)
                                x = half(X[u][0:T, :, :], l, T, 0)
                                dve.tensor_tensor(x, x, packed(2 * u + 1, l, T, T), ALU.subtract).then_inc(ev(f"xd{u}"), 1)
                            else:
                                dve.wait_ge(ev(f"xt{u}"), (LEVELS - 2) * n)
                                xt = half(XT[u][0:P // 2, :, :], l, T, 1)
                                dve.tensor_tensor(xt, xt, packed(2 * u, l, T, P // 2), ALU.subtract).then_inc(ev(f"xd{u}"), 1)
                        if last is not None:
                            if l == 1 and levels == LEVELS:
                                end_sums(last, P)
                            if l == 2 and levels == LEVELS:
                                end_gate(last, P)
                            if l == MIDDLE[levels]:
                                end_rows(last, P)
                            if l == (5 if levels == LEVELS else levels - 1):
                                end_add(last, P)
                    dve.wait_ge(ev("w_mm"), n)
                    dve.wait_ge(ev("out_a"), i)
                    dve.tensor_tensor(NV[0:T, :, :], v4(0, T), bc(nbt[0:T, :].rearrange("p (h a) -> p h a", a=1), [T, AH, P]),
                                      ALU.mult).then_inc(ev("nv"), 1)
                    dve.wait_ge(ev("nv"), n)
                    dve.wait_ge(ev("dend"), n)
                    dve.wait_ge(ev("upd_a"), i)
                    dve.tensor_tensor(NVd[0:T, :, :], NV[0:T, :, :], bc(dend[0:T, :].rearrange("p (h a) -> p h a", a=1),
                                                                        [T, AH, P]), ALU.mult).then_inc(ev("nvd"), 1)
                    if last is not None:
                        end_norm(last, P)
                    if T != P:
                        spread(1, range(AH + BH))
                    center(i, T)

                def whole_tile(i, last):
                    n = i + 1
                    tile(i, P, LEVELS, mask4, K.lcausal, last)
                    dve.wait_ge(ev("upd_a"), n)
                    for h in range(AH):
                        ins = dve.scalar_tensor_tensor(out=St[:, h, :], in0=St[:, h, :], scalar=eGB[:, h, P - 1:P],
                                                       in1=v4(4)[:, h, :], op0=ALU.mult, op1=ALU.add)
                    ins.then_inc(ev("state_a"), 1)
                    dve.wait_ge(ev("upd_b"), n)
                    for h in range(2):
                        r = slice(64 * h, 64 * h + 64)
                        ins = dve.tensor_tensor(Tt[r, :, r], Th[r, :, r], v4(5)[r, :, r], ALU.add)
                    ins.then_inc(ev("tt1"), 1)
                    dve.wait_ge(ev("tt1"), n)
                    dve.tensor_tensor(Tt[:, :, :], Tt[:, :, :], bc(K.rw_out[:, :, bass.ds(i, 1)], [P, NP, P]),
                                      ALU.mult).then_inc(ev("state_b"), 1)
                    if last is not None:
                        end_keep(last, P)

                for i in range(2):
                    whole_tile(i, i - 1 if i else None)
                with dve.Fori(2, TILES) as i:
                    whole_tile(i, i - 1)
                dve.wait_ge(ev("tr_mm"), 1)
                dve.tensor_copy(tr[:, :, :], v4(4)).then_inc(ev("tr"), 1)
                dve.wait_ge(ev("ld_sb"), 16)
                tile(TILES, SR, LEVELS_S, mask4s, K.lcausal_s, TILES - 1)
                end_keep(TILES - 1, P)
                end_sums(TILES, SR)
                end_gate(TILES, SR)

                def batch(b):
                    dve.wait_ge(ev("upd_s"), b + 1)
                    for h in range(AH):
                        ins = dve.scalar_tensor_tensor(out=Sb[:, b, h, :], in0=Sb[:, b, h, :], scalar=eGB[:, h, b * DS + DS - 1:(b + 1) * DS],
                                                       in1=v4(UPD_A[b % 2])[:, h, :], op0=ALU.mult, op1=ALU.add)
                    ins.then_inc(ev("sb_new"), 1)
                    for h in range(2):
                        r = slice(64 * h, 64 * h + 64)
                        ins = dve.tensor_tensor(Tb[r, b, :, :], Tb[r, b, :, :], v4(UPD_B[b % 2])[r, :, r], ALU.add)
                    ins.then_inc(ev("tb1"), 1)
                    dve.wait_ge(ev("tb1"), b + 1)
                    dve.tensor_tensor(Tb[:, b, :, :], Tb[:, b, :, :], bc(K.rw_out[:, :, TILES + b:TILES + b + 1], [P, NP, 64]),
                                      ALU.mult).then_inc(ev("tb_new"), 1)

                with_batches(batch, {2: lambda: end_rows(TILES, SR), 4: lambda: end_add(TILES, SR),
                                     5: lambda: end_norm(TILES, SR), 7: lambda: end_keep(TILES, SR)})

            @block.tensor
            def _(pe):
                def end_rows(f, T, used):
                    pe.wait_ge(ev("oa"), f + 1)
                    pe.wait_ge(ev("ob"), f + 1)
                    pe.wait_ge(ev("wr"), used)
                    pe.wait_ge(ev("rh"), used)
                    for c in range(KT):
                        mm = pe.transpose(v4(6 + c // 4, P, T)[:, c % 4, :], OR[0:T, c * P:(c + 1) * P], K.ident[0:T, 0:T])
                    mm.then_inc(ev("ot_mm"), 1)

                def end_project(f, T, c):
                    if c == 0:
                        if isinstance(f, int) and f == 0:
                            pe.wait_ge(ev("ld_wo"), 16)
                        pe.wait_ge(ev("ot"), f + 1)
                        pe.wait_ge(ev("ot2"), f + 1)
                    for kt in range(KT):
                        mm = pe.matmul(bank[6 + c][0:T, :], OT[:, kt, 0:T], wo[:, kt, 512 * c:512 * c + 512],
                                       start=(kt == 0), stop=(kt == KT - 1))
                    mm.then_inc(ev("prj"), 1)

                def end_norm(f, T):
                    pe.wait_ge(ev("xn1"), f + 1)
                    for c in range(KT):
                        mm = pe.transpose(v4(6 + c // 4, P, T)[:, c % 4, :], xn[0:T, c * P:(c + 1) * P], K.ident[0:T, 0:T])
                    mm.then_inc(ev("nt_mm"), 1)

                def tile(i, T, levels, ks, kd, last):
                    n = i + 1
                    pe.wait_ge(ev("ldc"), n)
                    pe.wait_ge(ev("nv"), i)
                    pe.wait_ge(ev("sqa"), i)
                    pe.wait_ge(ev("raw"), i)
                    pe.wait_ge(ev("cent"), i)
                    caus = K.causal if T == P else K.causal_s
                    for h in range(AH):
                        mm = pe.matmul(v4(0, P, T)[:, h, :], ld[0:T, h:h + 1].broadcast_to([T, P]), caus[0:T, 0:T], start=True, stop=True)
                    mm.then_inc(ev("gB"), 1)
                    pe.matmul(bank[1][0:T, 0:AH], caus[0:T, 0:T], ld[0:T, :], start=True, stop=True).then_inc(ev("gcol_mm"), 1)
                    pe.wait_ge(ev("ld_qk"), 32 * n)
                    for h in range(AH):
                        o = v4(2 + h // 2, T, T)[:, 2 * (h % 2):2 * (h % 2) + 2, :]
                        mm = pe.matmul(o, QK[:, 1, h, 0:T], QK[:, :, h, 0:T], start=True, stop=True)
                    mm.then_inc(ev("kkqk"), 1)
                    pe.wait_ge(ev("state_a"), i)
                    pe.wait_ge(ev("state_b"), i)
                    pe.wait_ge(ev("ld_v"), 16 * n)
                    for h in range(AH):
                        pe.transpose(v4(4, T)[:, h, :], QK[:, 1, h, 0:T], K.ident[:, :])
                        mm = pe.transpose(v4(5, T)[:, h, :], V[:, h, 0:T], K.ident[:, :])
                    mm.then_inc(ev("rows_a"), 1)
                    kept = 0 if isinstance(i, int) and i == 0 else i - 1
                    pe.wait_ge(ev("xk_a"), kept)
                    pe.wait_ge(ev("xk_b"), kept)
                    pe.wait_ge(ev("ld_rw"), 48 * n)
                    pe.wait_ge(ev("ld_r"), 16 * n)
                    for j in range(NP):
                        pe.transpose(v4(6, T)[:, j, :], RW[:, 2, j, 0:T], K.ident[:, :])
                        mm = pe.transpose(v4(7, T)[:, j, :], RW[:, 3, j, 0:T], K.ident[:, :])
                    mm.then_inc(ev("rows_b"), 1)
                    for h in range(BH):
                        if h == 0:
                            pe.wait_ge(ev("attn"), n)
                        if h == 2:
                            pe.wait_ge(ev("kr"), n)
                        if h == 3:
                            pe.wait_ge(ev("vr_a"), n)
                        if h == 4:
                            pe.wait_ge(ev("br"), n)
                        if h == 5:
                            pe.wait_ge(ev("krr"), n)
                        if h >= 6:
                            pe.wait_ge(ev("sc"), 8 * i + h - 5)
                        r = slice(64 * (h % 2), 64 * (h % 2) + 64)
                        o = v4(2 + h % 6, T, T)
                        pe.matmul(o[:, 0:2, :], RW[r, 2, h // 2, 0:T], RW[r, 0:2, h // 2, 0:T], start=True, stop=True)
                        pe.matmul(o[:, 2:4, :], RW[r, 3, h // 2, 0:T], RW[r, 0:2, h // 2, 0:T], start=True, stop=True
                                  ).then_inc(ev("score"), 1)
                    pe.wait_ge(ev("egb"), n)
                    pe.wait_ge(ev("eg"), n)
                    pe.wait_ge(ev("ld_vg"), 32 * n)
                    for j in range(NP):
                        pe.transpose(v4(0, T)[:, j, :], VG[:, 0, j, 0:T], K.ident[:, :])
                        mm = pe.transpose(v4(1, T)[:, j, :], VG[:, 1, j, 0:T], K.ident[:, :])
                    mm.then_inc(ev("rows_vg"), 1)
                    pe.wait_ge(ev("sc"), 8 * i + 5)
                    ks(6)
                    pe.wait_ge(ev("vr_b"), n)
                    if T == P:
                        pe.wait_ge(ev("th"), n)
                    pe.wait_ge(ev("sc"), 8 * n)
                    kd(7)
                    pe.wait_ge(ev("gr"), n)
                    for u in range(3):
                        pe.wait_ge(ev(f"xt1_{u}"), n)
                        for k in range(4):
                            mm = pe.transpose(v4(2 * u, T, T)[:, k, :], XT[u][0:T, k, 0:T], K.ident[0:T, 0:T])
                        mm.then_inc(ev(f"x1mm{u}"), 1)
                    for l in range(1, levels):
                        for u in range(3):
                            if l == 1:
                                pe.wait_ge(ev(f"xk{u}"), n)
                            else:
                                pe.wait_ge(ev(f"xd{u}"), (LEVELS - 1) * i + l - 1)
                            pe.wait_ge(ev(f"m{u}"), LEVELS * i + l + 1)
                            for k in range(4):
                                mm = pe.matmul(packed(2 * u, l, T, T)[:, k], M[u][0:T, k, 0:T], half(X[u][0:T, k, :], l, T, 0), start=True, stop=True)
                            mm.then_inc(ev(f"ymm{u}"), 1)
                            if l > 1:
                                for k in range(4):
                                    mm = pe.transpose(v4(2 * u + 1, T, T)[:, k, :], X[u][0:T, k, 0:T], K.ident[0:T, 0:T])
                                mm.then_inc(ev(f"xt_mm{u}"), 1)
                        for u in range(3):
                            pe.wait_ge(ev(f"y{u}"), (LEVELS - 1) * i + l)
                            if l > 1:
                                pe.wait_ge(ev(f"xt{u}"), (LEVELS - 2) * i + l - 1)
                            for k in range(4):
                                if l < LEVELS - 1:
                                    mm = pe.matmul(packed(2 * u + 1, l, T, T)[:, k], XT[u][0:T, k, 0:T], Y[u][0:T, k, 0:T // 2], start=True, stop=True)
                                else:
                                    mm = pe.matmul(packed(2 * u, l, T, P // 2)[:, k], Y[u][0:T, k, 0:P // 2], half(XT[u][0:T, k, :], l, T, 1), start=True, stop=True)
                            mm.then_inc(ev(f"zmm{u}"), 1)
                        if last is not None and l == MIDDLE[levels]:
                            end_rows(last, P, n)
                        if last is not None and l in (4, 5):
                            end_project(last, P, l - 4)
                    if levels < LEVELS:
                        for u in range(3):
                            pe.wait_ge(ev(f"xd{u}"), (LEVELS - 1) * i + levels - 1)
                            for k in range(4):
                                mm = pe.transpose(v4(2 * u + 1, T, T)[:, k, :], X[u][0:T, k, 0:T], K.ident[0:T, 0:T])
                            mm.then_inc(ev(f"xt_mm{u}"), 1)
                            pe.wait_ge(ev(f"xt{u}"), (LEVELS - 2) * i + levels - 1)
                        end_project(last, P, 0)
                        end_project(last, P, 1)
                    pe.wait_ge(ev("xd0"), (LEVELS - 1) * i + levels - 1)
                    pe.wait_ge(ev("wr"), n)
                    for h in range(AH):
                        mm = pe.matmul(v4(0, T)[:, h, :], XT[0][0:T, h, 0:T], Wr[0:T, h, :], start=True, stop=True)
                    mm.then_inc(ev("w_mm"), 1)
                    pe.wait_ge(ev("xd1"), (LEVELS - 1) * i + levels - 1)
                    pe.wait_ge(ev("xd2"), (LEVELS - 1) * i + levels - 1)
                    pe.wait_ge(ev("rh"), n)
                    for h in range(BH):
                        mm = pe.matmul(bank[2][0:T, 64 * h:64 * h + 64], XT[1 + h // 4][0:T, h % 4, 0:T],
                                       RH[0:T, 64 * h:64 * h + 64], start=True, stop=True)
                    mm.then_inc(ev("sa_mm"), 1)

                pe.wait_ge(ev("init"), 2)

                def whole_tile(i, last):
                    n = i + 1

                    def ks(b):
                        for h in range(AH):
                            mm = pe.matmul(v4(b)[:, h, :], QK[:, 1, h, :], St[:, h, :], start=True, stop=True)
                        mm.then_inc(ev("rhs_a"), 1)

                    def kd(b):
                        for j in range(NP):
                            pe.matmul(v4(b)[:, j, :], RW[:, 1, j, :], Th[:, j, :], start=(j == 0), stop=False, skip_group_check=True)
                            for h in (2 * j, 2 * j + 1):
                                mm = pe.matmul(bank[b][:, 64 * h:64 * h + 64], SC[:, h, 3, :], Vr[:, 64 * h:64 * h + 64],
                                               start=False, stop=(h == BH - 1), skip_group_check=True)
                        mm.then_inc(ev("rhs_b"), 1)
                    tile(i, P, LEVELS, ks, kd, last)
                    pe.wait_ge(ev("nv"), n)
                    pe.wait_ge(ev("qg"), n)
                    for h in range(AH):
                        pe.matmul(v4(1)[:, h, :], QG[:, h, :], St[:, h, :], start=True, stop=False)
                        mm = pe.matmul(v4(1)[:, h, :], attn[:, h, :], NV[:, h, :], start=False, stop=True)
                    mm.then_inc(ev("out_a"), 1)
                    pe.wait_ge(ev("sa"), n)
                    for j in range(NP):
                        pe.matmul(v4(3)[:, j, :], RW[:, 0, j, :], Th[:, j, :], start=(j == 0), stop=False, skip_group_check=True)
                        for h in (2 * j, 2 * j + 1):
                            o = bank[3][:, 64 * h:64 * h + 64]
                            pe.matmul(o, SC[:, h, 0, :], SA[:, 64 * h:64 * h + 64], start=False, stop=False, skip_group_check=True)
                            mm = pe.matmul(o, SC[:, h, 2, :], Vr[:, 64 * h:64 * h + 64], start=False, stop=(h == BH - 1), skip_group_check=True)
                    mm.then_inc(ev("out_b"), 1)
                    pe.wait_ge(ev("nvd"), n)
                    pe.wait_ge(ev("kr"), n)
                    for h in range(AH):
                        mm = pe.matmul(v4(4)[:, h, :], kr[:, h, :], NVd[:, h, :], start=True, stop=True)
                    mm.then_inc(ev("upd_a"), 1)
                    for j in range(NP):
                        c = slice(j * P, (j + 1) * P)
                        pe.matmul(v4(5)[:, j, :], Br[:, c], SA[:, c], start=True, stop=False)
                        mm = pe.matmul(v4(5)[:, j, :], Kr[:, c], Vr[:, c], start=False, stop=True)
                    mm.then_inc(ev("upd_b"), 1)
                    if last is not None:
                        end_norm(last, P)
                for i in range(2):
                    whole_tile(i, i - 1 if i else None)
                with pe.Fori(2, TILES) as i:
                    whole_tile(i, i - 1)
                pe.wait_ge(ev("state_b"), TILES)
                for j in range(NP):
                    mm = pe.transpose(v4(4)[:, j, :], Tt[:, j, :], K.ident[:, :])
                mm.then_inc(ev("tr_mm"), 1)
                pe.wait_ge(ev("tr"), 1)

                def over_batches(k, o, states, start):
                    pe.wait_ge(ev("q1"), k + 1)
                    for b in range(DB):
                        mm = pe.matmul(o, Q1[k % 2][:, b, :], states[:, b, :], start=start and b == 0, stop=(b == DB - 1))
                    mm.then_inc(ev("q1_used"), 1)

                def ks_s(bk):
                    for h in range(AH):
                        over_batches(h, v4(bk, SR)[:, h, :], Sb[:, :, h, :], True)
                    pe.wait_ge(ev("q1_used"), AH)
                    pe.sem_inc(ev("rhs_a"), 1)

                def kd_s(bk):
                    pe.wait_ge(ev("sc"), 8 * (TILES + 1))
                    pe.wait_ge(ev("ld_rb"), 16 * DB)
                    for r in range(4):
                        for b in range(2):
                            for j in range(NP):
                                o = bank[2 + r][:, b * 256 + j * 64:b * 256 + j * 64 + 64]
                                mm = pe.transpose(o, Rin[2 * r + b][:, j, :], K.ident[0:64, 0:64])
                        mm.then_inc(ev("tb_mm"), 1)
                    pe.wait_ge(ev("tb"), 4)
                    for h in range(BH):
                        c = slice(64 * h, 64 * h + 64)
                        pe.matmul(bank[bk][0:SR, c], SC[0:SR, h, 3, 0:SR], Vr[0:SR, c], start=True, stop=False)
                        over_batches(AH + h, bank[bk][0:SR, c], Tb[:, :, h // 2, :], False)
                    pe.wait_ge(ev("q1_used"), AH + BH)
                    pe.sem_inc(ev("rhs_b"), 1)
                tile(TILES, SR, LEVELS_S, ks_s, kd_s, TILES - 1)
                pe.wait_ge(ev("nv"), TILES + 1)
                for h in range(AH):
                    pe.matmul(v4(1, SR)[:, h, :], attn[0:SR, h, 0:SR], NV[0:SR, h, :], start=True, stop=False)
                    over_batches(AH + BH + h, v4(1, SR)[:, h, :], Sb[:, :, h, :], False)
                pe.wait_ge(ev("q1_used"), 2 * AH + BH)
                pe.sem_inc(ev("out_a"), 1)
                pe.wait_ge(ev("sa"), TILES + 1)
                for h in range(BH):
                    c = slice(64 * h, 64 * h + 64)
                    pe.matmul(bank[3][0:SR, c], SC[0:SR, h, 0, 0:SR], SA[0:SR, c], start=True, stop=False)
                    pe.matmul(bank[3][0:SR, c], SC[0:SR, h, 2, 0:SR], Vr[0:SR, c], start=False, stop=False)
                    over_batches(2 * AH + BH + h, bank[3][0:SR, c], Tb[:, :, h // 2, :], False)
                pe.wait_ge(ev("q1_used"), 2 * AH + 2 * BH)
                pe.sem_inc(ev("out_b"), 1)
                end_norm(TILES - 1, P)

                def turn_state(b):
                    pe.wait_ge(ev("tb_new"), b + 1)
                    if b < 2:
                        pe.wait_ge(ev(("cent", "nv")[b]), TILES + 1)
                    else:
                        pe.wait_ge(ev("rb_new"), b - 1)
                    for j in range(NP):
                        mm = pe.transpose(bank[TURN[b % 2]][0:64, j * P:(j + 1) * P], Tb[:, b, j, :], K.ident[:, :])
                    mm.then_inc(ev("rb_mm"), 1)

                def batch(b):
                    pe.wait_ge(ev("pick"), 3 * (b + 1))
                    if b == 1:
                        pe.wait_ge(ev("sqa"), TILES + 1)
                        pe.wait_ge(ev("raw"), TILES + 1)
                    if b >= 2:
                        pe.wait_ge(ev("tb_new"), b - 1)
                    nv, sa, v = PICK[b % 2]
                    for h in range(AH):
                        pe.matmul(v4(UPD_A[b % 2])[:, h, :], kr[0:SR, h, :], nv[0:SR, h, :], start=True, stop=True)
                    for j in range(NP):
                        c = slice(j * P, (j + 1) * P)
                        o = v4(UPD_B[b % 2])[:, j, :]
                        pe.matmul(o, Br[0:SR, c], sa[0:SR, c], start=True, stop=False)
                        mm = pe.matmul(o, Kr[0:SR, c], v[0:SR, c], start=False, stop=True)
                    mm.then_inc(ev("upd_s"), 1)
                    if b >= 1:
                        turn_state(b - 1)

                def rows():
                    pe.wait_ge(ev("xk_a"), TILES)
                    pe.wait_ge(ev("xk_b"), TILES)
                    end_rows(TILES, SR, TILES + 1)

                def project():
                    end_project(TILES, SR, 0)
                    end_project(TILES, SR, 1)
                with_batches(batch, {2: rows, 3: project, 6: lambda: end_norm(TILES, SR)})
                turn_state(DB - 1)


QKC, VC = CH * CQK, CH * CV
IG = 2 * QKC + 3 * VC
VA1 = CV + 1
BLK = 256
GF = 32


def phase_mlstm_in(nc, K, w_in, b_i, b_f, m0, S, p_m, s_m):
    with ExitStack() as ctx:
        sb = lambda n, s: ctx.enter_context(nc.sbuf_tensor("e_" + n, s, F32))
        parts = lambda n, s: [ctx.enter_context(nc.sbuf_tensor(f"e_{n}{h}", s, F32R)) for h in "hl"]
        ev = Events(nc, ctx, "e_")
        X = parts("x", [P, KT, XW])
        xs = sb("xs", [P, 2, TOK])
        W = [sb(f"w{b}", [P, KT, BLK]) for b in range(2)]
        WP = [parts(f"wp{b}", [P, KT, BLK]) for b in range(2)]
        wg = sb("wg", [P, KT, GF + CH])
        wgp = parts("wgp", [P, KT, GF + CH])
        QB = [sb(f"qb{t}", [P, TOK]) for t in range(2)]
        VB = sb("vb", [P, TILES + 1, BLK])
        GO = sb("go", [P, TILES + 1, BLK])
        T2 = sb("t2", [P, 2, 2, BLK])
        bias = sb("bias", [CH, 2])
        li, lf, bc_, m = [sb(n, [CH, TOK]) for n in ("li", "lf", "b", "m")]
        pad = sb("pad", [CH, 2, DB, DS + 1])
        ms = sb("ms", [CH, DB, DS + 1])
        m0t = sb("m0t", [CH, DB])
        mp = sb("mp", [CH, TILES])
        bank = [ctx.enter_context(nc.psum_tensor(f"e_bank{i}", [P, 512], F32)) for i in range(8)]
        NB = TILES + 1
        PAIRS = ((0, 2, P), (2, 2, P), (4, 2, P), (6, 2, P), (8, 1, SR))
        PLACES = ((0, 1, 2, 3, 4), (5, 6, 7, 2, 3))
        QK_BLOCKS, ROUNDS = 4, CH * CV // BLK // 2
        BEFORE = (5, 5, 5, 4, 4, 4, 1, 1)
        PER = (3, 3, 6, 6, 3, 3, 3, 3)

        def cols(b, r, n):
            return bank[b][0:r, 0:8 * NB].rearrange("p (n h) -> p n h", h=CH)[:, n, :]

        def two(b, c):
            return bank[b][0:c[2], 0:c[1] * BLK].rearrange("p (n c) -> p n c", c=BLK)

        def column(k):
            if k < QK_BLOCKS:
                return k * BLK
            k -= QK_BLOCKS
            return 2 * QKC + (k % 3) * VC + (k // 3) * BLK
        BLOCKS = QK_BLOCKS + 6 * ROUNDS

        def done_at(k, i):
            return 6 * k + i + 1 if k < QK_BLOCKS else 6 * QK_BLOCKS + 5 * (k - QK_BLOCKS) + i + 1

        def last_of(k):
            return done_at(k, 5 if k < QK_BLOCKS else 4)

        def free_at(k, i):
            if k < QK_BLOCKS:
                return i, k + 1 + (1 if i < 3 else 0)
            g, p = divmod(k - QK_BLOCKS, 6)
            b = PLACES[k % 2][i]
            return b, BEFORE[b] + PER[b] * g + (p if b in (2, 3) else p // 2) + 1

        def read(eng, k, i):
            b, n = free_at(k, i)
            eng.wait_ge(ev(f"free{b}"), n)

        with nc.Block() as block:
            @block.sync
            def _(sp):
                def load(k):
                    sp.wait_ge(ev(f"low{k % 2}"), k // 2)
                    sp.dma_start(W[k % 2][:, :, :], w_block(w_in, column(k), BLK)).then_inc(ev(f"ld_w{k % 2}"), 16)
                sp.wait_ge(ev("pad"), 3)
                sp.dma_start(wg[:, :, 0:CH], w_block(w_in, IG, CH)).then_inc(ev("ld_g"), 16)
                sp.dma_start(wg[:, :, GF:GF + CH], w_block(w_in, IG + CH, CH)).then_inc(ev("ld_g"), 16)
                sp.dma_start(bias[:, 0:1], b_i.rearrange("(h a) -> h a", a=1)).then_inc(ev("ld_b"), 16)
                sp.dma_start(bias[:, 1:2], b_f.rearrange("(h a) -> h a", a=1)).then_inc(ev("ld_b"), 16)
                sp.dma_start(m0t[:, :], m0.rearrange("b h -> h b"), allow_slow_non_contiguous=True).then_inc(ev("ld_b"), 16)
                for kt in range(KT):
                    if kt >= 2:
                        sp.wait_ge(ev("x_low"), kt - 1)
                    sp.dma_start(xs[:, kt % 2, :], S.xnT[:, kt, :]).then_inc(ev(f"ld_x{kt % 2}"), 16)
                    if kt == KT - 3:
                        load(0)
                load(1)
                for k in range(QK_BLOCKS):
                    load(k + 2)
                    for t in range(2):
                        read(sp, k, 3 * t + 2)
                        r = (k % 2) * BLK + t * P
                        sp.dma_start(S.ql[k // 2, r:r + P, :], QB[t][:, :]).then_inc(ev(f"out_q{t}"), 16)

                def store(c, dram, t, done):
                    sp.dma_start(dram[0:SEQ, c * BLK:c * BLK + BLK].rearrange("(n p) c -> p n c", p=P), t[:, 0:TILES, :]).then_inc(done, 16)
                    sp.dma_start(dram[SEQ:TOK, c * BLK:c * BLK + BLK], t[0:SR, TILES, :]).then_inc(done, 16)
                for c in range(2 * ROUNDS):
                    for q in range(3):
                        k = QK_BLOCKS + 3 * c + q + 2
                        if k < BLOCKS:
                            load(k)
                        if q == 0:
                            read(sp, QK_BLOCKS + 3 * c, 4)
                            store(c, S.v, VB, ev("out_v"))
                    sp.wait_ge(ev("gated"), 5 * (c + 1))
                    store(c, S.g, GO, ev("out_g"))
                sp.wait_ge(ev("m_end"), 1)
                sp.dma_start(p_m.rearrange("b h -> h b"), m[:, SEQ - 1:SEQ], allow_slow_non_contiguous=True).then_inc(ev("out_m"), 16)
                sp.dma_start(s_m.rearrange("b h -> h b"), ms[:, :, DS], allow_slow_non_contiguous=True).then_inc(ev("out_m"), 16)
                for n, k in (("out_q0", QK_BLOCKS), ("out_q1", QK_BLOCKS), ("out_v", 4 * ROUNDS), ("out_g", 4 * ROUNDS), ("out_m", 2)):
                    sp.wait_ge(ev(n), 16 * k)

            @block.gpsimd
            def _(pool):
                pool.memset(wg[:, :, :], 0.0).then_inc(ev("pad"), 1)
                for x in X:
                    pool.memset(x[:, :, TOK:XW].bitcast(F32), 0.0).then_inc(ev("pad"), 1)
                done = Seq(ev("pseq"), pool, 4)
                done.start(0)
                done(pool.memset(K.sel[:, :, :], 1.0))
                done(pool.affine_select(out=K.sel[:, :, :], in_=K.sel[:, :, :], compare_op=ALU.is_equal, fill=0.0, base=0,
                                        pattern=[[-1, CH], [0, P]], channel_multiplier=1))
                done(pool.memset(K.sel2[:, :, :], 1.0))
                done(pool.affine_select(out=K.sel2[:, :, :].rearrange("g j (u c) -> g (j u) c", u=2),
                                        in_=K.sel2[:, :, :].rearrange("g j (u c) -> g (j u) c", u=2),
                                        compare_op=ALU.is_equal, fill=0.0, base=0,
                                        pattern=[[-1, CH], [0, 64]], channel_multiplier=1))
                done.end()
                pool.wait_ge(ev("g_high"), 1)
                pool.tensor_tensor(wgp[1][:, :, :], wg[:, :, :], wgp[0][:, :, :].bitcast(F32), ALU.subtract).then_inc(ev("g_low"), 1)
                for k in range(BLOCKS):
                    b = k % 2
                    pool.wait_ge(ev(f"high{b}"), k // 2 + 1)
                    pool.tensor_tensor(WP[b][1][:, :, :], W[b][:, :, :], WP[b][0][:, :, :].bitcast(F32), ALU.subtract
                                       ).then_inc(ev(f"low{b}"), 1)

            @block.scalar
            def _(act):
                def high(k):
                    if k < BLOCKS:
                        b = k % 2
                        act.wait_ge(ev(f"ld_w{b}"), 16 * (k // 2 + 1))
                        act.wait_ge(ev(f"low{b}"), k // 2)
                        if k >= 2:
                            act.wait_ge(ev("bank_full"), last_of(k - 2))
                        act.activation(WP[b][0][:, :, :], W[b][:, :, :], ACT.Copy).then_inc(ev(f"high{b}"), 1)
                act.wait_ge(ev("ld_g"), 32)
                act.activation(wgp[0][:, :, :], wg[:, :, :], ACT.Copy).then_inc(ev("g_high"), 1)
                for kt in range(KT):
                    act.wait_ge(ev(f"ld_x{kt % 2}"), 16 * (kt // 2 + 1))
                    act.activation(X[0][:, kt, 0:TOK], xs[:, kt % 2, :], ACT.Copy).then_inc(ev("x_high"), 1)
                high(0)
                act.wait_ge(ev("bias"), 1)
                for g, (c, n) in enumerate(THIRDS):
                    act.wait_ge(ev("gate_mm"), g + 1)
                    act.activation(li[:, c:c + n], bank[g][0:CH, 0:n], ACT.Tanh, scale=1.0 / CAP, bias=bias[:, 0:1])
                    act.activation(lf[:, c:c + n], bank[g][GF:GF + CH, 0:n], ACT.Tanh, scale=1.0 / CAP,
                                   bias=bias[:, 1:2]).then_inc(ev(f"free{g}"), 1)
                act.wait_ge(ev("free2"), 1)
                act.activation(lf[:, :], lf[:, :], ACT.Exp, scale=-CAP).then_inc(ev("gate_e"), 1)
                act.wait_ge(ev("gate_e"), 1)
                act.activation(lf[:, :], lf[:, :], ACT.Ln, bias=1.0).then_inc(ev("gate_e"), 1)
                for k in range(QK_BLOCKS):
                    high(k + 1)
                    for t in range(2):
                        act.wait_ge(ev(f"out_q{t}"), 16 * k)
                        for g, (c, n) in enumerate(THIRDS):
                            i = 3 * t + g
                            act.wait_ge(ev("bank_full"), done_at(k, i))
                            act.activation(QB[t][:, c:c + n], bank[i][:, 0:n], ACT.Copy,
                                           scale=CQK ** -0.5 if k < 2 else 1.0).then_inc(ev(f"free{i}"), 1)
                    if k == 1:
                        act.wait_ge(ev("e_log"), 2)
                        act.activation(K.e[:, :], K.e[:, :], ACT.Exp).then_inc(ev("e_kept"), 1)
                act.wait_ge(ev("turned"), 1)
                for r, n in ((P, slice(0, TILES)), (SR, slice(TILES, NB))):
                    ins = act.activation(K.em[0:r, n, :], cols(6, r, n), ACT.Exp, scale=-1.0)
                ins.then_inc(ev("free6"), 1)
                for c in range(2 * ROUNDS):
                    for q in range(3):
                        k = QK_BLOCKS + 3 * c + q
                        high(k + 1)
                        for i, at in enumerate(PAIRS):
                            b = PLACES[k % 2][i]
                            r, n = at[2], slice(at[0], at[0] + at[1])
                            act.wait_ge(ev("bank_full"), done_at(k, i))
                            if q == 0:
                                if i == 0:
                                    act.wait_ge(ev("out_v"), 32 * c)
                                act.activation(VB[0:r, n, :], two(b, at), ACT.Copy).then_inc(ev(f"free{b}"), 1)
                            elif q == 1:
                                if i == 0:
                                    act.wait_ge(ev("out_g"), 32 * c)
                                act.activation(GO[0:r, n, :], two(b, at), ACT.Tanh, scale=0.5).then_inc(ev(f"free{b}"), 1)
                            else:
                                z = 5 * c + i
                                if z >= 2:
                                    act.wait_ge(ev("gated"), z - 1)
                                act.activation(T2[0:r, z % 2, 0:at[1], :], two(b, at), ACT.Tanh, scale=0.5).then_inc(ev("tz"), 1)

            @block.vector
            def _(dve):
                dve.wait_ge(ev("ld_b"), 48)
                dve.tensor_scalar(bias[:, :], bias[:, :], 1.0 / CAP, None, ALU.mult).then_inc(ev("bias"), 1)
                for kt in range(KT):
                    dve.wait_ge(ev("x_high"), kt + 1)
                    dve.tensor_tensor(X[1][:, kt, 0:TOK], xs[:, kt % 2, :], X[0][:, kt, 0:TOK].bitcast(F32), ALU.subtract).then_inc(ev("x_low"), 1)
                done = Seq(ev("dseq"), dve, 14)
                done.start(0)
                dve.wait_ge(ev("gate_e"), 2)
                done(dve.tensor_scalar(li[:, :], li[:, :], CAP, None, ALU.mult))
                done(dve.tensor_scalar(lf[:, :], lf[:, :], -1.0, None, ALU.mult))
                done(dve.tensor_tensor_scan(bc_[:, :], K.restart[0:CH, :], lf[:, :], 0.0, ALU.mult, ALU.add))
                done(dve.tensor_tensor_scan(m[:, 0:SEQ], lf[:, 0:SEQ], li[:, 0:SEQ], 0.0, ALU.add, ALU.max))
                done(dve.memset(pad[:, 0, :, 0], -1e30))
                done(dve.tensor_copy(pad[:, 1, :, 0], m0t[:, :]))
                done(dve.tensor_copy(pad[:, 0, :, 1:DS + 1], lf[:, SEQ:TOK].rearrange("h (b t) -> h b t", b=DB)))
                done(dve.tensor_copy(pad[:, 1, :, 1:DS + 1], li[:, SEQ:TOK].rearrange("h (b t) -> h b t", b=DB)))
                done(dve.tensor_tensor_scan(ms[:, :, :].rearrange("h b t -> h (b t)"), pad[:, 0, :, :].rearrange("h b t -> h (b t)"),
                                            pad[:, 1, :, :].rearrange("h b t -> h (b t)"), 0.0, ALU.add, ALU.max))
                done(dve.tensor_copy(m[:, SEQ:TOK].rearrange("h (b t) -> h b t", b=DB), ms[:, :, 1:DS + 1]))
                dve.sem_inc(ev("m_end"), 1)
                done(dve.tensor_tensor(K.u[:, :], bc_[:, :], m[:, :], ALU.subtract))
                done(dve.tensor_tensor(li[:, :], li[:, :], bc_[:, :], ALU.subtract))
                done(dve.memset(mp[:, 0:1], 0.0))
                done(dve.tensor_copy(mp[:, 1:TILES], m[:, P - 1:SEQ - P:P]))
                done.end()
                dve.sem_inc(ev("w"), 1)
                dve.tensor_tensor(K.e[:, 0:SEQ].rearrange("h (n t) -> h n t", n=TILES), K.u[:, 0:SEQ].rearrange("h (n t) -> h n t", n=TILES),
                                  mp[:, :].rearrange("h (n a) -> h n a", a=1).broadcast_to([CH, TILES, P]), ALU.add).then_inc(ev("e_log"), 1)
                dve.tensor_tensor(K.e[:, SEQ:TOK].rearrange("h (b t) -> h b t", b=DB), K.u[:, SEQ:TOK].rearrange("h (b t) -> h b t", b=DB),
                                  m0t[:, :].rearrange("h (b a) -> h b a", a=1).broadcast_to([CH, DB, DS]), ALU.add).then_inc(ev("e_log"), 1)
                dve.wait_ge(ev("turned"), 2)
                for r, n in ((P, slice(0, TILES)), (SR, slice(TILES, NB))):
                    ins = dve.tensor_copy(K.w[0:r, n, :], cols(7, r, n))
                ins.then_inc(ev("free7"), 1)
                for c in range(2 * ROUNDS):
                    k = QK_BLOCKS + 3 * c + 2
                    for i, at in enumerate(PAIRS):
                        b, z = PLACES[k % 2][i], 5 * c + i
                        r, n = at[2], slice(at[0], at[0] + at[1])
                        t2 = T2[0:r, z % 2, 0:at[1], :]
                        dve.wait_ge(ev("tz"), z + 1)
                        dve.scalar_tensor_tensor(out=t2, in0=t2, scalar=1.0, in1=two(b, at), op0=ALU.add, op1=ALU.mult).then_inc(ev(f"free{b}"), 1)
                        read(dve, k, i)
                        read(dve, k - 1, i)
                        dve.scalar_tensor_tensor(out=GO[0:r, n, :], in0=GO[0:r, n, :], scalar=1.0, in1=t2,
                                                 op0=ALU.add, op1=ALU.mult).then_inc(ev("gated"), 1)

            @block.tensor
            def _(pe):
                pe.wait_ge(ev("g_high"), 1)
                pe.wait_ge(ev("g_low"), 1)
                for kt in range(KT):
                    pe.wait_ge(ev("x_low"), kt + 1)
                    for g, (c, n) in enumerate(THIRDS):
                        mm = products(pe, bank[g][0:GF + CH, 0:n], (wgp[0][:, kt, :], wgp[1][:, kt, :]),
                                      (X[0][:, kt, c:c + n], X[1][:, kt, c:c + n]), kt == 0, kt == KT - 1)
                        if kt == KT - 1:
                            mm.then_inc(ev("gate_mm"), 1)
                pe.wait_ge(ev("pad"), 3)
                for k in range(QK_BLOCKS):
                    b = k % 2
                    pe.wait_ge(ev(f"high{b}"), k // 2 + 1)
                    pe.wait_ge(ev(f"low{b}"), k // 2 + 1)
                    for t in range(2):
                        for g, (c, n) in enumerate(THIRDS):
                            i = 3 * t + g
                            pe.wait_ge(ev(f"free{i}"), k + (1 if i < 3 else 0))
                            for kt in range(KT):
                                w = [x[:, kt, t * P:(t + 1) * P] for x in WP[b]]
                                mm = products(pe, bank[i][:, 0:n], w, [x[:, kt, c:c + n] for x in X], kt == 0, kt == KT - 1)
                            mm.then_inc(ev("bank_full"), 1)
                pe.wait_ge(ev("w"), 1)
                for src, b in ((m, 6), (li, 7)):
                    for n in range(NB):
                        r = P if n < TILES else SR
                        mm = pe.transpose(bank[b][0:r, 8 * n:8 * n + 8], src[:, n * P:n * P + r], K.ident[0:CH, 0:CH])
                    mm.then_inc(ev("turned"), 1)
                with pe.Fori(0, ROUNDS) as g:
                    for p in range(6):
                        b = p % 2
                        n = QK_BLOCKS // 2 + p // 2 + 1
                        pe.wait_ge(ev(f"high{b}"), 3 * g + n)
                        pe.wait_ge(ev(f"low{b}"), 3 * g + n)
                        for i, at in enumerate(PAIRS):
                            o = PLACES[b][i]
                            used = p // 2 if o not in (2, 3) else p
                            pe.wait_ge(ev(f"free{o}"), PER[o] * g + BEFORE[o] + used)
                            for t in range(at[1]):
                                tok = slice((at[0] + t) * P, (at[0] + t + 1) * P)
                                for kt in range(KT):
                                    mm = products(pe, bank[o][:, t * BLK:(t + 1) * BLK], [x[:, kt, tok] for x in X],
                                                  [w[:, kt, :] for w in WP[b]], kt == 0, kt == KT - 1)
                            mm.then_inc(ev("bank_full"), 1)


def phase_mix1(nc, K, w_out, norm_w, c0, n0, S, y_p, y_s, p_c, p_n, s_c, s_n):
    with ExitStack() as ctx:
        sb = lambda n, s: ctx.enter_context(nc.sbuf_tensor("f_" + n, s, F32))
        ev = Events(nc, ctx, "f_")
        QL = sb("ql", [P, 2, NP, P])
        VA = sb("va", [P, CH, VA1])
        GR = sb("gr", [P, D])
        XR = sb("xr", [P, D])
        parts = lambda n, s: [ctx.enter_context(nc.sbuf_tensor(f"f_{n}{h}", s, F32R)) for h in "hl"]
        wo = parts("wo", [P, KT, D])
        ws = sb("ws", [P, 4, D])
        nw = sb("nw", [P, D])
        ut, et = sb("ut", [CH, P]), sb("et", [CH, P])
        wt, emt = sb("wt", [P, CH]), sb("emt", [P, CH])
        Dm = sb("dm", [P, CH, P])
        PM = sb("pm", [P, CH, P])
        qe = sb("qe", [P, NP, P])
        ec = sb("ec", [P, NP, DB])
        wk = sb("wk", [P, CH])
        KW = sb("kw", [P, QKC])
        den = sb("den", [P, 2, CH])
        H = sb("h", [P, D])
        OT = parts("ot", [P, KT, P])
        C = sb("c", [P, NP, VA1])
        n1 = sb("n1", [P, 4])
        yo = sb("yo", [P, D])
        Cb = sb("cb", [P, DB, NP, VA1])
        Q1 = [ws[:, n, 0:DB * SR].rearrange("p (b t) -> p b t", b=DB) for n in range(2)]
        KM = [ws[:, n, 0:QKC] for n in range(2, 4)]
        bank = [ctx.enter_context(nc.psum_tensor(f"f_bank{i}", [P, 512], F32)) for i in range(8)]
        ORDER = (0, 2, 4, 6, 1, 3, 5, 7)
        place = {h: (6 + h % 2, VA1 * (h // 2)) if h < 6 else (3 + h % 2, 0) for h in range(CH)}

        def v4(b, r=P, c=P):
            return bank[b][0:r, :].rearrange("p (h c) -> p h c", h=4)[:, :, 0:c]

        def split(b, r):
            if b >= 6:
                t = bank[b][0:r, 0:3 * VA1].rearrange("p (h c) -> p h c", h=3)
                return slice(b % 2, 6, 2), t[:, :, 0:CV], t[:, :, CV]
            t = bank[b][0:r, 0:VA1].rearrange("p (h c) -> p h c", h=1)
            return slice(3 + b, 4 + b), t[:, :, 0:CV], t[:, :, CV]

        UPDATE = ((2, 5), (3, 4))

        def update_at(j, b3, b1, r=slice(0, P)):
            return bank[b3][r, VA1 * j:VA1 * (j + 1)] if j < 3 else bank[b1][r, 0:VA1]

        with nc.Block() as block:
            @block.sync
            def _(sp):
                def load_qk(c, T):
                    for m in range(2):
                        sp.dma_start(QL[:, m, :, 0:T], S.ql[m].rearrange("(j p) t -> p j t", p=P)[:, :, bass.ds(c, T)]).then_inc(ev("ld_q"), 16)

                def load_v(c, T):
                    sp.dma_start(VA[0:T, :, 0:CV], S.v[bass.ds(c, T), :].rearrange("t (h v) -> t h v", h=CH)).then_inc(ev("ld_v"), 16)

                def load_g(c, T):
                    sp.dma_start(GR[0:T, :], S.g[bass.ds(c, T), :]).then_inc(ev("ld_gr"), 16)

                def load_x(c, T):
                    sp.dma_start(XR[0:T, :], S.x1[bass.ds(c, T), :]).then_inc(ev("ld_x"), 16)

                def load_wo(kts):
                    for kt in kts:
                        if kt >= 4:
                            sp.wait_ge(ev(f"wo_low{kt % 2}"), kt // 2 - 1)
                        sp.dma_start(ws[:, kt % 4, :], w_out[kt * P:(kt + 1) * P, :]).then_inc(ev(f"ld_wo{kt % 4}"), 16)

                def during(i, ahead):
                    n, c = i + 1, i * P
                    sp.wait_ge(ev("qk"), n)
                    sp.wait_ge(ev("rows"), n)
                    sp.wait_ge(ev("qe"), n)
                    alone(sp, K)
                    load_qk(c + P, ahead)
                    if isinstance(i, int) and i == 0:
                        load_wo(range(4, KT))
                    else:
                        sp.wait_ge(ev("y"), i)
                        alone(sp, K)
                        sp.dma_start(y_p[0, bass.ds(c - P, P), :], yo[:, :]).then_inc(ev("stored"), 16)
                        alone(sp, K)
                        load_x(c, P)
                    sp.wait_ge(ev("num"), n)
                    sp.wait_ge(ev("upd"), n)
                    alone(sp, K)
                    load_v(c + P, ahead)
                    sp.wait_ge(ev("gate"), n)
                    alone(sp, K)
                    load_g(c + P, ahead)
                load_qk(0, P)
                load_v(0, P)
                load_g(0, P)
                load_x(0, P)
                sp.dma_start(nw[:, :], as_row(norm_w)).then_inc(ev("ld_nw"), 16)
                load_wo(range(4))
                during(0, P)
                for h in range(2):
                    r = slice(64 * h, 64 * h + 64)
                    for b in range(DB):
                        sp.dma_start(Cb[r, b, :, 0:CV], c0[b].rearrange("(j h) k v -> h k j v", h=2)[h]).then_inc(ev("ld_c"), 16)
                        sp.dma_start(Cb[r, b, :, CV], n0[b].rearrange("(j h) k -> h k j", h=2)[h], allow_slow_non_contiguous=True).then_inc(ev("ld_c"), 16)
                during(1, P)
                with sp.Fori(2, TILES - 1) as i:
                    during(i, P)
                during(TILES - 1, SR)
                sp.wait_ge(ev("y"), TILES)
                sp.dma_start(y_p[0, SEQ - P:SEQ, :], yo[:, :]).then_inc(ev("stored"), 16)
                load_x(SEQ, SR)
                sp.wait_ge(ev("state"), TILES)
                for h in range(2):
                    r = slice(64 * h, 64 * h + 64)
                    sp.dma_start(p_c[0].rearrange("(j h) k v -> h k j v", h=2)[h], C[r, :, 0:CV], allow_slow_non_contiguous=True).then_inc(ev("c_out"), 16)
                    sp.dma_start(p_n[0].rearrange("(j h) k -> h k j", h=2)[h], C[r, :, CV], allow_slow_non_contiguous=True).then_inc(ev("c_out"), 16)
                for b in range(DB):
                    if b == DB - 2:
                        sp.wait_ge(ev("y"), TILES + 1)
                        sp.dma_start(y_s.rearrange("b t d -> (b t) d"), yo[0:SR, :]).then_inc(ev("stored"), 16)
                    sp.wait_ge(ev("cb"), b + 1)
                    for h in range(2):
                        r = slice(64 * h, 64 * h + 64)
                        sp.dma_start(s_c[b].rearrange("(j h) k v -> h k j v", h=2)[h], Cb[r, b, :, 0:CV], allow_slow_non_contiguous=True).then_inc(ev("cb_out"), 16)
                        sp.dma_start(s_n[b].rearrange("(j h) k -> h k j", h=2)[h], Cb[r, b, :, CV], allow_slow_non_contiguous=True).then_inc(ev("cb_out"), 16)
                sp.wait_ge(ev("stored"), 16 * (TILES + 1))
                sp.wait_ge(ev("c_out"), 64)
                sp.wait_ge(ev("cb_out"), 64 * DB)

            @block.gpsimd
            def _(pool):
                pool.memset(VA[:, :, CV:VA1], 1.0).then_inc(ev("va1"), 1)
                pool.memset(C[:, :, :], 0.0).then_inc(ev("init"), 1)

                for kt in range(0, KT, 2):
                    pool.wait_ge(ev("wo_high"), kt + 1)
                    pool.tensor_tensor(wo[1][:, kt, :], ws[:, kt % 4, :], wo[0][:, kt, :].bitcast(F32), ALU.subtract).then_inc(ev("wo_low0"), 1)

                def norm(f, T):
                    pool.wait_ge(ev("n1"), f + 1)
                    pool.tensor_tensor(n1[0:T, 2:3], n1[0:T, 1:2], K.half_neg[0:T, 0:1], ALU.pow).then_inc(ev("n1r"), 1)
                with pool.Fori(0, TILES) as f:
                    norm(f, P)
                norm(TILES, SR)

            @block.scalar
            def _(act):
                def end_rows(f, T):
                    act.wait_ge(ev("prj"), 2 * f)
                    for b in range(2):
                        act.wait_ge(ev("ot_mm"), 2 * f + b + 1)
                        act.activation(OT[0][:, 4 * b:4 * b + 4, 0:T], v4(b, P, T), ACT.Copy).then_inc(ev("ot_high"), 1)

                def end_square(f, T):
                    act.wait_ge(ev("x2"), f + 1)
                    act.wait_ge(ev("stored"), 16 * f)
                    act.activation(yo[0:T, :], XR[0:T, :], ACT.Square, accum_out=n1[0:T, 0:1]).then_inc(ev("n1s"), 1)

                def tile(i, c, T, last):
                    n = i + 1
                    act.wait_ge(ev("ub"), i)
                    act.activation(ut[:, 0:T], K.u[:, bass.ds(c, T)], ACT.Copy).then_inc(ev("ut"), 1)
                    act.wait_ge(ev("eb"), i)
                    act.activation(et[:, 0:T], K.e[:, bass.ds(c, T)], ACT.Copy).then_inc(ev("et"), 1)
                    act.wait_ge(ev("dmin"), i)
                    act.activation(wt[0:T, :], K.w[0:T, bass.ds(i, 1), :].rearrange("p a h -> p (a h)"), ACT.Copy).then_inc(ev("wt"), 1)
                    act.wait_ge(ev("rden"), i)
                    act.activation(emt[0:T, :], K.em[0:T, bass.ds(i, 1), :].rearrange("p a h -> p (a h)"), ACT.Copy).then_inc(ev("emt"), 1)
                    act.wait_ge(ev("dmin"), n)
                    act.activation(Dm[0:T, :, 0:T], Dm[0:T, :, 0:T], ACT.Exp).then_inc(ev("dexp"), 1)
                    if last is not None:
                        end_rows(last, P)
                        end_square(last, P)
                    elif T == P:
                        for kt in range(KT):
                            act.wait_ge(ev(f"ld_wo{kt % 4}"), 16 * (kt // 4 + 1))
                            act.activation(wo[0][:, kt, :], ws[:, kt % 4, :], ACT.Copy).then_inc(ev("wo_high"), 1)
                    act.wait_ge(ev("num"), n)
                    for b in (6, 7, 3, 4):
                        hs, _, dn = split(b, T)
                        ins = act.activation(den[0:T, 0, hs], dn, ACT.Abs)
                    ins.then_inc(ev("den"), 1)
                tile(0, 0, P, None)
                tile(1, P, P, 0)
                with act.Fori(2, TILES) as i:
                    tile(i, i * P, P, i - 1)
                end_rows(TILES - 1, P)
                end_square(TILES - 1, P)
                tile(TILES, SEQ, SR, None)

                def batch(b):
                    if b >= 2:
                        act.wait_ge(ev("upd_s"), b - 1)
                    act.activation(KM[b % 2][0:SR, :], KW[0:SR, :], ACT.Copy, scale=K.same[:, b * DS:b * DS + 1]).then_inc(ev("pick"), 1)
                with_batches(batch, {2: lambda: end_rows(TILES, SR), 5: lambda: end_square(TILES, SR)})

            @block.vector
            def _(dve):
                bc = lambda t, s: t.broadcast_to(s)

                def end_rows(f, T):
                    for b in range(2):
                        dve.wait_ge(ev("ot_high"), 2 * f + b + 1)
                        dve.tensor_tensor(OT[1][:, 4 * b:4 * b + 4, 0:T], v4(b, P, T), OT[0][:, 4 * b:4 * b + 4, 0:T].bitcast(F32),
                                          ALU.subtract).then_inc(ev("ot_low"), 1)

                def end_add(f, T):
                    dve.wait_ge(ev("ld_x"), 16 * (f + 1))
                    for c in range(2):
                        dve.wait_ge(ev("prj"), 2 * f + c + 1)
                        ins = dve.tensor_tensor(XR[0:T, 512 * c:512 * c + 512], bank[6 + c][0:T, :], XR[0:T, 512 * c:512 * c + 512], ALU.add)
                        ins.then_inc(ev(f"x2_{c}" if c == 0 else "x2"), 1)

                def end_norm(f, T):
                    dve.wait_ge(ev("n1s"), f + 1)
                    dve.tensor_scalar(n1[0:T, 1:2], n1[0:T, 0:1], 1.0 / D, EPS, ALU.mult, ALU.add).then_inc(ev("n1"), 1)
                    dve.wait_ge(ev("n1r"), f + 1)
                    dve.scalar_tensor_tensor(out=yo[0:T, :], in0=XR[0:T, :], scalar=n1[0:T, 2:3], in1=nw[0:T, :],
                                             op0=ALU.mult, op1=ALU.mult).then_inc(ev("y"), 1)

                def tile(i, T, lmask, last):
                    n = i + 1
                    dve.wait_ge(ev("ub"), n)
                    dve.wait_ge(ev("wt"), n)
                    dve.wait_ge(ev("kw"), i)
                    dve.wait_ge(ev("pm"), 2 * i)
                    for h in range(CH):
                        ins = dve.scalar_tensor_tensor(out=Dm[0:T, h, 0:T], in0=v4(h // 4, T, T)[:, h % 4, :], scalar=wt[0:T, h:h + 1],
                                                       in1=lmask[0:T, 0:T], op0=ALU.add, op1=ALU.min)
                    ins.then_inc(ev("dmin"), 1)
                    dve.wait_ge(ev("eb"), n)
                    dve.wait_ge(ev("ld_q"), 32 * n)
                    dve.wait_ge(ev("num"), i)
                    dve.wait_ge(ev("state"), i)
                    dve.tensor_tensor(qe[:, :, 0:T], QL[:, 0, :, 0:T], v4(2, P, T), ALU.mult).then_inc(ev("qe"), 1)
                    if T == P:
                        dve.tensor_copy(ec[:, :, 0], v4(2)[:, :, P - 1]).then_inc(ev("ec"), 1)
                    else:
                        dve.tensor_copy(ec[:, :, :], v4(2, P, T)[:, :, DS - 1:SR:DS]).then_inc(ev("ec"), 1)
                    dve.wait_ge(ev("dexp"), n)
                    dve.wait_ge(ev("qk"), n)
                    for k in range(2):
                        dve.tensor_tensor(PM[0:T, k::2, 0:T], Dm[0:T, k::2, 0:T], v4(3 + k, T, T), ALU.mult).then_inc(ev("pm"), 1)
                    dve.wait_ge(ev("rows"), n)
                    dve.wait_ge(ev("upd"), i)
                    if T == P:
                        w = Dm[:, :, P - 1]
                    else:
                        dve.wait_ge(ev("pm"), 2 * n)
                        dve.tensor_tensor(Dm[0:T, :, 0:T], Dm[0:T, :, 0:T], bc(K.last[:, :].rearrange("s (a t) -> s a t", a=1),
                                                                            [T, CH, T]), ALU.mult).then_inc(ev("wk"), 1)
                        dve.wait_ge(ev("wk"), 1)
                        dve.tensor_reduce(wk[0:T, :], Dm[0:T, :, 0:T], AX_X, ALU.add).then_inc(ev("wk"), 1)
                        dve.wait_ge(ev("wk"), 2)
                        w = wk[0:T, :]
                    dve.tensor_tensor(KW[0:T, :].rearrange("p (h k) -> p h k", h=CH), bank[5][0:T, :].rearrange("p (h k) -> p h k", h=CH),
                                      bc(w.rearrange("p (h a) -> p h a", a=1), [T, CH, 64]), ALU.mult).then_inc(ev("kw"), 1)
                    if T != P:
                        for k, h in enumerate(ORDER):
                            if k >= 2:
                                dve.wait_ge(ev("q1_used"), k - 1)
                            dve.wait_ge(ev("qe"), n)
                            dve.scalar_tensor_tensor(out=Q1[k % 2][:, :, :], in0=bc(qe[:, h // 2, 0:T].rearrange("p (a t) -> p a t", a=1), [P, DB, SR]),
                                                     scalar=K.head_cols[:, h % 2:h % 2 + 1], in1=K.batch_cols[:, :, :],
                                                     op0=ALU.mult, op1=ALU.mult).then_inc(ev("q1"), 1)
                    if last is not None:
                        end_rows(last, P)
                        end_add(last, P)
                        end_norm(last, P)
                    elif T == P:
                        for kt in range(1, KT, 2):
                            dve.wait_ge(ev("wo_high"), kt + 1)
                            dve.tensor_tensor(wo[1][:, kt, :], ws[:, kt % 4, :], wo[0][:, kt, :].bitcast(F32), ALU.subtract).then_inc(ev("wo_low1"), 1)
                    dve.wait_ge(ev("den"), n)
                    dve.wait_ge(ev("emt"), n)
                    dve.tensor_tensor(den[0:T, 0, :], den[0:T, 0, :], emt[0:T, :], ALU.max).then_inc(ev("den2"), 1)
                    dve.wait_ge(ev("den2"), n)
                    dve.tensor_scalar(den[0:T, 0, :], den[0:T, 0, :], 4.0, None, ALU.mult).then_inc(ev("den3"), 1)
                    dve.wait_ge(ev("den3"), n)
                    dve.reciprocal(den[0:T, 1, :], den[0:T, 0, :]).then_inc(ev("rden"), 1)
                    dve.wait_ge(ev("rden"), n)
                    dve.wait_ge(ev("ot_mm"), 2 * i)
                    h3 = H[0:T, :].rearrange("p (h c) -> p h c", h=CH)
                    for b in (6, 7, 3, 4):
                        hs, nm, _ = split(b, T)
                        w = nm.shape[1]
                        ins = dve.tensor_tensor(h3[:, hs, :], nm, bc(den[0:T, 1, hs].rearrange("p (h a) -> p h a", a=1), [T, w, CV]), ALU.mult)
                    ins.then_inc(ev("hr"), 1)
                    dve.wait_ge(ev("hr"), n)
                    dve.wait_ge(ev("ld_gr"), 16 * n)
                    dve.tensor_tensor(H[0:T, :], H[0:T, :], GR[0:T, :], ALU.mult).then_inc(ev("gate"), 1)
                    if T == P:
                        dve.wait_ge(ev("upd"), n)
                        dve.wait_ge(ev("ec"), n)
                        for j in range(NP):
                            src = update_at(j, *UPDATE[0])
                            ins = dve.scalar_tensor_tensor(out=C[:, j, :], in0=C[:, j, :], scalar=ec[:, j, 0:1], in1=src,
                                                           op0=ALU.mult, op1=ALU.add)
                        ins.then_inc(ev("state"), 1)
                dve.wait_ge(ev("ld_nw"), 16)
                for i in range(2):
                    tile(i, P, K.lcausal, i - 1 if i else None)
                with dve.Fori(2, TILES) as i:
                    tile(i, P, K.lcausal, i - 1)
                end_rows(TILES - 1, P)
                end_add(TILES - 1, P)
                end_norm(TILES - 1, P)
                tile(TILES, SR, K.lcausal_s, None)

                def batch(b):
                    dve.wait_ge(ev("upd_s"), b + 1)
                    for j in range(NP):
                        src = update_at(j, *UPDATE[b % 2])
                        ins = dve.scalar_tensor_tensor(out=Cb[:, b, j, :], in0=Cb[:, b, j, :], scalar=ec[:, j, b:b + 1], in1=src,
                                                       op0=ALU.mult, op1=ALU.add)
                    ins.then_inc(ev("cb"), 1)
                with_batches(batch, {2: lambda: end_rows(TILES, SR), 5: lambda: end_add(TILES, SR), 6: lambda: end_norm(TILES, SR)})

            @block.tensor
            def _(pe):
                def update(T, keys, banks, name):
                    for h in range(CH):
                        r = slice(64 * (h % 2), 64 * (h % 2) + 64)
                        mm = pe.matmul(update_at(h // 2, *banks, r), keys[0:T, 64 * h:64 * h + 64], VA[0:T, h, :], start=True, stop=True)
                    mm.then_inc(ev(name), 1)

                def end_rows(f, T, masked):
                    pe.wait_ge(ev("gate"), f + 1)
                    pe.wait_ge(ev("dmin"), masked)
                    pe.wait_ge(ev("ot_low"), 2 * f)
                    for c in range(KT):
                        mm = pe.transpose(v4(c // 4, P, T)[:, c % 4, :], H[0:T, c * P:(c + 1) * P], K.ident[0:T, 0:T])
                        if c % 4 == 3:
                            mm.then_inc(ev("ot_mm"), 1)

                def end_project(f, T):
                    if isinstance(f, int) and f == 0:
                        pe.wait_ge(ev("wo_high"), KT)
                        pe.wait_ge(ev("wo_low0"), KT // 2)
                        pe.wait_ge(ev("wo_low1"), KT // 2)
                    pe.wait_ge(ev("hr"), f + 1)
                    for c in range(2):
                        for kt in range(KT):
                            if c == 0 and kt % 4 == 0:
                                pe.wait_ge(ev("ot_low"), 2 * f + kt // 4 + 1)
                            mm = products(pe, bank[6 + c][0:T, :], [o[:, kt, 0:T] for o in OT],
                                          [w[:, kt, 512 * c:512 * c + 512] for w in wo], kt == 0, kt == KT - 1)
                        mm.then_inc(ev("prj"), 1)

                def tile(i, T, last):
                    n = i + 1
                    kept = i if T != P else i - 1 if not isinstance(i, int) or i > 0 else 0
                    pe.wait_ge(ev("ut"), n)
                    pe.wait_ge(ev("ot_low"), 2 * kept)
                    for h in range(CH):
                        mm = pe.matmul(v4(h // 4, T, T)[:, h % 4, :], K.sel[:, h, 0:T], ut[:, 0:T], start=True, stop=True)
                    mm.then_inc(ev("ub"), 1)
                    pe.wait_ge(ev("hr"), i)
                    pe.wait_ge(ev("ld_q"), 32 * n)
                    for h in range(CH):
                        r = slice(64 * (h % 2), 64 * (h % 2) + 64)
                        mm = pe.matmul(v4(3 + h % 2, T, T)[:, h // 2, :], QL[r, 1, h // 2, 0:T], QL[r, 0, h // 2, 0:T], start=True, stop=True)
                    mm.then_inc(ev("qk"), 1)
                    pe.wait_ge(ev("et"), n)
                    pe.wait_ge(ev("state"), i)
                    for j in range(NP):
                        mm = pe.matmul(v4(2, P, T)[:, j, :], K.sel2[:, j, :], et[:, 0:T], start=True, stop=True)
                    mm.then_inc(ev("eb"), 1)
                    for j in range(NP):
                        mm = pe.transpose(v4(5, T)[:, j, :], QL[:, 1, j, 0:T], K.ident[:, :])
                    mm.then_inc(ev("rows"), 1)
                    pe.wait_ge(ev("ld_v"), 16 * n)
                    pe.wait_ge(ev("qe"), n)
                    if last is not None:
                        end_rows(last, P, n)
                        end_project(last, P)
                    pe.wait_ge(ev("x2_0"), i)
                    pe.wait_ge(ev("pm"), 2 * n)
                    for k, h in enumerate(ORDER):
                        if h == 1:
                            pe.wait_ge(ev("x2"), i)
                        r = slice(64 * (h % 2), 64 * (h % 2) + 64)
                        b, c = place[h]
                        o = bank[b][0:T, c:c + VA1]
                        pe.matmul(o, PM[0:T, h, 0:T], VA[0:T, h, :], start=True, stop=False)
                        if T == P:
                            mm = pe.matmul(o, qe[r, h // 2, :], C[r, h // 2, :], start=False, stop=True)
                        else:
                            pe.wait_ge(ev("q1"), k + 1)
                            for b in range(DB):
                                mm = pe.matmul(o, Q1[k % 2][:, b, :], Cb[:, b, h // 2, :], start=False, stop=(b == DB - 1))
                            mm.then_inc(ev("q1_used"), 1)
                    if T == P:
                        mm.then_inc(ev("num"), 1)
                        pe.wait_ge(ev("kw"), n)
                        pe.wait_ge(ev("ec"), n)
                        update(T, KW, UPDATE[0], "upd")
                    else:
                        pe.wait_ge(ev("q1_used"), CH)
                        pe.sem_inc(ev("num"), 1)
                pe.wait_ge(ev("va1"), 1)
                pe.wait_ge(ev("init"), 1)
                tile(0, P, None)
                tile(1, P, 0)
                with pe.Fori(2, TILES) as i:
                    tile(i, P, i - 1)
                end_rows(TILES - 1, P, TILES)
                end_project(TILES - 1, P)
                pe.wait_ge(ev("ld_c"), 32 * DB * 2)
                tile(TILES, SR, None)

                def batch(b):
                    pe.wait_ge(ev("pick"), b + 1)
                    if b == 0:
                        pe.wait_ge(ev("kw"), TILES + 1)
                        pe.wait_ge(ev("ec"), TILES + 1)
                    elif b == 1:
                        pe.wait_ge(ev("hr"), TILES + 1)
                    else:
                        pe.wait_ge(ev("cb"), b - 1)
                    update(SR, KM[b % 2], UPDATE[b % 2], "upd_s")
                with_batches(batch, {2: lambda: end_rows(TILES, SR, TILES + 1), 4: lambda: end_project(TILES, SR)})


_INS = ("x_prompt", "x_sample", "state_gdn_conv", "state_gdn", "state_rwkv_shift", "state_rwkv",
        "state_mlstm_c", "state_mlstm_n", "state_mlstm_m",
        "norm0_w", "w_in0", "w_out0", "gdn_conv_w", "gdn_a_log", "gdn_dt_bias", "gdn_norm_w",
        "rwkv_mu", "rwkv_w0", "rwkv_w2", "rwkv_a0", "rwkv_a2", "rwkv_k_k", "rwkv_k_a", "rwkv_r_k",
        "rwkv_ln_w", "rwkv_ln_b", "norm1_w", "w_in1", "w_out1", "mlstm_b_i", "mlstm_b_f", "norm_f_w")
_OUTS = (("y_prompt", (1, SEQ, D)), ("y_sample", (DB, DS, D)),
         ("p_conv", (1, CONV - 1, AQKV)), ("p_gdn", (1, AH, P, P)), ("p_shift", (1, D)), ("p_rwkv", (1, BH, 64, 64)),
         ("p_c", (1, CH, CQK, CV)), ("p_n", (1, CH, CQK)), ("p_m", (1, CH)),
         ("s_conv", (DB, CONV - 1, AQKV)), ("s_gdn", (DB, AH, P, P)), ("s_shift", (DB, D)), ("s_rwkv", (DB, BH, 64, 64)),
         ("s_c", (DB, CH, CQK, CV)), ("s_n", (DB, CH, CQK)), ("s_m", (DB, CH)))


class Scope:
    pass


def build(nc, A, O):
    K, S = Scope(), Scope()
    dram = lambda name, shape: nc.dram_tensor("scratch_" + name, shape, F32, kind="Internal").ap()
    S.qkv, S.z, S.rw = dram("qkv", [3, AKEY, TOK]), dram("z", [TOK, AKEY]), dram("rw", [6, BW, TOK])
    S.x1, S.xnT = dram("x1", [TOK, D]), dram("xnT", [P, KT, TOK])
    S.ql, S.v, S.g = dram("ql", [2, CH * CQK, TOK]), dram("v", [TOK, D]), dram("g", [TOK, D])
    chip = lambda ctx, name, shape: ctx.enter_context(nc.sbuf_tensor("k_" + name, shape, F32))
    NB = TILES + 1

    with ExitStack() as kept:
        (K.ident, K.ones, K.half_neg, K.pair_ones, K.causal, K.strict, K.same, K.causal_s, K.strict_s, K.last, K.restart,
         K.batch_cols, K.head_cols, K.lcausal, K.lcausal_s) = [chip(kept, name, shape) for name, shape in CONSTS]
        K.idle = {n: kept.enter_context(nc.semaphore("idle_" + n)) for n in ("SP", "Pool", "PE", "DVE", "Activation")}
        with ExitStack() as layer:
            K.beta, K.logd, K.bonus = [chip(layer, n, [P, NB, h]) for n, h in (("beta", AH), ("logd", AH), ("bonus", BH))]
            K.rw_mid, K.rw_in, K.rw_out = [chip(layer, n, [P, NP, h]) for n, h in (("rw_mid", TILES), ("rw_in", TILES), ("rw_out", TILES + DB))]
            with ExitStack() as rows:
                K.xh, K.xl = [rows.enter_context(nc.sbuf_tensor(n, [P, KT, XW], F32R)) for n in ("k_xh", "k_xl")]
                phase_norm(nc, K, A["x_prompt"], A["x_sample"], A["state_rwkv_shift"], A["norm0_w"], O["p_shift"], O["s_shift"])
                phase_gdn_in(nc, K, A["w_in0"], A["gdn_conv_w"], A["state_gdn_conv"], A["gdn_a_log"], A["gdn_dt_bias"], S,
                             O["p_conv"], O["s_conv"])
                phase_rwkv_in(nc, K, A["w_in0"], A["rwkv_mu"], A["rwkv_w0"], A["rwkv_w2"], A["rwkv_a0"], A["rwkv_a2"],
                              A["rwkv_k_k"], A["rwkv_k_a"], A["rwkv_r_k"], S)
            phase_mix0(nc, K, A["w_out0"], A["norm1_w"], A["gdn_norm_w"], A["rwkv_ln_w"], A["rwkv_ln_b"],
                       A["x_prompt"], A["x_sample"], A["state_gdn"], A["state_rwkv"], S,
                       O["p_gdn"], O["p_rwkv"], O["s_gdn"], O["s_rwkv"])
        with ExitStack() as layer:
            K.sel, K.sel2 = chip(layer, "sel", [CH, CH, P]), chip(layer, "sel2", [CH, NP, P])
            K.w, K.em = chip(layer, "w", [P, NB, CH]), chip(layer, "em", [P, NB, CH])
            K.u, K.e = chip(layer, "u", [CH, TOK]), chip(layer, "e", [CH, TOK])
            phase_mlstm_in(nc, K, A["w_in1"], A["mlstm_b_i"], A["mlstm_b_f"], A["state_mlstm_m"], S, O["p_m"], O["s_m"])
            phase_mix1(nc, K, A["w_out1"], A["norm_f_w"], A["state_mlstm_c"], A["state_mlstm_n"], S,
                       O["y_prompt"], O["y_sample"], O["p_c"], O["p_n"], O["s_c"], O["s_n"])


def kernel(**inputs):
    import numpy as _np
    import concourse.bacc as _bacc
    from concourse import mybir as _mybir
    from concourse.bass_utils import run_bass_kernel_spmd as _run

    nc = _bacc.Bacc("TRN2", target_bir_lowering=False, num_devices=1)
    arrays, A, O = {}, {}, {}
    for name in _INS:
        arrays[f"in_{name}_dram"] = a = _np.ascontiguousarray(inputs[name])
        A[name] = nc.dram_tensor(f"in_{name}_dram", a.shape, _mybir.dt.from_np(a.dtype), kind="ExternalInput").ap()
    for name, shape in _OUTS:
        O[name] = nc.dram_tensor(f"out_{name}_dram", shape, _mybir.dt.float32, kind="ExternalOutput").ap()
    build(nc, A, O)
    r = _run(nc, [arrays], core_ids=[0])
    return tuple(r.results[0][f"out_{name}_dram"] for name, _ in _OUTS)
```
